# Optimizing a Trainium2 kernel written in Bass

```python
import jax, jax.numpy as jnp
from jax import lax
import numpy as np

D_MODEL = 1024
BATCH = 1
SEQ = 512
DEPTH = 2

N_SUB = 3
HALF_STEP = 0.5
D_FF = 2816
CONV_WIDTH = 4
EPS = 1e-6
LRU_WIDTH = D_MODEL
LRU_HEADS = 8
LRU_BLOCK = LRU_WIDTH // LRU_HEADS
LRU_C = 8.0
SSD_WIDTH = D_MODEL
SSD_HEADDIM = 64
SSD_HEADS = SSD_WIDTH // SSD_HEADDIM
SSD_GROUPS = 2
SSD_STATE = 128
SSD_CHUNK = 128
SSD_CONV_DIM = SSD_WIDTH + 2 * SSD_GROUPS * SSD_STATE
HYB_SPLITS = (LRU_WIDTH, 2 * LRU_WIDTH, 2 * LRU_WIDTH + SSD_WIDTH, 2 * LRU_WIDTH + SSD_WIDTH + SSD_CONV_DIM)
HYB_IN = HYB_SPLITS[-1] + SSD_HEADS
HYB_OUT = LRU_WIDTH + SSD_WIDTH
MLSTM_WIDTH = 2 * D_MODEL
MLSTM_HEADS = 4
MLSTM_HEADDIM = MLSTM_WIDTH // MLSTM_HEADS
MLSTM_QKV_BLOCK = 4
MLSTM_CHUNK = 64
N_EVEN = (DEPTH + 1) // 2
N_ODD = DEPTH // 2


def rms_norm(x, g):
    xf = x.astype(jnp.float32)
    y = xf * lax.rsqrt(jnp.mean(xf * xf, axis=-1, keepdims=True) + EPS)
    return (y * g.astype(jnp.float32)).astype(x.dtype)

def head_layer_norm(h, g):
    mu = jnp.mean(h, axis=-1, keepdims=True)
    hc = h - mu
    var = jnp.mean(hc * hc, axis=-1, keepdims=True)
    return hc * lax.rsqrt(var + EPS) * g.astype(jnp.float32)

def causal_conv(x, w, b):
    width, ch = w.shape
    y = lax.conv_general_dilated(x, w[:, None, :].astype(x.dtype), window_strides=(1,),
                                 padding=((width - 1, 0),), dimension_numbers=('NWC', 'WIO', 'NWC'),
                                 feature_group_count=ch)
    return y + b

def block_diag_linear(x, w):
    nb, bi, bo = w.shape
    xb = x.reshape(x.shape[:-1] + (nb, bi))
    return jnp.einsum('...ni,nio->...no', xb, w).reshape(x.shape[:-1] + (nb * bo,))

def swiglu(h, w_gate, w_up, w_down):
    return (jax.nn.silu(h @ w_gate) * (h @ w_up)) @ w_down

def rg_lru(x, w_a, b_a, w_x, b_x, lam):
    xf = x.astype(jnp.float32)
    r = jax.nn.sigmoid(block_diag_linear(xf, w_a.astype(jnp.float32)) + b_a.astype(jnp.float32))
    i = jax.nn.sigmoid(block_diag_linear(xf, w_x.astype(jnp.float32)) + b_x.astype(jnp.float32))
    log_a = -LRU_C * r * jax.nn.softplus(-lam.astype(jnp.float32))
    a = jnp.exp(log_a)
    u = jnp.sqrt(-jnp.expm1(2.0 * log_a)) * (i * xf)

    def combine(left, right):
        a_l, u_l = left
        a_r, u_r = right
        return a_l * a_r, a_r * u_l + u_r

    _, h = lax.associative_scan(combine, (a, u), axis=1)
    return h

def segsum(x):
    t = x.shape[-1]
    cs = jnp.cumsum(x, axis=-1)
    diff = cs[..., :, None] - cs[..., None, :]
    mask = jnp.tril(jnp.ones((t, t), dtype=bool))
    return jnp.where(mask, diff, -jnp.inf)

def ssd_chunked(x, dt, a, bm, cm):
    bsz, seq, nh, hp = x.shape
    ng, ns = bm.shape[-2:]
    ne = nh // ng
    nc = seq // SSD_CHUNK
    ln = SSD_CHUNK
    xc = (x * dt[..., None]).reshape(bsz, nc, ln, ng, ne, hp)
    bc = bm.reshape(bsz, nc, ln, ng, ns)
    cc = cm.reshape(bsz, nc, ln, ng, ns)
    ac = (dt * a).reshape(bsz, nc, ln, ng, ne).transpose(0, 3, 4, 1, 2)
    acs = jnp.cumsum(ac, axis=-1)
    decay_in = jnp.exp(segsum(ac))
    cb = jnp.einsum('bclgn,bcsgn->bgcls', cc, bc)
    y_diag = jnp.einsum('bgecls,bcsgep->bclgep', cb[:, :, None] * decay_in, xc)
    decay_states = jnp.exp(acs[..., -1:] - acs).transpose(0, 3, 4, 1, 2)
    states = jnp.einsum('bclgn,bclgep->bcgepn', bc, xc * decay_states[..., None])
    chunk_tot = jnp.pad(acs[..., -1], ((0, 0), (0, 0), (0, 0), (1, 0)))
    decay_chunk = jnp.exp(segsum(chunk_tot))
    states = jnp.pad(states, ((0, 0), (1, 0), (0, 0), (0, 0), (0, 0), (0, 0)))
    prev_states = jnp.einsum('bgezj,bjgepn->bzgepn', decay_chunk, states)[:, :-1]
    decay_out = jnp.exp(acs).transpose(0, 3, 4, 1, 2)
    y_off = jnp.einsum('bclgn,bcgepn->bclgep', cc, prev_states) * decay_out[..., None]
    return (y_diag + y_off).reshape(bsz, seq, nh, hp)

def mlstm_chunkwise(q, k, v, i_pre, f_pre):
    bsz, nh, seq, dh = q.shape
    nc = seq // MLSTM_CHUNK
    ln = MLSTM_CHUNK
    k = k * (dh ** -0.5)
    log_f = jax.nn.log_sigmoid(f_pre)

    def to_chunks(t):
        return jnp.moveaxis(t.reshape((bsz, nh, nc, ln) + t.shape[3:]), 2, 0)

    causal = jnp.tril(jnp.ones((ln, ln), dtype=bool))

    def step(carry, inp):
        c_st, n_st, m_st = carry
        q_c, k_c, v_c, i_c, lf_c = inp
        bcum = jnp.cumsum(lf_c, axis=-1)
        log_d = jnp.where(causal, bcum[..., :, None] - bcum[..., None, :] + i_c[..., None, :], -jnp.inf)
        g = bcum + m_st[..., None]
        m = jnp.maximum(g, jnp.max(log_d, axis=-1))
        w_inter = jnp.exp(g - m)
        s_mat = jnp.einsum('bhtd,bhsd->bhts', q_c, k_c) * jnp.exp(log_d - m[..., None])
        num = w_inter[..., None] * jnp.einsum('bhtd,bhdv->bhtv', q_c, c_st) + jnp.einsum('bhts,bhsv->bhtv', s_mat, v_c)
        den = w_inter * jnp.einsum('bhtd,bhd->bht', q_c, n_st) + jnp.sum(s_mat, axis=-1)
        h_out = num / jnp.maximum(jnp.abs(den), jnp.exp(-m))[..., None]
        b_last = bcum[..., -1]
        log_w = b_last[..., None] - bcum + i_c
        m_new = jnp.maximum(b_last + m_st, jnp.max(log_w, axis=-1))
        w_s = jnp.exp(log_w - m_new[..., None])
        decay = jnp.exp(b_last + m_st - m_new)
        c_new = decay[..., None, None] * c_st + jnp.einsum('bhs,bhsd,bhsv->bhdv', w_s, k_c, v_c)
        n_new = decay[..., None] * n_st + jnp.einsum('bhs,bhsd->bhd', w_s, k_c)
        return (c_new, n_new, m_new), h_out

    init = (jnp.zeros((bsz, nh, dh, dh), jnp.float32), jnp.zeros((bsz, nh, dh), jnp.float32),
            jnp.zeros((bsz, nh), jnp.float32))
    _, hc = lax.scan(step, init, (to_chunks(q), to_chunks(k), to_chunks(v), to_chunks(i_pre), to_chunks(log_f)))
    return jnp.moveaxis(hc, 0, 2).reshape(bsz, nh, seq, dh)

def hybrid_mixer(h, w_in, w_out, lru_conv_w, lru_conv_b, lru_wa, lru_ba, lru_wx, lru_bx, lru_lambda,
                 ssd_conv_w, ssd_conv_b, ssd_dt_bias, ssd_a_log, ssd_d, ssd_norm_g):
    bsz, seq, _ = h.shape
    f32 = jnp.float32
    gate_lru, x_lru, z_ssd, xbc, dt_raw = jnp.split(h @ w_in, HYB_SPLITS, axis=-1)
    x_lru = causal_conv(x_lru, lru_conv_w, lru_conv_b)
    y_lru = rg_lru(x_lru, lru_wa, lru_ba, lru_wx, lru_bx, lru_lambda) * jax.nn.gelu(gate_lru.astype(f32))
    xbc = jax.nn.silu(causal_conv(xbc, ssd_conv_w, ssd_conv_b)).astype(f32)
    gn = SSD_GROUPS * SSD_STATE
    xs = xbc[..., :SSD_WIDTH].reshape(bsz, seq, SSD_HEADS, SSD_HEADDIM)
    bm = xbc[..., SSD_WIDTH:SSD_WIDTH + gn].reshape(bsz, seq, SSD_GROUPS, SSD_STATE)
    cm = xbc[..., SSD_WIDTH + gn:].reshape(bsz, seq, SSD_GROUPS, SSD_STATE)
    dt = jax.nn.softplus(dt_raw.astype(f32) + ssd_dt_bias.astype(f32))
    a = -jnp.exp(ssd_a_log.astype(f32))
    y = ssd_chunked(xs, dt, a, bm, cm) + ssd_d.astype(f32)[:, None] * xs
    y = y.reshape(bsz, seq, SSD_WIDTH) * jax.nn.silu(z_ssd.astype(f32))
    y = rms_norm(y.reshape(bsz, seq, SSD_GROUPS, SSD_WIDTH // SSD_GROUPS),
                 ssd_norm_g.reshape(SSD_GROUPS, SSD_WIDTH // SSD_GROUPS)).reshape(bsz, seq, SSD_WIDTH)
    y_cat = jnp.concatenate([y_lru, y], axis=-1).astype(h.dtype)
    return y_cat @ w_out

def mlstm_block(h, w_up, conv_w, conv_b, wq, wk, wv, w_gates, b_gates, norm_g, skip, w_down):
    bsz, seq, _ = h.shape
    f32 = jnp.float32
    xm, z = jnp.split(h @ w_up, 2, axis=-1)
    xc = jax.nn.silu(causal_conv(xm, conv_w, conv_b))
    q = block_diag_linear(xc, wq)
    k = block_diag_linear(xc, wk)
    v = block_diag_linear(xm, wv)
    gates = (q @ w_gates[:MLSTM_WIDTH] + k @ w_gates[MLSTM_WIDTH:2 * MLSTM_WIDTH]
             + v @ w_gates[2 * MLSTM_WIDTH:] + b_gates).astype(f32).transpose(0, 2, 1)
    i_pre = gates[:, :MLSTM_HEADS]
    f_pre = gates[:, MLSTM_HEADS:]

    def heads(t):
        return t.astype(f32).reshape(bsz, seq, MLSTM_HEADS, MLSTM_HEADDIM).transpose(0, 2, 1, 3)

    hh = mlstm_chunkwise(heads(q), heads(k), heads(v), i_pre, f_pre)
    hh = head_layer_norm(hh.transpose(0, 2, 1, 3), norm_g.reshape(MLSTM_HEADS, MLSTM_HEADDIM))
    hh = hh.reshape(bsz, seq, MLSTM_WIDTH) + skip.astype(f32) * xc.astype(f32)
    return (hh * jax.nn.silu(z.astype(f32))).astype(h.dtype) @ w_down

def first_inputs(seed: int = 0) -> dict:
    key = jax.random.key(seed)
    ks = iter(jax.random.split(key, 64))
    f32 = jnp.float32

    def nrm(shape, fan_in, scale=1.0):
        return jax.random.normal(next(ks), shape, f32) * (scale * fan_in ** -0.5)

    def small(shape, s=0.02):
        return jax.random.normal(next(ks), shape, f32) * s

    def gain(shape):
        return 1.0 + small(shape, 0.05)

    x = jax.random.normal(next(ks), (BATCH, SEQ, D_MODEL), f32)
    c = jax.random.normal(next(ks), (BATCH, D_MODEL), f32)
    ada_w = nrm((DEPTH, D_MODEL, N_SUB * 3 * D_MODEL), D_MODEL, 0.5)
    ada_b = small((DEPTH, N_SUB * 3 * D_MODEL))
    norm_g = gain((DEPTH, N_SUB, D_MODEL))
    ffn_w_gate = nrm((DEPTH, 2, D_MODEL, D_FF), D_MODEL)
    ffn_w_up = nrm((DEPTH, 2, D_MODEL, D_FF), D_MODEL)
    ffn_w_down = nrm((DEPTH, 2, D_FF, D_MODEL), D_FF)
    hyb_w_in = nrm((N_EVEN, D_MODEL, HYB_IN), D_MODEL)
    hyb_w_out = nrm((N_EVEN, HYB_OUT, D_MODEL), HYB_OUT)
    lru_conv_w = nrm((N_EVEN, CONV_WIDTH, LRU_WIDTH), CONV_WIDTH)
    lru_conv_b = small((N_EVEN, LRU_WIDTH))
    lru_wa = nrm((N_EVEN, LRU_HEADS, LRU_BLOCK, LRU_BLOCK), LRU_BLOCK)
    lru_ba = small((N_EVEN, LRU_WIDTH))
    lru_wx = nrm((N_EVEN, LRU_HEADS, LRU_BLOCK, LRU_BLOCK), LRU_BLOCK)
    lru_bx = small((N_EVEN, LRU_WIDTH))
    a_pow = jax.random.uniform(next(ks), (N_EVEN, LRU_WIDTH), f32, minval=0.9, maxval=0.999)
    s_a = a_pow ** (1.0 / LRU_C)
    lru_lambda = jnp.log(s_a) - jnp.log1p(-s_a)
    ssd_conv_w = nrm((N_EVEN, CONV_WIDTH, SSD_CONV_DIM), CONV_WIDTH)
    ssd_conv_b = small((N_EVEN, SSD_CONV_DIM))
    dt0 = jnp.exp(jax.random.uniform(next(ks), (N_EVEN, SSD_HEADS), f32,
                                     minval=float(np.log(1e-3)), maxval=float(np.log(1e-1))))
    ssd_dt_bias = dt0 + jnp.log(-jnp.expm1(-dt0))
    ssd_a_log = jnp.log(jax.random.uniform(next(ks), (N_EVEN, SSD_HEADS), f32, minval=1.0, maxval=16.0))
    ssd_d = gain((N_EVEN, SSD_HEADS))
    ssd_norm_g = gain((N_EVEN, SSD_WIDTH))
    mlstm_w_up = nrm((N_ODD, D_MODEL, 2 * MLSTM_WIDTH), D_MODEL)
    mlstm_conv_w = nrm((N_ODD, CONV_WIDTH, MLSTM_WIDTH), CONV_WIDTH)
    mlstm_conv_b = small((N_ODD, MLSTM_WIDTH))
    nblk = MLSTM_WIDTH // MLSTM_QKV_BLOCK
    mlstm_wq = nrm((N_ODD, nblk, MLSTM_QKV_BLOCK, MLSTM_QKV_BLOCK), MLSTM_QKV_BLOCK)
    mlstm_wk = nrm((N_ODD, nblk, MLSTM_QKV_BLOCK, MLSTM_QKV_BLOCK), MLSTM_QKV_BLOCK)
    mlstm_wv = nrm((N_ODD, nblk, MLSTM_QKV_BLOCK, MLSTM_QKV_BLOCK), MLSTM_QKV_BLOCK)
    mlstm_w_gates = nrm((N_ODD, 3 * MLSTM_WIDTH, 2 * MLSTM_HEADS), 3 * MLSTM_WIDTH, 0.5)
    f_bias = jnp.broadcast_to(jnp.linspace(3.0, 6.0, MLSTM_HEADS, dtype=f32), (N_ODD, MLSTM_HEADS))
    mlstm_b_gates = jnp.concatenate([small((N_ODD, MLSTM_HEADS), 0.1),
                                     f_bias + small((N_ODD, MLSTM_HEADS), 0.02)], axis=-1)
    mlstm_norm_g = gain((N_ODD, MLSTM_WIDTH))
    mlstm_skip = gain((N_ODD, MLSTM_WIDTH))
    mlstm_w_down = nrm((N_ODD, MLSTM_WIDTH, D_MODEL), MLSTM_WIDTH)
    final_norm_g = gain((D_MODEL,))
    return {'x': x, 'c': c, 'ada_w': ada_w, 'ada_b': ada_b, 'norm_g': norm_g,
            'ffn_w_gate': ffn_w_gate, 'ffn_w_up': ffn_w_up, 'ffn_w_down': ffn_w_down,
            'hyb_w_in': hyb_w_in, 'hyb_w_out': hyb_w_out,
            'lru_conv_w': lru_conv_w, 'lru_conv_b': lru_conv_b, 'lru_wa': lru_wa, 'lru_ba': lru_ba,
            'lru_wx': lru_wx, 'lru_bx': lru_bx, 'lru_lambda': lru_lambda,
            'ssd_conv_w': ssd_conv_w, 'ssd_conv_b': ssd_conv_b, 'ssd_dt_bias': ssd_dt_bias,
            'ssd_a_log': ssd_a_log, 'ssd_d': ssd_d, 'ssd_norm_g': ssd_norm_g,
            'mlstm_w_up': mlstm_w_up, 'mlstm_conv_w': mlstm_conv_w, 'mlstm_conv_b': mlstm_conv_b,
            'mlstm_wq': mlstm_wq, 'mlstm_wk': mlstm_wk, 'mlstm_wv': mlstm_wv,
            'mlstm_w_gates': mlstm_w_gates, 'mlstm_b_gates': mlstm_b_gates,
            'mlstm_norm_g': mlstm_norm_g, 'mlstm_skip': mlstm_skip, 'mlstm_w_down': mlstm_w_down,
            'final_norm_g': final_norm_g}

def first_block(x, c, ada_w, ada_b, norm_g, ffn_w_gate, ffn_w_up, ffn_w_down, hyb_w_in, hyb_w_out,
              lru_conv_w, lru_conv_b, lru_wa, lru_ba, lru_wx, lru_bx, lru_lambda,
              ssd_conv_w, ssd_conv_b, ssd_dt_bias, ssd_a_log, ssd_d, ssd_norm_g,
              mlstm_w_up, mlstm_conv_w, mlstm_conv_b, mlstm_wq, mlstm_wk, mlstm_wv,
              mlstm_w_gates, mlstm_b_gates, mlstm_norm_g, mlstm_skip, mlstm_w_down, final_norm_g):
    bsz = x.shape[0]
    c_act = jax.nn.silu(c)
    for layer in range(DEPTH):
        mod = (c_act @ ada_w[layer] + ada_b[layer]).reshape(bsz, N_SUB, 3, D_MODEL)[:, :, :, None, :]

        def modulate(t, sub):
            return rms_norm(t, norm_g[layer, sub]) * (1.0 + mod[:, sub, 1]) + mod[:, sub, 0]

        h = modulate(x, 0)
        x = x + HALF_STEP * (1.0 + mod[:, 0, 2]) * swiglu(h, ffn_w_gate[layer, 0], ffn_w_up[layer, 0], ffn_w_down[layer, 0])
        h = modulate(x, 1)
        if layer % 2 == 0:
            e = layer // 2
            y = hybrid_mixer(h, hyb_w_in[e], hyb_w_out[e], lru_conv_w[e], lru_conv_b[e], lru_wa[e], lru_ba[e],
                             lru_wx[e], lru_bx[e], lru_lambda[e], ssd_conv_w[e], ssd_conv_b[e],
                             ssd_dt_bias[e], ssd_a_log[e], ssd_d[e], ssd_norm_g[e])
        else:
            o = layer // 2
            y = mlstm_block(h, mlstm_w_up[o], mlstm_conv_w[o], mlstm_conv_b[o], mlstm_wq[o], mlstm_wk[o],
                            mlstm_wv[o], mlstm_w_gates[o], mlstm_b_gates[o], mlstm_norm_g[o],
                            mlstm_skip[o], mlstm_w_down[o])
        x = x + (1.0 + mod[:, 1, 2]) * y.astype(x.dtype)
        h = modulate(x, 2)
        x = x + HALF_STEP * (1.0 + mod[:, 2, 2]) * swiglu(h, ffn_w_gate[layer, 1], ffn_w_up[layer, 1], ffn_w_down[layer, 1])
    return rms_norm(x, final_norm_g)


DEPTH_2 = 1

HEAD_DIM = 64
ATTN_GROUPS = ((128, 1), (512, 4), (2048, 16))
ATTN_HEADS_PER_GROUP = 4
ATTN_HEADS = ATTN_HEADS_PER_GROUP * len(ATTN_GROUPS)
ATTN_WIDTH = ATTN_HEADS * HEAD_DIM
ATTN_OUT_WIDTH = ATTN_HEADS_PER_GROUP * HEAD_DIM
ATTN_BLOCK = 128
ROPE_THETA = 500000.0
ROPE_DIM = HEAD_DIM // 4
RWKV_HEADS = D_MODEL // HEAD_DIM
RWKV_WIDTH = RWKV_HEADS * HEAD_DIM
DECAY_LORA = 64
ICLR_LORA = 64
GATE_LORA = 128
D_FF_2 = 4 * D_MODEL
NORM_EPS = 1e-6
GN_EPS = 64e-5
NEG_INF = -1e30
SPLITS = (ATTN_WIDTH, ATTN_WIDTH, ATTN_WIDTH,
          RWKV_WIDTH, RWKV_WIDTH, RWKV_WIDTH,
          DECAY_LORA, ICLR_LORA, GATE_LORA,
          D_MODEL, D_MODEL)
ATTN_QKV_WIDTH = 3 * ATTN_WIDTH
SHIFT_WIDTH = 3 * RWKV_WIDTH + DECAY_LORA + ICLR_LORA + GATE_LORA
IN_WIDTH = sum(SPLITS)


def rms_norm_2(t, gain):
    t32 = t.astype(jnp.float32)
    y = t32 * lax.rsqrt(jnp.mean(t32 * t32, axis=-1, keepdims=True) + NORM_EPS)
    return (y * gain.astype(jnp.float32)).astype(t.dtype)

def partial_rope(t, positions):
    half = ROPE_DIM // 2
    inv = ROPE_THETA ** (-jnp.arange(half, dtype=jnp.float32) * 2.0 / ROPE_DIM)
    ang = positions.astype(jnp.float32)[..., None] * inv
    cos = jnp.cos(ang)[:, :, None, :]
    sin = jnp.sin(ang)[:, :, None, :]
    t32 = t.astype(jnp.float32)
    x1 = t32[..., :half]
    x2 = t32[..., half:ROPE_DIM]
    out = jnp.concatenate([x1 * cos - x2 * sin, x1 * sin + x2 * cos, t32[..., ROPE_DIM:]], axis=-1)
    return out.astype(t.dtype)

def dilated_band_attention(q, k, v, dilation, span):
    B, S, H, Dh = q.shape
    unit = dilation * ATTN_BLOCK
    Sp = -(-S // unit) * unit
    L = Sp // dilation
    nb = L // ATTN_BLOCK

    def to_blocks(t):
        t = jnp.pad(t.astype(jnp.float32), ((0, 0), (0, Sp - S), (0, 0), (0, 0)))
        t = t.reshape(B, L, dilation, H, Dh).transpose(0, 2, 1, 3, 4)
        return t.reshape(B, dilation, nb, ATTN_BLOCK, H, Dh)

    qb, kb, vb = to_blocks(q), to_blocks(k), to_blocks(v)

    def with_prev(t):
        prev = jnp.pad(t[:, :, :-1], ((0, 0), (0, 0), (1, 0), (0, 0), (0, 0), (0, 0)))
        return jnp.concatenate([prev, t], axis=3)

    kw, vw = with_prev(kb), with_prev(vb)
    s = jnp.einsum('bdnqhe,bdnkhe->bdnhqk', qb, kw) * (HEAD_DIM ** -0.5)
    qi = jnp.arange(ATTN_BLOCK)[:, None]
    kj = jnp.arange(2 * ATTN_BLOCK)[None, :]
    lag = qi + ATTN_BLOCK - kj
    band = (lag >= 0) & (lag <= span)
    has_prev = (jnp.arange(nb) > 0)[:, None, None] | (kj >= ATTN_BLOCK)[None]
    mask = band[None] & has_prev
    s = jnp.where(mask[None, None, :, None], s, NEG_INF)
    m = jnp.max(s, axis=-1, keepdims=True)
    p = jnp.exp(s - m)
    l = jnp.sum(p, axis=-1, keepdims=True)
    o = jnp.einsum('bdnhqk,bdnkhe->bdnqhe', p / l, vw)
    lse = jnp.swapaxes((m + jnp.log(l))[..., 0], -1, -2)

    def from_blocks(t):
        t = t.reshape((B, dilation, L) + t.shape[4:])
        t = jnp.swapaxes(t, 1, 2)
        return t.reshape((B, Sp) + t.shape[3:])[:, :S]

    return from_blocks(o), from_blocks(lse)

def dilated_attention_mixer(q, k, v, positions):
    B, S = q.shape[:2]
    q = partial_rope(q, positions)
    k = partial_rope(k, positions)
    outs, lses = [], []
    for g, (window, dilation) in enumerate(ATTN_GROUPS):
        sl = slice(g * ATTN_HEADS_PER_GROUP, (g + 1) * ATTN_HEADS_PER_GROUP)
        o, lse = dilated_band_attention(q[:, :, sl], k[:, :, sl], v[:, :, sl], dilation, window // dilation)
        outs.append(o)
        lses.append(lse)
    o = jnp.stack(outs)
    w = jax.nn.softmax(jnp.stack(lses), axis=0)
    out = jnp.sum(w[..., None] * o, axis=0)
    return out.reshape(B, S, ATTN_OUT_WIDTH).astype(q.dtype)

def token_shift(u, mu):
    prev = jnp.pad(u, ((0, 0), (1, 0), (0, 0)))[:, :-1]
    return u + (prev - u) * mu

def wkv7_scan(r, w, k, v, a, b):
    B, S, H, N = r.shape
    xs = tuple(jnp.moveaxis(t, 1, 0) for t in (r, w, k, v, a, b))

    def step(state, inp):
        r_t, w_t, k_t, v_t, a_t, b_t = inp
        sa = jnp.einsum('bhvk,bhk->bhv', state, a_t)
        state = (state * w_t[:, :, None, :] + sa[..., None] * b_t[:, :, None, :]
                 + v_t[..., None] * k_t[:, :, None, :])
        return state, jnp.einsum('bhvk,bhk->bhv', state, r_t)

    s0 = jnp.zeros((B, H, N, N), jnp.float32)
    _, ys = lax.scan(step, s0, xs)
    return jnp.moveaxis(ys, 0, 1)

def rwkv7_mixer(r, k, v, dw, da, dg, w0, w2, a0, a2, g2, k_k, k_a, r_k, gn_w, gn_b):
    B, S, C = r.shape
    H, N = RWKV_HEADS, HEAD_DIM
    f32 = jnp.float32
    w_log = -jax.nn.softplus(-(w0 + jnp.tanh(dw) @ w2).astype(f32)) - 0.5
    decay = jnp.exp(-jnp.exp(w_log))
    a = jax.nn.sigmoid((a0 + da @ a2).astype(f32))
    g = (jax.nn.sigmoid(dg) @ g2).astype(f32)
    kk = (k * k_k).astype(f32).reshape(B, S, H, N)
    kk = kk / jnp.maximum(jnp.sqrt(jnp.sum(kk * kk, axis=-1, keepdims=True)), 1e-12)
    k = k.astype(f32) * (1.0 + (a - 1.0) * k_a.astype(f32))
    heads = lambda t: t.astype(f32).reshape(B, S, H, N)
    rh, kh, vh, wh, ah = heads(r), heads(k), heads(v), heads(decay), heads(a)
    y = wkv7_scan(rh, wh, kh, vh, -kk, kk * ah)
    mu = jnp.mean(y, axis=-1, keepdims=True)
    var = jnp.mean(jnp.square(y - mu), axis=-1, keepdims=True)
    y = ((y - mu) * lax.rsqrt(var + GN_EPS)).reshape(B, S, C) * gn_w + gn_b
    bonus = jnp.sum(rh * kh * r_k.astype(f32), axis=-1, keepdims=True) * vh
    y = y + bonus.reshape(B, S, C)
    return (y * g).astype(r.dtype)

def second_inputs(seed: int = 0) -> dict:
    key = jax.random.key(seed)
    ks = jax.random.split(key, 32)
    f32 = jnp.float32
    L, D = DEPTH_2, D_MODEL
    nrm = lambda kk, shape, scale: jax.random.normal(kk, shape, f32) * scale
    x = nrm(ks[0], (BATCH, SEQ, D), 1.0)
    c = nrm(ks[1], (BATCH, D), 1.0)
    offset = jax.random.randint(ks[2], (BATCH, 1), 0, 4096, dtype=jnp.int32)
    positions = offset + jnp.arange(SEQ, dtype=jnp.int32)[None, :]
    return {
        "x": x,
        "c": c,
        "positions": positions,
        "ada_w": nrm(ks[3], (L, D, 6 * D), 0.5 * D ** -0.5),
        "ada_b": nrm(ks[4], (L, 6 * D), 0.02),
        "norm_mix_pre": 1.0 + nrm(ks[5], (L, D), 0.05),
        "norm_mix_post": 1.0 + nrm(ks[6], (L, D), 0.05),
        "norm_ffn_pre": 1.0 + nrm(ks[7], (L, D), 0.05),
        "norm_ffn_post": 1.0 + nrm(ks[8], (L, D), 0.05),
        "w_in": nrm(ks[9], (L, D, IN_WIDTH), D ** -0.5),
        "shift_mu": jax.random.uniform(ks[10], (L, SHIFT_WIDTH), f32),
        "decay_w0": jax.random.uniform(ks[11], (L, RWKV_WIDTH), f32, -6.0, 1.0),
        "decay_w2": nrm(ks[12], (L, DECAY_LORA, RWKV_WIDTH), DECAY_LORA ** -0.5),
        "iclr_a0": nrm(ks[13], (L, RWKV_WIDTH), 0.1),
        "iclr_a2": nrm(ks[14], (L, ICLR_LORA, RWKV_WIDTH), ICLR_LORA ** -0.5),
        "gate_g2": nrm(ks[15], (L, GATE_LORA, RWKV_WIDTH), GATE_LORA ** -0.5),
        "k_k": 0.85 + nrm(ks[16], (L, RWKV_WIDTH), 0.05),
        "k_a": 1.0 + nrm(ks[17], (L, RWKV_WIDTH), 0.05),
        "r_k": nrm(ks[18], (L, RWKV_HEADS, HEAD_DIM), 0.1),
        "gn_w": 1.0 + nrm(ks[19], (L, RWKV_WIDTH), 0.05),
        "gn_b": nrm(ks[20], (L, RWKV_WIDTH), 0.02),
        "w_branch": jnp.concatenate([nrm(ks[21], (L, ATTN_OUT_WIDTH, D), ATTN_OUT_WIDTH ** -0.5),
                                     nrm(ks[22], (L, RWKV_WIDTH, D), RWKV_WIDTH ** -0.5)], axis=1),
        "w_out": nrm(ks[23], (L, D, D), D ** -0.5),
        "w_ff1": nrm(ks[24], (L, D, D_FF_2), D ** -0.5),
        "w_ff2": nrm(ks[25], (L, D_FF_2, D), D_FF_2 ** -0.5),
    }

def second_block(x, c, positions, ada_w, ada_b, norm_mix_pre, norm_mix_post, norm_ffn_pre,
              norm_ffn_post, w_in, shift_mu, decay_w0, decay_w2, iclr_a0, iclr_a2, gate_g2,
              k_k, k_a, r_k, gn_w, gn_b, w_branch, w_out, w_ff1, w_ff2):
    B, S, D = x.shape
    for l in range(DEPTH_2):
        mod = jax.nn.silu(c) @ ada_w[l] + ada_b[l]
        sh1, sc1, gt1, sh2, sc2, gt2 = [m[:, None, :] for m in jnp.split(mod, 6, axis=-1)]

        h = rms_norm_2(x, norm_mix_pre[l]) * (1.0 + sc1) + sh1
        proj = h @ w_in[l]
        attn_part = proj[..., :ATTN_QKV_WIDTH]
        rwkv_part = token_shift(proj[..., ATTN_QKV_WIDTH:ATTN_QKV_WIDTH + SHIFT_WIDTH], shift_mu[l])
        gate_part = proj[..., ATTN_QKV_WIDTH + SHIFT_WIDTH:]
        q, k, v = [t.reshape(B, S, ATTN_HEADS, HEAD_DIM) for t in jnp.split(attn_part, 3, axis=-1)]
        cuts = np.cumsum([RWKV_WIDTH, RWKV_WIDTH, RWKV_WIDTH, DECAY_LORA, ICLR_LORA])
        r_r, r_k_, r_v, dw, da, dg = jnp.split(rwkv_part, cuts, axis=-1)
        g_attn, g_rwkv = jnp.split(gate_part, 2, axis=-1)

        o_attn = dilated_attention_mixer(q, k, v, positions)
        o_rwkv = rwkv7_mixer(r_r, r_k_, r_v, dw, da, dg, decay_w0[l], decay_w2[l], iclr_a0[l],
                             iclr_a2[l], gate_g2[l], k_k[l], k_a[l], r_k[l], gn_w[l], gn_b[l])
        wb = w_branch[l]
        merged = (jax.nn.sigmoid(g_attn) * (o_attn @ wb[:ATTN_OUT_WIDTH])
                  + jax.nn.sigmoid(g_rwkv) * (o_rwkv @ wb[ATTN_OUT_WIDTH:]))
        mix_out = merged @ w_out[l]
        x = (x + gt1 * rms_norm_2(mix_out, norm_mix_post[l])).astype(x.dtype)

        h = rms_norm_2(x, norm_ffn_pre[l]) * (1.0 + sc2) + sh2
        f = jnp.square(jax.nn.relu(h @ w_ff1[l])) @ w_ff2[l]
        x = (x + gt2 * rms_norm_2(f, norm_ffn_post[l])).astype(x.dtype)
    return x


def setup_inputs(seed=0):
    out = dict(first_inputs(seed))
    for name, value in second_inputs(seed + 1).items():
        if name != "x":
            out[name + "_2"] = value
    return out


def reference(
    x, c, ada_w, ada_b, norm_g, ffn_w_gate, ffn_w_up, ffn_w_down, hyb_w_in, hyb_w_out,
    lru_conv_w, lru_conv_b, lru_wa, lru_ba, lru_wx, lru_bx, lru_lambda, ssd_conv_w, ssd_conv_b,
    ssd_dt_bias, ssd_a_log, ssd_d, ssd_norm_g, mlstm_w_up, mlstm_conv_w, mlstm_conv_b, mlstm_wq,
    mlstm_wk, mlstm_wv, mlstm_w_gates, mlstm_b_gates, mlstm_norm_g, mlstm_skip, mlstm_w_down,
    final_norm_g, c_2, positions_2, ada_w_2, ada_b_2, norm_mix_pre_2, norm_mix_post_2,
    norm_ffn_pre_2, norm_ffn_post_2, w_in_2, shift_mu_2, decay_w0_2, decay_w2_2, iclr_a0_2,
    iclr_a2_2, gate_g2_2, k_k_2, k_a_2, r_k_2, gn_w_2, gn_b_2, w_branch_2, w_out_2, w_ff1_2,
    w_ff2_2,
):
    x = first_block(
        x, c, ada_w, ada_b, norm_g, ffn_w_gate, ffn_w_up, ffn_w_down, hyb_w_in, hyb_w_out,
        lru_conv_w, lru_conv_b, lru_wa, lru_ba, lru_wx, lru_bx, lru_lambda, ssd_conv_w,
        ssd_conv_b, ssd_dt_bias, ssd_a_log, ssd_d, ssd_norm_g, mlstm_w_up, mlstm_conv_w,
        mlstm_conv_b, mlstm_wq, mlstm_wk, mlstm_wv, mlstm_w_gates, mlstm_b_gates, mlstm_norm_g,
        mlstm_skip, mlstm_w_down, final_norm_g,
    )
    return second_block(
        x, c_2, positions_2, ada_w_2, ada_b_2, norm_mix_pre_2, norm_mix_post_2, norm_ffn_pre_2,
        norm_ffn_post_2, w_in_2, shift_mu_2, decay_w0_2, decay_w2_2, iclr_a0_2, iclr_a2_2,
        gate_g2_2, k_k_2, k_a_2, r_k_2, gn_w_2, gn_b_2, w_branch_2, w_out_2, w_ff1_2, w_ff2_2,
    )


_drawn_inputs = setup_inputs


def setup_inputs(seed=0):
    import zlib

    import numpy as np

    out = dict(_drawn_inputs(seed))
    spreads = {}
    factors = {'lru_ba': 8.0,
     'lru_bx': 8.0,
     'ssd_conv_b': 2.992,
     'ssd_d': 3.202,
     'mlstm_conv_b': 3.139,
     'mlstm_norm_g': 2.741,
     'mlstm_skip': 4.074,
     'norm_mix_post_2': 3.839,
     'norm_ffn_pre_2': 3.513,
     'norm_ffn_post_2': 4.148,
     'iclr_a0_2': 5.989,
     'gn_w_2': 4.386,
     'gn_b_2': 8.0}
    for name, (base, spread) in spreads.items():
        noise = np.random.default_rng([zlib.crc32(name.encode()), seed]).standard_normal(out[name].shape)
        drawn = base * np.exp(spread * noise) if base else spread * noise
        out[name] = __import__('jax').numpy.asarray(drawn.astype(out[name].dtype))
    for name, factor in factors.items():
        out[name] = (out[name] * factor).astype(out[name].dtype)
    return out
```

```python
from contextlib import ExitStack, contextmanager

import numpy as np

import concourse.bass as bass
from concourse import mybir

F32 = mybir.dt.float32
F32R = mybir.dt.float32r
I32 = mybir.dt.int32
ALU = mybir.AluOpType
ACT = mybir.ActivationFunctionType
AX_X = mybir.AxisListType.X

P = 128
S = 512
NT = S // P
D = 1024
DC = D // P
FF = 2816
FC = FF // P
RING = 4
SPLIT = 2
KB_MAX = FC // 2
SLOT_BYTES = KB_MAX * P * 4
EPS = 1e-6
ADA_GROUPS = (2 * 9 * D + 6 * D) // S
ADA_FIRST = 2 * 9 * D // S

SSD_H, SSD_P, SSD_G = 16, 64, 2
SSD_PAIRS = SSD_H // SSD_G // 2
XBC = DC + 2 * SSD_G
HYB = DC + XBC + 2 * DC
CONV = 4
ML_H = 4
MLC = 2 * D // P
HC = MLC // ML_H
HEADS, HD = 12, 64
GROUPS = 3
DILATION = (1, 4, 16)
ROPE = HD // 4
THETA = 500000.0
QKV = 3 * HEADS * HD // P
LEVELS = 6
GN_EPS = 64e-5
FF2 = 4 * D // P
ML_F = 32

COLUMNS = [("ada_b", 192), ("norm_g", 48), ("final_g", 8), ("mix_pre", 8), ("mix_post", 8), ("ffn_pre", 8),
           ("ffn_post", 8), ("c", 8), ("c2", 8),
           ("hyb_conv_w", 80), ("hyb_conv_b", 20), ("lru_ba", 8), ("lru_bx", 8), ("lru_lambda", 8),
           ("ssd_d", 8), ("ssd_norm_g", 8), ("ssd_dt_bias", 1), ("ssd_a_log", 1),
           ("ml_conv_w", 64), ("ml_conv_b", 16), ("ml_norm_g", 16), ("ml_skip", 16), ("ml_bi", 1), ("ml_bf", 1),
           ("rope_inv", 1), ("shift_mu", 44), ("w0", 8), ("a0", 8), ("k_k", 8), ("k_a", 8), ("r_k", 8), ("gn_w", 8), ("gn_b", 8)]


def column_map():
    at, out = 0, {}
    for name, n in COLUMNS:
        out[name] = (at, n)
        at += n
    return out, at


class Count:

    def __init__(self, sem):
        self.sem, self.base = sem, 0

    def __call__(self, n):
        return self.base + n


class Chain:

    def __init__(self, eng, count, start=0):
        self.eng, self.count, self.n, self.start = eng, count, 0, start

    def __call__(self, ins):
        self.n += 1
        ins.then_inc(self.count.sem, 1)
        self.eng.wait_ge(self.count.sem, self.count(self.start + self.n))


@contextmanager
def stage(K):
    K.stage_sems = []
    yield
    K.nc.clear_and_free_semaphores(K.stage_sems)
    K.stage_sems = None
    K.nc.all_engine_barrier()


class Core:
    pass


def setup(nc, ctx, dram):
    K = Core()
    K.nc, K.dram, K.ctx = nc, dram, ctx
    K.top = [nc.sbuf_base]

    def at(name, shape, dtype, offset):
        return nc.alloc_sbuf_tensor_at(name, shape, dtype, offset=offset)

    def sb(name, shape, dtype=F32):
        n = int(np.prod(shape[1:])) * 4
        K.top[0] = (K.top[0] + 31) // 32 * 32
        t = at(name, shape, dtype, K.top[0])
        K.top[0] += n
        return t

    K.at, K.sb = at, sb
    K.stage_sems = None

    def sem(name):
        if K.stage_sems is None:
            return ctx.enter_context(nc.semaphore(name))
        K.stage_sems.append(nc.alloc_semaphore(name=name))
        return K.stage_sems[-1]
    K.sem = sem
    K.count = lambda name: Count(K.sem(name))
    K.cols_at, ncols = column_map()
    K.x = sb("residual", [P, DC, S])
    K.h_at = (K.top[0] + 31) // 32 * 32
    K.h_hi = sb("h_hi", [P, DC, S], F32R)
    K.h_lo = sb("h_lo", [P, DC, S], F32R)
    K.w_raw = sb("w_raw", [P, RING, KB_MAX * P])
    K.w_hi_at = (K.top[0] + 31) // 32 * 32
    K.w_hi = sb("w_hi", [P, SPLIT, KB_MAX * P], F32R)
    K.w_lo_at = (K.top[0] + 31) // 32 * 32
    K.w_lo = sb("w_lo", [P, SPLIT, KB_MAX * P], F32R)
    K.cols = sb("cols", [P, ncols])
    K.consts = sb("consts", [P, NCONST])
    K.mods = sb("mods", [P, 192])
    K.gain = sb("gain", [P, DC])
    K.coef = sb("coef", [P, DC])
    K.c_act = sb("c_act", [P, 16])
    K.arena = (K.top[0] + 31) // 32 * 32
    K.ident = K.consts[:, 0:P]
    K.ones = K.consts[:, P:2 * P]
    K.causal = K.consts[:, 2 * P:3 * P]
    K.ps = [nc.alloc_psum_tensor(f"bank{i}", [P, S], F32) for i in range(8)]

    K.w_loaded = [K.sem(f"w_loaded{i}") for i in range(RING)]
    K.hi_done = K.count("w_hi_done")
    K.lo_done = K.count("w_lo_done")
    K.tile_mm = K.count("tile_mm")
    K.bank_free = K.count("bank_free")
    K.norm_counts = [K.count("norm_" + n) for n in ("squares", "sum", "order", "rstd", "value", "hi", "scaled")]
    K.silu_done, K.gu_hi_done = K.count("silu_done"), K.count("gu_hi_done")
    K.tile0 = 0
    return K


CONSTANTS = ["ident", "ones", "causal"]
NCONST = len(CONSTANTS) * P


def col(K, name, i=0, n=1):
    a, _ = K.cols_at[name]
    return K.cols[:, a + i:a + i + n]


def load_tile(K, sp, w, kb, t, slot, value):
    if value is not None:
        sp.wait_ge(K.lo_done.sem, value)
    sp.dma_start(K.w_raw[:, slot, 0:kb * P], w[bass.ds(t, 1)].rearrange("o p n -> p (o n)")).then_inc(K.w_loaded[slot], 16)


def split_hi(K, act, kb, slot, half, g):
    act.wait_ge(K.w_loaded[slot], 16 * (g // RING + 1) if isinstance(g, int) else (g + (RING - slot)) * (16 // RING))
    act.wait_ge(K.tile_mm.sem, g + PRIMED - 1)
    K.nc.scalar.activation(K.w_hi[:, half, 0:kb * P], K.w_raw[:, slot, 0:kb * P], ACT.Copy).then_inc(K.hi_done.sem, 1)


def split_lo(K, dve, kb, slot, half, g):
    dve.wait_ge(K.hi_done.sem, g + PRIMED + 1)
    K.nc.vector.tensor_tensor(K.w_lo[:, half, 0:kb * P], K.w_raw[:, slot, 0:kb * P],
                              K.w_hi[:, half, 0:kb * P].bitcast(F32), ALU.subtract).then_inc(K.lo_done.sem, 1)


PRIMED = 4


def rolled(eng, n, body):
    if n > 2:
        with eng.Fori(0, n - 1) as i:
            body(i, False)
    elif n == 2:
        body(0, False)
    body(n - 1, True)


def gemm(K, w, kb, n_tiles, nxt, mm, pe_wait, act_evac=None, dve_evac=None, turn=4, pre=None):
    nc = K.nc
    g0 = K.tile0
    n = n_tiles // turn
    assert n_tiles % turn == 0 and g0 % RING == 0 and turn % RING == 0
    with nc.Block() as block:
        @block.sync
        def _(sp):
            def body(i, last):
                if last:
                    if nxt is None:
                        return
                    for j in range(RING):
                        load_tile(K, sp, nxt[0], nxt[1], j, j, g0 + n_tiles + j + PRIMED - RING + 1)
                    return
                for j in range(turn):
                    load_tile(K, sp, w, kb, turn * i + j + RING, j % RING, g0 + turn * i + j + PRIMED + 1)
            if turn == RING:
                rolled(sp, n, body)
            else:
                with sp.Fori(0, n - 1) as i:
                    body(i, False)
                for j in range(turn - RING):
                    load_tile(K, sp, w, kb, n_tiles - turn + j + RING, j % RING, g0 + n_tiles - turn + j + PRIMED + 1)
                body(n - 1, True)

        @block.scalar
        def _(act):
            def body(i, last):
                for j in range(turn):
                    t = turn * i + j
                    if not (last and j == turn - 1):
                        split_hi(K, act, kb, (j + 1) % RING, (j + 1) % SPLIT, g0 + t + 1)
                    elif nxt is not None:
                        split_hi(K, act, nxt[1], 0, 0, g0 + t + 1)
                    if act_evac:
                        act_evac(act, i, j, t, g0 + t + PRIMED + 1)
            rolled(act, n, body)

        @block.vector
        def _(dve):
            def body(i, last):
                for j in range(turn):
                    t = turn * i + j
                    if not (last and j == turn - 1):
                        split_lo(K, dve, kb, (j + 1) % RING, (j + 1) % SPLIT, g0 + t + 1)
                    elif nxt is not None:
                        split_lo(K, dve, nxt[1], 0, 0, g0 + t + 1)
                    if dve_evac:
                        dve_evac(dve, i, j, t, g0 + t + PRIMED + 1)
            rolled(dve, n, body)

        @block.tensor
        def _(pe):
            if pre:
                pre(pe)

            def body(i, last):
                for j in range(turn):
                    t = turn * i + j
                    pe.wait_ge(K.lo_done.sem, g0 + t + PRIMED + 1)
                    pe_wait(pe, i, j, t)
                    for k in range(kb):
                        hi, lo, bank, start, stop = mm(k, j)
                        wh = K.w_hi[:, j % SPLIT, k * P:(k + 1) * P]
                        wl = K.w_lo[:, j % SPLIT, k * P:(k + 1) * P]
                        nc.tensor.matmul(K.ps[bank][:], wh, hi, start=start, stop=False)
                        nc.tensor.matmul(K.ps[bank][:], wh, lo, start=False, stop=False)
                        last_mm = nc.tensor.matmul(K.ps[bank][:], wl, hi, start=False, stop=stop)
                    last_mm.then_inc(K.tile_mm.sem, 1)
            rolled(pe, n, body)
    K.tile0 += n_tiles
    for c in (K.hi_done, K.lo_done, K.tile_mm):
        c.base = K.tile0 + PRIMED


def first_block(K, first):
    nc, dram = K.nc, K.dram
    loaded = K.sem("inputs_loaded")
    silu_done = K.sem("c_silu_done")
    ada_loaded = [K.sem(f"ada_loaded{i}") for i in range(4)]
    ada_step = K.sem("ada_step")
    ada_mm = K.count("ada_mm")
    zero_done = K.sem("zero_done")
    ada = K.at("ada_tiles", [P, 4, 4 * S], F32, K.arena)
    acc = K.at("ada_acc", [P, 2, S], F32, K.arena + 4 * 4 * S * 4)
    tiny = K.at("prime", [P, 8], F32, K.arena + 4 * 4 * S * 4 + 2 * S * 4)
    mod_ps = K.ps[0]
    with nc.Block() as block:
        @block.sync
        def _(sp):
            sp.dma_start(K.cols[:], dram["cols"]).then_inc(loaded, 16)
            sp.dma_start(K.consts[:], dram["consts"]).then_inc(loaded, 16)
            for j in range(4):
                sp.dma_start(ada[:, j, :], dram["ada"][j]).then_inc(ada_loaded[j], 16)
            sp.dma_start(K.x[:], dram["x"]).then_inc(loaded, 16)
            for j in range(RING):
                load_tile(K, sp, first[0], first[1], j, j, None)
            with sp.Fori(0, ADA_GROUPS // 2 - 1) as i:
                for j in range(4):
                    sp.wait_ge(ada_step, 16 * i + 4 * (j + 1))
                    sp.dma_start(ada[:, j, :], dram["ada"][bass.ds(4 * i + j + 4, 1)].rearrange("o p n -> p (o n)")).then_inc(ada_loaded[j], 16)

        @block.scalar
        def _(act):
            act.wait_ge(loaded, 48)
            nc.scalar.activation(K.c_act[:], K.cols[:, K.cols_at["c"][0]:K.cols_at["c"][0] + 16], ACT.Silu).then_inc(silu_done, 1)
            nc.scalar.activation(tiny[:, 4:5], K.consts[:, 0:1], ACT.Copy).then_inc(K.hi_done.sem, PRIMED)
            act.wait_ge(K.tile_mm.sem, PRIMED)
            split_hi(K, act, first[1], 0, 0, 0)

        @block.vector
        def _(dve):
            nc.vector.memset(tiny[:, 0:1], 0.0).then_inc(K.lo_done.sem, PRIMED)
            nc.vector.memset(tiny[:, 1:2], 0.0).then_inc(K.tile_mm.sem, PRIMED)
            nc.vector.memset(tiny[:, 2:3], 0.0).then_inc(K.bank_free.sem, PRIMED)
            nc.vector.memset(tiny[:, 3:4], 0.0).then_inc(ada_mm.sem, 2)
            for n, c in enumerate((K.prod_done, K.conv_step)):
                nc.vector.memset(tiny[:, 5 + n:6 + n], 0.0).then_inc(c.sem, 2 * PRIMED)
            split_lo(K, dve, first[1], 0, 0, 0)
            dve.wait_ge(silu_done, 1)

            def group(i, gq, c0):
                dve.wait_ge(ada_mm.sem, 2 * i + gq + 1)
                for h in range(2):
                    dve.wait_ge(ada_loaded[2 * gq + h], 16 * i + 16)
                    for k in range(4):
                        tile = ada[:, 2 * gq + h, k * S:(k + 1) * S]
                        cc = K.c_act[:, c0 + 4 * h + k:c0 + 4 * h + k + 1]
                        if h == k == 0:
                            ins = nc.vector.tensor_scalar(acc[:, gq, :], tile, cc, None, ALU.mult)
                        else:
                            dve.wait_ge(ada_step, 16 * i + 8 * gq + 4 * h + k)
                            ins = nc.vector.scalar_tensor_tensor(acc[:, gq, :], tile, cc, acc[:, gq, :], ALU.mult, ALU.add)
                        ins.then_inc(ada_step, 1)

            with dve.Fori(0, ADA_FIRST // 2) as i:
                for gq in range(2):
                    group(i, gq, 0)
            with dve.Fori(ADA_FIRST // 2, ADA_GROUPS // 2) as i:
                for gq in range(2):
                    group(i, gq, 8)
            dve.wait_ge(ada_mm.sem, ADA_GROUPS + 2)
            a, n = K.cols_at["ada_b"]
            nc.vector.tensor_tensor(K.mods[:], mod_ps[:, 0:192], K.cols[:, a:a + n], ALU.add).then_inc(zero_done, 1)

        @block.tensor
        def _(pe):
            pe.wait_ge(loaded, 48)
            with pe.Fori(0, ADA_GROUPS // 2) as i:
                for gq in range(2):
                    pe.wait_ge(ada_step, 16 * i + 8 * (gq + 1))
                    for m in range(4):
                        last = nc.tensor.matmul(mod_ps[:, bass.ds(8 * i + 4 * gq + m, 1)], acc[:, gq, m * P:(m + 1) * P],
                                                K.ones[:, 0:1], start=True, stop=True)
                    last.then_inc(ada_mm.sem, 1)
    for c in (K.hi_done, K.lo_done, K.tile_mm, K.bank_free):
        c.base = PRIMED
    for c in (K.prod_done, K.conv_step):
        c.base = 2 * PRIMED


def norm(K, name, src, mode, gain=None, scale=None, shift=None, gate=None, half=None, split=None):
    nc = K.nc
    sq_done, sum_done, order, rstd_done, val_done, hi_done, t_done = K.norm_counts
    buf = K.at(f"{name}_buf", [P, DC, S], F32, K.norm_at)
    rstd = K.at(f"{name}_rstd_t", [P, S], F32, K.norm_at + DC * S * 4)
    total = K.ps[0]
    with nc.Block() as block:
        @block.scalar
        def _(act):
            for c in range(0, DC, 2):
                nc.scalar.activation(buf[:, c:c + 2, :], src[:, c:c + 2, :], ACT.Square).then_inc(sq_done.sem, 1)
            act.wait_ge(order.sem, order(4))
            nc.scalar.activation(rstd[:], rstd[:], ACT.Sqrt).then_inc(rstd_done.sem, 1)
            if mode == "modulate":
                for c in range(DC):
                    act.wait_ge(t_done.sem, t_done(c // 4 + 1))
                    nc.scalar.activation(buf[:, c, :], buf[:, c, :], ACT.Identity, bias=shift[:, c:c + 1],
                                         scale=K.gain[:, c:c + 1]).then_inc(val_done.sem, 1)
                    act.wait_ge(val_done.sem, val_done(c + 1))
                    nc.scalar.activation(split[0][:, c, :], buf[:, c, :], ACT.Copy).then_inc(hi_done.sem, 1)

        @block.tensor
        def _(pe):
            for c in range(DC):
                pe.wait_ge(sq_done.sem, sq_done(c // 2 + 1))
                last = nc.tensor.matmul(total[:], K.ones, buf[:, c, :], start=c == 0, stop=c == DC - 1)
            last.then_inc(sum_done.sem, 1)

        @block.vector
        def _(dve):
            link = Chain(dve, order)
            if mode == "modulate":
                link(nc.vector.scalar_tensor_tensor(K.gain[:], scale, 1.0, gain, ALU.add, ALU.mult))
                link(nc.vector.tensor_scalar(K.coef[:], gate, 1.0, half, ALU.add, ALU.mult))
            elif mode == "add":
                link(nc.vector.tensor_tensor(K.gain[:], gain, gate, ALU.mult))
                link(nc.vector.tensor_copy(K.coef[:], gate))
            else:
                link(nc.vector.tensor_copy(K.gain[:], gain))
                link(nc.vector.tensor_copy(K.coef[:], gain))
            dve.wait_ge(sum_done.sem, sum_done(1))
            link(nc.vector.tensor_scalar(rstd[:], total[:], 1.0 / D, EPS, ALU.mult, ALU.add))
            link(nc.vector.reciprocal(rstd[:], rstd[:]))
            dve.wait_ge(rstd_done.sem, rstd_done(1))
            for c in range(0, DC, 4):
                nc.vector.tensor_tensor(buf[:, c:c + 4, :], src[:, c:c + 4, :],
                                        rstd[:, None, :].to_broadcast([P, 4, S]), ALU.mult).then_inc(t_done.sem, 1)
            if mode == "modulate":
                for c in range(DC):
                    dve.wait_ge(hi_done.sem, hi_done(c + 1))
                    nc.vector.tensor_tensor(split[1][:, c, :], buf[:, c, :], split[0][:, c, :].bitcast(F32), ALU.subtract)
            else:
                for c in range(DC):
                    dve.wait_ge(t_done.sem, t_done(c // 4 + 1))
                    if mode == "plain":
                        nc.vector.tensor_scalar(src[:, c, :], buf[:, c, :], K.gain[:, c:c + 1], None, ALU.mult)
                    else:
                        nc.vector.scalar_tensor_tensor(K.x[:, c, :], buf[:, c, :], K.gain[:, c:c + 1], K.x[:, c, :],
                                                       ALU.mult, ALU.add)
    for c, n in zip(K.norm_counts, (DC // 2, 1, 4, 1) + ((DC, DC) if mode == "modulate" else (0, 0)) + (DC // 4,)):
        c.base += n


def swiglu(K, name, w_gu, w_down, nxt):
    nc = K.nc
    sil_done, guhi_done = K.silu_done, K.gu_hi_done
    gu_hi = K.at(f"{name}_gu_hi", [P, FC, S], F32R, K.arena)
    gu_lo = K.at(f"{name}_gu_lo", [P, FC, S], F32R, K.arena + FC * S * 4)
    sil = K.at(f"{name}_sil_t", [P, 2, S], F32, K.arena + 2 * FC * S * 4)
    prod = K.at(f"{name}_prod_t", [P, 2, S], F32, K.arena + 2 * FC * S * 4 + 2 * S * 4)
    done = K.prod_done

    def mm(k, j):
        return K.h_hi[:, k, :], K.h_lo[:, k, :], j, k == 0, k == DC - 1

    def pe_wait(pe, i, j, t):
        if j % 2 == 0:
            pe.wait_ge(done.sem, done(2 * i + j // 2 - 1))

    def act_evac(act, i, j, t, mm_done):
        f = 2 * i + j // 2
        if j % 2 == 0:
            act.wait_ge(K.tile_mm.sem, mm_done)
            act.wait_ge(done.sem, done(f - 1))
            nc.scalar.activation(sil[:, j // 2, :], K.ps[j][:], ACT.Silu).then_inc(sil_done.sem, 1)
        else:
            act.wait_ge(done.sem, done(f + 1))
            nc.scalar.activation(gu_hi[:, bass.ds(f, 1), :], prod[:, j // 2:j // 2 + 1, :], ACT.Copy).then_inc(guhi_done.sem, 1)

    def dve_evac(dve, i, j, t, mm_done):
        f = 2 * i + j // 2
        if j % 2 == 1:
            dve.wait_ge(K.tile_mm.sem, mm_done)
            dve.wait_ge(sil_done.sem, sil_done(f + 1))
            nc.vector.tensor_tensor(prod[:, j // 2, :], sil[:, j // 2, :], K.ps[j][:], ALU.mult).then_inc(done.sem, 1)
            dve.wait_ge(guhi_done.sem, guhi_done(f + 1))
            nc.vector.tensor_tensor(gu_lo[:, bass.ds(f, 1), :], prod[:, j // 2:j // 2 + 1, :],
                                    gu_hi[:, bass.ds(f, 1), :].bitcast(F32), ALU.subtract)

    gemm(K, w_gu, DC, 2 * FC, (w_down, KB_MAX), mm, pe_wait, act_evac, dve_evac)
    for c in (done, sil_done, guhi_done):
        c.base += FC

    def mm2(k, j):
        kc = (j % 2) * KB_MAX + k
        return gu_hi[:, kc, :], gu_lo[:, kc, :], j // 2, kc == 0, kc == FC - 1

    project(K, w_down, KB_MAX, 2, mm2, nxt, lambda o: (K.coef[:, bass.ds(o, 1)]))


def project(K, w, kb, tpo, mm, nxt, coef, turn=4):
    nc = K.nc
    banks = turn // tpo
    free = K.bank_free

    def pe_wait(pe, i, j, t):
        if j % tpo == 0:
            pe.wait_ge(free.sem, free(banks * i + j // tpo - banks + 1))

    def dve_evac(dve, i, j, t, mm_done):
        if j % tpo == tpo - 1:
            o = banks * i + j // tpo
            dve.wait_ge(K.tile_mm.sem, mm_done)
            nc.vector.scalar_tensor_tensor(K.x[:, bass.ds(o, 1), :], K.ps[j // tpo][:, None, :], coef(o), K.x[:, bass.ds(o, 1), :],
                                           ALU.mult, ALU.add).then_inc(free.sem, 1)

    gemm(K, w, kb, DC * tpo, nxt, mm, pe_wait, None, dve_evac, turn=turn)
    free.base += DC


def conv_evacs(K, raw, dst, dst0, o0, weights, bias, n_all, ring=True):
    nc, free = K.nc, K.bank_free
    steps = K.conv_step
    wa, ba = K.cols_at[weights][0], K.cols_at[bias][0]

    def act_evac(act, i, j, t, mm_done):
        act.wait_ge(K.tile_mm.sem, mm_done)
        o = j % 2
        if ring:
            act.wait_ge(steps.sem, steps(CONV * (4 * i + j - 1)))
        else:
            o = t
        nc.scalar.activation(raw[:, bass.ds(o, 1), CONV - 1:], K.ps[j][:, None, :], ACT.Copy).then_inc(free.sem, 1)

    def dve_evac(dve, i, j, t, mm_done):
        o = 4 * i + j
        dve.wait_ge(free.sem, free(o + 1))
        y = dst[:, bass.ds(dst0 + o, 1), :]
        for tap in range(CONV):
            src = raw[:, bass.ds(j % 2 if ring else o, 1), tap:tap + S]
            w = K.cols[:, bass.ds(wa + tap * n_all + o0 + o, 1)]
            if tap == 0:
                ins = nc.vector.tensor_scalar(y, src, w, K.cols[:, bass.ds(ba + o0 + o, 1)], ALU.mult, ALU.add)
            else:
                dve.wait_ge(steps.sem, steps(CONV * o + tap))
                ins = nc.vector.scalar_tensor_tensor(y, src, w, y, ALU.mult, ALU.add)
            ins.then_inc(steps.sem, 1)

    return act_evac, dve_evac


def stream_out(K, w, n, nxt, act_evac, dve_evac=None, pre=None):
    free = K.bank_free

    def mm(k, j):
        return K.h_hi[:, k, :], K.h_lo[:, k, :], j, k == 0, k == DC - 1

    def pe_wait(pe, i, j, t):
        pe.wait_ge(free.sem, free(t - RING + 1))

    gemm(K, w, DC, n, nxt, mm, pe_wait, act_evac, dve_evac, pre=pre)
    free.base += n


def act_out(K, dst, dst0, func):
    def act_evac(act, i, j, t, mm_done):
        act.wait_ge(K.tile_mm.sem, mm_done)
        K.nc.scalar.activation(dst[:, bass.ds(dst0 + t, 1), :], K.ps[j][:, None, :], func).then_inc(K.bank_free.sem, 1)
    return act_evac


LOG1P_TERMS = 8
NEG = -1e30


def softplus_steps(nc, link, z, out, e, q, exp_of):
    v = nc.vector
    link(v.tensor_scalar(q, z, -1.0, None, ALU.mult))
    link(v.tensor_tensor(e, z, q, ALU.max))
    exp_of()
    link(v.tensor_scalar(q, e, 2.0, None, ALU.add))
    link(v.reciprocal(q, q))
    link(v.tensor_tensor(e, e, q, ALU.mult))
    link(v.tensor_tensor(q, e, e, ALU.mult))
    link(v.tensor_scalar(out, q, 1.0 / (2 * LOG1P_TERMS - 1), None, ALU.mult))
    for n in range(LOG1P_TERMS - 2, 0, -1):
        link(v.scalar_tensor_tensor(out, out, 1.0 / (2 * n + 1), q, ALU.add, ALU.mult))
    link(v.scalar_tensor_tensor(out, out, 1.0, e, ALU.add, ALU.mult))
    link(v.tensor_scalar(q, z, 0.0, None, ALU.max))
    link(v.scalar_tensor_tensor(out, out, 2.0, q, ALU.mult, ALU.add))


def hybrid(K, nxt):
    nc, d = K.nc, K.dram
    A = K.arena
    proj = K.at("proj", [P, HYB, S], F32, A)
    B = A + HYB * S * 4
    raw = K.at("conv_raw", [P, 2, S + CONV - 1], F32, B + 20 * 1024)
    w_dt = K.at("w_dt", [P, DC, SSD_H], F32, B + 26 * 1024)
    wax = K.at("lru_wax", [P, 2, 2 * P], F32, B + 27 * 1024)
    dt_raw = K.at("dt_raw", [SSD_H, S], F32, B + 30 * 1024)
    small = K.sem("hyb_small_loaded")
    wax_loaded = [K.sem(f"lru_wax_loaded{i}") for i in range(2)]
    pad_done = K.sem("conv_pad_zeroed")
    dt_mm = K.sem("dt_mm")
    XB, GATE, Z = DC, DC + XBC, DC + XBC + DC

    with nc.Block() as block:
        @block.sync
        def _(sp):
            sp.dma_start(w_dt[:], d["w_dt"]).then_inc(small, 16)
            for j in range(2):
                sp.dma_start(wax[:, j, :], d["lru_wax"][j]).then_inc(wax_loaded[j], 16)
            sp.wait_ge(small, 16)

        @block.vector
        def _(dve):
            nc.vector.memset(raw[:, :, 0:CONV - 1], 0.0).then_inc(pad_done, 1)

    def dt_product(pe):
        for k in range(2 * DC):
            h = (K.h_hi, K.h_lo)[k // DC]
            last = nc.tensor.matmul(K.ps[7][0:SSD_H, :], w_dt[:, k % DC, :], h[:, k % DC, :].bitcast(F32),
                                    start=k == 0, stop=k == 2 * DC - 1)
        last.then_inc(dt_mm, 1)

    ae, de = conv_evacs(K, raw, proj, 0, 0, "hyb_conv_w", "hyb_conv_b", DC + XBC)
    stream_out(K, d["w_hyb"][0:DC], DC, (d["w_hyb"][XB:GATE], DC), ae, de, pre=dt_product)
    K.conv_step.base += CONV * DC
    ae, de = conv_evacs(K, raw, proj, XB, XB, "hyb_conv_w", "hyb_conv_b", DC + XBC)
    stream_out(K, d["w_hyb"][XB:GATE], XBC, (d["w_hyb"][GATE:Z], DC), ae, de)
    K.conv_step.base += CONV * XBC
    stream_out(K, d["w_hyb"][GATE:Z], DC, (d["w_hyb"][Z:HYB], DC), act_out(K, proj, GATE, ACT.Gelu_apprx_tanh))
    stream_out(K, d["w_hyb"][Z:HYB], DC, (d["w_hout"], DC), act_out(K, proj, Z, ACT.Silu))
    lru(K, proj, GATE, wax, wax_loaded, dt_raw, dt_mm)
    ssd(K, proj, XB, Z, B, dt_raw)
    hybrid_out(K, proj, GATE, nxt)


def lru(K, proj, GATE, wax, wax_loaded, dt_raw, dt_mm):
    nc, d = K.nc, K.dram
    B = K.arena + HYB * S * 4
    r_all = K.at("lru_r", [P, DC, S], F32, B)
    ix = K.at("lru_ix", [P, DC, S], F32, K.h_at)
    m2 = K.at("lru_m2", [P, DC, S], F32, K.h_at + DC * S * 4)
    i_t = K.at("lru_i", [P, 2, S], F32, B + DC * S * 4)
    lam = K.at("lru_lam", [P, 4, DC], F32, B + 25 * 1024)
    mm_done, sig_done, ix_done = K.count("lru_mm"), K.count("lru_sig"), K.sem("lru_ix_done")
    lam_order, lam_abs, lam_exp = K.count("lru_lam_order"), K.sem("lru_lam_abs"), K.sem("lru_lam_exp")
    a_done, q_done, root_done, u_done, h_done = (K.sem(f"lru_{n}") for n in ("a", "q", "root", "u", "h"))
    dt_out = K.sem("dt_out")
    la = K.cols_at["lru_lambda"][0]
    ba, bx = K.cols_at["lru_ba"][0], K.cols_at["lru_bx"][0]
    z, e, q, out = (lam[:, k, :] for k in range(4))
    with nc.Block() as block:
        @block.sync
        def _(sp):
            with sp.Fori(0, DC // 2 - 1) as i:
                for j in range(2):
                    sp.wait_ge(mm_done.sem, 2 * i + j + 1)
                    sp.dma_start(wax[:, j:j + 1, :], d["lru_wax"][bass.ds(2 * i + j + 2, 1)].rearrange("o p n -> p o n")).then_inc(wax_loaded[j], 16)

        @block.tensor
        def _(pe):
            def head(i, j, first):
                pe.wait_ge(wax_loaded[j], 16 * i + 16)
                if not first:
                    pe.wait_ge(sig_done.sem, 4 * i + 2 * j - 2)
                c = 2 * i + j
                nc.tensor.matmul(K.ps[2 * j][:], wax[:, j, 0:P], proj[:, bass.ds(c, 1), :], start=True, stop=True)
                nc.tensor.matmul(K.ps[2 * j + 1][:], wax[:, j, P:2 * P], proj[:, bass.ds(c, 1), :], start=True, stop=True).then_inc(mm_done.sem, 1)
            for j in range(2):
                head(0, j, True)
            with pe.Fori(1, DC // 2) as i:
                for j in range(2):
                    head(i, j, False)

        @block.scalar
        def _(act):
            act.wait_ge(dt_mm, 1)
            nc.scalar.activation(dt_raw[:], K.ps[7][0:SSD_H, :], ACT.Copy).then_inc(dt_out, 1)
            act.wait_ge(lam_abs, 1)
            nc.scalar.activation(e, e, ACT.Exp, scale=-1.0).then_inc(lam_exp, 1)

            def head(i, j, first):
                c = 2 * i + j
                act.wait_ge(mm_done.sem, c + 1)
                nc.scalar.activation(r_all[:, bass.ds(c, 1), :], K.ps[2 * j][:, None, :], ACT.Sigmoid, bias=K.cols[:, bass.ds(ba + c, 1)]).then_inc(sig_done.sem, 1)
                if not first:
                    act.wait_ge(ix_done, c - 1)
                nc.scalar.activation(i_t[:, j, :], K.ps[2 * j + 1][:], ACT.Sigmoid, bias=K.cols[:, bass.ds(bx + c, 1)]).then_inc(sig_done.sem, 1)
            for j in range(2):
                head(0, j, True)
            with act.Fori(1, DC // 2) as i:
                for j in range(2):
                    head(i, j, False)
            act.wait_ge(lam_order.sem, LRU_LAM_STEPS)
            act.wait_ge(ix_done, DC)
            with act.Fori(0, DC) as c:
                nc.scalar.activation(proj[:, bass.ds(c, 1), :], r_all[:, bass.ds(c, 1), :], ACT.Exp, scale=lam[:, 3, bass.ds(c, 1)]).then_inc(a_done, 1)
                nc.scalar.activation(m2[:, bass.ds(c, 1), :], r_all[:, bass.ds(c, 1), :], ACT.Tanh, scale=lam[:, 3, bass.ds(c, 1)]).then_inc(a_done, 1)
            act.wait_ge(q_done, 2)
            nc.scalar.activation(m2[:], m2[:], ACT.Sqrt, scale=-1.0).then_inc(root_done, 1)

        @block.vector
        def _(dve):
            link = Chain(dve, lam_order)

            def exp_of():
                nc.vector.tensor_copy(q, e).then_inc(lam_abs, 1)
                dve.wait_ge(lam_exp, 1)
            link(nc.vector.tensor_scalar(z, K.cols[:, la:la + DC], -1.0, None, ALU.mult))
            softplus_steps(nc, link, z, out, e, q, exp_of)
            link(nc.vector.tensor_scalar(out, out, -8.0, None, ALU.mult))
            assert link.n == LRU_LAM_STEPS, link.n
            with dve.Fori(0, DC // 2) as i:
                for j in range(2):
                    c = 2 * i + j
                    dve.wait_ge(sig_done.sem, 4 * i + 2 * j + 2)
                    nc.vector.tensor_tensor(ix[:, bass.ds(c, 1), :], i_t[:, j:j + 1, :], proj[:, bass.ds(c, 1), :], ALU.mult).then_inc(ix_done, 1)
            dve.wait_ge(a_done, 2 * DC)
            nc.vector.tensor_tensor(r_all[:], proj[:, 0:DC, :], proj[:, 0:DC, :], ALU.mult).then_inc(q_done, 1)
            dve.wait_ge(q_done, 1)
            nc.vector.scalar_tensor_tensor(m2[:], r_all[:], 1.0, m2[:], ALU.add, ALU.mult).then_inc(q_done, 1)
            dve.wait_ge(root_done, 1)
            nc.vector.tensor_tensor(ix[:], ix[:], m2[:], ALU.mult).then_inc(u_done, 1)
            dve.wait_ge(u_done, 1)
            for c in range(DC):
                nc.vector.tensor_tensor_scan(r_all[:, c, :], proj[:, c, :], ix[:, c, :], 0.0, ALU.mult, ALU.add).then_inc(h_done, 1)
            dve.wait_ge(h_done, DC)
            nc.vector.tensor_tensor(proj[:, GATE:GATE + DC, :], proj[:, GATE:GATE + DC, :], r_all[:], ALU.mult)


LRU_LAM_STEPS = 10 + LOG1P_TERMS


def ssd(K, proj, XB, Z, B, dt_raw):
    nc, d = K.nc, K.dram
    H16 = SSD_H
    off = [B, K.h_at]

    def sb(name, shape, where=0):
        t = K.at("ssd_" + name, shape, F32, off[where])
        off[where] += (int(np.prod(shape[1:])) * 4 + 31) // 32 * 32
        return t
    acs, wst = sb("acs", [H16, S]), sb("wst", [H16, S], 1)
    toks = sb("toks", [P, 3, NT, H16])
    edec = sb("edec", [P, NT, H16])
    b_tok, cbm = sb("b_tok", [P, SSD_G, S]), sb("cbm", [P, SSD_G, S])
    xs, xdt, xw = sb("xs", [P, S]), sb("xdt", [P, NT, P]), sb("xw", [P, NT, P])
    rows = sb("rows", [H16, 2, S])
    arg, eb = sb("arg", [P, 2, S]), sb("eb", [P, 2, S], 1)
    state = sb("state", [P, NT - 1, P], 1)
    dt = sb("dt", [H16, S], 1)
    e, q, z = sb("e", [H16, S], 1), sb("q", [H16, S], 1), sb("z", [H16, S], 1)
    diag = sb("diag", [H16, NT, H16], 1)
    aneg = sb("aneg", [H16, 1], 1)
    assert off[0] <= B + 30 * 1024 and off[1] <= K.h_at + 32 * 1024
    CSTEP = S // NT
    order = K.count("ssd_order")
    abs_done, exp_done, silu_done, tr_done, cb_done, prep_done, wexp_done, wdone, diag_done = (
        K.sem(f"ssd_{n}") for n in ("abs", "exp", "silu", "tr", "cb", "prep", "wexp", "w", "diag"))
    dtb, alog = (K.cols[0:H16, K.cols_at[n][0]:K.cols_at[n][0] + 1] for n in ("ssd_dt_bias", "ssd_a_log"))

    rows_done, bc_mm, arg_done, eb_done, e_done, m_done, cd_done, xs_done, xt_done, xdt_done, st_mm, st_done, y_mm, y_done, z_done = (
        K.count(f"ssd_{n}") for n in ("rows", "bc", "arg", "eb", "decay", "m", "cd", "xs", "xt", "xdt", "st_mm", "state", "y_mm", "y", "z"))
    def tile(t, c):
        return t[:, c * CSTEP:(c + 1) * CSTEP]

    with nc.Block() as block:
        @block.scalar
        def _(act):
            nc.scalar.activation(proj[:, XB:XB + XBC, :], proj[:, XB:XB + XBC, :], ACT.Silu).then_inc(silu_done, 1)
            nc.scalar.activation(aneg[:], alog, ACT.Exp).then_inc(exp_done, 1)
            act.wait_ge(abs_done, 1)
            nc.scalar.activation(e[:], e[:], ACT.Exp, scale=-1.0).then_inc(exp_done, 1)
            act.wait_ge(wdone, 1)
            nc.scalar.activation(wst[:], wst[:], ACT.Exp, scale=-1.0).then_inc(wexp_done, 1)
            act.wait_ge(cb_done, 2)
            nc.scalar.activation(edec[:], K.ps[5][:, 0:NT * H16].rearrange("p (c h) -> p c h", c=NT), ACT.Exp).then_inc(prep_done, 1)

        @block.vector
        def _(dve):
            v = nc.vector
            link = Chain(dve, order)

            def exp_of():
                v.tensor_copy(q[:], e[:]).then_inc(abs_done, 1)
                dve.wait_ge(exp_done, 2)
            link(v.tensor_scalar(z[:], dt_raw[:], dtb, None, ALU.add))
            softplus_steps(nc, link, z[:], dt[:], e[:], q[:], exp_of)
            link(v.tensor_scalar(aneg[:], aneg[:], -1.0, None, ALU.mult))
            link(v.tensor_scalar(z[:], dt[:], aneg[:, 0:1], None, ALU.mult))
            for c in range(NT):
                ins = v.tensor_tensor_scan(tile(acs, c), K.ones[0:H16, :], tile(z, c), 0.0, ALU.mult, ALU.add)
            link(ins)
            for c in range(NT):
                end = acs[:, (c + 1) * CSTEP - 1:(c + 1) * CSTEP]
                v.tensor_scalar(diag[:, c, :], K.ident[0:H16, 0:H16], end, None, ALU.mult)
                ins = v.tensor_scalar(tile(wst, c), tile(acs, c), end, None, ALU.subtract)
            ins.then_inc(wdone, 1)
            dve.wait_ge(wexp_done, 1)
            v.tensor_tensor(wst[:], wst[:], dt[:], ALU.mult).then_inc(wdone, 1)
            dve.wait_ge(tr_done, 1)
            v.tensor_copy(toks[:], K.ps[0][:, 0:3 * NT * H16].rearrange("p (k c h) -> p k c h", k=3, c=NT))
            dve.wait_ge(cb_done, 1)
            for g in range(SSD_G):
                v.tensor_copy(b_tok[:, g, :], K.ps[1 + g][:])
                ins = v.tensor_tensor(cbm[:, g, :].rearrange("p (c l) -> p c l", c=NT), K.ps[3 + g][:].rearrange("p (c l) -> p c l", c=NT),
                                      K.causal[:, None, :].to_broadcast([P, NT, P]), ALU.mult)
            ins.then_inc(y_done.sem, 1)

        @block.tensor
        def _(pe):
            pe.wait_ge(silu_done, 1)
            for g in range(SSD_G):
                bt, ct = proj[:, XB + DC + g, :], proj[:, XB + DC + SSD_G + g, :]
                for c in range(NT):
                    nc.tensor.transpose(K.ps[1 + g][:, c * P:(c + 1) * P], tile(bt, c), K.ident)
                    last = nc.tensor.matmul(K.ps[3 + g][:, c * P:(c + 1) * P], tile(bt, c), tile(ct, c), start=True, stop=True)
            last.then_inc(cb_done, 1)
            pe.wait_ge(wdone, 2)
            for k, t in enumerate((acs, dt, wst)):
                for c in range(NT):
                    last = nc.tensor.transpose(K.ps[0][:, (k * NT + c) * H16:(k * NT + c + 1) * H16], tile(t, c), K.ident[0:H16, 0:H16])
            last.then_inc(tr_done, 1)
            nc.tensor.matmul(K.ps[5][:, 0:NT * H16], K.ones[0:H16, :], diag[:], start=True, stop=True).then_inc(cb_done, 1)

    dcol = K.cols_at["ssd_d"][0]
    toks_v = toks[:]
    for g in range(SSD_G):
        n0 = g * SSD_PAIRS
        ct = proj[:, XB + DC + SSD_G + g, :]
        with nc.Block() as block:
            @block.gpsimd
            def _(pool):
                with pool.Fori(0, SSD_PAIRS) as i:
                    pool.wait_ge(y_done.sem, i + n0 + 1)
                    nc.gpsimd.tensor_copy(xs[:, None, :], proj[:, bass.ds(XB + n0 + i, 1), :]).then_inc(xs_done.sem, 1)

            @block.tensor
            def _(pe):
                with pe.Fori(0, SSD_PAIRS) as i:
                    pe.wait_ge(rows_done.sem, 2 * (i + n0) + 2)
                    for hd in range(2):
                        last = nc.tensor.matmul(K.ps[hd][:], K.ones[0:H16, :], rows[:, hd, :], start=True, stop=True)
                    last.then_inc(bc_mm.sem, 1)
                    pe.wait_ge(xs_done.sem, i + n0 + 1)
                    for c in range(NT):
                        last = nc.tensor.transpose(K.ps[2][:, c * P:(c + 1) * P], tile(xs, c), K.ident)
                    last.then_inc(xt_done.sem, 1)
                    pe.wait_ge(xdt_done.sem, 2 * (i + n0) + 2)
                    for c in range(NT - 1):
                        last = nc.tensor.matmul(K.ps[4][:, c * P:(c + 1) * P], tile(b_tok[:, g, :], c), xw[:, c, :], start=True, stop=True)
                    last.then_inc(st_mm.sem, 1)
                    pe.wait_ge(m_done.sem, i + n0 + 1)
                    pe.wait_ge(cd_done.sem, i + n0 + 1)
                    pe.wait_ge(st_done.sem, (1 + 2 * (NT - 2)) * (i + n0 + 1))
                    for hd in range(2):
                        lo, hi = hd * SSD_P, (hd + 1) * SSD_P
                        for c in range(NT):
                            dst = K.ps[3][lo:hi, c * P:(c + 1) * P]
                            last = nc.tensor.matmul(dst, xdt[:, c, lo:hi], tile(arg[:, hd, :], c), start=True, stop=c == 0)
                            if c:
                                last = nc.tensor.matmul(dst, state[:, c - 1, lo:hi], tile(eb[:, hd, :], c), start=False, stop=True)
                    last.then_inc(y_mm.sem, 1)

            @block.scalar
            def _(act):
                with act.Fori(0, SSD_PAIRS) as i:
                    act.wait_ge(bc_mm.sem, i + n0 + 1)
                    act.wait_ge(y_done.sem, i + n0 + 1)
                    for hd in range(2):
                        nc.scalar.activation(eb[:, hd, :], K.ps[hd][:], ACT.Exp).then_inc(eb_done.sem, 1)
                    act.wait_ge(arg_done.sem, 2 * NT * (i + n0) + 2 * NT)
                    nc.scalar.activation(arg[:], arg[:], ACT.Exp).then_inc(e_done.sem, 1)

            @block.vector
            def _(dve):
                v = nc.vector
                with dve.Fori(0, SSD_PAIRS) as i:
                    h0 = 8 * g + 2 * i
                    for hd in range(2):
                        v.tensor_scalar(rows[:, hd, :], acs[:], K.consts[0:H16, bass.ds(h0 + hd, 1)], None, ALU.mult).then_inc(rows_done.sem, 1)
                    dve.wait_ge(eb_done.sem, 2 * (i + n0) + 2)
                    for hd in range(2):
                        for c in range(NT):
                            v.tensor_scalar(tile(arg[:, hd, :], c), tile(K.ps[hd], c), toks[:, 0, c, bass.ds(h0 + hd, 1)], 0.0,
                                            ALU.subtract, ALU.min).then_inc(arg_done.sem, 1)
                    dve.wait_ge(xt_done.sem, i + n0 + 1)
                    for k, t in ((1, xdt), (2, xw)):
                        v.tensor_tensor(t[:].rearrange("p c (h w) -> p c h w", h=2), K.ps[2][:].rearrange("p (c h w) -> p c h w", c=NT, h=2),
                                        toks_v[:, k, :, bass.ds(h0, 2)][:, :, :, None].to_broadcast([P, NT, 2, SSD_P]), ALU.mult).then_inc(xdt_done.sem, 1)
                    dve.wait_ge(st_mm.sem, i + n0 + 1)
                    per = 1 + 2 * (NT - 2)
                    v.tensor_copy(state[:, 0, :], K.ps[4][:, 0:P]).then_inc(st_done.sem, 1)
                    for c in range(1, NT - 1):
                        dve.wait_ge(st_done.sem, per * (i + n0) + 1 + 2 * (c - 1))
                        for hd in range(2):
                            lo, hi = hd * SSD_P, (hd + 1) * SSD_P
                            v.scalar_tensor_tensor(state[:, c, lo:hi], state[:, c - 1, lo:hi], edec[:, c, bass.ds(h0 + hd, 1)],
                                                   K.ps[4][:, c * P + lo:c * P + hi], ALU.mult, ALU.add).then_inc(st_done.sem, 1)
                    dve.wait_ge(e_done.sem, i + n0 + 1)
                    v.tensor_tensor(arg[:], arg[:], cbm[:, g:g + 1, :].to_broadcast([P, 2, S]), ALU.mult).then_inc(m_done.sem, 1)
                    v.tensor_tensor(eb[:], eb[:], ct[:, None, :].to_broadcast([P, 2, S]), ALU.mult).then_inc(cd_done.sem, 1)
                    dve.wait_ge(y_mm.sem, i + n0 + 1)
                    v.scalar_tensor_tensor(xdt[:].rearrange("p c w -> p (c w)"), xs[:], K.cols[:, bass.ds(dcol + n0 + i, 1)], K.ps[3][:], ALU.mult, ALU.add).then_inc(z_done.sem, 1)
                    dve.wait_ge(z_done.sem, i + n0 + 1)
                    zc = proj[:, bass.ds(Z + n0 + i, 1), :]
                    v.tensor_tensor(zc, zc, xdt[:].rearrange("p c w -> p (c w)")[:, None, :], ALU.mult).then_inc(y_done.sem, 1)


def hybrid_out(K, proj, GATE, nxt):
    nc = K.nc
    n = 2 * DC
    hi = K.at("hyb_hi", [P, n, S], F32R, K.h_at)
    lo = K.at("hyb_lo", [P, n, S], F32R, K.arena)
    B = K.arena + HYB * S * 4
    sq = K.at("hyb_sq", [P, DC, S], F32, B)
    rstd = K.at("hyb_rstd", [P, SSD_G, S], F32, B + DC * S * 4)
    sq_done, sum_done, r_done, root_done, v_done, hi_done = (K.sem(f"hyb_{k}") for k in ("sq", "sum", "r", "root", "v", "hi"))
    per = DC // SSD_G
    ng = K.cols_at["ssd_norm_g"][0]
    with nc.Block() as block:
        @block.scalar
        def _(act):
            for g in range(SSD_G):
                nc.scalar.activation(sq[:, per * g:per * (g + 1), :], proj[:, GATE + DC + per * g:GATE + DC + per * (g + 1), :], ACT.Square).then_inc(sq_done, 1)
            with act.Fori(0, DC) as c:
                nc.scalar.activation(hi[:, bass.ds(c, 1), :], proj[:, bass.ds(GATE + c, 1), :], ACT.Copy).then_inc(hi_done, 1)
            act.wait_ge(r_done, 4)
            nc.scalar.activation(rstd[:], rstd[:], ACT.Sqrt).then_inc(root_done, 1)
            with act.Fori(0, DC) as c:
                act.wait_ge(v_done, c + 1)
                nc.scalar.activation(hi[:, bass.ds(DC + c, 1), :], proj[:, bass.ds(GATE + DC + c, 1), :], ACT.Copy).then_inc(hi_done, 1)

        @block.tensor
        def _(pe):
            for g in range(SSD_G):
                pe.wait_ge(sq_done, g + 1)
                for c in range(per):
                    last = nc.tensor.matmul(K.ps[g][:], K.ones, sq[:, per * g + c, :], start=c == 0, stop=c == per - 1)
                last.then_inc(sum_done, 1)

        @block.vector
        def _(dve):
            v = nc.vector

            def low(c):
                v.tensor_tensor(lo[:, bass.ds(c, 1), :], proj[:, bass.ds(GATE + c, 1), :], hi[:, bass.ds(c, 1), :].bitcast(F32), ALU.subtract)
            for g in range(SSD_G):
                dve.wait_ge(sum_done, g + 1)
                v.tensor_scalar(rstd[:, g, :], K.ps[g][:], 1.0 / (per * P), EPS, ALU.mult, ALU.add).then_inc(r_done, 1)
            dve.wait_ge(r_done, 2)
            for g in range(SSD_G):
                v.reciprocal(rstd[:, g, :], rstd[:, g, :]).then_inc(r_done, 1)
            with dve.Fori(0, DC) as c:
                dve.wait_ge(hi_done, c + 1)
                low(c)
            dve.wait_ge(root_done, 1)
            for g in range(SSD_G):
                with dve.Fori(per * g, per * (g + 1)) as c:
                    y = proj[:, bass.ds(GATE + DC + c, 1), :]
                    v.scalar_tensor_tensor(y, y, K.cols[:, bass.ds(ng + c, 1)], rstd[:, g:g + 1, :], ALU.mult, ALU.mult).then_inc(v_done, 1)
            with dve.Fori(0, DC) as c:
                dve.wait_ge(hi_done, DC + 1 + c)
                low(c + DC)

    def mm(k, j):
        kc = (j % 2) * DC + k
        return hi[:, kc, :], lo[:, kc, :], j // 2, kc == 0, kc == n - 1

    project(K, K.dram["w_hout"], DC, 2, mm, nxt, lambda o: K.coef[:, bass.ds(o, 1)])


def mlstm(K, nxt):
    nc, d = K.nc, K.dram
    A = K.arena
    PAD = S + CONV - 1
    xm = K.at("ml_xm", [P, MLC, PAD], F32, A)
    xc = K.at("ml_xc", [P, MLC, S], F32, A + MLC * PAD * 4)
    B = A + MLC * (PAD + S) * 4
    at = [B]

    def sb(name, shape):
        t = K.at("ml_" + name, shape, F32, at[0])
        at[0] += (int(np.prod(shape[1:])) * 4 + 31) // 32 * 32
        return t
    r_row, m_row = sb("r_row", [ML_H, S]), sb("m_row", [ML_H, S])
    ccol = sb("ccol", [P, NT, ML_H])
    sel = sb("sel", [P, S])
    bd = sb("bd", [P, HC, 3 * P])
    mix = at[0]
    q, k, v, e = (sb(n, [P, HC, S]) for n in "qkve")
    pad_done = K.sem("ml_pad_zeroed")

    with nc.Block() as block:
        @block.vector
        def _(dve):
            nc.vector.memset(xm[:, :, 0:CONV - 1], 0.0).then_inc(pad_done, 1)

    ae, de = conv_evacs(K, xm, xc, 0, 0, "ml_conv_w", "ml_conv_b", MLC, ring=False)
    stream_out(K, d["w_xm"], MLC, (d["w_z"], DC), ae, de)
    K.conv_step.base += CONV * MLC
    head_written = K.sem("mlh_y")
    ml_gates(K, xm, xc, r_row, m_row, ccol, mix, head_written)
    ml_heads(K, xm, xc, r_row, m_row, ccol, sel, bd, q, k, v, e, head_written)

    hi = K.at("ml_hi", [P, MLC, S], F32R, A + MLC * PAD * 4)
    lo = K.at("ml_lo", [P, MLC, S], F32R, B)
    sz = K.at("ml_sz", [P, 2, S], F32, B + MLC * S * 4)
    y_done, hi_done = K.count("ml_y"), K.sem("ml_hi_done")
    free = K.bank_free

    def act_evac(act, i, j, t, mm_done):
        act.wait_ge(K.tile_mm.sem, mm_done)
        nc.scalar.activation(sz[:, j % 2, :], K.ps[j][:], ACT.Silu).then_inc(free.sem, 1)
        act.wait_ge(y_done.sem, t + 1)
        nc.scalar.activation(hi[:, bass.ds(t, 1), :], xm[:, bass.ds(t, 1), CONV - 1:], ACT.Copy).then_inc(hi_done, 1)

    def dve_evac(dve, i, j, t, mm_done):
        y = xm[:, bass.ds(t, 1), CONV - 1:]
        dve.wait_ge(free.sem, free(t + 1))
        nc.vector.tensor_tensor(y, y, sz[:, j % 2:j % 2 + 1, :], ALU.mult).then_inc(y_done.sem, 1)
        dve.wait_ge(hi_done, t + 1)
        nc.vector.tensor_tensor(lo[:, bass.ds(t, 1), :], y, hi[:, bass.ds(t, 1), :].bitcast(F32), ALU.subtract)

    stream_out(K, d["w_z"], MLC, (d["w_mdown"], DC), act_evac, dve_evac)

    def mm(kk, j):
        kc = (j % 2) * DC + kk
        return hi[:, kc, :], lo[:, kc, :], j // 2, kc == 0, kc == MLC - 1

    project(K, d["w_mdown"], DC, 2, mm, nxt, lambda o: K.coef[:, bass.ds(o, 1)])


def ml_gates(K, xm, xc, r_row, m_row, ccol, base, head_written):
    nc, d = K.nc, K.dram
    at = [base]

    def sb(name, shape):
        t = K.at("mlg_" + name, shape, F32, at[0])
        at[0] += (int(np.prod(shape[1:])) * 4 + 31) // 32 * 32
        return t
    qkv = sb("qkv", [P, 2, 3, S])
    w = sb("w", [P, 2, 3 * P])
    wg = sb("wg", [P, 2, 6 * ML_F])
    acc = sb("acc", [2 * ML_F, S])
    i_pre, z, lf, e, t2, zero = (sb(n, [ML_H, S]) for n in ("i", "z", "lf", "e", "t2", "zero"))
    silu_done, w_loaded = K.sem("mlg_silu"), [K.sem(f"mlg_w{j}") for j in range(2)]
    qkv_mm, qkv_done, gate_mm, acc_done = (K.count(f"mlg_{n}") for n in ("qkv_mm", "qkv", "gate_mm", "acc"))
    order, abs_done, exp_done, m_done, tr_done = K.count("mlg_order"), K.sem("mlg_abs"), K.sem("mlg_exp"), K.sem("mlg_m"), K.sem("mlg_tr")
    bi, bf = (K.cols[0:ML_H, K.cols_at[n][0]:K.cols_at[n][0] + 1] for n in ("ml_bi", "ml_bf"))
    with nc.Block() as block:
        @block.sync
        def _(sp):
            def load(c, j):
                sp.dma_start(w[:, j:j + 1, :], d["w_qkv"][bass.ds(c, 1)].rearrange("o p n -> p o n")).then_inc(w_loaded[j], 16)
                sp.dma_start(wg[:, j:j + 1, :], d["w_gates"][bass.ds(c, 1)].rearrange("o p n -> p o n")).then_inc(w_loaded[j], 16)
            for j in range(2):
                load(j, j)
            with sp.Fori(0, MLC // 2 - 1) as i:
                for j in range(2):
                    sp.wait_ge(gate_mm.sem, 2 * i + j + 1)
                    load(2 * i + j + 2, j)

        @block.scalar
        def _(act):
            for c in range(0, MLC, HC):
                nc.scalar.activation(xc[:, c:c + HC, :], xc[:, c:c + HC, :], ACT.Silu).then_inc(silu_done, 1)
            with act.Fori(0, MLC // 2) as i:
                for j in range(2):
                    act.wait_ge(qkv_mm.sem, 2 * i + j + 1)
                    for n in range(3):
                        nc.scalar.activation(qkv[:, j, n, :], K.ps[3 * j + n][:], ACT.Copy).then_inc(qkv_done.sem, 1)
            act.wait_ge(abs_done, 1)
            nc.scalar.activation(e[:], e[:], ACT.Exp, scale=-1.0).then_inc(exp_done, 1)
            act.wait_ge(m_done, 1)
            nc.scalar.activation(m_row[:], m_row[:], ACT.Exp, scale=-1.0)

        @block.tensor
        def _(pe):
            pe.wait_ge(silu_done, ML_H)

            def body(i, first):
                for j in range(2):
                    pe.wait_ge(w_loaded[j], 32 * i + 32)
                    c = 2 * i + j
                    if not first:
                        pe.wait_ge(qkv_done.sem, 3 * (c - 1))
                    for n, src in enumerate((xc[:, bass.ds(c, 1), :], xc[:, bass.ds(c, 1), :], xm[:, bass.ds(c, 1), CONV - 1:])):
                        last = nc.tensor.matmul(K.ps[3 * j + n][:], w[:, j, n * P:(n + 1) * P], src, start=True, stop=True)
                    last.then_inc(qkv_mm.sem, 1)
                for j in range(2):
                    c = 2 * i + j
                    pe.wait_ge(qkv_done.sem, 3 * (c + 1))
                    if not first:
                        pe.wait_ge(acc_done.sem, c)
                    for n in range(3):
                        last = nc.tensor.matmul(K.ps[6 + j][0:2 * ML_F, :], wg[:, j, 2 * n * ML_F:2 * (n + 1) * ML_F], qkv[:, j, n, :], start=n == 0, stop=n == 2)
                    last.then_inc(gate_mm.sem, 1)
            body(0, True)
            with pe.Fori(1, MLC // 2) as i:
                body(i, False)
            pe.wait_ge(order.sem, ML_GATE_STEPS)
            for c in range(NT):
                last = nc.tensor.transpose(K.ps[0][:, c * ML_H:(c + 1) * ML_H], t2[:, c * P:(c + 1) * P], K.ident[0:ML_H, 0:ML_H])
            last.then_inc(tr_done, 1)

        @block.vector
        def _(dve):
            v = nc.vector
            link = Chain(dve, order)
            v.memset(acc[:], 0.0).then_inc(acc_done.sem, 1)
            with dve.Fori(0, MLC // 2) as i:
                for j in range(2):
                    c = 2 * i + j
                    dve.wait_ge(gate_mm.sem, c + 1)
                    dve.wait_ge(acc_done.sem, c + 1)
                    v.tensor_tensor(acc[:], acc[:], K.ps[6 + j][0:2 * ML_F, :], ALU.add).then_inc(acc_done.sem, 1)
            dve.wait_ge(acc_done.sem, MLC + 1)
            link(v.memset(zero[:], 0.0))
            link(v.tensor_scalar(i_pre[:], acc[0:ML_H, :], bi, None, ALU.add))
            link(v.tensor_copy(z[:], acc[ML_F:ML_F + ML_H, :]))
            link(v.tensor_scalar(z[:], z[:], bf, -1.0, ALU.add, ALU.mult))

            def exp_of():
                v.tensor_copy(t2[:], e[:]).then_inc(abs_done, 1)
                dve.wait_ge(exp_done, 1)
            softplus_steps(nc, link, z[:], lf[:], e[:], t2[:], exp_of)
            link(v.tensor_scalar(lf[:], lf[:], -1.0, None, ALU.mult))
            link(v.tensor_tensor_scan(z[:], lf[:], zero[:], 0.0, ALU.add, ALU.add))
            link(v.tensor_tensor_scan(m_row[:], lf[:], i_pre[:], 0.0, ALU.add, ALU.max))
            link(v.tensor_tensor(r_row[:], z[:], m_row[:], ALU.subtract))
            v.tensor_tensor(e[:], z[:], m_row[:], ALU.add).then_inc(m_done, 1)
            link(v.tensor_tensor(t2[:], z[:], i_pre[:], ALU.subtract))
            assert link.n == ML_GATE_STEPS, link.n
            dve.wait_ge(tr_done, 1)
            v.tensor_copy(ccol[:], K.ps[0][:, 0:NT * ML_H].rearrange("p (c h) -> p c h", c=NT)).then_inc(head_written, 1)


ML_GATE_STEPS = 17 + LOG1P_TERMS


def ml_heads(K, xm, xc, r_row, m_row, ccol, sel, bd, q, k, v, e, head_written):
    nc, d = K.nc, K.dram
    names = ("bd_free", "xs", "q_mm", "k_mm", "q", "k", "v_mm", "v", "sel", "bc", "arg", "e", "s_mm", "s", "den_mm", "rec", "num_mm", "h",
             "mean_mm", "hc", "sq", "var_mm", "r", "root", "mu")
    N = {n: K.count("mlh_" + n) for n in names}
    bd_loaded = K.sem("mlh_bd_loaded")
    gcol, scol = K.cols_at["ml_norm_g"][0], K.cols_at["ml_skip"][0]
    h_t, sq, xs = q, k, e
    mu = sel
    rows = slice(0, ML_H)
    with nc.Block() as block:
        @block.sync
        def _(sp):
            def load(h):
                sp.dma_start(bd[:], d["w_qkv"][bass.ds(HC * h, HC)].rearrange("c p n -> p c n")).then_inc(bd_loaded, 16)
            load(0)
            with sp.Fori(0, ML_H - 1) as h:
                sp.wait_ge(N["v_mm"].sem, h + 1)
                load(h + 1)

        @block.gpsimd
        def _(pool):
            with pool.Fori(0, ML_H) as h:
                pool.wait_ge(head_written, 4 * h + 1)
                nc.gpsimd.tensor_copy(xs[:], xm[:, bass.ds(HC * h, HC), CONV - 1:]).then_inc(N["xs"].sem, 1)

        @block.tensor
        def _(pe):
            mmul = nc.tensor.matmul
            with pe.Fori(0, ML_H) as h:
                pe.wait_ge(bd_loaded, 16 * h + 16)
                pe.wait_ge(head_written, 4 * h + 1)
                for c in range(HC):
                    last = mmul(K.ps[c][:], bd[:, c, 0:P], xc[:, bass.ds(HC * h + c, 1), :], start=True, stop=True)
                    last.then_inc(N["q_mm"].sem, 1)
                for c in range(HC):
                    last = mmul(K.ps[4 + c][:], bd[:, c, P:2 * P], xc[:, bass.ds(HC * h + c, 1), :], start=True, stop=True)
                    last.then_inc(N["k_mm"].sem, 1)
                pe.wait_ge(N["xs"].sem, h + 1)
                for t in range(NT):
                    pe.wait_ge(N["q"].sem, 4 * h + t + 1)
                    for c in range(HC):
                        last = mmul(K.ps[t][:, c * P:(c + 1) * P], xs[:, c, t * P:(t + 1) * P], bd[:, c, 2 * P:3 * P], start=True, stop=True)
                last.then_inc(N["v_mm"].sem, 1)
                pe.wait_ge(N["k"].sem, 4 * h + 4)
                pe.wait_ge(N["sel"].sem, 2 * h + 1)
                mmul(K.ps[4][:], K.ones[rows, :], sel[rows, :], start=True, stop=True).then_inc(N["bc"].sem, 1)
                pe.wait_ge(N["sel"].sem, 2 * h + 2)
                mmul(K.ps[5][:], K.ones[rows, :], sel[rows, :], start=True, stop=True).then_inc(N["bc"].sem, 1)
                for sb in range(NT):
                    pe.wait_ge(N["v"].sem, 4 * h + sb + 1)
                    for c in range(HC):
                        last = mmul(K.ps[sb][:, sb * P:], k[:, c, sb * P:(sb + 1) * P], q[:, c, sb * P:], start=c == 0, stop=c == HC - 1)
                    last.then_inc(N["s_mm"].sem, 1)
                for sb in range(NT):
                    pe.wait_ge(N["s"].sem, 4 * h + sb + 1)
                    last = mmul(K.ps[6][:, sb * P:], K.ones, e[:, sb, sb * P:], start=sb == 0, stop=sb == NT - 1, skip_group_check=True)
                last.then_inc(N["den_mm"].sem, 1)
                for c in range(HC):
                    for sb in range(NT):
                        last = mmul(K.ps[c][:, sb * P:], v[:, sb, c * P:(c + 1) * P], e[:, sb, sb * P:], start=sb == 0, stop=sb == NT - 1, skip_group_check=True)
                    last.then_inc(N["num_mm"].sem, 1)
                for c in range(HC):
                    pe.wait_ge(N["h"].sem, 4 * h + c + 1)
                    last = mmul(K.ps[7][:], K.ones, h_t[:, c, :], start=c == 0, stop=c == HC - 1)
                last.then_inc(N["mean_mm"].sem, 1)
                pe.wait_ge(N["sq"].sem, h + 1)
                for c in range(HC):
                    last = mmul(K.ps[4][:], K.ones, sq[:, c, :], start=c == 0, stop=c == HC - 1)
                last.then_inc(N["var_mm"].sem, 1)

        @block.scalar
        def _(act):
            with act.Fori(0, ML_H) as h:
                for c in range(HC):
                    act.wait_ge(N["q_mm"].sem, 4 * h + c + 1)
                    nc.scalar.activation(q[:, c, :], K.ps[c][:], ACT.Copy).then_inc(N["q"].sem, 1)
                for c in range(HC):
                    act.wait_ge(N["k_mm"].sem, 4 * h + c + 1)
                    nc.scalar.activation(k[:, c, :], K.ps[4 + c][:], ACT.Copy, scale=float(HC * P) ** -0.5).then_inc(N["k"].sem, 1)
                for sb in range(NT):
                    act.wait_ge(N["arg"].sem, 4 * h + sb + 1)
                    nc.scalar.activation(e[:, sb, sb * P:], e[:, sb, sb * P:], ACT.Exp).then_inc(N["e"].sem, 1)
                act.wait_ge(N["hc"].sem, h + 1)
                nc.scalar.activation(sq[:], h_t[:], ACT.Square).then_inc(N["sq"].sem, 1)
                act.wait_ge(N["r"].sem, 2 * h + 2)
                nc.scalar.activation(mu[:], mu[:], ACT.Sqrt).then_inc(N["root"].sem, 1)

        @block.vector
        def _(dve):
            vv = nc.vector
            with dve.Fori(0, ML_H) as h:
                one = K.consts[rows, bass.ds(h, 1)]
                dve.wait_ge(N["v_mm"].sem, h + 1)
                for t in range(NT):
                    vv.tensor_copy(v[:, t, :], K.ps[t][:]).then_inc(N["v"].sem, 1)
                vv.tensor_scalar(sel[rows, :], r_row[:], one, None, ALU.mult).then_inc(N["sel"].sem, 1)
                dve.wait_ge(N["bc"].sem, 2 * h + 1)
                vv.tensor_scalar(sel[rows, :], m_row[:], one, None, ALU.mult).then_inc(N["sel"].sem, 1)
                for sb in range(NT):
                    vv.tensor_scalar(e[:, sb, sb * P:], K.ps[4][:, sb * P:], ccol[:, sb, bass.ds(h, 1)], 0.0, ALU.subtract, ALU.min).then_inc(N["arg"].sem, 1)
                for sb in range(NT):
                    dve.wait_ge(N["e"].sem, 4 * h + sb + 1)
                    blk = e[:, sb, sb * P:(sb + 1) * P]
                    vv.tensor_tensor(blk, blk, K.causal, ALU.mult).then_inc(N["mu"].sem, 1)
                    dve.wait_ge(N["s_mm"].sem, 4 * h + sb + 1)
                    dve.wait_ge(N["mu"].sem, 7 * h + sb + 1)
                    vv.tensor_tensor(e[:, sb, sb * P:], e[:, sb, sb * P:], K.ps[sb][:, sb * P:], ALU.mult).then_inc(N["s"].sem, 1)
                rec = sel
                dve.wait_ge(N["den_mm"].sem, h + 1)
                vv.tensor_scalar(rec[:], K.ps[6][:], -1.0, None, ALU.mult).then_inc(N["rec"].sem, 1)
                dve.wait_ge(N["rec"].sem, 4 * h + 1)
                vv.tensor_tensor(rec[:], rec[:], K.ps[6][:], ALU.max).then_inc(N["rec"].sem, 1)
                dve.wait_ge(N["rec"].sem, 4 * h + 2)
                dve.wait_ge(N["bc"].sem, 2 * h + 2)
                vv.tensor_tensor(rec[:], rec[:], K.ps[5][:], ALU.max).then_inc(N["rec"].sem, 1)
                dve.wait_ge(N["rec"].sem, 4 * h + 3)
                vv.reciprocal(rec[:], rec[:]).then_inc(N["rec"].sem, 1)
                dve.wait_ge(N["rec"].sem, 4 * h + 4)
                for c in range(HC):
                    dve.wait_ge(N["num_mm"].sem, 4 * h + c + 1)
                    vv.tensor_tensor(h_t[:, c, :], K.ps[c][:], rec[:], ALU.mult).then_inc(N["h"].sem, 1)
                dve.wait_ge(N["mean_mm"].sem, h + 1)
                dve.wait_ge(N["h"].sem, 4 * h + 4)
                vv.tensor_scalar(mu[:], K.ps[7][:], 1.0 / (HC * P), None, ALU.mult).then_inc(N["mu"].sem, 1)
                dve.wait_ge(N["mu"].sem, 7 * h + 5)
                vv.tensor_tensor(h_t[:], h_t[:], mu[:, None, :].to_broadcast([P, HC, S]), ALU.subtract).then_inc(N["hc"].sem, 1)
                dve.wait_ge(N["var_mm"].sem, h + 1)
                vv.tensor_scalar(mu[:], K.ps[4][:], 1.0 / (HC * P), EPS, ALU.mult, ALU.add).then_inc(N["r"].sem, 1)
                dve.wait_ge(N["r"].sem, 2 * h + 1)
                vv.reciprocal(mu[:], mu[:]).then_inc(N["r"].sem, 1)
                dve.wait_ge(N["root"].sem, h + 1)
                vv.tensor_tensor(h_t[:], h_t[:], mu[:, None, :].to_broadcast([P, HC, S]), ALU.mult).then_inc(N["mu"].sem, 1)
                dve.wait_ge(N["mu"].sem, 7 * h + 6)
                for c in range(HC):
                    ins = vv.tensor_scalar(h_t[:, c, :], h_t[:, c, :], K.cols[:, bass.ds(gcol + HC * h + c, 1)], None, ALU.mult)
                ins.then_inc(N["mu"].sem, 1)
                dve.wait_ge(N["mu"].sem, 7 * h + 7)
                for c in range(HC):
                    vv.scalar_tensor_tensor(xm[:, bass.ds(HC * h + c, 1), CONV - 1:], xc[:, bass.ds(HC * h + c, 1), :],
                                            K.cols[:, bass.ds(scol + HC * h + c, 1)], h_t[:, c:c + 1, :], ALU.mult, ALU.add).then_inc(head_written, 1)


def second_block(K):
    nc, d = K.nc, K.dram
    A = K.arena
    o_hi = K.at("oa_hi", [P, 2, S], F32R, A)
    o_lo = K.at("oa_lo", [P, 2, S], F32R, A + 4096)
    p1 = K.at("attn_proj", [P, 2 + QKV, S], F32, A + 8192)
    raw1 = K.at("shift_raw1", [P, 2, S + 1], F32, A + 8192 + (2 + QKV) * S * 4)
    rkv = K.at("rkv", [P, 3 * DC, S], F32, A + 8192 + 4096)
    raw2 = K.at("shift_raw2", [P, 2, S + 1], F32, A + 8192 + 4096 + 3 * DC * S * 4)
    lora = p1[:, 0:2, :]
    m = [K.mods[:, 144 + 8 * n:152 + 8 * n] for n in range(6)]
    sh1, sc1, gt1, sh2, sc2, gt2 = m
    norm(K, "n20", K.x, "modulate", gain=col(K, "mix_pre", 0, 8), scale=sc1, shift=sh1, gate=gt1, half=1.0, split=(K.h_hi, K.h_lo))
    mu0 = K.cols_at["shift_mu"][0]
    shifted = K.count("shifted")
    for n, (w, n_tiles, raw, dst, o0, nxt) in enumerate((("w_attn", 2 + QKV, raw1, p1, 0, "w_rkv"), ("w_rkv", 3 * DC, raw2, rkv, 2 + QKV, "w_gate2"))):
        pad = K.sem(f"shift_pad{n}")
        with nc.Block() as block:
            @block.vector
            def _(dve):
                nc.vector.memset(raw[:, :, 0:1], 0.0).then_inc(pad, 1)
                if n == 0:
                    nc.vector.memset(K.gain[:, 0:1], 0.0).then_inc(shifted.sem, 4)
                    shifted.base = 4
        ae, de = shift_evacs(K, raw, dst, mu0 + o0, shifted)
        stream_out(K, d[w], n_tiles, (d[nxt], DC), ae, de)
        shifted.base += 2 * n_tiles
        if n == 0:
            with stage(K):
                attention(K, p1, o_hi, o_lo, A + 8192 + (2 + QKV) * S * 4)
    with stage(K):
        rwkv(K, lora, rkv, A + 8192 + 4096 + 3 * DC * S * 4)

    G = A + 8192 + 4096 + 3 * DC * S * 4
    gates = K.at("branch_gates", [P, 2 * DC, S], F32, G)
    r_hi = K.at("or_hi", [P, DC, S], F32R, A + 8192 + 4096 + DC * S * 4)
    r_lo = K.at("or_lo", [P, DC, S], F32R, A + 8192 + 4096 + 2 * DC * S * 4)
    sp_hi = K.sem("or_hi_done")
    with nc.Block() as block:
        @block.scalar
        def _(act):
            for c in range(0, DC, 2):
                nc.scalar.activation(r_hi[:, c:c + 2, :], rkv[:, c:c + 2, :], ACT.Copy).then_inc(sp_hi, 1)

        @block.vector
        def _(dve):
            for c in range(0, DC, 2):
                dve.wait_ge(sp_hi, c // 2 + 1)
                nc.vector.tensor_tensor(r_lo[:, c:c + 2, :], rkv[:, c:c + 2, :], r_hi[:, c:c + 2, :].bitcast(F32), ALU.subtract)
    stream_out(K, d["w_gate2"], 2 * DC, (d["w_branch"], 2 + DC), act_out(K, gates, 0, ACT.Sigmoid))

    free, merged, hi_done = K.bank_free, K.count("merged"), K.sem("merged_hi")

    def mm(k, j):
        if k < 2:
            return o_hi[:, k, :], o_lo[:, k, :], 2 * j, k == 0, k == 1
        return r_hi[:, k - 2, :], r_lo[:, k - 2, :], 2 * j + 1, k == 2, k == 1 + DC

    def pe_wait(pe, i, j, t):
        pe.wait_ge(free.sem, free(t - RING + 1))

    def act_evac(act, i, j, t, mm_done):
        act.wait_ge(merged.sem, 2 * t + 2)
        nc.scalar.activation(K.h_hi[:, bass.ds(t, 1), :], gates[:, bass.ds(t, 1), :], ACT.Copy).then_inc(hi_done, 1)

    def dve_evac(dve, i, j, t, mm_done):
        ga, gr = gates[:, bass.ds(t, 1), :], gates[:, bass.ds(DC + t, 1), :]
        dve.wait_ge(K.tile_mm.sem, mm_done)
        nc.vector.tensor_tensor(ga, ga, K.ps[2 * j][:, None, :], ALU.mult).then_inc(merged.sem, 1)
        nc.vector.tensor_tensor(gr, gr, K.ps[2 * j + 1][:, None, :], ALU.mult).then_inc(free.sem, 1)
        dve.wait_ge(merged.sem, 2 * t + 1)
        dve.wait_ge(free.sem, free(t + 1))
        nc.vector.tensor_tensor(ga, ga, gr, ALU.add).then_inc(merged.sem, 1)
        dve.wait_ge(hi_done, t + 1)
        nc.vector.tensor_tensor(K.h_lo[:, bass.ds(t, 1), :], ga, K.h_hi[:, bass.ds(t, 1), :].bitcast(F32), ALU.subtract)

    gemm(K, d["w_branch"], 2 + DC, DC, (d["w_out2"], DC), mm, pe_wait, act_evac, dve_evac)
    free.base += DC
    mix = K.at("mix_out", [P, DC, S], F32, G)
    stream_out(K, d["w_out2"], DC, (d["w_ff10"], DC), act_out(K, mix, 0, ACT.Copy))
    norm(K, "n2p", mix, "add", gain=col(K, "mix_post", 0, 8), gate=gt1)

    norm(K, "n21", K.x, "modulate", gain=col(K, "ffn_pre", 0, 8), scale=sc2, shift=sh2, gate=gt2, half=1.0, split=(K.h_hi, K.h_lo))
    HF = FF2 // 2
    u_hi = K.at("u_hi", [P, HF, S], F32R, A)
    u_lo = K.at("u_lo", [P, HF, S], F32R, A + HF * S * 4)
    f = K.at("ffn_out", [P, DC, S], F32, A + 2 * HF * S * 4)
    rel = K.at("relu", [P, 2, S], F32, A + (2 * HF + DC) * S * 4)
    squared = K.count("squared")
    uhi = K.count("u_hi_done")
    for half in range(2):
        def act_evac(act, i, j, t, mm_done):
            act.wait_ge(K.tile_mm.sem, mm_done)
            nc.scalar.activation(rel[:, j % 2, :], K.ps[j][:], ACT.Relu).then_inc(free.sem, 1)
            act.wait_ge(squared.sem, squared(t + 1))
            nc.scalar.activation(u_hi[:, bass.ds(t, 1), :], rel[:, j % 2:j % 2 + 1, :], ACT.Copy).then_inc(uhi.sem, 1)

        def dve_evac(dve, i, j, t, mm_done):
            r = rel[:, j % 2:j % 2 + 1, :]
            dve.wait_ge(free.sem, free(t + 1))
            nc.vector.tensor_tensor(r, r, r, ALU.mult).then_inc(squared.sem, 1)
            dve.wait_ge(uhi.sem, uhi(t + 1))
            nc.vector.tensor_tensor(u_lo[:, bass.ds(t, 1), :], r, u_hi[:, bass.ds(t, 1), :].bitcast(F32), ALU.subtract)

        stream_out(K, d[f"w_ff1{half}"], HF, (d[f"w_ff2{half}"], DC), act_evac, dve_evac)
        squared.base += HF
        uhi.base += HF

        def mm(k, j):
            kc = (j % 2) * DC + k
            return u_hi[:, kc, :], u_lo[:, kc, :], j // 2, kc == 0, kc == HF - 1

        def pe_wait(pe, i, j, t):
            if j % 2 == 0:
                pe.wait_ge(free.sem, free(2 * i + j // 2 - 1))

        def dve_evac2(dve, i, j, t, mm_done):
            if j % 2 == 1:
                o = f[:, bass.ds(2 * i + j // 2, 1), :]
                dve.wait_ge(K.tile_mm.sem, mm_done)
                if half == 0:
                    ins = nc.vector.tensor_copy(o, K.ps[j // 2][:, None, :])
                else:
                    ins = nc.vector.tensor_tensor(o, o, K.ps[j // 2][:, None, :], ALU.add)
                ins.then_inc(free.sem, 1)

        gemm(K, d[f"w_ff2{half}"], DC, 2 * DC, (d["w_ff11"], DC) if half == 0 else None, mm, pe_wait, None, dve_evac2)
        free.base += DC
    norm(K, "n2f", f, "add", gain=col(K, "ffn_post", 0, 8), gate=gt2)


def shift_evacs(K, raw, dst, mu0, shifted):
    nc, free = K.nc, K.bank_free

    def act_evac(act, i, j, t, mm_done):
        act.wait_ge(K.tile_mm.sem, mm_done)
        act.wait_ge(shifted.sem, shifted(2 * (t - 1)))
        nc.scalar.activation(raw[:, j % 2, 1:], K.ps[j][:], ACT.Copy).then_inc(free.sem, 1)

    def dve_evac(dve, i, j, t, mm_done):
        u, prev = raw[:, j % 2:j % 2 + 1, 1:], raw[:, j % 2:j % 2 + 1, 0:S]
        o = dst[:, bass.ds(t, 1), :]
        dve.wait_ge(free.sem, free(t + 1))
        nc.vector.tensor_tensor(o, prev, u, ALU.subtract).then_inc(shifted.sem, 1)
        dve.wait_ge(shifted.sem, shifted(2 * t + 1))
        nc.vector.scalar_tensor_tensor(o, o, K.cols[:, bass.ds(mu0 + t, 1)], u, ALU.mult, ALU.add).then_inc(shifted.sem, 1)

    return act_evac, dve_evac


TWO_PI = (6.28125, 1.93500518798828125e-03, 3.0199160983e-07)
ROUND = 12582912.0


def attention(K, p1, o_hi, o_lo, base):
    nc, d = K.nc, K.dram
    at = [base]

    def sb(name, shape, dt=F32):
        t = K.at("at_" + name, shape, dt, at[0])
        at[0] += (int(np.prod(shape[1:])) * 4 + 31) // 32 * 32
        return t
    masks, mats = sb("masks", [P, 3 * P]), sb("mats", [P, 3 * P])
    cos, sin = sb("cos", [P, S]), sb("sin", [P, S])
    qp, kp, vp = sb("qp", [P, S]), sb("kp", [P, S]), sb("vp", [P, S])
    t1, t2 = sb("t1", [P, S]), sb("t2", [P, S])
    v_tok = sb("v_tok", [P, NT, P])
    sm = sb("sm", [P, 2, NT, P])
    pT = sb("pT", [P, 2, NT, P])
    o = sb("o", [P, GROUPS, 2, S])
    mx, l, lse = sb("mx", [P, GROUPS, NT, 4]), sb("l", [P, GROUPS, NT, 4]), sb("lse", [P, GROUPS, NT, 4])
    m2, rl = sb("m2", [P, NT]), sb("rl", [P, NT])
    rows, wrow = sb("rows", [4, GROUPS, S]), sb("wrow", [4, 2, S])
    pos = K.at("at_pos", [P, S], I32, at[0] - 5 * 2048)
    assert at[0] - base < 58 * 1024, at[0] - base
    rot = mats[:, 0:P]
    loaded, order = K.sem("at_loaded"), K.count("at_order")
    trig_done, half_done = K.sem("at_trig"), K.sem("at_half")
    inv = K.cols[:, K.cols_at["rope_inv"][0]:K.cols_at["rope_inv"][0] + 1]
    with nc.Block() as block:
        @block.sync
        def _(sp):
            sp.dma_start(masks[:], d["attn_masks"]).then_inc(loaded, 16)
            sp.dma_start(mats[:], d["attn_mats"]).then_inc(loaded, 16)
            sp.dma_start(pos[:], d["positions"].to_broadcast([P, S])).then_inc(loaded, 16)
            sp.wait_ge(loaded, 48)

        @block.vector
        def _(dve):
            v = nc.vector
            link = Chain(dve, order)
            dve.wait_ge(loaded, 48)
            link(v.tensor_copy(t1[:], pos[:]))
            link(v.tensor_scalar(t1[:], t1[:], inv, None, ALU.mult))
            link(v.tensor_scalar(t2[:], t1[:], float(0.5 / np.pi), ROUND, ALU.mult, ALU.add))
            link(v.tensor_scalar(t2[:], t2[:], -ROUND, None, ALU.add))
            for part in TWO_PI:
                link(v.scalar_tensor_tensor(t1[:], t2[:], -part, t1[:], ALU.mult, ALU.add))
            link(v.tensor_scalar(t1[:], t1[:], float(np.float32(3.1415925)), -float(np.float32(3.1415925)), ALU.min, ALU.max))
            dve.wait_ge(trig_done, 2)
            link(v.tensor_tensor(cos[:], cos[:], cos[:], ALU.mult))
            link(v.tensor_scalar(cos[:], cos[:], -2.0, 1.0, ALU.mult, ALU.add))

        @block.scalar
        def _(act):
            act.wait_ge(order.sem, 8)
            nc.scalar.activation(sin[:], t1[:], ACT.Sin).then_inc(trig_done, 1)
            nc.scalar.activation(cos[:], t1[:], ACT.Sin, scale=0.5).then_inc(trig_done, 1)

    names = ("rot", "tq", "qk", "vp", "vt_mm", "vt", "s_mm", "sm", "max", "arg", "p", "sum", "rl", "pn", "pt_mm", "pt", "pv", "o")
    N = {n: K.count("ath_" + n) for n in names}
    for g in range(GROUPS):
        dil = DILATION[g]
        wide = 2 if g == 0 else 1

        def permuted(t):
            return t.rearrange("p (r j) -> p j r", r=dil) if dil > 1 else t

        def by_token(t):
            return t.rearrange("p (j r) -> p j r", r=dil) if dil > 1 else t

        b = {n: c.base for n, c in N.items()}
        with nc.Block() as block:
            @block.gpsimd
            def _(pool):
                with pool.Fori(0, 2) as i:
                    pool.wait_ge(N["o"].sem, b["o"] + i + 1)
                    nc.gpsimd.tensor_copy(permuted(vp[:]), by_token(p1[:, bass.ds(2 + 12 + 2 * g + i, 1), :].rearrange("p o s -> p (o s)"))).then_inc(N["vp"].sem, 1)

            @block.tensor
            def _(pe):
                with pe.Fori(0, 2) as i:
                    pe.wait_ge(N["o"].sem, b["o"] + i + 1)
                    for n in range(2):
                        nc.tensor.matmul(K.ps[n][:], rot, p1[:, bass.ds(2 + 6 * n + 2 * g + i, 1), :], start=True, stop=True).then_inc(N["rot"].sem, 1)
                    pe.wait_ge(N["vp"].sem, b["vp"] + i + 1)
                    for t in range(NT):
                        last = nc.tensor.transpose(K.ps[2][:, t * P:(t + 1) * P], vp[:, t * P:(t + 1) * P], K.ident)
                    last.then_inc(N["vt_mm"].sem, 1)
                    pe.wait_ge(N["qk"].sem, b["qk"] + 2 * i + 2)
                    for hd in range(2):
                        hr = slice(hd * HD, (hd + 1) * HD)
                        for w in range(wide):
                            for t in range(w, NT):
                                last = nc.tensor.matmul(K.ps[3 + w][:, t * P:(t + 1) * P], qp[hr, t * P:(t + 1) * P], kp[hr, (t - w) * P:(t - w + 1) * P], start=True, stop=True)
                        last.then_inc(N["s_mm"].sem, 1)
                        pe.wait_ge(N["pn"].sem, b["pn"] + 2 * i + hd + 1)
                        for w in range(wide):
                            for t in range(w, NT):
                                last = nc.tensor.transpose(K.ps[5 + w][:, t * P:(t + 1) * P], sm[:, w, t, :], K.ident)
                        last.then_inc(N["pt_mm"].sem, 1)
                        pe.wait_ge(N["pt"].sem, b["pt"] + wide * (2 * i + hd + 1))
                        pe.wait_ge(N["vt"].sem, b["vt"] + i + 1)
                        for t in range(NT):
                            for w in range(min(wide, t + 1)):
                                last = nc.tensor.matmul(K.ps[7][hr, t * P:(t + 1) * P], v_tok[:, t - w, hr], pT[:, w, t, :], start=w == 0, stop=w == min(wide, t + 1) - 1)
                        last.then_inc(N["pv"].sem, 1)

            @block.scalar
            def _(act):
                with act.Fori(0, 2) as i:
                    act.wait_ge(N["vt_mm"].sem, b["vt_mm"] + i + 1)
                    nc.scalar.activation(v_tok[:].rearrange("p t c -> p (t c)"), K.ps[2][:], ACT.Copy).then_inc(N["vt"].sem, 1)
                    for hd in range(2):
                        act.wait_ge(N["arg"].sem, b["arg"] + 2 * i + hd + 1)
                        nc.scalar.activation(sm[:, 0:wide], sm[:, 0:wide], ACT.Exp, scale=float(HD) ** -0.5).then_inc(N["p"].sem, 1)
                        act.wait_ge(N["pt_mm"].sem, b["pt_mm"] + 2 * i + hd + 1)
                        for w in range(wide):
                            nc.scalar.activation(pT[:, w, w:, :].rearrange("p t k -> p (t k)"), K.ps[5 + w][:, w * P:], ACT.Copy).then_inc(N["pt"].sem, 1)

            @block.vector
            def _(dve):
                v = nc.vector
                if g == 0:
                    v.memset(m2[:], 0.0).then_inc(N["o"].sem, 1)
                with dve.Fori(0, 2) as i:
                    for n, dst in ((0, qp), (1, kp)):
                        v.tensor_tensor(t1[:], p1[:, bass.ds(2 + 6 * n + 2 * g + i, 1), :].rearrange("p o s -> p (o s)"), cos[:], ALU.mult).then_inc(N["tq"].sem, 1)
                        dve.wait_ge(N["rot"].sem, b["rot"] + 2 * i + n + 1)
                        v.tensor_tensor(t2[:], K.ps[n][:], sin[:], ALU.mult).then_inc(N["tq"].sem, 1)
                        dve.wait_ge(N["tq"].sem, b["tq"] + 4 * i + 2 * n + 2)
                        v.tensor_tensor(permuted(dst[:]), by_token(t1[:]), by_token(t2[:]), ALU.add).then_inc(N["qk"].sem, 1)
                        dve.wait_ge(N["qk"].sem, b["qk"] + 2 * i + n + 1)
                    for hd in range(2):
                        u = 2 * i + hd
                        mxc, lc = mx[:, g, :, bass.ds(u, 1)], l[:, g, :, bass.ds(u, 1)]
                        dve.wait_ge(N["s_mm"].sem, b["s_mm"] + u + 1)
                        mask = masks[:, P:2 * P] if g == 2 else masks[:, 0:P]
                        v.tensor_tensor(sm[:, 0], K.ps[3][:].rearrange("p (t k) -> p t k", t=NT), mask[:, None, :].to_broadcast([P, NT, P]), ALU.add).then_inc(N["sm"].sem, 1)
                        if wide == 2:
                            v.memset(sm[:, 1, 0, :], NEG).then_inc(N["sm"].sem, 1)
                            v.tensor_tensor(sm[:, 1, 1:, :], K.ps[4][:, P:].rearrange("p (t k) -> p t k", t=NT - 1),
                                            masks[:, None, 2 * P:3 * P].to_broadcast([P, NT - 1, P]), ALU.add).then_inc(N["sm"].sem, 1)
                        per = 3 if wide == 2 else 1
                        dve.wait_ge(N["sm"].sem, b["sm"] + per * (u + 1))
                        v.tensor_reduce(mxc, sm[:, 0], AX_X, ALU.max).then_inc(N["max"].sem, 1)
                        if wide == 2:
                            v.tensor_reduce(m2[:], sm[:, 1], AX_X, ALU.max).then_inc(N["max"].sem, 1)
                            dve.wait_ge(N["max"].sem, b["max"] + 3 * u + 2)
                            v.tensor_tensor(mxc, mxc, m2[:, :, None], ALU.max).then_inc(N["max"].sem, 1)
                        dve.wait_ge(N["max"].sem, b["max"] + per * (u + 1))
                        for w in range(wide):
                            ins = v.tensor_tensor(sm[:, w], sm[:, w], mxc.to_broadcast([P, NT, P]), ALU.subtract)
                        ins.then_inc(N["arg"].sem, 1)
                        dve.wait_ge(N["p"].sem, b["p"] + u + 1)
                        v.tensor_reduce(lc, sm[:, 0], AX_X, ALU.add).then_inc(N["sum"].sem, 1)
                        if wide == 2:
                            v.tensor_reduce(m2[:], sm[:, 1], AX_X, ALU.add).then_inc(N["sum"].sem, 1)
                            dve.wait_ge(N["sum"].sem, b["sum"] + 3 * u + 2)
                            v.tensor_tensor(lc, lc, m2[:, :, None], ALU.add).then_inc(N["sum"].sem, 1)
                        dve.wait_ge(N["sum"].sem, b["sum"] + per * (u + 1))
                        v.tensor_scalar(rl[:, :, None], lc, 1.0, None, ALU.mult).then_inc(N["rl"].sem, 1)
                        dve.wait_ge(N["rl"].sem, b["rl"] + 2 * u + 1)
                        v.reciprocal(rl[:], rl[:]).then_inc(N["rl"].sem, 1)
                        dve.wait_ge(N["rl"].sem, b["rl"] + 2 * u + 2)
                        for w in range(wide):
                            ins = v.tensor_tensor(sm[:, w], sm[:, w], rl[:, :, None].to_broadcast([P, NT, P]), ALU.mult)
                        ins.then_inc(N["pn"].sem, 1)
                    dve.wait_ge(N["pv"].sem, b["pv"] + 2 * i + 2)
                    v.tensor_copy(by_token(o[:, g, bass.ds(i, 1), :].rearrange("p o s -> p (o s)")), permuted(K.ps[7][:])).then_inc(N["o"].sem, 1)
        per = 3 if wide == 2 else 1
        for n, k in (("rot", 4), ("tq", 8), ("qk", 4), ("vp", 2), ("vt_mm", 2), ("vt", 2), ("s_mm", 4), ("sm", 4 * per), ("max", 4 * per), ("arg", 4), ("p", 4),
                     ("sum", 4 * per), ("rl", 8), ("pn", 4), ("pt_mm", 4), ("pt", 4 * wide), ("pv", 4), ("o", 2)):
            N[n].base += k

    order2, ln_done, tr_done, e_done, bc_done, fin, hi_done = (K.count("atw_order"), *(K.sem("atw_" + n) for n in ("ln", "tr", "e", "bc", "fin", "hi")))
    rows_done = K.sem("atw_rows")
    with nc.Block() as block:
        @block.scalar
        def _(act):
            nc.scalar.activation(l[:], l[:], ACT.Ln).then_inc(ln_done, 1)
            act.wait_ge(order2.sem, 7)
            nc.scalar.activation(rows[:], rows[:], ACT.Exp).then_inc(e_done, 1)
            for c in range(2):
                act.wait_ge(fin, c + 1)
                nc.scalar.activation(o_hi[:, c, :], o[:, 0, c, :], ACT.Copy).then_inc(hi_done, 1)

        @block.tensor
        def _(pe):
            pe.wait_ge(order2.sem, 1)
            for g in range(GROUPS):
                for t in range(NT):
                    last = nc.tensor.transpose(K.ps[g][0:4, t * P:(t + 1) * P], lse[:, g, t, :], K.ident)
            last.then_inc(tr_done, 1)
            pe.wait_ge(order2.sem, 11)
            for c in range(2):
                for g in range(GROUPS):
                    nc.tensor.matmul(K.ps[GROUPS * c + g][:], mats[0:4, (1 + c) * P:(2 + c) * P], rows[:, g, :], start=True, stop=True).then_inc(bc_done, 1)

        @block.vector
        def _(dve):
            v = nc.vector
            link = Chain(dve, order2)
            dve.wait_ge(ln_done, 1)
            link(v.scalar_tensor_tensor(lse[:], mx[:], float(HD) ** -0.5, l[:], ALU.mult, ALU.add))
            dve.wait_ge(tr_done, 1)
            for g in range(GROUPS):
                dil = DILATION[g]
                src, dst = K.ps[g][0:4, :], rows[:, g, :]
                if dil > 1:
                    src, dst = src.rearrange("p (r j) -> p j r", r=dil), dst.rearrange("p (j r) -> p j r", r=dil)
                ins = v.tensor_copy(dst, src)
            link(ins)
            link(v.tensor_tensor(wrow[:, 0, :], rows[:, 0, :], rows[:, 1, :], ALU.max))
            link(v.tensor_tensor(wrow[:, 0, :], wrow[:, 0, :], rows[:, 2, :], ALU.max))
            for g in range(GROUPS):
                link(v.tensor_tensor(rows[:, g, :], rows[:, g, :], wrow[:, 0, :], ALU.subtract))
            dve.wait_ge(e_done, 1)
            link(v.tensor_tensor(wrow[:, 0, :], rows[:, 0, :], rows[:, 1, :], ALU.add))
            link(v.tensor_tensor(wrow[:, 0, :], wrow[:, 0, :], rows[:, 2, :], ALU.add))
            link(v.reciprocal(wrow[:, 1, :], wrow[:, 0, :]))
            link(v.tensor_tensor(rows[:], rows[:], wrow[:, 1:2, :].to_broadcast([4, GROUPS, S]), ALU.mult))
            for c in range(2):
                for g in range(GROUPS):
                    dve.wait_ge(bc_done, GROUPS * c + g + 1)
                    link(v.tensor_tensor(o[:, g, c, :], o[:, g, c, :], K.ps[GROUPS * c + g][:], ALU.mult))
                link(v.tensor_tensor(o[:, 0, c, :], o[:, 0, c, :], o[:, 1, c, :], ALU.add))
                v.tensor_tensor(o[:, 0, c, :], o[:, 0, c, :], o[:, 2, c, :], ALU.add).then_inc(fin, 1)
            for c in range(2):
                dve.wait_ge(hi_done, c + 1)
                v.tensor_tensor(o_lo[:, c, :], o[:, 0, c, :], o_hi[:, c, :].bitcast(F32), ALU.subtract)


RWKV_DECAY = -float(np.exp(-0.5))


def rwkv(K, lora, rkv, base):
    nc, d = K.nc, K.dram
    at = [base]

    def sb(name, shape):
        t = K.at("rw_" + name, shape, F32, at[0])
        at[0] += (int(np.prod(shape[1:])) * 4 + 31) // 32 * 32
        return t
    masks = sb("masks", [P, 10 * P + 2 * LEVELS])
    w = sb("w", [P, 2 * P])
    log_w, a, kkn, kc, bc, ac, rc, bonus = (sb(n, [P, S]) for n in ("logw", "a", "kk", "k", "b", "a_dec", "r", "bonus"))
    at_, bt, kt, vt = (sb(n, [P, NT, P]) for n in ("a_tok", "b_tok", "k_tok", "v_tok"))
    spare = [a + SLOT_BYTES + n * S * 4 for a in (K.w_hi_at, K.w_lo_at) for n in range(2)]
    abT = [sb("abT0", [P, NT, P]), K.at("rw_abT1", [P, NT, P], F32, spare[0])]
    T = [sb("T0", [P, NT, P]), K.at("rw_T1", [P, NT, P], F32, spare[1])]
    TT = [sb("TT0", [P, NT, P]), K.at("rw_TT1", [P, NT, P], F32, spare[2])]
    off = [sb("off0", [P, NT, P]), K.at("rw_off1", [P, NT, P], F32, spare[3])]
    W = [sb("W0", [P, NT, P]), sb("W1", [P, NT, P])]
    qs, y = sb("q", [P, S]), sb("y", [P, S])
    G, H = sb("G", [P, NT, HD]), sb("H", [P, NT, HD])
    sh, s1 = sb("sh", [P, P]), sb("s1", [P, HD])
    mid, pm, pl, ka1 = sb("mid", [P, NT]), sb("pm", [P, NT]), sb("pl", [P, NT]), sb("ka1", [P, DC])
    assert at[0] <= K.nc.sbuf_usable_end, at[0] - K.nc.sbuf_usable_end
    akT, rbT, rkT, cat, xu = abT, T, off, W, TT
    vs = y
    strict, pair_t, pair = masks[:, 0:P], masks[:, P:2 * P], masks[:, 2 * P:3 * P]
    level = [masks[:, (3 + n) * P:(4 + n) * P] for n in range(LEVELS)]
    same = masks[:, 9 * P:10 * P]
    first_half = [masks[:, 10 * P + n:10 * P + n + 1] for n in range(LEVELS)]
    second_half = [masks[:, 10 * P + LEVELS + n:10 * P + LEVELS + n + 1] for n in range(LEVELS)]
    B = [[K.ps[4 * hd + n] for n in range(4)] for hd in range(2)]

    def half(x, lv, second):
        return x.rearrange("p t (n h b) -> p t n h b", h=2, b=2 << lv)[:, :, :, second, :]

    def half_of_chunk(x, lv, second):
        return x.rearrange("p (n h b) -> p n h b", h=2, b=2 << lv)[:, :, second, :]

    PER = {"lora": 1, "sig": 2, "kk": 1, "sq": 1, "ss": 1, "root": 1, "kkn": 4, "k2": 2, "rk": 1, "rk_mm": 1, "bonus": 1, "logw": 1, "cs": 4, "csm": 3,
           "exp": 4, "dec": 5, "vs": 1, "tr": 4, "tok": 4, "score": 10, "mask": 12, "ident": 4, "off": 2 * LEVELS, "w_mm": 2 * LEVELS, "w": 2 * LEVELS,
           "dT": 2 * LEVELS - 2, "dTT": 2 * LEVELS, "T": 2 * LEVELS - 2, "TT": 2 * LEVELS, "akv": 2, "cat": 4, "xu_mm": 2, "xu": 2, "qy": 2, "gh": 4, "qev": 8,
           "s": 10, "y_mm": 3, "s_mm": 2, "yadd": 1, "mean": 1, "yc": 1, "ysq": 1, "var": 1, "r": 2, "yroot": 1, "yn": 3, "g_mm": 1, "out": 1}
    N = {n: K.count("rw_" + n) for n in PER}
    seen = dict.fromkeys(PER, 0)

    def sig(ins, name):
        seen[name] += 1
        ins.then_inc(N[name].sem, 1)

    def after(eng, i, name, n):
        eng.wait_ge(N[name].sem, PER[name] * i + n)

    loaded, lora_act, ka_done = K.sem("rw_loaded"), K.sem("rw_lora_act"), K.sem("rw_ka")
    w_loaded = K.sem("rw_w_loaded")
    with nc.Block() as block:
        @block.sync
        def _(sp):
            sp.dma_start(masks[:], d["rwkv_masks"]).then_inc(loaded, 16)
            sp.dma_start(w[:], d["w_lora"][0]).then_inc(w_loaded, 16)
            sp.wait_ge(loaded, 16)

        @block.scalar
        def _(act):
            nc.scalar.activation(lora[0:HD, 0, :], lora[0:HD, 0, :], ACT.Tanh).then_inc(lora_act, 1)
            nc.scalar.activation(lora[:, 1, :], lora[:, 1, :], ACT.Sigmoid).then_inc(lora_act, 1)

        @block.vector
        def _(dve):
            nc.vector.tensor_scalar(ka1[:], col(K, "k_a", 0, 8), -1.0, 1.0, ALU.mult, ALU.add).then_inc(ka_done, 1)
            for x in (sh, *W, *off):
                nc.vector.memset(x[:], 0.0)
            nc.vector.memset(pm[:], 0.0).then_inc(N["out"].sem, 1)

    def t4(x):
        return x.rearrange("p (t k) -> p t k", t=NT)

    def tl(x, t):
        return x[:, t * P:(t + 1) * P]

    halves = [slice(0, HD), slice(HD, P)]
    with nc.Block() as block:
        @block.sync
        def _(sp):
            with sp.Fori(0, DC - 1) as i:
                after(sp, i, "g_mm", 1)
                sp.dma_start(w[:], d["w_lora"][bass.ds(i + 1, 1)].rearrange("o p n -> p (o n)")).then_inc(w_loaded, 16)

        @block.gpsimd
        def _(pool):
            with pool.Fori(0, DC) as i:
                after(pool, i, "out", 1)
                sig(nc.gpsimd.tensor_copy(vs[:], rkv[:, bass.ds(2 * DC + i, 1), :].rearrange("p o s -> p (o s)")), "vs")
                for lv in range(LEVELS):
                    for hd in range(2):
                        if lv == 0:
                            after(pool, i, "mask", 3 * hd + 1)
                        else:
                            after(pool, i, "w_mm", 2 * (lv - 1) + hd + 1)
                        mask = half_of_chunk(level[lv], lv, 1)
                        sig(nc.gpsimd.tensor_tensor(half(off[hd][:], lv, 1), half(abT[hd][:], lv, 1),
                                                    mask[:, None].to_broadcast([P, NT] + list(mask.shape[1:])), ALU.mult), "off")

        @block.tensor
        def _(pe):
            mm = nc.tensor.matmul
            with pe.Fori(0, DC) as i:
                pe.wait_ge(w_loaded, 16 * i + 16)
                after(pe, i, "out", 1)
                mm(K.ps[0][:], w[0:HD, 0:P], lora[0:HD, 0, :], start=True, stop=True)
                sig(mm(K.ps[1][:], w[HD:P, 0:P], lora[HD:P, 0, :], start=True, stop=True), "lora")
                after(pe, i, "sq", 1)
                sig(mm(K.ps[2][:], same, T[0][:].rearrange("p t k -> p (t k)"), start=True, stop=True), "ss")
                after(pe, i, "rk", 1)
                sig(mm(K.ps[3][:], same, TT[0][:].rearrange("p t k -> p (t k)"), start=True, stop=True), "rk_mm")
                for n, (src, name, k) in enumerate(((vs, "vs", 1), (ac, "dec", 3), (kc, "dec", 4), (bc, "dec", 5))):
                    after(pe, i, name, k)
                    for t in range(NT):
                        last = nc.tensor.transpose(tl(K.ps[4 + n], t), tl(src, t), K.ident)
                    sig(last, "tr")
                def scores(hd, bank, x, z):
                    for t in range(NT):
                        last = mm(tl(B[hd][bank], t), tl(x, t)[halves[hd]], tl(z, t)[halves[hd]], start=True, stop=True)
                    sig(last, "score")
                after(pe, i, "tok", 4)
                after(pe, i, "dec", 5)
                after(pe, i, "bonus", 1)
                for hd in range(2):
                    scores(hd, 0, bc, ac)
                    scores(hd, 1, ac, bc)
                for lv in range(LEVELS):
                    for hd in range(2):
                        after(pe, i, "off", 2 * lv + hd + 1)
                        after(pe, i, "ident", 2 * hd + 2) if lv == 0 else after(pe, i, "T", 2 * (lv - 1) + hd + 1)
                        for t in range(NT):
                            last = mm(tl(B[hd][2], t), off[hd][:, t, :], T[hd][:, t, :], start=True, stop=True)
                        sig(last, "w_mm")
                    for hd in range(2):
                        after(pe, i, "w", 2 * lv + hd + 1)
                        if lv:
                            after(pe, i, "TT", 2 * (lv - 1) + hd + 1)
                        if lv < LEVELS - 1:
                            for t in range(NT):
                                last = mm(tl(B[hd][3], t), TT[hd][:, t, :], W[hd][:, t, :], start=True, stop=True)
                            sig(last, "dT")
                        for t in range(NT):
                            last = mm(tl(B[hd][0], t), W[hd][:, t, :], TT[hd][:, t, :], start=True, stop=True)
                        sig(last, "dTT")
                    if lv == LEVELS - 2:
                        for hd in range(2):
                            scores(hd, 1, kc, ac)
                for hd in range(2):
                    scores(hd, 2, bc, rc)
                    scores(hd, 3, kc, rc)
                for hd, hr in enumerate(halves):
                    after(pe, i, "TT", 2 * (LEVELS - 1) + hd + 1)
                    after(pe, i, "mask", 6 + hd + 1)
                    for t in range(NT):
                        last = mm(B[hd][0][:, t * HD:(t + 1) * HD], akT[hd][:, t, :], vt[:, t, hr], start=True, stop=True)
                    sig(last, "akv")
                for hd in range(2):
                    after(pe, i, "cat", 2 * hd + 2)
                    for t in range(NT):
                        last = mm(tl(B[hd][1], t), TT[hd][:, t, :], cat[hd][:, t, :], start=True, stop=True)
                    sig(last, "xu_mm")
                for hd, hr in enumerate(halves):
                    xr, ur = hr, halves[1 - hd]
                    after(pe, i, "xu", hd + 1)
                    after(pe, i, "mask", 8 + 2 * hd + 2)
                    for t in range(NT):
                        mm(tl(B[hd][2], t), xu[hd][:, t, :], rbT[hd][:, t, :], start=True, stop=False, skip_group_check=True)
                        last = mm(tl(B[hd][2], t)[ur], vt[:, t, hr], rkT[hd][:, t, :], start=False, stop=True, skip_group_check=True)
                    sig(last, "qy")
                    for t in range(NT):
                        last = mm(B[hd][3][hr, t * HD:(t + 1) * HD], xu[hd][:, t, xr], bt[:, t, hr], start=True, stop=True)
                    sig(last, "gh")
                    for t in range(NT):
                        mm(B[hd][0][hr, t * HD:(t + 1) * HD], bt[:, t, hr], xu[hd][:, t, ur], start=True, stop=False)
                        last = mm(B[hd][0][hr, t * HD:(t + 1) * HD], kt[:, t, hr], vt[:, t, hr], start=False, stop=True)
                    sig(last, "gh")
                after(pe, i, "qev", 8)
                for t in range(1, NT):
                    after(pe, i, "s", 2 + 4 * (t - 1))
                    sig(mm(tl(K.ps[5], t), sh[:], tl(qs, t), start=True, stop=True), "y_mm")
                    if t < NT - 1:
                        for hr in halves:
                            last = mm(K.ps[6][hr, 0:HD], G[hr, t, :], sh[hr, hr], start=True, stop=True)
                        sig(last, "s_mm")
                after(pe, i, "yadd", 1)
                sig(mm(K.ps[0][:], same, y[:], start=True, stop=True), "mean")
                after(pe, i, "ysq", 1)
                sig(mm(K.ps[1][:], same, T[0][:].rearrange("p t k -> p (t k)"), start=True, stop=True), "var")
                sig(mm(K.ps[2][:], w[:, P:2 * P], lora[:, 1, :], start=True, stop=True), "g_mm")

        @block.scalar
        def _(act):
            A = nc.scalar.activation
            w0, a0 = K.cols_at["w0"][0], K.cols_at["a0"][0]
            with act.Fori(0, DC) as i:
                after(act, i, "kk", 1)
                sig(A(T[0][:].rearrange("p t k -> p (t k)"), kkn[:], ACT.Square), "sq")
                after(act, i, "lora", 1)
                sig(A(log_w[:], K.ps[0][:], ACT.Sigmoid, bias=K.cols[:, bass.ds(w0 + i, 1)]), "sig")
                sig(A(a[:], K.ps[1][:], ACT.Sigmoid, bias=K.cols[:, bass.ds(a0 + i, 1)]), "sig")
                after(act, i, "ss", 1)
                sig(A(T[0][:].rearrange("p t k -> p (t k)"), K.ps[2][:], ACT.Sqrt), "root")
                after(act, i, "csm", 3)
                sig(A(rc[:], bc[:], ACT.Exp), "exp")
                sig(A(pm[:], mid[:], ACT.Exp), "exp")
                act.wait_ge(N["exp"].sem, PER["exp"] * i + 1)
                sig(A(bc[:], bc[:], ACT.Exp, scale=-1.0), "exp")
                sig(A(ac[:], ac[:], ACT.Exp), "exp")
                for n, dst in ((0, vt), (2, kt)):
                    after(act, i, "tr", n + 1)
                    sig(A(dst[:].rearrange("p t k -> p (t k)"), K.ps[4 + n][:], ACT.Copy), "tok")
                for lv in range(LEVELS):
                    for hd in range(2):
                        after(act, i, "w_mm", 2 * lv + hd + 1)
                        if lv:
                            after(act, i, "dTT", 2 * (lv - 1) + hd + 1)
                        sig(A(half(W[hd][:], lv, 0), half(t4(B[hd][2][:]), lv, 0), ACT.Identity, scale=second_half[lv]), "w")
                for hd, hr in enumerate(halves):
                    after(act, i, "dTT", 2 * (LEVELS - 1) + hd + 1)
                    sig(A(cat[hd][:, :, hr], at_[:, :, hr], ACT.Copy), "cat")
                    after(act, i, "akv", hd + 1)
                    sig(A(cat[hd][:, :, halves[1 - hd]], B[hd][0][:, 0:NT * HD].rearrange("p (t k) -> p t k", t=NT), ACT.Copy), "cat")
                for hd in range(2):
                    after(act, i, "xu_mm", hd + 1)
                    sig(A(xu[hd][:].rearrange("p t k -> p (t k)"), B[hd][1][:], ACT.Copy), "xu")
                after(act, i, "yc", 1)
                sig(A(T[0][:].rearrange("p t k -> p (t k)"), y[:], ACT.Square), "ysq")
                after(act, i, "r", 2)
                sig(A(qs[:], qs[:], ACT.Sqrt), "yroot")

        @block.vector
        def _(dve):
            v = nc.vector
            c = {n: K.cols_at[n][0] for n in ("k_k", "k_a", "r_k", "gn_w", "gn_b")}
            Tf, TTf = T[0][:].rearrange("p t k -> p (t k)"), TT[0][:].rearrange("p t k -> p (t k)")
            with dve.Fori(0, DC) as i:
                def colv(n):
                    return K.cols[:, bass.ds(c[n] + i, 1)]

                def chunk(n):
                    return rkv[:, bass.ds(n * DC + i, 1), :].rearrange("p o s -> p (o s)")
                r, k, vv = chunk(0), chunk(1), chunk(2)
                sig(v.tensor_scalar(kkn[:], k, colv("k_k"), None, ALU.mult), "kk")
                after(dve, i, "sig", 2)
                sig(v.tensor_scalar(kc[:], a[:], colv("k_a"), ka1[:, bass.ds(i, 1)], ALU.mult, ALU.add), "k2")
                sig(v.tensor_scalar(log_w[:], log_w[:], RWKV_DECAY, None, ALU.mult), "logw")
                after(dve, i, "logw", 1)
                for t in range(NT):
                    sig(v.tensor_tensor_scan(tl(bc, t), K.ones, tl(log_w, t), 0.0, ALU.mult, ALU.add), "cs")
                after(dve, i, "k2", 1)
                sig(v.tensor_tensor(kc[:], kc[:], k, ALU.mult), "k2")
                after(dve, i, "cs", 4)
                sig(v.tensor_copy(mid[:], t4(bc[:])[:, :, P // 2 - 1]), "csm")
                after(dve, i, "csm", 1)
                sig(v.tensor_tensor(t4(bc[:]), t4(bc[:]), mid[:, :, None].to_broadcast([P, NT, P]), ALU.subtract), "csm")
                after(dve, i, "csm", 2)
                sig(v.tensor_tensor(ac[:], bc[:], log_w[:], ALU.subtract), "csm")
                after(dve, i, "k2", 2)
                sig(v.scalar_tensor_tensor(TTf, r, colv("r_k"), kc[:], ALU.mult, ALU.mult), "rk")
                after(dve, i, "root", 1)
                sig(v.tensor_scalar(Tf, Tf, 1e-12, None, ALU.max), "kkn")
                after(dve, i, "kkn", 1)
                sig(v.reciprocal(Tf, Tf), "kkn")
                after(dve, i, "kkn", 2)
                sig(v.tensor_tensor(kkn[:], kkn[:], Tf, ALU.mult), "kkn")
                after(dve, i, "kkn", 3)
                sig(v.tensor_tensor(a[:], a[:], kkn[:], ALU.mult), "kkn")
                after(dve, i, "rk_mm", 1)
                sig(v.tensor_tensor(bonus[:], K.ps[3][:], vv, ALU.mult), "bonus")
                after(dve, i, "exp", 4)
                sig(v.tensor_copy(pl[:], t4(rc[:])[:, :, P - 1]), "dec")
                after(dve, i, "dec", 1)
                sig(v.tensor_tensor(rc[:], rc[:], r, ALU.mult), "dec")
                sig(v.scalar_tensor_tensor(ac[:], kkn[:], -1.0, ac[:], ALU.mult, ALU.mult), "dec")
                sig(v.tensor_tensor(kc[:], kc[:], bc[:], ALU.mult), "dec")
                after(dve, i, "dec", 4)
                after(dve, i, "kkn", 4)
                sig(v.tensor_tensor(bc[:], bc[:], a[:], ALU.mult), "dec")
                for n, dst in ((1, at_), (3, bt)):
                    after(dve, i, "tr", n + 1)
                    sig(v.tensor_copy(dst[:].rearrange("p t k -> p (t k)"), K.ps[4 + n][:]), "tok")
                def masked(n, bank, dst, mask):
                    after(dve, i, "score", n)
                    sig(v.tensor_tensor(dst[:], t4(bank[:]), mask[:, None, :].to_broadcast([P, NT, P]), ALU.mult), "mask")
                eye = K.ident[:, None, :].to_broadcast([P, NT, P])
                for hd in range(2):
                    masked(2 * hd + 1, B[hd][0], abT[hd], strict)
                    masked(2 * hd + 2, B[hd][1], T[hd], pair_t)
                    after(dve, i, "mask", 3 * hd + 2)
                    sig(v.tensor_tensor(T[hd][:], T[hd][:], eye, ALU.add), "ident")
                    sig(v.tensor_tensor(TT[hd][:], abT[hd][:], pair[:, None, :].to_broadcast([P, NT, P]), ALU.mult), "mask")
                    after(dve, i, "mask", 3 * hd + 3)
                    sig(v.tensor_tensor(TT[hd][:], TT[hd][:], eye, ALU.add), "ident")
                for lv in range(LEVELS):
                    for hd in range(2):
                        if lv < LEVELS - 1:
                            after(dve, i, "dT", 2 * lv + hd + 1)
                            x = half(T[hd][:], lv, 0)
                            sig(v.tensor_tensor(x, x, half(t4(B[hd][3][:]), lv, 0), ALU.add), "T")
                        after(dve, i, "dTT", 2 * lv + hd + 1)
                        x = half(TT[hd][:], lv, 1)
                        sig(v.scalar_tensor_tensor(x, half(t4(B[hd][0][:]), lv, 1), first_half[lv], x, ALU.mult, ALU.add), "TT")
                for hd in range(2):
                    masked(4 + hd + 1, B[hd][1], akT[hd], strict)
                for hd in range(2):
                    masked(6 + 2 * hd + 1, B[hd][2], rbT[hd], K.causal)
                    masked(6 + 2 * hd + 2, B[hd][3], rkT[hd], K.causal)
                for hd, hr in enumerate(halves):
                    ur = halves[1 - hd]
                    after(dve, i, "qy", hd + 1)
                    sig(v.tensor_tensor(qs[hr, :], B[hd][2][hr, :], rc[hr, :], ALU.add), "qev")
                    sig(v.tensor_copy(y[hr, :], B[hd][2][ur, :]), "qev")
                    after(dve, i, "gh", 2 * hd + 2)
                    sig(v.tensor_copy(G[hr, :, :], B[hd][3][hr, 0:NT * HD].rearrange("p (t k) -> p t k", t=NT)), "qev")
                    sig(v.tensor_tensor(H[hr, :, :], B[hd][0][hr, 0:NT * HD].rearrange("p (t k) -> p t k", t=NT),
                                        pl[hr, :, None].to_broadcast([HD, NT, HD]), ALU.mult), "qev")
                after(dve, i, "qev", 8)
                for hr in halves:
                    sig(v.tensor_scalar(sh[hr, hr], H[hr, 0, :], pm[hr, 1:2], None, ALU.mult), "s")
                for t in range(1, NT - 1):
                    after(dve, i, "s", 2 + 4 * (t - 1))
                    for hr in halves:
                        ins = v.scalar_tensor_tensor(s1[hr, :], sh[hr, hr], pl[hr, t:t + 1], H[hr, t, :], ALU.mult, ALU.add)
                    sig(ins, "s")
                    after(dve, i, "s", 3 + 4 * (t - 1))
                    after(dve, i, "s_mm", t)
                    sig(v.scalar_tensor_tensor(s1[:], K.ps[6][:, 0:HD], pl[:, t:t + 1], s1[:], ALU.mult, ALU.add), "s")
                    after(dve, i, "s", 4 + 4 * (t - 1))
                    for hr in halves:
                        sig(v.tensor_scalar(sh[hr, hr], s1[hr, :], pm[hr, t + 1:t + 2], None, ALU.mult), "s")
                after(dve, i, "y_mm", NT - 1)
                sig(v.tensor_tensor(y[:, P:], y[:, P:], K.ps[5][:, P:], ALU.add), "yadd")
                after(dve, i, "yadd", 1)
                after(dve, i, "mean", 1)
                sig(v.scalar_tensor_tensor(y[:], K.ps[0][:], -1.0 / HD, y[:], ALU.mult, ALU.add), "yc")
                after(dve, i, "var", 1)
                sig(v.tensor_scalar(qs[:], K.ps[1][:], 1.0 / HD, GN_EPS, ALU.mult, ALU.add), "r")
                after(dve, i, "r", 1)
                sig(v.reciprocal(qs[:], qs[:]), "r")
                after(dve, i, "yroot", 1)
                sig(v.tensor_tensor(y[:], y[:], qs[:], ALU.mult), "yn")
                after(dve, i, "yn", 1)
                sig(v.tensor_scalar(y[:], y[:], colv("gn_w"), colv("gn_b"), ALU.mult, ALU.add), "yn")
                after(dve, i, "yn", 2)
                sig(v.tensor_tensor(y[:], y[:], bonus[:], ALU.add), "yn")
                after(dve, i, "yn", 3)
                after(dve, i, "g_mm", 1)
                sig(v.tensor_tensor(r, y[:], K.ps[2][:], ALU.mult), "out")
    assert seen == PER, {n: (seen[n], PER[n]) for n in PER if seen[n] != PER[n]}


def mod(K, layer, sub, which):
    a = layer * 72 + sub * 24 + which * 8
    return K.mods[:, a:a + 8]


def build(nc, dram, plan=None):
    with ExitStack() as ctx:
        K = setup(nc, ctx, dram)
        K.prod_done = K.count("prod_done")
        K.conv_step = K.count("conv_step")
        K.norm_at = K.arena
        d = dram
        heads = {"f00": (d.get("gu00"), DC), "hyb": (d["w_hyb"][0:DC] if "w_hyb" in d else None, DC), "f01": (d.get("gu01"), DC),
                 "f10": (d.get("gu10"), DC), "ml": (d.get("w_xm"), DC), "f11": (d.get("gu11"), DC), "b2": (d.get("w_attn"), DC)}
        plan = plan or ["f00", "hyb", "f01", "f10", "ml", "f11", "final", "b2"]
        with stage(K):
            first_block(K, heads[plan[0]])
        for n, step in enumerate(plan):
            nxt = next((heads[k] for k in plan[n + 1:] if k in heads), None)
            if step == "final":
                norm(K, "nf", K.x, "plain", gain=col(K, "final_g", 0, 8))
                continue
            if step == "b2":
                second_block(K)
                continue
            layer, sub = {"f00": (0, 0), "hyb": (0, 1), "f01": (0, 2), "f10": (1, 0), "ml": (1, 1), "f11": (1, 2)}[step]
            half = 0.5 if step[0] == "f" else 1.0
            norm(K, f"n{layer}{sub}", K.x, "modulate", gain=col(K, "norm_g", layer * 24 + sub * 8, 8), scale=mod(K, layer, sub, 1),
                 shift=mod(K, layer, sub, 0), gate=mod(K, layer, sub, 2), half=half, split=(K.h_hi, K.h_lo))
            if step == "hyb":
                with stage(K):
                    hybrid(K, nxt)
            elif step == "ml":
                with stage(K):
                    mlstm(K, nxt)
            else:
                s = sub // 2
                swiglu(K, step, d[f"gu{layer}{s}"], d[f"dn{layer}{s}"], nxt)
        stored = K.sem("out_stored")
        with nc.Block() as block:
            @block.sync
            def _(sp):
                for c in range(0, DC, 2):
                    sp.dma_start(d["out"][:, c:c + 2, :], K.x[:, c:c + 2, :]).then_inc(stored, 16)
                sp.wait_ge(stored, 16 * DC // 2)


def tiles_of(w, kb):
    k, n = w.shape
    return np.ascontiguousarray(w.reshape(k // P // kb, kb, P, n // P, P).transpose(3, 0, 2, 1, 4)).reshape(-1, P, kb * P)


def chunks(v):
    return np.asarray(v).reshape(-1, P).T


def interleave(a, b):
    return np.stack([a, b], axis=1).reshape((-1,) + a.shape[1:])


def layout(I):
    I = {k: np.asarray(v) for k, v in I.items()}
    out = {}
    mu = I["shift_mu_2"][0]
    inv = (np.float32(THETA) ** (-np.arange(ROPE // 2, dtype=np.float32) * np.float32(2.0) / np.float32(ROPE))).astype(np.float32)
    vec = {"ada_b": np.concatenate([I["ada_b"][0], I["ada_b"][1], I["ada_b_2"][0]]), "norm_g": I["norm_g"], "final_g": I["final_norm_g"],
           "mix_pre": I["norm_mix_pre_2"], "mix_post": I["norm_mix_post_2"], "ffn_pre": I["norm_ffn_pre_2"],
           "ffn_post": I["norm_ffn_post_2"], "c": I["c"], "c2": I["c_2"],
           "hyb_conv_w": np.concatenate([I["lru_conv_w"][0], I["ssd_conv_w"][0]], axis=1),
           "hyb_conv_b": np.concatenate([I["lru_conv_b"][0], I["ssd_conv_b"][0]]),
           "lru_ba": I["lru_ba"], "lru_bx": I["lru_bx"], "lru_lambda": I["lru_lambda"],
           "ssd_d": np.repeat(I["ssd_d"][0], SSD_P), "ssd_norm_g": I["ssd_norm_g"],
           "ssd_dt_bias": np.pad(I["ssd_dt_bias"][0], (0, P - SSD_H)), "ssd_a_log": np.pad(I["ssd_a_log"][0], (0, P - SSD_H)),
           "ml_conv_w": I["mlstm_conv_w"], "ml_conv_b": I["mlstm_conv_b"], "ml_norm_g": I["mlstm_norm_g"], "ml_skip": I["mlstm_skip"],
           "ml_bi": np.pad(I["mlstm_b_gates"][0, :ML_H], (0, P - ML_H)), "ml_bf": np.pad(I["mlstm_b_gates"][0, ML_H:], (0, P - ML_H)),
           "rope_inv": np.tile(np.pad(np.tile(inv, 2), (0, HD - ROPE)), 2),
           "shift_mu": np.concatenate([mu[3 * D:], np.zeros(QKV * P, np.float32), mu[:3 * D]]),
           "w0": I["decay_w0_2"], "a0": I["iclr_a0_2"], "k_k": I["k_k_2"], "k_a": I["k_a_2"], "r_k": I["r_k_2"], "gn_w": I["gn_w_2"], "gn_b": I["gn_b_2"]}
    out["cols"] = np.ascontiguousarray(np.concatenate([chunks(vec[n]) for n, _ in COLUMNS], axis=1))
    row, column = np.arange(P)[:, None], np.arange(P)[None, :]
    masks = {"ident": row == column, "ones": np.ones((P, P)), "causal": row <= column}
    out["consts"] = np.concatenate([masks[n] for n in CONSTANTS], axis=1).astype(np.float32)
    ada = [I["ada_w"][0], I["ada_w"][1], I["ada_w_2"][0]]
    out["ada"] = np.concatenate([w.reshape(2, 4, P, -1, S).transpose(3, 0, 2, 1, 4).reshape(-1, P, 4 * S) for w in ada])
    out["x"] = np.ascontiguousarray(I["x"][0].T.reshape(DC, P, S).transpose(1, 0, 2))
    for l in range(2):
        for s in range(2):
            out[f"gu{l}{s}"] = interleave(tiles_of(I["ffn_w_gate"][l, s], DC), tiles_of(I["ffn_w_up"][l, s], DC))
            out[f"dn{l}{s}"] = tiles_of(I["ffn_w_down"][l, s], KB_MAX)
    w_in = I["hyb_w_in"][0]
    gate, x_lru, z, xbc = w_in[:, :D], w_in[:, D:2 * D], w_in[:, 2 * D:3 * D], w_in[:, 3 * D:3 * D + XBC * P]
    out["w_hyb"] = tiles_of(np.concatenate([x_lru, xbc, gate, z], axis=1), DC)
    out["w_dt"] = np.ascontiguousarray(w_in[:, 3 * D + XBC * P:].reshape(DC, P, SSD_H).transpose(1, 0, 2))
    out["lru_wax"] = np.ascontiguousarray(np.concatenate([I["lru_wa"][0], I["lru_wx"][0]], axis=2))
    out["w_hout"] = tiles_of(I["hyb_w_out"][0], DC)
    up = I["mlstm_w_up"][0]
    out["w_xm"], out["w_z"] = tiles_of(up[:, :2 * D], DC), tiles_of(up[:, 2 * D:], DC)
    out["w_mdown"] = tiles_of(I["mlstm_w_down"][0], DC)
    qkv = np.zeros((MLC, P, 3, P), np.float32)
    for k, n in enumerate(("mlstm_wq", "mlstm_wk", "mlstm_wv")):
        w = I[n][0]
        b = w.shape[1]
        blocks = w.reshape(MLC, P // b, b, b)
        for r in range(P // b):
            qkv[:, r * b:(r + 1) * b, k, r * b:(r + 1) * b] = blocks[:, r]
    out["w_qkv"] = qkv.reshape(MLC, P, 3 * P)
    wg = I["mlstm_w_gates"][0].reshape(3, MLC, P, 2 * ML_H).transpose(1, 2, 0, 3)
    gates = np.zeros((MLC, P, 3, 2 * ML_F), np.float32)
    gates[..., :ML_H], gates[..., ML_F:ML_F + ML_H] = wg[..., :ML_H], wg[..., ML_H:]
    w2 = I["w_in_2"][0]
    n_attn, n_rwkv = QKV * P, 3 * D
    lora, gate2 = w2[:, n_attn + n_rwkv:-2 * D], w2[:, -2 * D:]
    out["w_attn"] = tiles_of(np.concatenate([lora, w2[:, :n_attn]], axis=1), DC)
    out["w_rkv"] = tiles_of(w2[:, n_attn:n_attn + n_rwkv], DC)
    out["w_gate2"] = tiles_of(gate2, DC)
    out["w_lora"] = np.concatenate([np.concatenate([I["decay_w2_2"][0], I["iclr_a2_2"][0]]).reshape(P, DC, P),
                                    I["gate_g2_2"][0].reshape(P, DC, P)], axis=2).transpose(1, 0, 2).copy()
    out["w_branch"] = tiles_of(I["w_branch_2"][0], 2 + DC)
    out["w_out2"] = tiles_of(I["w_out_2"][0], DC)
    ff2 = I["w_ff2_2"][0]
    for h in range(2):
        out[f"w_ff1{h}"] = tiles_of(I["w_ff1_2"][0][:, h * 2 * D:(h + 1) * 2 * D], DC)
        out[f"w_ff2{h}"] = tiles_of(ff2[h * 2 * D:(h + 1) * 2 * D], DC)
    out["positions"] = I["positions_2"].reshape(1, S)
    no = np.float32(NEG)
    own, sub = column <= row, (column <= row) & (column // 32 == row // 32)
    band = column >= row
    out["attn_masks"] = np.concatenate([np.where(m, np.float32(0), no) for m in (own, sub, band)], axis=1).astype(np.float32)
    rot = np.zeros((P, P), np.float32)
    for h in range(0, P, HD):
        for j in range(ROPE // 2):
            rot[h + ROPE // 2 + j, h + j], rot[h + j, h + ROPE // 2 + j] = -1.0, 1.0
    head_of = np.zeros((P, 2 * P), np.float32)
    for c in range(2):
        for h in range(2):
            head_of[2 * c + h, c * P + h * HD:c * P + (h + 1) * HD] = 1.0
    out["attn_mats"] = np.concatenate([rot, head_of], axis=1)
    off = [(row // (2 * b) == column // (2 * b)) & (row % (2 * b) < b) & (column % (2 * b) >= b) for b in (1, 2, 4, 8, 16, 32, 64)]
    same = row // HD == column // HD
    rows = [row % (2 * b) < b for b in (2, 4, 8, 16, 32, 64)]
    out["rwkv_masks"] = np.concatenate([row < column, off[0].T, off[0], *off[1:], same, *rows, *(~r for r in rows)], axis=1).astype(np.float32)
    out["w_gates"] = gates.reshape(MLC, P, 6 * ML_F)
    return out


def kernel(**inputs):
    import numpy as _np
    import concourse.bacc as _bacc
    from concourse import mybir as _mybir
    from concourse.bass_utils import run_bass_kernel_spmd as _run

    nc = _bacc.Bacc("TRN2", target_bir_lowering=False, num_devices=1)
    arrays, dram = {}, {}
    for name, a in layout(inputs).items():
        a = _np.ascontiguousarray(a)
        arrays[f"in_{name}"] = a
        dram[name] = nc.dram_tensor(f"in_{name}", a.shape, _mybir.dt.from_np(a.dtype), kind="ExternalInput").ap()
    dram["out"] = nc.dram_tensor("out", [P, DC, S], F32, kind="ExternalOutput").ap()
    build(nc, dram)
    r = _run(nc, [arrays], core_ids=[0])
    return r.results[0]["out"].transpose(1, 0, 2).reshape(1, D, S).transpose(0, 2, 1)
```

```python
from contextlib import ExitStack, contextmanager

import numpy as np

import concourse.bass as bass
from concourse import mybir

F32 = mybir.dt.float32
F32R = mybir.dt.float32r
I32 = mybir.dt.int32
ALU = mybir.AluOpType
ACT = mybir.ActivationFunctionType
AX_X = mybir.AxisListType.X

P = 128
S = 512
NT = S // P
D = 1024
DC = D // P
FF = 2816
FC = FF // P
RING = 4
SPLIT = 2
KB_MAX = FC // 2
SLOT_BYTES = KB_MAX * P * 4
EPS = 1e-6
ADA_GROUPS = (2 * 9 * D + 6 * D) // S
ADA_FIRST = 2 * 9 * D // S
ADA_TILES = 4
ADA_UP_FRONT = (*range(3 * D // S), ADA_GROUPS - 1)

SSD_H, SSD_P, SSD_G = 16, 64, 2
SSD_PAIRS = SSD_H // SSD_G // 2
XBC = DC + 2 * SSD_G
HYB = DC + XBC + 2 * DC
CONV = 4
ML_H = 4
MLC = 2 * D // P
HC = MLC // ML_H
HEADS, HD = 12, 64
GROUPS = 3
DILATION = (1, 4, 16)
ROPE = HD // 4
THETA = 500000.0
QKV = 3 * HEADS * HD // P
LEVELS = 6
GN_EPS = 64e-5
FF2 = 4 * D // P
ML_F = 32

COLUMNS = [("ada_b", 192), ("norm_g", 48), ("final_g", 8), ("mix_pre", 8), ("mix_post", 8), ("ffn_pre", 8),
           ("ffn_post", 8), ("c", 8), ("c2", 8),
           ("hyb_conv_w", 80), ("hyb_conv_b", 20), ("lru_ba", 8), ("lru_bx", 8), ("lru_lambda", 8),
           ("ssd_d", 8), ("ssd_norm_g", 8), ("ssd_dt_bias", 1), ("ssd_a_log", 1),
           ("ml_conv_w", 64), ("ml_conv_b", 16), ("ml_norm_g", 16), ("ml_skip", 16), ("ml_bi", 1), ("ml_bf", 1),
           ("rope_inv", 1), ("shift_mu", 44), ("w0", 8), ("a0", 8), ("k_k", 8), ("k_a", 8), ("r_k", 8), ("gn_w", 8), ("gn_b", 8)]


def column_map():
    at, out = 0, {}
    for name, n in COLUMNS:
        out[name] = (at, n)
        at += n
    return out, at


class Count:

    def __init__(self, sem):
        self.sem, self.base = sem, 0

    def __call__(self, n):
        return self.base + n


class Chain:

    def __init__(self, eng, count, start=0):
        self.eng, self.count, self.n, self.start = eng, count, 0, start

    def __call__(self, ins):
        self.n += 1
        ins.then_inc(self.count.sem, 1)
        self.eng.wait_ge(self.count.sem, self.count(self.start + self.n))


@contextmanager
def stage(K):
    K.stage_sems = []
    yield
    K.nc.clear_and_free_semaphores(K.stage_sems)
    K.stage_sems = None
    K.nc.all_engine_barrier()


class Core:
    pass


def setup(nc, ctx, dram):
    K = Core()
    K.nc, K.dram, K.ctx = nc, dram, ctx
    K.top = [nc.sbuf_base]

    def at(name, shape, dtype, offset):
        return nc.alloc_sbuf_tensor_at(name, shape, dtype, offset=offset)

    def sb(name, shape, dtype=F32):
        n = int(np.prod(shape[1:])) * 4
        K.top[0] = (K.top[0] + 31) // 32 * 32
        t = at(name, shape, dtype, K.top[0])
        K.top[0] += n
        return t

    K.at, K.sb = at, sb
    K.stage_sems = None

    def sem(name):
        if K.stage_sems is None:
            return ctx.enter_context(nc.semaphore(name))
        K.stage_sems.append(nc.alloc_semaphore(name=name))
        return K.stage_sems[-1]
    K.sem = sem
    K.count = lambda name: Count(K.sem(name))
    K.cols_at, ncols = column_map()
    K.x = sb("residual", [P, DC, S])
    K.h_at = (K.top[0] + 31) // 32 * 32
    K.h_hi = sb("h_hi", [P, DC, S], F32R)
    K.h_lo_at = (K.top[0] + 31) // 32 * 32
    K.h_lo = sb("h_lo", [P, DC, S], F32R)
    K.w_raw_at = (K.top[0] + 31) // 32 * 32
    K.w_raw = sb("w_raw", [P, RING, KB_MAX * P])
    K.w_hi_at = (K.top[0] + 31) // 32 * 32
    K.w_hi = sb("w_hi", [P, SPLIT, KB_MAX * P], F32R)
    K.w_lo_at = (K.top[0] + 31) // 32 * 32
    K.w_lo = sb("w_lo", [P, SPLIT, KB_MAX * P], F32R)
    K.cols = sb("cols", [P, ncols])
    K.consts = sb("consts", [P, NCONST])
    K.mods = sb("mods", [P, 192])
    K.gain = sb("gain", [P, DC])
    K.coef = sb("coef", [P, DC])
    K.c_act = sb("c_act", [P, 16])
    K.arena = (K.top[0] + 31) // 32 * 32
    K.ident = K.consts[:, 0:P]
    K.ones = K.consts[:, P:2 * P]
    K.causal = K.consts[:, 2 * P:3 * P]
    K.ps = [nc.alloc_psum_tensor(f"bank{i}", [P, S], F32) for i in range(8)]

    K.w_loaded = [K.sem(f"w_loaded{i}") for i in range(RING)]
    K.hi_done = K.count("w_hi_done")
    K.lo_done = K.count("w_lo_done")
    K.tile_mm = K.count("tile_mm")
    K.bank_free = K.count("bank_free")
    K.ada_loaded, K.ada_base = [K.sem(f"ada_loaded{i}") for i in range(2)], 0
    K.ada_step, K.ada_mm, K.ada_out = K.count("ada_step"), K.count("ada_mm"), K.count("ada_out")
    K.sq_done, K.sq_added = K.count("sq_done"), K.count("sq_added")
    K.rms_sum, K.rms_step, K.rms_root, K.rms_diag, K.rms_row = (K.count("rms_" + n) for n in ("sum", "step", "root", "diag", "row"))
    K.scaled, K.h_hi_done, K.h_ready, K.x_written = (K.count(n) for n in ("h_scaled", "h_hi_done", "h_ready", "x_written"))
    K.rs, K.pad4 = sb("rms_rs", [P, NT]), sb("rms_pad", [P, NT])
    K.t = at("h_scaled", [P, DC, S], F32, K.h_lo_at)
    K.diag = at("rms_diag", [P, NT, P], F32, K.h_at + 3 * S * 4)
    K.arena = (K.top[0] + 31) // 32 * 32
    K.silu_done, K.gu_hi_done = K.count("silu_done"), K.count("gu_hi_done")
    K.tile0 = 0
    return K


CONSTANTS = ["ident", "ones", "causal"]
NCONST = len(CONSTANTS) * P


def col(K, name, i=0, n=1):
    a, _ = K.cols_at[name]
    return K.cols[:, a + i:a + i + n]


def load_tile(K, sp, w, kb, t, slot, value):
    if value is not None:
        sp.wait_ge(K.lo_done.sem, value)
    sp.dma_start(K.w_raw[:, slot, 0:kb * P], w[bass.ds(t, 1)].rearrange("o p n -> p (o n)")).then_inc(K.w_loaded[slot], 16)


def split_hi(K, act, kb, slot, half, g):
    act.wait_ge(K.w_loaded[slot], 16 * (g // RING + 1) if isinstance(g, int) else (g + (RING - slot)) * (16 // RING))
    act.wait_ge(K.tile_mm.sem, g + PRIMED - 1)
    K.nc.scalar.activation(K.w_hi[:, half, 0:kb * P], K.w_raw[:, slot, 0:kb * P], ACT.Copy).then_inc(K.hi_done.sem, 1)


def split_lo(K, dve, kb, slot, half, g):
    dve.wait_ge(K.hi_done.sem, g + PRIMED + 1)
    K.nc.vector.tensor_tensor(K.w_lo[:, half, 0:kb * P], K.w_raw[:, slot, 0:kb * P],
                              K.w_hi[:, half, 0:kb * P].bitcast(F32), ALU.subtract).then_inc(K.lo_done.sem, 1)


PRIMED = 4


def rolled(eng, n, body):
    if n > 2:
        with eng.Fori(0, n - 1) as i:
            body(i, False)
    elif n == 2:
        body(0, False)
    body(n - 1, True)


def gemm(K, w, kb, n_tiles, nxt, mm, pe_wait, act_evac=None, dve_evac=None, turn=4, post=None, side=None, head=None, squares=None, fetched=RING, fetch=RING):
    nc = K.nc
    g0 = K.tile0
    n = n_tiles // turn
    assert n_tiles % turn == 0 and g0 % RING == 0 and turn % RING == 0
    with nc.Block() as block:
        @block.sync
        def _(sp):
            if side:
                side.first_loads(sp)
            for j in range(fetched, RING):
                load_tile(K, sp, w, kb, j, j, None)

            def body(i, last):
                for j in range(turn):
                    ahead = turn * i + j + RING
                    if not last or j < turn - RING:
                        load_tile(K, sp, w, kb, ahead, j % RING, g0 + ahead + PRIMED - RING + 1)
                    elif nxt is not None and j - turn + RING < fetch:
                        load_tile(K, sp, nxt[0], nxt[1], j - turn + RING, j % RING, g0 + ahead + PRIMED - RING + 1)
                    if side:
                        side.load(sp, i, j, last)
            rolled(sp, n, body)

        @block.scalar
        def _(act):
            if head:
                head.act(act)

            def body(i, last):
                for j in range(turn):
                    t = turn * i + j
                    if not (last and j == turn - 1):
                        split_hi(K, act, kb, (j + 1) % RING, (j + 1) % SPLIT, g0 + t + 1)
                    elif nxt is not None:
                        split_hi(K, act, nxt[1], 0, 0, g0 + t + 1)
                    if act_evac:
                        act_evac(act, i, j, t, g0 + t + PRIMED + 1)
            rolled(act, n, body)

        @block.vector
        def _(dve):
            if head:
                head.dve(dve)

            def body(i, last):
                for j in range(turn):
                    t = turn * i + j
                    if not (last and j == turn - 1):
                        split_lo(K, dve, kb, (j + 1) % RING, (j + 1) % SPLIT, g0 + t + 1)
                    elif nxt is not None:
                        split_lo(K, dve, nxt[1], 0, 0, g0 + t + 1)
                    if dve_evac:
                        dve_evac(dve, i, j, t, g0 + t + PRIMED + 1)
                    if side:
                        side.accumulate(dve, i, j)
            rolled(dve, n, body)

        @block.tensor
        def _(pe):
            if head:
                head.pe(pe)

            def body(i, last):
                for j in range(turn):
                    t = turn * i + j
                    pe.wait_ge(K.lo_done.sem, g0 + t + PRIMED + 1)
                    pe_wait(pe, i, j, t)
                    for k in range(kb):
                        hi, lo, bank, start, stop = mm(k, j)
                        if head:
                            pe.wait_ge(K.h_ready.sem, K.h_ready(k + 1))
                        wh = K.w_hi[:, j % SPLIT, k * P:(k + 1) * P]
                        wl = K.w_lo[:, j % SPLIT, k * P:(k + 1) * P]
                        nc.tensor.matmul(K.ps[bank][:], wh, hi, start=start, stop=False)
                        nc.tensor.matmul(K.ps[bank][:], wh, lo, start=False, stop=False)
                        last_mm = nc.tensor.matmul(K.ps[bank][:], wl, hi, start=False, stop=stop)
                    last_mm.then_inc(K.tile_mm.sem, 1)
                    if side and j == turn - 1:
                        side.reduce(pe, i)
            rolled(pe, n, body)
            if post:
                post(pe)

        if squares:
            @block.gpsimd
            def _(pool):
                squares.clear(pool)

                def body(i, last):
                    for j in range(squares.per):
                        squares.add(pool, squares.per * i + j, j % 2)
                rolled(pool, DC // squares.per, body)
    if side:
        side.advance(n)
    if squares:
        squares.advance()
    if head:
        head.advance()
    K.tile0 += n_tiles
    for c in (K.hi_done, K.lo_done, K.tile_mm):
        c.base = K.tile0 + PRIMED


class Modulation:
    SLOT = (0, 1, 0, 1)
    STEP = ((0, 1), (2,), (3,), ())

    def __init__(self, K, group, c0, base):
        self.K, self.group, self.c0 = K, group, c0
        self.tiles = K.at(f"ada_tiles{group}", [P, 2, 2 * S], F32, base)
        self.acc = K.at(f"ada_acc{group}", [P, S], F32, base + 4 * S * 4)

    def fetch(self, sp, group, tile):
        sp.dma_start(self.tiles[:, self.SLOT[tile], :],
                     self.K.dram["ada"][bass.ds(ADA_TILES * group + tile, 1)].rearrange("o p n -> p (o n)")).then_inc(self.K.ada_loaded[self.SLOT[tile]], 16)

    def first_loads(self, sp):
        for tile in range(2):
            self.fetch(sp, self.group, tile)

    def load(self, sp, i, j, last):
        if last and j >= 2:
            return
        sp.wait_ge(self.K.ada_step.sem, self.K.ada_step(8 * i + 2 * j + 2))
        self.fetch(sp, self.group + i + (j >= 2), (j + 2) % ADA_TILES)

    def accumulate(self, dve, i, j):
        K, v = self.K, self.K.nc.vector
        for tile in self.STEP[j]:
            slot = self.SLOT[tile]
            dve.wait_ge(K.ada_loaded[slot], 32 * i + (K.ada_base + tile // 2 + 1) * 16)
            for k in range(2):
                n = 2 * tile + k
                block = self.tiles[:, slot, k * S:(k + 1) * S]
                c = K.c_act[:, self.c0 + n:self.c0 + n + 1]
                if n == 0:
                    ins = v.tensor_scalar(self.acc[:], block, c, None, ALU.mult)
                else:
                    dve.wait_ge(K.ada_step.sem, K.ada_step(8 * i + n))
                    ins = v.scalar_tensor_tensor(self.acc[:], block, c, self.acc[:], ALU.mult, ALU.add)
                ins.then_inc(K.ada_step.sem, 1)
        if j == 3:
            dve.wait_ge(K.ada_mm.sem, K.ada_mm(i + 1))
            at = 4 * (self.group + i)
            v.tensor_tensor(K.mods[:, bass.ds(at, 4)], K.ps[7][:, 0:4], K.cols[:, bass.ds(K.cols_at["ada_b"][0] + at, 4)],
                            ALU.add).then_inc(K.ada_out.sem, 1)

    def reduce(self, pe, i):
        K = self.K
        pe.wait_ge(K.ada_step.sem, K.ada_step(8 * i + 8))
        pe.wait_ge(K.ada_out.sem, K.ada_out(i))
        for m in range(4):
            last = K.nc.tensor.matmul(K.ps[7][:, m:m + 1], self.acc[:, m * P:(m + 1) * P], K.ones[:, 0:1], start=True, stop=True)
        last.then_inc(K.ada_mm.sem, 1)

    def advance(self, turns):
        K = self.K
        self.group += turns
        K.ada_base += 2 * turns
        for c, per in ((K.ada_step, 8), (K.ada_mm, 1), (K.ada_out, 1)):
            c.base += per * turns


def first_block(K, first):
    nc, dram = K.nc, K.dram
    loaded, x_loaded = K.sem("inputs_loaded"), K.sem("x_loaded")
    silu_done = K.sem("c_silu_done")
    n_up = len(ADA_UP_FRONT)
    ada_loaded = [K.sem(f"ada_up_front{g}") for g in ADA_UP_FRONT]
    step, reduced, out = K.count("ada_up_step"), K.sem("ada_up_reduced"), K.sem("ada_up_out")
    GROUP_BYTES = ADA_TILES * 2 * S * 4
    acc = K.at("ada_up_acc", [P, n_up, S], F32, K.h_at)
    tiny = K.at("prime", [P, 8], F32, K.h_at + n_up * S * 4)
    ada = [K.at(f"ada_up{n}", [P, ADA_TILES, 2 * S], F32, K.arena + n * GROUP_BYTES if n < n_up - 1 else K.h_at + n_up * S * 4 + 32)
           for n in range(n_up)]
    mod_ps = K.ps[0]
    squares = Squares(K, "first", K.arena + (n_up - 1) * GROUP_BYTES + 3 * S * 4)
    K.sq_added.base = PRIMED
    with nc.Block() as block:
        @block.sync
        def _(sp):
            sp.dma_start(K.cols[:], dram["cols"]).then_inc(loaded, 16)
            sp.dma_start(K.consts[:], dram["consts"]).then_inc(loaded, 16)
            for n, g in enumerate(ADA_UP_FRONT):
                sp.dma_start(ada[n][:], dram["ada"][ADA_TILES * g:ADA_TILES * (g + 1)].rearrange("t p n -> p t n")).then_inc(ada_loaded[n], 16)
                if n == 1:
                    sp.dma_start(K.x[:], dram["x"]).then_inc(x_loaded, 16)
            for j in range(RING):
                load_tile(K, sp, first[0], first[1], j, j, None)
            sp.wait_ge(x_loaded, 16)

        @block.scalar
        def _(act):
            act.wait_ge(loaded, 32)
            nc.scalar.activation(K.c_act[:], K.cols[:, K.cols_at["c"][0]:K.cols_at["c"][0] + 16], ACT.Silu).then_inc(silu_done, 1)
            nc.scalar.activation(tiny[:, 4:5], K.consts[:, 0:1], ACT.Copy).then_inc(K.hi_done.sem, PRIMED)
            act.wait_ge(K.tile_mm.sem, PRIMED)
            split_hi(K, act, first[1], 0, 0, 0)
            act.wait_ge(x_loaded, 16)
            for c in range(DC):
                squares.by_act(act, K.x[:, c:c + 1, :], c, c % 2)

        @block.gpsimd
        def _(pool):
            nc.gpsimd.memset(tiny[:, 7:8], 0.0).then_inc(K.sq_added.sem, PRIMED)
            squares.clear(pool)
            for c in range(DC):
                squares.add(pool, c, c % 2)

        @block.vector
        def _(dve):
            v = nc.vector
            v.memset(tiny[:, 0:1], 0.0).then_inc(K.lo_done.sem, PRIMED)
            v.memset(tiny[:, 1:2], 0.0).then_inc(K.tile_mm.sem, PRIMED)
            v.memset(tiny[:, 2:3], 0.0).then_inc(K.bank_free.sem, PRIMED)
            v.memset(tiny[:, 3:4], 0.0).then_inc(K.ada_out.sem, 1)
            for n, c in enumerate((K.prod_done, K.conv_step)):
                v.memset(tiny[:, 5 + n:6 + n], 0.0).then_inc(c.sem, 2 * PRIMED)
            dve.wait_ge(silu_done, 1)
            link = Chain(dve, step)
            for n, g in enumerate(ADA_UP_FRONT):
                dve.wait_ge(ada_loaded[n], 16)
                for k in range(2 * ADA_TILES):
                    block_k = ada[n][:, k // 2, (k % 2) * S:(k % 2 + 1) * S]
                    c0 = (0 if g < ADA_FIRST else DC) + k
                    if k == 0:
                        link(v.tensor_scalar(acc[:, n], block_k, K.c_act[:, c0:c0 + 1], None, ALU.mult))
                    else:
                        link(v.scalar_tensor_tensor(acc[:, n], block_k, K.c_act[:, c0:c0 + 1], acc[:, n], ALU.mult, ALU.add))
            split_lo(K, dve, first[1], 0, 0, 0)
            dve.wait_ge(reduced, n_up)
            for n, g in enumerate(ADA_UP_FRONT):
                a = K.cols_at["ada_b"][0] + 4 * g
                v.tensor_tensor(K.mods[:, 4 * g:4 * g + 4], mod_ps[:, 4 * n:4 * n + 4], K.cols[:, a:a + 4], ALU.add).then_inc(out, 1)
            dve.wait_ge(out, n_up)

        @block.tensor
        def _(pe):
            pe.wait_ge(loaded, 32)
            for n in range(n_up):
                pe.wait_ge(step.sem, 2 * ADA_TILES * (n + 1))
                for m in range(4):
                    last = nc.tensor.matmul(mod_ps[:, 4 * n + m:4 * n + m + 1], acc[:, n, m * P:(m + 1) * P],
                                            K.ones[:, 0:1], start=True, stop=True)
                last.then_inc(reduced, 1)
    for c in (K.hi_done, K.lo_done, K.tile_mm, K.bank_free):
        c.base = PRIMED
    K.ada_out.base = 1
    squares.advance()
    for c in (K.prod_done, K.conv_step):
        c.base = 2 * PRIMED


class Squares:

    def __init__(self, K, name, base, per=2):
        self.K, self.per = K, per
        self.sq = K.at(f"sq_{name}", [P, 2, S], F32, base)
        self.acc = K.at(f"sq_acc_{name}", [P, S], F32, base + 2 * S * 4)

    def clear(self, pool):
        self.K.nc.gpsimd.memset(self.acc[:], 0.0).then_inc(self.K.sq_added.sem, 1)

    def by_act(self, act, src, o, slot):
        act.wait_ge(self.K.sq_added.sem, self.K.sq_added(o))
        self.K.nc.scalar.activation(self.sq[:, slot:slot + 1, :], src, ACT.Square).then_inc(self.K.sq_done.sem, 1)

    def by_dve(self, dve, src, o, slot):
        dve.wait_ge(self.K.sq_added.sem, self.K.sq_added(o))
        self.K.nc.vector.tensor_tensor(self.sq[:, slot:slot + 1, :], src, src, ALU.mult).then_inc(self.K.sq_done.sem, 1)

    def add(self, pool, o, slot):
        K = self.K
        pool.wait_ge(K.sq_done.sem, K.sq_done(o + 1))
        pool.wait_ge(K.sq_added.sem, K.sq_added(o + 1))
        K.nc.gpsimd.tensor_tensor(self.acc[:], self.acc[:], self.sq[:, slot, :], ALU.add).then_inc(K.sq_added.sem, 1)

    def advance(self):
        self.K.sq_done.base += DC
        self.K.sq_added.base += DC + 1
        self.K.sq_acc = self.acc


class Rms:
    SUM, ROW = 4, 5

    def __init__(self, K):
        self.K, self.acc = K, K.sq_acc

    def rms_pe(self, pe):
        K, mm = self.K, self.K.nc.tensor.matmul
        pe.wait_ge(K.sq_added.sem, K.sq_added(0))
        for t in range(NT):
            last = mm(K.ps[self.SUM][:, t:t + 1], self.acc[:, t * P:(t + 1) * P], K.ones[:, 0:1], start=True, stop=True)
        last.then_inc(K.rms_sum.sem, 1)
        pe.wait_ge(K.rms_diag.sem, K.rms_diag(1))
        mm(K.ps[self.ROW][:], K.ones, K.diag[:].rearrange("p t k -> p (t k)"), start=True, stop=True).then_inc(K.rms_row.sem, 1)

    def rms_act(self, act):
        K = self.K
        K.nc.scalar.activation(K.pad4[:], K.consts[:, 0:NT], ACT.Sqrt)
        act.wait_ge(K.rms_step.sem, K.rms_step(1))
        K.nc.scalar.activation(K.rs[:], K.rs[:], ACT.Sqrt).then_inc(K.rms_root.sem, 1)

    def rms_dve(self, dve):
        K, v = self.K, self.K.nc.vector
        dve.wait_ge(K.rms_sum.sem, K.rms_sum(1))
        v.tensor_scalar(K.rs[:], K.ps[self.SUM][:, 0:NT], 1.0 / D, EPS, ALU.mult, ALU.add).then_inc(K.rms_step.sem, 1)
        dve.wait_ge(K.rms_root.sem, K.rms_root(1))
        v.reciprocal(K.rs[:], K.rs[:]).then_inc(K.rms_step.sem, 1)
        dve.wait_ge(K.rms_step.sem, K.rms_step(2))
        v.tensor_tensor(K.diag[:], K.ident[:, None, :].to_broadcast([P, NT, P]), K.rs[:, :, None].to_broadcast([P, NT, P]),
                        ALU.mult).then_inc(K.rms_diag.sem, 1)
        dve.wait_ge(K.rms_row.sem, K.rms_row(1))

    def rms_advance(self):
        K = self.K
        for c, n in ((K.rms_sum, 1), (K.rms_step, 2), (K.rms_root, 1), (K.rms_diag, 1), (K.rms_row, 1)):
            c.base += n


class Modulated(Rms):

    def __init__(self, K, gain, scale, shift, gate, half):
        super().__init__(K)
        self.gain, self.scale, self.shift, self.gate, self.half = gain, scale, shift, gate, half

    def pe(self, pe):
        self.rms_pe(pe)

    def act(self, act):
        K = self.K
        self.rms_act(act)
        for c in range(DC):
            act.wait_ge(K.scaled.sem, K.scaled(c + 1))
            K.nc.scalar.activation(K.h_hi[:, c, :], K.t[:, c, :], ACT.Identity, bias=self.shift[:, c:c + 1]).then_inc(K.h_hi_done.sem, 1)

    def dve(self, dve):
        K, v = self.K, self.K.nc.vector
        v.scalar_tensor_tensor(K.gain[:], self.scale, 1.0, self.gain, ALU.add, ALU.mult).then_inc(K.x_written.sem, 1)
        v.tensor_scalar(K.coef[:], self.gate, 1.0, self.half, ALU.add, ALU.mult).then_inc(K.x_written.sem, 1)
        self.rms_dve(dve)
        dve.wait_ge(K.x_written.sem, K.x_written(2))

        def scale(c):
            v.scalar_tensor_tensor(K.t[:, c, :], K.x[:, c, :], K.gain[:, c:c + 1], K.ps[self.ROW][:], ALU.mult, ALU.mult).then_inc(K.scaled.sem, 1)
        scale(0)
        scale(1)
        for c in range(DC):
            if c + 2 < DC:
                scale(c + 2)
            dve.wait_ge(K.h_hi_done.sem, K.h_hi_done(c + 1))
            v.scalar_tensor_tensor(K.h_lo[:, c, :], K.t[:, c, :], self.shift[:, c:c + 1], K.h_hi[:, c, :].bitcast(F32),
                                   ALU.add, ALU.subtract).then_inc(K.h_ready.sem, 1)

    def advance(self):
        self.rms_advance()
        self.K.x_written.base += 2
        for c in (self.K.scaled, self.K.h_hi_done, self.K.h_ready):
            c.base += DC


def norm(K, name, src, gain, gate=None, squares=None, store=None):
    nc = K.nc
    rms = Rms(K)
    t = K.t
    with nc.Block() as block:
        @block.tensor
        def _(pe):
            rms.rms_pe(pe)

        @block.scalar
        def _(act):
            rms.rms_act(act)
            if squares:
                for c in range(DC):
                    act.wait_ge(K.x_written.sem, K.x_written(c + 2))
                    squares.by_act(act, K.x[:, c:c + 1, :], c, c % 2)

        if squares:
            @block.gpsimd
            def _(pool):
                squares.clear(pool)
                for c in range(DC):
                    squares.add(pool, c, c % 2)

        if store:
            @block.sync
            def _(sp):
                for c in range(DC):
                    sp.wait_ge(K.x_written.sem, K.x_written(c + 2))
                    sp.dma_start(K.dram["out"][:, c, :], K.x[:, c, :]).then_inc(store, 16)
                sp.wait_ge(store, 16 * DC)

        @block.vector
        def _(dve):
            v = nc.vector
            if gate is None:
                v.tensor_copy(K.gain[:], gain).then_inc(K.x_written.sem, 1)
            else:
                v.tensor_tensor(K.gain[:], gain, gate, ALU.mult).then_inc(K.x_written.sem, 1)
            rms.rms_dve(dve)
            dve.wait_ge(K.x_written.sem, K.x_written(1))
            for c in range(DC):
                dst = K.x if gate is None else t
                ins = v.scalar_tensor_tensor(dst[:, c, :], src[:, c, :], K.gain[:, c:c + 1], K.ps[rms.ROW][:], ALU.mult, ALU.mult)
                if gate is None:
                    ins.then_inc(K.x_written.sem, 1)
                    continue
                ins.then_inc(K.scaled.sem, 1)
                dve.wait_ge(K.scaled.sem, K.scaled(c + 1))
                v.tensor_tensor(K.x[:, c, :], K.x[:, c, :], t[:, c, :], ALU.add).then_inc(K.x_written.sem, 1)
    rms.rms_advance()
    K.x_written.base += DC + 1
    if gate is not None:
        K.scaled.base += DC
    if squares:
        squares.advance()


def swiglu(K, name, w_gu, w_down, nxt, head, ada=None):
    nc = K.nc
    sil_done, guhi_done = K.silu_done, K.gu_hi_done
    gu_hi = K.at(f"{name}_gu_hi", [P, FC, S], F32R, K.arena)
    gu_lo = K.at(f"{name}_gu_lo", [P, FC, S], F32R, K.arena + FC * S * 4)
    sil = K.at(f"{name}_sil_t", [P, 2, S], F32, K.arena + 2 * FC * S * 4)
    prod = K.at(f"{name}_prod_t", [P, 2, S], F32, K.arena + 2 * FC * S * 4 + 2 * S * 4)
    side = Modulation(K, ada[0], ada[1], K.arena + 2 * FC * S * 4 + 4 * S * 4) if ada else None
    done = K.prod_done

    def mm(k, j):
        return K.h_hi[:, k, :], K.h_lo[:, k, :], j, k == 0, k == DC - 1

    def pe_wait(pe, i, j, t):
        if j % 2 == 0:
            pe.wait_ge(done.sem, done(2 * i + j // 2 - 1))

    def act_evac(act, i, j, t, mm_done):
        f = 2 * i + j // 2
        if j % 2 == 0:
            act.wait_ge(K.tile_mm.sem, mm_done)
            act.wait_ge(done.sem, done(f - 1))
            nc.scalar.activation(sil[:, j // 2, :], K.ps[j][:], ACT.Silu).then_inc(sil_done.sem, 1)
        else:
            act.wait_ge(done.sem, done(f + 1))
            nc.scalar.activation(gu_hi[:, bass.ds(f, 1), :], prod[:, j // 2:j // 2 + 1, :], ACT.Copy).then_inc(guhi_done.sem, 1)

    def dve_evac(dve, i, j, t, mm_done):
        f = 2 * i + j // 2
        if j % 2 == 1:
            dve.wait_ge(K.tile_mm.sem, mm_done)
            dve.wait_ge(sil_done.sem, sil_done(f + 1))
            nc.vector.tensor_tensor(prod[:, j // 2, :], sil[:, j // 2, :], K.ps[j][:], ALU.mult).then_inc(done.sem, 1)
            dve.wait_ge(guhi_done.sem, guhi_done(f + 1))
            nc.vector.tensor_tensor(gu_lo[:, bass.ds(f, 1), :], prod[:, j // 2:j // 2 + 1, :],
                                    gu_hi[:, bass.ds(f, 1), :].bitcast(F32), ALU.subtract)

    gemm(K, w_gu, DC, 2 * FC, (w_down, KB_MAX), mm, pe_wait, act_evac, dve_evac, side=side, head=head)
    for c in (done, sil_done, guhi_done):
        c.base += FC

    def mm2(k, j):
        kc = (j % 2) * KB_MAX + k
        return gu_hi[:, kc, :], gu_lo[:, kc, :], j // 2, kc == 0, kc == FC - 1

    project(K, w_down, KB_MAX, 2, mm2, nxt, lambda o: (K.coef[:, bass.ds(o, 1)]),
            Squares(K, name, K.h_at), side=side if ada and ada[2] > 2 * FC // RING else None)


def project(K, w, kb, tpo, mm, nxt, coef, squares, turn=4, side=None):
    nc = K.nc
    banks = turn // tpo
    free = K.bank_free

    def pe_wait(pe, i, j, t):
        if j % tpo == 0:
            pe.wait_ge(free.sem, free(banks * i + j // tpo - banks + 1))

    def dve_evac(dve, i, j, t, mm_done):
        if j % tpo == tpo - 1:
            o = banks * i + j // tpo
            dve.wait_ge(K.tile_mm.sem, mm_done)
            nc.vector.scalar_tensor_tensor(K.x[:, bass.ds(o, 1), :], K.ps[j // tpo][:, None, :], coef(o), K.x[:, bass.ds(o, 1), :],
                                           ALU.mult, ALU.add).then_inc(free.sem, 1)

    def act_evac(act, i, j, t, mm_done):
        if j % tpo == tpo - 1:
            o = banks * i + j // tpo
            act.wait_ge(free.sem, free(o + 1))
            squares.by_act(act, K.x[:, bass.ds(o, 1), :], o, j // tpo % 2)

    gemm(K, w, kb, DC * tpo, nxt, mm, pe_wait, act_evac, dve_evac, turn=turn, side=side, squares=squares)
    free.base += DC


def conv_evacs(K, raw, dst, dst0, o0, weights, bias, n_all, ring=True):
    nc, free = K.nc, K.bank_free
    steps = K.conv_step
    wa, ba = K.cols_at[weights][0], K.cols_at[bias][0]

    def act_evac(act, i, j, t, mm_done):
        act.wait_ge(K.tile_mm.sem, mm_done)
        o = j % 2
        if ring:
            act.wait_ge(steps.sem, steps(CONV * (4 * i + j - 1)))
        else:
            o = t
        nc.scalar.activation(raw[:, bass.ds(o, 1), CONV - 1:], K.ps[j][:, None, :], ACT.Copy).then_inc(free.sem, 1)

    def dve_evac(dve, i, j, t, mm_done):
        o = 4 * i + j
        dve.wait_ge(free.sem, free(o + 1))
        y = dst[:, bass.ds(dst0 + o, 1), :]
        for tap in range(CONV):
            src = raw[:, bass.ds(j % 2 if ring else o, 1), tap:tap + S]
            w = K.cols[:, bass.ds(wa + tap * n_all + o0 + o, 1)]
            if tap == 0:
                ins = nc.vector.tensor_scalar(y, src, w, K.cols[:, bass.ds(ba + o0 + o, 1)], ALU.mult, ALU.add)
            else:
                dve.wait_ge(steps.sem, steps(CONV * o + tap))
                ins = nc.vector.scalar_tensor_tensor(y, src, w, y, ALU.mult, ALU.add)
            ins.then_inc(steps.sem, 1)

    return act_evac, dve_evac


def stream_out(K, w, n, nxt, act_evac, dve_evac=None, post=None, head=None, squares=None, fetched=RING, fetch=RING):
    free = K.bank_free

    def mm(k, j):
        return K.h_hi[:, k, :], K.h_lo[:, k, :], j, k == 0, k == DC - 1

    def pe_wait(pe, i, j, t):
        pe.wait_ge(free.sem, free(t - RING + 1))

    gemm(K, w, DC, n, nxt, mm, pe_wait, act_evac, dve_evac, post=post, head=head, squares=squares,
         fetched=fetched, fetch=fetch)
    free.base += n


def act_out(K, dst, dst0, func):
    def act_evac(act, i, j, t, mm_done):
        act.wait_ge(K.tile_mm.sem, mm_done)
        K.nc.scalar.activation(dst[:, bass.ds(dst0 + t, 1), :], K.ps[j][:, None, :], func).then_inc(K.bank_free.sem, 1)
    return act_evac


LOG1P_TERMS = 8
NEG = -1e30


def softplus_steps(nc, link, z, out, e, q, exp_of):
    v = nc.vector
    link(v.tensor_scalar(q, z, -1.0, None, ALU.mult))
    link(v.tensor_tensor(e, z, q, ALU.max))
    exp_of()
    link(v.tensor_scalar(q, e, 2.0, None, ALU.add))
    link(v.reciprocal(q, q))
    link(v.tensor_tensor(e, e, q, ALU.mult))
    link(v.tensor_tensor(q, e, e, ALU.mult))
    link(v.tensor_scalar(out, q, 1.0 / (2 * LOG1P_TERMS - 1), None, ALU.mult))
    for n in range(LOG1P_TERMS - 2, 0, -1):
        link(v.scalar_tensor_tensor(out, out, 1.0 / (2 * n + 1), q, ALU.add, ALU.mult))
    link(v.scalar_tensor_tensor(out, out, 1.0, e, ALU.add, ALU.mult))
    link(v.tensor_scalar(q, z, 0.0, None, ALU.max))
    link(v.scalar_tensor_tensor(out, out, 2.0, q, ALU.mult, ALU.add))


def hybrid(K, nxt, head):
    nc, d = K.nc, K.dram
    A = K.arena
    proj = K.at("proj", [P, HYB, S], F32, A)
    B = A + HYB * S * 4
    raw = K.at("conv_raw", [P, 2, S + CONV - 1], F32, B + 20 * 1024)
    w_dt = K.at("w_dt", [P, DC, SSD_H], F32, B + 26 * 1024)
    w_dt_hi = K.at("w_dt_hi", [P, DC, SSD_H], F32R, B + 26 * 1024 + 512)
    w_dt_lo = K.at("w_dt_lo", [P, DC, SSD_H], F32R, B + 24 * 1024 + 512)
    wax = K.at("lru_wax", [P, 2, 2 * P], F32, B + 27 * 1024)
    dt_raw = K.at("dt_raw", [SSD_H, S], F32, B + 30 * 1024)
    small = K.sem("hyb_small_loaded")
    wax_loaded = [K.sem(f"lru_wax_loaded{i}") for i in range(2)]
    pad_done = K.sem("conv_pad_zeroed")
    dt_mm = K.sem("dt_mm")
    XB, GATE, Z = DC, DC + XBC, DC + XBC + DC

    with nc.Block() as block:
        @block.sync
        def _(sp):
            sp.dma_start(w_dt[:], d["w_dt"]).then_inc(small, 16)
            for j in range(2):
                sp.dma_start(wax[:, j, :], d["lru_wax"][j]).then_inc(wax_loaded[j], 16)
            sp.wait_ge(small, 16)

        @block.scalar
        def _(act):
            act.wait_ge(small, 16)
            nc.scalar.activation(w_dt_hi[:], w_dt[:], ACT.Copy).then_inc(pad_done, 1)

        @block.vector
        def _(dve):
            nc.vector.memset(raw[:, :, 0:CONV - 1], 0.0)
            dve.wait_ge(pad_done, 1)
            nc.vector.tensor_tensor(w_dt_lo[:], w_dt[:], w_dt_hi[:].bitcast(F32), ALU.subtract).then_inc(pad_done, 1)

    def dt_product(pe):
        passes = [(w, h, k) for k in range(DC) for w, h in ((w_dt_hi, K.h_hi), (w_dt_hi, K.h_lo), (w_dt_lo, K.h_hi))]
        for n, (w, h, k) in enumerate(passes):
            last = nc.tensor.matmul(K.ps[7][0:SSD_H, :], w[:, k, :], h[:, k, :], start=n == 0, stop=n == len(passes) - 1)
        last.then_inc(dt_mm, 1)

    ae, de = conv_evacs(K, raw, proj, 0, 0, "hyb_conv_w", "hyb_conv_b", DC + XBC)
    stream_out(K, d["w_hyb"][0:DC], DC, (d["w_hyb"][XB:GATE], DC), ae, de, post=dt_product, head=head)
    K.conv_step.base += CONV * DC
    ae, de = conv_evacs(K, raw, proj, XB, XB, "hyb_conv_w", "hyb_conv_b", DC + XBC)
    stream_out(K, d["w_hyb"][XB:GATE], XBC, (d["w_hyb"][GATE:Z], DC), ae, de)
    K.conv_step.base += CONV * XBC
    stream_out(K, d["w_hyb"][GATE:Z], DC, (d["w_hyb"][Z:HYB], DC), act_out(K, proj, GATE, ACT.Gelu_apprx_tanh))
    stream_out(K, d["w_hyb"][Z:HYB], DC, (d["w_hout"], DC), act_out(K, proj, Z, ACT.Silu))
    lru(K, proj, GATE, wax, wax_loaded, dt_raw, dt_mm)
    ssd(K, proj, XB, Z, B, dt_raw)
    hybrid_out(K, proj, GATE, nxt)


def lru(K, proj, GATE, wax, wax_loaded, dt_raw, dt_mm):
    nc, d = K.nc, K.dram
    B = K.arena + HYB * S * 4
    r_all = K.at("lru_r", [P, DC, S], F32, B)
    ix = K.at("lru_ix", [P, DC, S], F32, K.h_at)
    m2 = K.at("lru_m2", [P, DC, S], F32, K.h_at + DC * S * 4)
    i_t = K.at("lru_i", [P, 2, S], F32, B + DC * S * 4)
    lam = K.at("lru_lam", [P, 4, DC], F32, B + 25 * 1024)
    mm_done, sig_done, ix_done = K.count("lru_mm"), K.count("lru_sig"), K.sem("lru_ix_done")
    lam_order, lam_abs, lam_exp = K.count("lru_lam_order"), K.sem("lru_lam_abs"), K.sem("lru_lam_exp")
    a_done, q_done, root_done, u_done, h_done = (K.sem(f"lru_{n}") for n in ("a", "q", "root", "u", "h"))
    dt_out = K.sem("dt_out")
    la = K.cols_at["lru_lambda"][0]
    ba, bx = K.cols_at["lru_ba"][0], K.cols_at["lru_bx"][0]
    z, e, q, out = (lam[:, k, :] for k in range(4))
    with nc.Block() as block:
        @block.sync
        def _(sp):
            with sp.Fori(0, DC // 2 - 1) as i:
                for j in range(2):
                    sp.wait_ge(mm_done.sem, 2 * i + j + 1)
                    sp.dma_start(wax[:, j:j + 1, :], d["lru_wax"][bass.ds(2 * i + j + 2, 1)].rearrange("o p n -> p o n")).then_inc(wax_loaded[j], 16)

        @block.tensor
        def _(pe):
            def head(i, j, first):
                pe.wait_ge(wax_loaded[j], 16 * i + 16)
                if not first:
                    pe.wait_ge(sig_done.sem, 4 * i + 2 * j - 2)
                c = 2 * i + j
                nc.tensor.matmul(K.ps[2 * j][:], wax[:, j, 0:P], proj[:, bass.ds(c, 1), :], start=True, stop=True)
                nc.tensor.matmul(K.ps[2 * j + 1][:], wax[:, j, P:2 * P], proj[:, bass.ds(c, 1), :], start=True, stop=True).then_inc(mm_done.sem, 1)
            for j in range(2):
                head(0, j, True)
            with pe.Fori(1, DC // 2) as i:
                for j in range(2):
                    head(i, j, False)

        @block.scalar
        def _(act):
            act.wait_ge(dt_mm, 1)
            nc.scalar.activation(dt_raw[:], K.ps[7][0:SSD_H, :], ACT.Copy).then_inc(dt_out, 1)
            act.wait_ge(lam_abs, 1)
            nc.scalar.activation(e, e, ACT.Exp, scale=-1.0).then_inc(lam_exp, 1)

            def head(i, j, first):
                c = 2 * i + j
                act.wait_ge(mm_done.sem, c + 1)
                nc.scalar.activation(r_all[:, bass.ds(c, 1), :], K.ps[2 * j][:, None, :], ACT.Sigmoid, bias=K.cols[:, bass.ds(ba + c, 1)]).then_inc(sig_done.sem, 1)
                if not first:
                    act.wait_ge(ix_done, c - 1)
                nc.scalar.activation(i_t[:, j, :], K.ps[2 * j + 1][:], ACT.Sigmoid, bias=K.cols[:, bass.ds(bx + c, 1)]).then_inc(sig_done.sem, 1)
            for j in range(2):
                head(0, j, True)
            with act.Fori(1, DC // 2) as i:
                for j in range(2):
                    head(i, j, False)
            act.wait_ge(lam_order.sem, LRU_LAM_STEPS)
            act.wait_ge(ix_done, DC)
            with act.Fori(0, DC) as c:
                nc.scalar.activation(proj[:, bass.ds(c, 1), :], r_all[:, bass.ds(c, 1), :], ACT.Exp, scale=lam[:, 3, bass.ds(c, 1)]).then_inc(a_done, 1)
                nc.scalar.activation(m2[:, bass.ds(c, 1), :], r_all[:, bass.ds(c, 1), :], ACT.Tanh, scale=lam[:, 3, bass.ds(c, 1)]).then_inc(a_done, 1)
            act.wait_ge(q_done, 2)
            nc.scalar.activation(m2[:], m2[:], ACT.Sqrt, scale=-1.0).then_inc(root_done, 1)

        @block.vector
        def _(dve):
            link = Chain(dve, lam_order)

            def exp_of():
                nc.vector.tensor_copy(q, e).then_inc(lam_abs, 1)
                dve.wait_ge(lam_exp, 1)
            link(nc.vector.tensor_scalar(z, K.cols[:, la:la + DC], -1.0, None, ALU.mult))
            softplus_steps(nc, link, z, out, e, q, exp_of)
            link(nc.vector.tensor_scalar(out, out, -8.0, None, ALU.mult))
            assert link.n == LRU_LAM_STEPS, link.n
            with dve.Fori(0, DC // 2) as i:
                for j in range(2):
                    c = 2 * i + j
                    dve.wait_ge(sig_done.sem, 4 * i + 2 * j + 2)
                    nc.vector.tensor_tensor(ix[:, bass.ds(c, 1), :], i_t[:, j:j + 1, :], proj[:, bass.ds(c, 1), :], ALU.mult).then_inc(ix_done, 1)
            dve.wait_ge(a_done, 2 * DC)
            nc.vector.tensor_tensor(r_all[:], proj[:, 0:DC, :], proj[:, 0:DC, :], ALU.mult).then_inc(q_done, 1)
            dve.wait_ge(q_done, 1)
            nc.vector.scalar_tensor_tensor(m2[:], r_all[:], 1.0, m2[:], ALU.add, ALU.mult).then_inc(q_done, 1)
            dve.wait_ge(root_done, 1)
            nc.vector.tensor_tensor(ix[:], ix[:], m2[:], ALU.mult).then_inc(u_done, 1)
            dve.wait_ge(u_done, 1)
            for c in range(DC):
                nc.vector.tensor_tensor_scan(r_all[:, c, :], proj[:, c, :], ix[:, c, :], 0.0, ALU.mult, ALU.add).then_inc(h_done, 1)
            dve.wait_ge(h_done, DC)
            nc.vector.tensor_tensor(proj[:, GATE:GATE + DC, :], proj[:, GATE:GATE + DC, :], r_all[:], ALU.mult)


LRU_LAM_STEPS = 10 + LOG1P_TERMS


def ssd(K, proj, XB, Z, B, dt_raw):
    nc, d = K.nc, K.dram
    H16 = SSD_H
    off = [B, K.h_at]

    def sb(name, shape, where=0):
        t = K.at("ssd_" + name, shape, F32, off[where])
        off[where] += (int(np.prod(shape[1:])) * 4 + 31) // 32 * 32
        return t
    acs, wst = sb("acs", [H16, S]), sb("wst", [H16, S], 1)
    toks = sb("toks", [P, 3, NT, H16])
    edec = sb("edec", [P, NT, H16])
    b_tok, cbm = sb("b_tok", [P, SSD_G, S]), sb("cbm", [P, SSD_G, S])
    xs, xdt, xw = sb("xs", [P, S]), sb("xdt", [P, NT, P]), sb("xw", [P, NT, P])
    rows = sb("rows", [H16, 2, S])
    arg, eb = sb("arg", [P, 2, S]), sb("eb", [P, 2, S], 1)
    state = sb("state", [P, NT - 1, P], 1)
    dt = sb("dt", [H16, S], 1)
    e, q, z = sb("e", [H16, S], 1), sb("q", [H16, S], 1), sb("z", [H16, S], 1)
    diag = sb("diag", [H16, NT, H16], 1)
    aneg = sb("aneg", [H16, 1], 1)
    assert off[0] <= B + 30 * 1024 and off[1] <= K.h_at + 32 * 1024
    CSTEP = S // NT
    order = K.count("ssd_order")
    abs_done, exp_done, silu_done, tr_done, cb_done, prep_done, wexp_done, wdone, diag_done = (
        K.sem(f"ssd_{n}") for n in ("abs", "exp", "silu", "tr", "cb", "prep", "wexp", "w", "diag"))
    dtb, alog = (K.cols[0:H16, K.cols_at[n][0]:K.cols_at[n][0] + 1] for n in ("ssd_dt_bias", "ssd_a_log"))

    rows_done, bc_mm, arg_done, eb_done, e_done, m_done, cd_done, xs_done, xt_done, xdt_done, st_mm, st_done, y_mm, y_done, z_done = (
        K.count(f"ssd_{n}") for n in ("rows", "bc", "arg", "eb", "decay", "m", "cd", "xs", "xt", "xdt", "st_mm", "state", "y_mm", "y", "z"))
    def tile(t, c):
        return t[:, c * CSTEP:(c + 1) * CSTEP]

    with nc.Block() as block:
        @block.scalar
        def _(act):
            nc.scalar.activation(proj[:, XB:XB + XBC, :], proj[:, XB:XB + XBC, :], ACT.Silu).then_inc(silu_done, 1)
            nc.scalar.activation(aneg[:], alog, ACT.Exp).then_inc(exp_done, 1)
            act.wait_ge(abs_done, 1)
            nc.scalar.activation(e[:], e[:], ACT.Exp, scale=-1.0).then_inc(exp_done, 1)
            act.wait_ge(wdone, 1)
            nc.scalar.activation(wst[:], wst[:], ACT.Exp, scale=-1.0).then_inc(wexp_done, 1)
            act.wait_ge(cb_done, 2)
            nc.scalar.activation(edec[:], K.ps[5][:, 0:NT * H16].rearrange("p (c h) -> p c h", c=NT), ACT.Exp).then_inc(prep_done, 1)

        @block.vector
        def _(dve):
            v = nc.vector
            link = Chain(dve, order)

            def exp_of():
                v.tensor_copy(q[:], e[:]).then_inc(abs_done, 1)
                dve.wait_ge(exp_done, 2)
            link(v.tensor_scalar(z[:], dt_raw[:], dtb, None, ALU.add))
            softplus_steps(nc, link, z[:], dt[:], e[:], q[:], exp_of)
            link(v.tensor_scalar(aneg[:], aneg[:], -1.0, None, ALU.mult))
            link(v.tensor_scalar(z[:], dt[:], aneg[:, 0:1], None, ALU.mult))
            for c in range(NT):
                ins = v.tensor_tensor_scan(tile(acs, c), K.ones[0:H16, :], tile(z, c), 0.0, ALU.mult, ALU.add)
            link(ins)
            for c in range(NT):
                end = acs[:, (c + 1) * CSTEP - 1:(c + 1) * CSTEP]
                v.tensor_scalar(diag[:, c, :], K.ident[0:H16, 0:H16], end, None, ALU.mult)
                ins = v.tensor_scalar(tile(wst, c), tile(acs, c), end, None, ALU.subtract)
            ins.then_inc(wdone, 1)
            dve.wait_ge(wexp_done, 1)
            v.tensor_tensor(wst[:], wst[:], dt[:], ALU.mult).then_inc(wdone, 1)
            dve.wait_ge(tr_done, 1)
            v.tensor_copy(toks[:], K.ps[0][:, 0:3 * NT * H16].rearrange("p (k c h) -> p k c h", k=3, c=NT))
            dve.wait_ge(cb_done, 1)
            for g in range(SSD_G):
                v.tensor_copy(b_tok[:, g, :], K.ps[1 + g][:])
                ins = v.tensor_tensor(cbm[:, g, :].rearrange("p (c l) -> p c l", c=NT), K.ps[3 + g][:].rearrange("p (c l) -> p c l", c=NT),
                                      K.causal[:, None, :].to_broadcast([P, NT, P]), ALU.mult)
            ins.then_inc(y_done.sem, 1)

        @block.tensor
        def _(pe):
            pe.wait_ge(silu_done, 1)
            for g in range(SSD_G):
                bt, ct = proj[:, XB + DC + g, :], proj[:, XB + DC + SSD_G + g, :]
                for c in range(NT):
                    nc.tensor.transpose(K.ps[1 + g][:, c * P:(c + 1) * P], tile(bt, c), K.ident)
                    last = nc.tensor.matmul(K.ps[3 + g][:, c * P:(c + 1) * P], tile(bt, c), tile(ct, c), start=True, stop=True)
            last.then_inc(cb_done, 1)
            pe.wait_ge(wdone, 2)
            for k, t in enumerate((acs, dt, wst)):
                for c in range(NT):
                    last = nc.tensor.transpose(K.ps[0][:, (k * NT + c) * H16:(k * NT + c + 1) * H16], tile(t, c), K.ident[0:H16, 0:H16])
            last.then_inc(tr_done, 1)
            nc.tensor.matmul(K.ps[5][:, 0:NT * H16], K.ones[0:H16, :], diag[:], start=True, stop=True).then_inc(cb_done, 1)

    dcol = K.cols_at["ssd_d"][0]
    toks_v = toks[:]
    for g in range(SSD_G):
        n0 = g * SSD_PAIRS
        ct = proj[:, XB + DC + SSD_G + g, :]
        with nc.Block() as block:
            @block.gpsimd
            def _(pool):
                with pool.Fori(0, SSD_PAIRS) as i:
                    pool.wait_ge(y_done.sem, i + n0 + 1)
                    nc.gpsimd.tensor_copy(xs[:, None, :], proj[:, bass.ds(XB + n0 + i, 1), :]).then_inc(xs_done.sem, 1)

            @block.tensor
            def _(pe):
                with pe.Fori(0, SSD_PAIRS) as i:
                    pe.wait_ge(rows_done.sem, 2 * (i + n0) + 2)
                    for hd in range(2):
                        last = nc.tensor.matmul(K.ps[hd][:], K.ones[0:H16, :], rows[:, hd, :], start=True, stop=True)
                    last.then_inc(bc_mm.sem, 1)
                    pe.wait_ge(xs_done.sem, i + n0 + 1)
                    for c in range(NT):
                        last = nc.tensor.transpose(K.ps[2][:, c * P:(c + 1) * P], tile(xs, c), K.ident)
                    last.then_inc(xt_done.sem, 1)
                    pe.wait_ge(xdt_done.sem, 2 * (i + n0) + 2)
                    for c in range(NT - 1):
                        last = nc.tensor.matmul(K.ps[4][:, c * P:(c + 1) * P], tile(b_tok[:, g, :], c), xw[:, c, :], start=True, stop=True)
                    last.then_inc(st_mm.sem, 1)
                    pe.wait_ge(m_done.sem, i + n0 + 1)
                    pe.wait_ge(cd_done.sem, i + n0 + 1)
                    pe.wait_ge(st_done.sem, (1 + 2 * (NT - 2)) * (i + n0 + 1))
                    for hd in range(2):
                        lo, hi = hd * SSD_P, (hd + 1) * SSD_P
                        for c in range(NT):
                            dst = K.ps[3][lo:hi, c * P:(c + 1) * P]
                            last = nc.tensor.matmul(dst, xdt[:, c, lo:hi], tile(arg[:, hd, :], c), start=True, stop=c == 0)
                            if c:
                                last = nc.tensor.matmul(dst, state[:, c - 1, lo:hi], tile(eb[:, hd, :], c), start=False, stop=True)
                    last.then_inc(y_mm.sem, 1)

            @block.scalar
            def _(act):
                with act.Fori(0, SSD_PAIRS) as i:
                    act.wait_ge(bc_mm.sem, i + n0 + 1)
                    act.wait_ge(y_done.sem, i + n0 + 1)
                    for hd in range(2):
                        nc.scalar.activation(eb[:, hd, :], K.ps[hd][:], ACT.Exp).then_inc(eb_done.sem, 1)
                    act.wait_ge(arg_done.sem, 2 * NT * (i + n0) + 2 * NT)
                    nc.scalar.activation(arg[:], arg[:], ACT.Exp).then_inc(e_done.sem, 1)

            @block.vector
            def _(dve):
                v = nc.vector
                with dve.Fori(0, SSD_PAIRS) as i:
                    h0 = 8 * g + 2 * i
                    for hd in range(2):
                        v.tensor_scalar(rows[:, hd, :], acs[:], K.consts[0:H16, bass.ds(h0 + hd, 1)], None, ALU.mult).then_inc(rows_done.sem, 1)
                    dve.wait_ge(eb_done.sem, 2 * (i + n0) + 2)
                    for hd in range(2):
                        for c in range(NT):
                            v.tensor_scalar(tile(arg[:, hd, :], c), tile(K.ps[hd], c), toks[:, 0, c, bass.ds(h0 + hd, 1)], 0.0,
                                            ALU.subtract, ALU.min).then_inc(arg_done.sem, 1)
                    dve.wait_ge(xt_done.sem, i + n0 + 1)
                    for k, t in ((1, xdt), (2, xw)):
                        v.tensor_tensor(t[:].rearrange("p c (h w) -> p c h w", h=2), K.ps[2][:].rearrange("p (c h w) -> p c h w", c=NT, h=2),
                                        toks_v[:, k, :, bass.ds(h0, 2)][:, :, :, None].to_broadcast([P, NT, 2, SSD_P]), ALU.mult).then_inc(xdt_done.sem, 1)
                    dve.wait_ge(st_mm.sem, i + n0 + 1)
                    per = 1 + 2 * (NT - 2)
                    v.tensor_copy(state[:, 0, :], K.ps[4][:, 0:P]).then_inc(st_done.sem, 1)
                    for c in range(1, NT - 1):
                        dve.wait_ge(st_done.sem, per * (i + n0) + 1 + 2 * (c - 1))
                        for hd in range(2):
                            lo, hi = hd * SSD_P, (hd + 1) * SSD_P
                            v.scalar_tensor_tensor(state[:, c, lo:hi], state[:, c - 1, lo:hi], edec[:, c, bass.ds(h0 + hd, 1)],
                                                   K.ps[4][:, c * P + lo:c * P + hi], ALU.mult, ALU.add).then_inc(st_done.sem, 1)
                    dve.wait_ge(e_done.sem, i + n0 + 1)
                    v.tensor_tensor(arg[:], arg[:], cbm[:, g:g + 1, :].to_broadcast([P, 2, S]), ALU.mult).then_inc(m_done.sem, 1)
                    v.tensor_tensor(eb[:], eb[:], ct[:, None, :].to_broadcast([P, 2, S]), ALU.mult).then_inc(cd_done.sem, 1)
                    dve.wait_ge(y_mm.sem, i + n0 + 1)
                    v.scalar_tensor_tensor(xdt[:].rearrange("p c w -> p (c w)"), xs[:], K.cols[:, bass.ds(dcol + n0 + i, 1)], K.ps[3][:], ALU.mult, ALU.add).then_inc(z_done.sem, 1)
                    dve.wait_ge(z_done.sem, i + n0 + 1)
                    zc = proj[:, bass.ds(Z + n0 + i, 1), :]
                    v.tensor_tensor(zc, zc, xdt[:].rearrange("p c w -> p (c w)")[:, None, :], ALU.mult).then_inc(y_done.sem, 1)


def hybrid_out(K, proj, GATE, nxt):
    nc = K.nc
    n = 2 * DC
    hi = K.at("hyb_hi", [P, n, S], F32R, K.h_at)
    lo = K.at("hyb_lo", [P, n, S], F32R, K.arena)
    B = K.arena + HYB * S * 4
    sq = K.at("hyb_sq", [P, DC, S], F32, B)
    rstd = K.at("hyb_rstd", [P, SSD_G, S], F32, B + DC * S * 4)
    sq_done, sum_done, r_done, root_done, v_done, hi_done = (K.sem(f"hyb_{k}") for k in ("sq", "sum", "r", "root", "v", "hi"))
    per = DC // SSD_G
    ng = K.cols_at["ssd_norm_g"][0]
    with nc.Block() as block:
        @block.scalar
        def _(act):
            for g in range(SSD_G):
                nc.scalar.activation(sq[:, per * g:per * (g + 1), :], proj[:, GATE + DC + per * g:GATE + DC + per * (g + 1), :], ACT.Square).then_inc(sq_done, 1)
            with act.Fori(0, DC) as c:
                nc.scalar.activation(hi[:, bass.ds(c, 1), :], proj[:, bass.ds(GATE + c, 1), :], ACT.Copy).then_inc(hi_done, 1)
            act.wait_ge(r_done, 4)
            nc.scalar.activation(rstd[:], rstd[:], ACT.Sqrt).then_inc(root_done, 1)
            with act.Fori(0, DC) as c:
                act.wait_ge(v_done, c + 1)
                nc.scalar.activation(hi[:, bass.ds(DC + c, 1), :], proj[:, bass.ds(GATE + DC + c, 1), :], ACT.Copy).then_inc(hi_done, 1)

        @block.tensor
        def _(pe):
            for g in range(SSD_G):
                pe.wait_ge(sq_done, g + 1)
                for c in range(per):
                    last = nc.tensor.matmul(K.ps[g][:], K.ones, sq[:, per * g + c, :], start=c == 0, stop=c == per - 1)
                last.then_inc(sum_done, 1)

        @block.vector
        def _(dve):
            v = nc.vector

            def low(c):
                v.tensor_tensor(lo[:, bass.ds(c, 1), :], proj[:, bass.ds(GATE + c, 1), :], hi[:, bass.ds(c, 1), :].bitcast(F32), ALU.subtract)
            for g in range(SSD_G):
                dve.wait_ge(sum_done, g + 1)
                v.tensor_scalar(rstd[:, g, :], K.ps[g][:], 1.0 / (per * P), EPS, ALU.mult, ALU.add).then_inc(r_done, 1)
            dve.wait_ge(r_done, 2)
            for g in range(SSD_G):
                v.reciprocal(rstd[:, g, :], rstd[:, g, :]).then_inc(r_done, 1)
            with dve.Fori(0, DC) as c:
                dve.wait_ge(hi_done, c + 1)
                low(c)
            dve.wait_ge(root_done, 1)
            for g in range(SSD_G):
                with dve.Fori(per * g, per * (g + 1)) as c:
                    y = proj[:, bass.ds(GATE + DC + c, 1), :]
                    v.scalar_tensor_tensor(y, y, K.cols[:, bass.ds(ng + c, 1)], rstd[:, g:g + 1, :], ALU.mult, ALU.mult).then_inc(v_done, 1)
            with dve.Fori(0, DC) as c:
                dve.wait_ge(hi_done, DC + 1 + c)
                low(c + DC)

    def mm(k, j):
        kc = (j % 2) * DC + k
        return hi[:, kc, :], lo[:, kc, :], j // 2, kc == 0, kc == n - 1

    project(K, K.dram["w_hout"], DC, 2, mm, nxt, lambda o: K.coef[:, bass.ds(o, 1)], Squares(K, "hyb", K.arena + n * S * 4))


def mlstm(K, nxt, head):
    nc, d = K.nc, K.dram
    A = K.arena
    PAD = S + CONV - 1
    xm = K.at("ml_xm", [P, MLC, PAD], F32, A)
    xc = K.at("ml_xc", [P, MLC, S], F32, A + MLC * PAD * 4)
    B = A + MLC * (PAD + S) * 4
    at = [B]

    def sb(name, shape):
        t = K.at("ml_" + name, shape, F32, at[0])
        at[0] += (int(np.prod(shape[1:])) * 4 + 31) // 32 * 32
        return t
    r_row, m_row = sb("r_row", [ML_H, S]), sb("m_row", [ML_H, S])
    ccol = sb("ccol", [P, NT, ML_H])
    sel = sb("sel", [P, S])
    bd = sb("bd", [P, HC, 3 * P])
    mix = at[0]
    q, k, v, e = (sb(n, [P, HC, S]) for n in "qkve")
    pad_done = K.sem("ml_pad_zeroed")

    with nc.Block() as block:
        @block.vector
        def _(dve):
            nc.vector.memset(xm[:, :, 0:CONV - 1], 0.0).then_inc(pad_done, 1)

    ae, de = conv_evacs(K, xm, xc, 0, 0, "ml_conv_w", "ml_conv_b", MLC, ring=False)
    stream_out(K, d["w_xm"], MLC, (d["w_z"], DC), ae, de, head=head)
    K.conv_step.base += CONV * MLC
    head_written = K.sem("mlh_y")
    ml_gates(K, xm, xc, r_row, m_row, ccol, mix, head_written)
    ml_heads(K, xm, xc, r_row, m_row, ccol, sel, bd, q, k, v, e, head_written)

    hi = K.at("ml_hi", [P, MLC, S], F32R, A + MLC * PAD * 4)
    lo = K.at("ml_lo", [P, MLC, S], F32R, B)
    sz = K.at("ml_sz", [P, 2, S], F32, B + MLC * S * 4)
    y_done, hi_done = K.count("ml_y"), K.sem("ml_hi_done")
    free = K.bank_free

    def act_evac(act, i, j, t, mm_done):
        act.wait_ge(K.tile_mm.sem, mm_done)
        nc.scalar.activation(sz[:, j % 2, :], K.ps[j][:], ACT.Silu).then_inc(free.sem, 1)
        act.wait_ge(y_done.sem, t + 1)
        nc.scalar.activation(hi[:, bass.ds(t, 1), :], xm[:, bass.ds(t, 1), CONV - 1:], ACT.Copy).then_inc(hi_done, 1)

    def dve_evac(dve, i, j, t, mm_done):
        y = xm[:, bass.ds(t, 1), CONV - 1:]
        dve.wait_ge(free.sem, free(t + 1))
        nc.vector.tensor_tensor(y, y, sz[:, j % 2:j % 2 + 1, :], ALU.mult).then_inc(y_done.sem, 1)
        dve.wait_ge(hi_done, t + 1)
        nc.vector.tensor_tensor(lo[:, bass.ds(t, 1), :], y, hi[:, bass.ds(t, 1), :].bitcast(F32), ALU.subtract)

    stream_out(K, d["w_z"], MLC, (d["w_mdown"], DC), act_evac, dve_evac)

    def mm(kk, j):
        kc = (j % 2) * DC + kk
        return hi[:, kc, :], lo[:, kc, :], j // 2, kc == 0, kc == MLC - 1

    project(K, d["w_mdown"], DC, 2, mm, nxt, lambda o: K.coef[:, bass.ds(o, 1)], Squares(K, "ml", K.h_at))


def ml_gates(K, xm, xc, r_row, m_row, ccol, base, head_written):
    nc, d = K.nc, K.dram
    at = [base]

    def sb(name, shape):
        t = K.at("mlg_" + name, shape, F32, at[0])
        at[0] += (int(np.prod(shape[1:])) * 4 + 31) // 32 * 32
        return t
    qkv = sb("qkv", [P, 2, 3, S])
    w = sb("w", [P, 2, 3 * P])
    wg = sb("wg", [P, 2, 6 * ML_F])
    acc = sb("acc", [2 * ML_F, S])
    i_pre, z, lf, e, t2, zero = (sb(n, [ML_H, S]) for n in ("i", "z", "lf", "e", "t2", "zero"))
    silu_done, w_loaded = K.sem("mlg_silu"), [K.sem(f"mlg_w{j}") for j in range(2)]
    qkv_mm, qkv_done, gate_mm, acc_done = (K.count(f"mlg_{n}") for n in ("qkv_mm", "qkv", "gate_mm", "acc"))
    order, abs_done, exp_done, m_done, tr_done = K.count("mlg_order"), K.sem("mlg_abs"), K.sem("mlg_exp"), K.sem("mlg_m"), K.sem("mlg_tr")
    bi, bf = (K.cols[0:ML_H, K.cols_at[n][0]:K.cols_at[n][0] + 1] for n in ("ml_bi", "ml_bf"))
    with nc.Block() as block:
        @block.sync
        def _(sp):
            def load(c, j):
                sp.dma_start(w[:, j:j + 1, :], d["w_qkv"][bass.ds(c, 1)].rearrange("o p n -> p o n")).then_inc(w_loaded[j], 16)
                sp.dma_start(wg[:, j:j + 1, :], d["w_gates"][bass.ds(c, 1)].rearrange("o p n -> p o n")).then_inc(w_loaded[j], 16)
            for j in range(2):
                load(j, j)
            with sp.Fori(0, MLC // 2 - 1) as i:
                for j in range(2):
                    sp.wait_ge(gate_mm.sem, 2 * i + j + 1)
                    load(2 * i + j + 2, j)

        @block.scalar
        def _(act):
            for c in range(0, MLC, HC):
                nc.scalar.activation(xc[:, c:c + HC, :], xc[:, c:c + HC, :], ACT.Silu).then_inc(silu_done, 1)
            with act.Fori(0, MLC // 2) as i:
                for j in range(2):
                    act.wait_ge(qkv_mm.sem, 2 * i + j + 1)
                    for n in range(3):
                        nc.scalar.activation(qkv[:, j, n, :], K.ps[3 * j + n][:], ACT.Copy).then_inc(qkv_done.sem, 1)
            act.wait_ge(abs_done, 1)
            nc.scalar.activation(e[:], e[:], ACT.Exp, scale=-1.0).then_inc(exp_done, 1)
            act.wait_ge(m_done, 1)
            nc.scalar.activation(m_row[:], m_row[:], ACT.Exp, scale=-1.0)

        @block.tensor
        def _(pe):
            pe.wait_ge(silu_done, ML_H)

            def body(i, first):
                for j in range(2):
                    pe.wait_ge(w_loaded[j], 32 * i + 32)
                    c = 2 * i + j
                    if not first:
                        pe.wait_ge(qkv_done.sem, 3 * (c - 1))
                    for n, src in enumerate((xc[:, bass.ds(c, 1), :], xc[:, bass.ds(c, 1), :], xm[:, bass.ds(c, 1), CONV - 1:])):
                        last = nc.tensor.matmul(K.ps[3 * j + n][:], w[:, j, n * P:(n + 1) * P], src, start=True, stop=True)
                    last.then_inc(qkv_mm.sem, 1)
                for j in range(2):
                    c = 2 * i + j
                    pe.wait_ge(qkv_done.sem, 3 * (c + 1))
                    if not first:
                        pe.wait_ge(acc_done.sem, c)
                    for n in range(3):
                        last = nc.tensor.matmul(K.ps[6 + j][0:2 * ML_F, :], wg[:, j, 2 * n * ML_F:2 * (n + 1) * ML_F], qkv[:, j, n, :], start=n == 0, stop=n == 2)
                    last.then_inc(gate_mm.sem, 1)
            body(0, True)
            with pe.Fori(1, MLC // 2) as i:
                body(i, False)
            pe.wait_ge(order.sem, ML_GATE_STEPS)
            for c in range(NT):
                last = nc.tensor.transpose(K.ps[0][:, c * ML_H:(c + 1) * ML_H], t2[:, c * P:(c + 1) * P], K.ident[0:ML_H, 0:ML_H])
            last.then_inc(tr_done, 1)

        @block.vector
        def _(dve):
            v = nc.vector
            link = Chain(dve, order)
            v.memset(acc[:], 0.0).then_inc(acc_done.sem, 1)
            with dve.Fori(0, MLC // 2) as i:
                for j in range(2):
                    c = 2 * i + j
                    dve.wait_ge(gate_mm.sem, c + 1)
                    dve.wait_ge(acc_done.sem, c + 1)
                    v.tensor_tensor(acc[:], acc[:], K.ps[6 + j][0:2 * ML_F, :], ALU.add).then_inc(acc_done.sem, 1)
            dve.wait_ge(acc_done.sem, MLC + 1)
            link(v.memset(zero[:], 0.0))
            link(v.tensor_scalar(i_pre[:], acc[0:ML_H, :], bi, None, ALU.add))
            link(v.tensor_copy(z[:], acc[ML_F:ML_F + ML_H, :]))
            link(v.tensor_scalar(z[:], z[:], bf, -1.0, ALU.add, ALU.mult))

            def exp_of():
                v.tensor_copy(t2[:], e[:]).then_inc(abs_done, 1)
                dve.wait_ge(exp_done, 1)
            softplus_steps(nc, link, z[:], lf[:], e[:], t2[:], exp_of)
            link(v.tensor_scalar(lf[:], lf[:], -1.0, None, ALU.mult))
            link(v.tensor_tensor_scan(z[:], lf[:], zero[:], 0.0, ALU.add, ALU.add))
            link(v.tensor_tensor_scan(m_row[:], lf[:], i_pre[:], 0.0, ALU.add, ALU.max))
            link(v.tensor_tensor(r_row[:], z[:], m_row[:], ALU.subtract))
            v.tensor_tensor(e[:], z[:], m_row[:], ALU.add).then_inc(m_done, 1)
            link(v.tensor_tensor(t2[:], z[:], i_pre[:], ALU.subtract))
            assert link.n == ML_GATE_STEPS, link.n
            dve.wait_ge(tr_done, 1)
            v.tensor_copy(ccol[:], K.ps[0][:, 0:NT * ML_H].rearrange("p (c h) -> p c h", c=NT)).then_inc(head_written, 1)


ML_GATE_STEPS = 17 + LOG1P_TERMS


def ml_heads(K, xm, xc, r_row, m_row, ccol, sel, bd, q, k, v, e, head_written):
    nc, d = K.nc, K.dram
    names = ("bd_free", "xs", "q_mm", "k_mm", "q", "k", "v_mm", "v", "sel", "bc", "arg", "e", "s_mm", "s", "den_mm", "rec", "num_mm", "h",
             "mean_mm", "hc", "sq", "var_mm", "r", "root", "mu")
    N = {n: K.count("mlh_" + n) for n in names}
    bd_loaded = K.sem("mlh_bd_loaded")
    gcol, scol = K.cols_at["ml_norm_g"][0], K.cols_at["ml_skip"][0]
    h_t, sq, xs = q, k, e
    mu = sel
    rows = slice(0, ML_H)
    with nc.Block() as block:
        @block.sync
        def _(sp):
            def load(h):
                sp.dma_start(bd[:], d["w_qkv"][bass.ds(HC * h, HC)].rearrange("c p n -> p c n")).then_inc(bd_loaded, 16)
            load(0)
            with sp.Fori(0, ML_H - 1) as h:
                sp.wait_ge(N["v_mm"].sem, h + 1)
                load(h + 1)

        @block.gpsimd
        def _(pool):
            with pool.Fori(0, ML_H) as h:
                pool.wait_ge(head_written, 4 * h + 1)
                nc.gpsimd.tensor_copy(xs[:], xm[:, bass.ds(HC * h, HC), CONV - 1:]).then_inc(N["xs"].sem, 1)

        @block.tensor
        def _(pe):
            mmul = nc.tensor.matmul
            with pe.Fori(0, ML_H) as h:
                pe.wait_ge(bd_loaded, 16 * h + 16)
                pe.wait_ge(head_written, 4 * h + 1)
                for c in range(HC):
                    last = mmul(K.ps[c][:], bd[:, c, 0:P], xc[:, bass.ds(HC * h + c, 1), :], start=True, stop=True)
                    last.then_inc(N["q_mm"].sem, 1)
                for c in range(HC):
                    last = mmul(K.ps[4 + c][:], bd[:, c, P:2 * P], xc[:, bass.ds(HC * h + c, 1), :], start=True, stop=True)
                    last.then_inc(N["k_mm"].sem, 1)
                pe.wait_ge(N["xs"].sem, h + 1)
                for t in range(NT):
                    pe.wait_ge(N["q"].sem, 4 * h + t + 1)
                    for c in range(HC):
                        last = mmul(K.ps[t][:, c * P:(c + 1) * P], xs[:, c, t * P:(t + 1) * P], bd[:, c, 2 * P:3 * P], start=True, stop=True)
                last.then_inc(N["v_mm"].sem, 1)
                pe.wait_ge(N["k"].sem, 4 * h + 4)
                pe.wait_ge(N["sel"].sem, 2 * h + 1)
                mmul(K.ps[4][:], K.ones[rows, :], sel[rows, :], start=True, stop=True).then_inc(N["bc"].sem, 1)
                pe.wait_ge(N["sel"].sem, 2 * h + 2)
                mmul(K.ps[5][:], K.ones[rows, :], sel[rows, :], start=True, stop=True).then_inc(N["bc"].sem, 1)
                for sb in range(NT):
                    pe.wait_ge(N["v"].sem, 4 * h + sb + 1)
                    for c in range(HC):
                        last = mmul(K.ps[sb][:, sb * P:], k[:, c, sb * P:(sb + 1) * P], q[:, c, sb * P:], start=c == 0, stop=c == HC - 1)
                    last.then_inc(N["s_mm"].sem, 1)
                for sb in range(NT):
                    pe.wait_ge(N["s"].sem, 4 * h + sb + 1)
                    last = mmul(K.ps[6][:, sb * P:], K.ones, e[:, sb, sb * P:], start=sb == 0, stop=sb == NT - 1, skip_group_check=True)
                last.then_inc(N["den_mm"].sem, 1)
                for c in range(HC):
                    for sb in range(NT):
                        last = mmul(K.ps[c][:, sb * P:], v[:, sb, c * P:(c + 1) * P], e[:, sb, sb * P:], start=sb == 0, stop=sb == NT - 1, skip_group_check=True)
                    last.then_inc(N["num_mm"].sem, 1)
                for c in range(HC):
                    pe.wait_ge(N["h"].sem, 4 * h + c + 1)
                    last = mmul(K.ps[7][:], K.ones, h_t[:, c, :], start=c == 0, stop=c == HC - 1)
                last.then_inc(N["mean_mm"].sem, 1)
                pe.wait_ge(N["sq"].sem, h + 1)
                for c in range(HC):
                    last = mmul(K.ps[4][:], K.ones, sq[:, c, :], start=c == 0, stop=c == HC - 1)
                last.then_inc(N["var_mm"].sem, 1)

        @block.scalar
        def _(act):
            with act.Fori(0, ML_H) as h:
                for c in range(HC):
                    act.wait_ge(N["q_mm"].sem, 4 * h + c + 1)
                    nc.scalar.activation(q[:, c, :], K.ps[c][:], ACT.Copy).then_inc(N["q"].sem, 1)
                for c in range(HC):
                    act.wait_ge(N["k_mm"].sem, 4 * h + c + 1)
                    nc.scalar.activation(k[:, c, :], K.ps[4 + c][:], ACT.Copy, scale=float(HC * P) ** -0.5).then_inc(N["k"].sem, 1)
                for sb in range(NT):
                    act.wait_ge(N["arg"].sem, 4 * h + sb + 1)
                    nc.scalar.activation(e[:, sb, sb * P:], e[:, sb, sb * P:], ACT.Exp).then_inc(N["e"].sem, 1)
                act.wait_ge(N["hc"].sem, h + 1)
                nc.scalar.activation(sq[:], h_t[:], ACT.Square).then_inc(N["sq"].sem, 1)
                act.wait_ge(N["r"].sem, 2 * h + 2)
                nc.scalar.activation(mu[:], mu[:], ACT.Sqrt).then_inc(N["root"].sem, 1)

        @block.vector
        def _(dve):
            vv = nc.vector
            with dve.Fori(0, ML_H) as h:
                one = K.consts[rows, bass.ds(h, 1)]
                dve.wait_ge(N["v_mm"].sem, h + 1)
                for t in range(NT):
                    vv.tensor_copy(v[:, t, :], K.ps[t][:]).then_inc(N["v"].sem, 1)
                vv.tensor_scalar(sel[rows, :], r_row[:], one, None, ALU.mult).then_inc(N["sel"].sem, 1)
                dve.wait_ge(N["bc"].sem, 2 * h + 1)
                vv.tensor_scalar(sel[rows, :], m_row[:], one, None, ALU.mult).then_inc(N["sel"].sem, 1)
                for sb in range(NT):
                    vv.tensor_scalar(e[:, sb, sb * P:], K.ps[4][:, sb * P:], ccol[:, sb, bass.ds(h, 1)], 0.0, ALU.subtract, ALU.min).then_inc(N["arg"].sem, 1)
                for sb in range(NT):
                    dve.wait_ge(N["e"].sem, 4 * h + sb + 1)
                    blk = e[:, sb, sb * P:(sb + 1) * P]
                    vv.tensor_tensor(blk, blk, K.causal, ALU.mult).then_inc(N["mu"].sem, 1)
                    dve.wait_ge(N["s_mm"].sem, 4 * h + sb + 1)
                    dve.wait_ge(N["mu"].sem, 7 * h + sb + 1)
                    vv.tensor_tensor(e[:, sb, sb * P:], e[:, sb, sb * P:], K.ps[sb][:, sb * P:], ALU.mult).then_inc(N["s"].sem, 1)
                rec = sel
                dve.wait_ge(N["den_mm"].sem, h + 1)
                vv.tensor_scalar(rec[:], K.ps[6][:], -1.0, None, ALU.mult).then_inc(N["rec"].sem, 1)
                dve.wait_ge(N["rec"].sem, 4 * h + 1)
                vv.tensor_tensor(rec[:], rec[:], K.ps[6][:], ALU.max).then_inc(N["rec"].sem, 1)
                dve.wait_ge(N["rec"].sem, 4 * h + 2)
                dve.wait_ge(N["bc"].sem, 2 * h + 2)
                vv.tensor_tensor(rec[:], rec[:], K.ps[5][:], ALU.max).then_inc(N["rec"].sem, 1)
                dve.wait_ge(N["rec"].sem, 4 * h + 3)
                vv.reciprocal(rec[:], rec[:]).then_inc(N["rec"].sem, 1)
                dve.wait_ge(N["rec"].sem, 4 * h + 4)
                for c in range(HC):
                    dve.wait_ge(N["num_mm"].sem, 4 * h + c + 1)
                    vv.tensor_tensor(h_t[:, c, :], K.ps[c][:], rec[:], ALU.mult).then_inc(N["h"].sem, 1)
                dve.wait_ge(N["mean_mm"].sem, h + 1)
                dve.wait_ge(N["h"].sem, 4 * h + 4)
                vv.tensor_scalar(mu[:], K.ps[7][:], 1.0 / (HC * P), None, ALU.mult).then_inc(N["mu"].sem, 1)
                dve.wait_ge(N["mu"].sem, 7 * h + 5)
                vv.tensor_tensor(h_t[:], h_t[:], mu[:, None, :].to_broadcast([P, HC, S]), ALU.subtract).then_inc(N["hc"].sem, 1)
                dve.wait_ge(N["var_mm"].sem, h + 1)
                vv.tensor_scalar(mu[:], K.ps[4][:], 1.0 / (HC * P), EPS, ALU.mult, ALU.add).then_inc(N["r"].sem, 1)
                dve.wait_ge(N["r"].sem, 2 * h + 1)
                vv.reciprocal(mu[:], mu[:]).then_inc(N["r"].sem, 1)
                dve.wait_ge(N["root"].sem, h + 1)
                vv.tensor_tensor(h_t[:], h_t[:], mu[:, None, :].to_broadcast([P, HC, S]), ALU.mult).then_inc(N["mu"].sem, 1)
                dve.wait_ge(N["mu"].sem, 7 * h + 6)
                for c in range(HC):
                    ins = vv.tensor_scalar(h_t[:, c, :], h_t[:, c, :], K.cols[:, bass.ds(gcol + HC * h + c, 1)], None, ALU.mult)
                ins.then_inc(N["mu"].sem, 1)
                dve.wait_ge(N["mu"].sem, 7 * h + 7)
                for c in range(HC):
                    vv.scalar_tensor_tensor(xm[:, bass.ds(HC * h + c, 1), CONV - 1:], xc[:, bass.ds(HC * h + c, 1), :],
                                            K.cols[:, bass.ds(scol + HC * h + c, 1)], h_t[:, c:c + 1, :], ALU.mult, ALU.add).then_inc(head_written, 1)


def second_block(K):
    nc, d = K.nc, K.dram
    A = K.arena
    o_hi = K.at("oa_hi", [P, 2, S], F32R, A)
    o_lo = K.at("oa_lo", [P, 2, S], F32R, A + 4096)
    p1 = K.at("attn_proj", [P, 2 + QKV, S], F32, A + 8192)
    raw1 = K.at("shift_raw1", [P, 2, S + 1], F32, A + 8192 + (2 + QKV) * S * 4)
    rkv = K.at("rkv", [P, 3 * DC, S], F32, A + 8192 + 4096)
    raw2 = K.at("shift_raw2", [P, 2, S + 1], F32, A + 8192 + 4096 + 3 * DC * S * 4)
    lora = p1[:, 0:2, :]
    m = [K.mods[:, 144 + 8 * n:152 + 8 * n] for n in range(6)]
    sh1, sc1, gt1, sh2, sc2, gt2 = m
    head = Modulated(K, col(K, "mix_pre", 0, 8), sc1, sh1, gt1, 1.0)
    mu0 = K.cols_at["shift_mu"][0]
    shifted = K.count("shifted")
    for n, (w, n_tiles, raw, dst, o0, nxt) in enumerate((("w_attn", 2 + QKV, raw1, p1, 0, "w_rkv"), ("w_rkv", 3 * DC, raw2, rkv, 2 + QKV, "w_gate2"))):
        pad = K.sem(f"shift_pad{n}")
        with nc.Block() as block:
            @block.vector
            def _(dve):
                nc.vector.memset(raw[:, :, 0:1], 0.0).then_inc(pad, 1)
                if n == 0:
                    nc.vector.memset(K.pad4[:], 0.0).then_inc(shifted.sem, 4)
                    shifted.base = 4
        ae, de = shift_evacs(K, raw, dst, mu0 + o0, shifted)
        stream_out(K, d[w], n_tiles, (d[nxt], DC), ae, de, head=head if n == 0 else None, fetch=RING if n == 0 else RWKV_FETCH)
        shifted.base += 2 * n_tiles
        if n == 0:
            with stage(K):
                attention(K, p1, o_hi, o_lo, A + 8192 + (2 + QKV) * S * 4)
    with stage(K):
        rwkv(K, lora, rkv, A + 8192 + 4096 + 3 * DC * S * 4)

    G = A + 8192 + 4096 + 3 * DC * S * 4
    gates = K.at("branch_gates", [P, 2 * DC, S], F32, G)
    r_hi = K.at("or_hi", [P, DC, S], F32R, A + 8192 + 4096 + DC * S * 4)
    r_lo = K.at("or_lo", [P, DC, S], F32R, A + 8192 + 4096 + 2 * DC * S * 4)
    sp_hi = K.sem("or_hi_done")
    with nc.Block() as block:
        @block.scalar
        def _(act):
            for c in range(0, DC, 2):
                nc.scalar.activation(r_hi[:, c:c + 2, :], rkv[:, c:c + 2, :], ACT.Copy).then_inc(sp_hi, 1)

        @block.vector
        def _(dve):
            for c in range(0, DC, 2):
                dve.wait_ge(sp_hi, c // 2 + 1)
                nc.vector.tensor_tensor(r_lo[:, c:c + 2, :], rkv[:, c:c + 2, :], r_hi[:, c:c + 2, :].bitcast(F32), ALU.subtract)
    stream_out(K, d["w_gate2"], 2 * DC, (d["w_branch"], 2 + DC), act_out(K, gates, 0, ACT.Sigmoid), fetched=RWKV_FETCH)

    free, merged, hi_done = K.bank_free, K.count("merged"), K.sem("merged_hi")

    def mm(k, j):
        if k < 2:
            return o_hi[:, k, :], o_lo[:, k, :], 2 * j, k == 0, k == 1
        return r_hi[:, k - 2, :], r_lo[:, k - 2, :], 2 * j + 1, k == 2, k == 1 + DC

    def pe_wait(pe, i, j, t):
        pe.wait_ge(free.sem, free(t - RING + 1))

    def act_evac(act, i, j, t, mm_done):
        act.wait_ge(merged.sem, 2 * t + 2)
        nc.scalar.activation(K.h_hi[:, bass.ds(t, 1), :], gates[:, bass.ds(t, 1), :], ACT.Copy).then_inc(hi_done, 1)

    def dve_evac(dve, i, j, t, mm_done):
        ga, gr = gates[:, bass.ds(t, 1), :], gates[:, bass.ds(DC + t, 1), :]
        dve.wait_ge(K.tile_mm.sem, mm_done)
        nc.vector.tensor_tensor(ga, ga, K.ps[2 * j][:, None, :], ALU.mult).then_inc(merged.sem, 1)
        nc.vector.tensor_tensor(gr, gr, K.ps[2 * j + 1][:, None, :], ALU.mult).then_inc(free.sem, 1)
        dve.wait_ge(merged.sem, 2 * t + 1)
        dve.wait_ge(free.sem, free(t + 1))
        nc.vector.tensor_tensor(ga, ga, gr, ALU.add).then_inc(merged.sem, 1)
        dve.wait_ge(hi_done, t + 1)
        nc.vector.tensor_tensor(K.h_lo[:, bass.ds(t, 1), :], ga, K.h_hi[:, bass.ds(t, 1), :].bitcast(F32), ALU.subtract)

    gemm(K, d["w_branch"], 2 + DC, DC, (d["w_out2"], DC), mm, pe_wait, act_evac, dve_evac)
    free.base += DC
    mix = K.at("mix_out", [P, DC, S], F32, G)
    squares = Squares(K, "mix", A + 8192 + 4096, RING)

    def square_mix(dve, i, j, t, mm_done):
        dve.wait_ge(free.sem, free(t + 1))
        squares.by_dve(dve, mix[:, bass.ds(t, 1), :], t, j % 2)
    stream_out(K, d["w_out2"], DC, (d["w_ff10"], DC), act_out(K, mix, 0, ACT.Copy), square_mix, squares=squares)
    norm(K, "n2p", mix, col(K, "mix_post", 0, 8), gate=gt1, squares=Squares(K, "x2", K.h_at + 4 * S * 4))

    head = Modulated(K, col(K, "ffn_pre", 0, 8), sc2, sh2, gt2, 1.0)
    HF = FF2 // 2
    u_hi = K.at("u_hi", [P, HF, S], F32R, A)
    u_lo = K.at("u_lo", [P, HF, S], F32R, A + HF * S * 4)
    f = K.at("ffn_out", [P, DC, S], F32, A + 2 * HF * S * 4)
    rel = K.at("relu", [P, 2, S], F32, A + (2 * HF + DC) * S * 4)
    squared = K.count("squared")
    uhi = K.count("u_hi_done")
    for half in range(2):
        def act_evac(act, i, j, t, mm_done):
            act.wait_ge(K.tile_mm.sem, mm_done)
            nc.scalar.activation(rel[:, j % 2, :], K.ps[j][:], ACT.Relu).then_inc(free.sem, 1)
            act.wait_ge(squared.sem, squared(t + 1))
            nc.scalar.activation(u_hi[:, bass.ds(t, 1), :], rel[:, j % 2:j % 2 + 1, :], ACT.Copy).then_inc(uhi.sem, 1)

        def dve_evac(dve, i, j, t, mm_done):
            r = rel[:, j % 2:j % 2 + 1, :]
            dve.wait_ge(free.sem, free(t + 1))
            nc.vector.tensor_tensor(r, r, r, ALU.mult).then_inc(squared.sem, 1)
            dve.wait_ge(uhi.sem, uhi(t + 1))
            nc.vector.tensor_tensor(u_lo[:, bass.ds(t, 1), :], r, u_hi[:, bass.ds(t, 1), :].bitcast(F32), ALU.subtract)

        stream_out(K, d[f"w_ff1{half}"], HF, (d[f"w_ff2{half}"], DC), act_evac, dve_evac, head=head if half == 0 else None)
        squared.base += HF
        uhi.base += HF

        def mm(k, j):
            kc = (j % 2) * DC + k
            return u_hi[:, kc, :], u_lo[:, kc, :], j // 2, kc == 0, kc == HF - 1

        def pe_wait(pe, i, j, t):
            if j % 2 == 0:
                pe.wait_ge(free.sem, free(2 * i + j // 2 - 1))

        def dve_evac2(dve, i, j, t, mm_done):
            if j % 2 == 1:
                o = f[:, bass.ds(2 * i + j // 2, 1), :]
                dve.wait_ge(K.tile_mm.sem, mm_done)
                if half == 0:
                    ins = nc.vector.tensor_copy(o, K.ps[j // 2][:, None, :])
                else:
                    ins = nc.vector.tensor_tensor(o, o, K.ps[j // 2][:, None, :], ALU.add)
                ins.then_inc(free.sem, 1)

        squares = Squares(K, "ffn", K.h_at) if half else None

        def square_f(act, i, j, t, mm_done):
            if j % 2 == 1:
                o = 2 * i + j // 2
                act.wait_ge(free.sem, free(o + 1))
                squares.by_act(act, f[:, bass.ds(o, 1), :], o, j // 2)

        gemm(K, d[f"w_ff2{half}"], DC, 2 * DC, (d["w_ff11"], DC) if half == 0 else None, mm, pe_wait, square_f if half else None, dve_evac2,
             squares=squares)
        free.base += DC
    norm(K, "n2f", f, col(K, "ffn_post", 0, 8), gate=gt2, store=K.stored)


def shift_evacs(K, raw, dst, mu0, shifted):
    nc, free = K.nc, K.bank_free

    def act_evac(act, i, j, t, mm_done):
        act.wait_ge(K.tile_mm.sem, mm_done)
        act.wait_ge(shifted.sem, shifted(2 * (t - 1)))
        nc.scalar.activation(raw[:, j % 2, 1:], K.ps[j][:], ACT.Copy).then_inc(free.sem, 1)

    def dve_evac(dve, i, j, t, mm_done):
        u, prev = raw[:, j % 2:j % 2 + 1, 1:], raw[:, j % 2:j % 2 + 1, 0:S]
        o = dst[:, bass.ds(t, 1), :]
        dve.wait_ge(free.sem, free(t + 1))
        nc.vector.tensor_tensor(o, prev, u, ALU.subtract).then_inc(shifted.sem, 1)
        dve.wait_ge(shifted.sem, shifted(2 * t + 1))
        nc.vector.scalar_tensor_tensor(o, o, K.cols[:, bass.ds(mu0 + t, 1)], u, ALU.mult, ALU.add).then_inc(shifted.sem, 1)

    return act_evac, dve_evac


TWO_PI = (6.28125, 1.93500518798828125e-03, 3.0199160983e-07)
ROUND = 12582912.0


def attention(K, p1, o_hi, o_lo, base):
    nc, d = K.nc, K.dram
    at = [base]

    def sb(name, shape, dt=F32):
        t = K.at("at_" + name, shape, dt, at[0])
        at[0] += (int(np.prod(shape[1:])) * 4 + 31) // 32 * 32
        return t
    masks, mats = sb("masks", [P, 3 * P]), sb("mats", [P, 3 * P])
    cos, sin = sb("cos", [P, S]), sb("sin", [P, S])
    qp, kp, vp = sb("qp", [P, S]), sb("kp", [P, S]), sb("vp", [P, S])
    t1, t2 = sb("t1", [P, S]), sb("t2", [P, S])
    v_tok = sb("v_tok", [P, NT, P])
    sm = sb("sm", [P, 2, NT, P])
    pT = sb("pT", [P, 2, NT, P])
    o = sb("o", [P, GROUPS, 2, S])
    mx, l, lse = sb("mx", [P, GROUPS, NT, 4]), sb("l", [P, GROUPS, NT, 4]), sb("lse", [P, GROUPS, NT, 4])
    m2, rl = sb("m2", [P, NT]), sb("rl", [P, NT])
    rows, wrow = sb("rows", [4, GROUPS, S]), sb("wrow", [4, 2, S])
    pos = K.at("at_pos", [P, S], I32, at[0] - 5 * 2048)
    assert at[0] - base < 58 * 1024, at[0] - base
    rot = mats[:, 0:P]
    loaded, order = K.sem("at_loaded"), K.count("at_order")
    trig_done, half_done = K.sem("at_trig"), K.sem("at_half")
    inv = K.cols[:, K.cols_at["rope_inv"][0]:K.cols_at["rope_inv"][0] + 1]
    with nc.Block() as block:
        @block.sync
        def _(sp):
            sp.dma_start(masks[:], d["attn_masks"]).then_inc(loaded, 16)
            sp.dma_start(mats[:], d["attn_mats"]).then_inc(loaded, 16)
            sp.dma_start(pos[:], d["positions"].to_broadcast([P, S])).then_inc(loaded, 16)
            sp.wait_ge(loaded, 48)

        @block.vector
        def _(dve):
            v = nc.vector
            link = Chain(dve, order)
            dve.wait_ge(loaded, 48)
            link(v.tensor_copy(t1[:], pos[:]))
            link(v.tensor_scalar(t1[:], t1[:], inv, None, ALU.mult))
            link(v.tensor_scalar(t2[:], t1[:], float(0.5 / np.pi), ROUND, ALU.mult, ALU.add))
            link(v.tensor_scalar(t2[:], t2[:], -ROUND, None, ALU.add))
            for part in TWO_PI:
                link(v.scalar_tensor_tensor(t1[:], t2[:], -part, t1[:], ALU.mult, ALU.add))
            link(v.tensor_scalar(t1[:], t1[:], float(np.float32(3.1415925)), -float(np.float32(3.1415925)), ALU.min, ALU.max))
            dve.wait_ge(trig_done, 2)
            link(v.tensor_tensor(cos[:], cos[:], cos[:], ALU.mult))
            link(v.tensor_scalar(cos[:], cos[:], -2.0, 1.0, ALU.mult, ALU.add))

        @block.scalar
        def _(act):
            act.wait_ge(order.sem, 8)
            nc.scalar.activation(sin[:], t1[:], ACT.Sin).then_inc(trig_done, 1)
            nc.scalar.activation(cos[:], t1[:], ACT.Sin, scale=0.5).then_inc(trig_done, 1)

    names = ("rot", "tq", "qk", "vp", "vt_mm", "vt", "s_mm", "sm", "max", "arg", "p", "sum", "rl", "pn", "pt_mm", "pt", "pv", "o")
    N = {n: K.count("ath_" + n) for n in names}
    for g in range(GROUPS):
        dil = DILATION[g]
        wide = 2 if g == 0 else 1

        def permuted(t):
            return t.rearrange("p (r j) -> p j r", r=dil) if dil > 1 else t

        def by_token(t):
            return t.rearrange("p (j r) -> p j r", r=dil) if dil > 1 else t

        b = {n: c.base for n, c in N.items()}
        with nc.Block() as block:
            @block.gpsimd
            def _(pool):
                with pool.Fori(0, 2) as i:
                    pool.wait_ge(N["o"].sem, b["o"] + i + 1)
                    nc.gpsimd.tensor_copy(permuted(vp[:]), by_token(p1[:, bass.ds(2 + 12 + 2 * g + i, 1), :].rearrange("p o s -> p (o s)"))).then_inc(N["vp"].sem, 1)

            @block.tensor
            def _(pe):
                with pe.Fori(0, 2) as i:
                    pe.wait_ge(N["o"].sem, b["o"] + i + 1)
                    for n in range(2):
                        nc.tensor.matmul(K.ps[n][:], rot, p1[:, bass.ds(2 + 6 * n + 2 * g + i, 1), :], start=True, stop=True).then_inc(N["rot"].sem, 1)
                    pe.wait_ge(N["vp"].sem, b["vp"] + i + 1)
                    for t in range(NT):
                        last = nc.tensor.transpose(K.ps[2][:, t * P:(t + 1) * P], vp[:, t * P:(t + 1) * P], K.ident)
                    last.then_inc(N["vt_mm"].sem, 1)
                    pe.wait_ge(N["qk"].sem, b["qk"] + 2 * i + 2)
                    for hd in range(2):
                        hr = slice(hd * HD, (hd + 1) * HD)
                        for w in range(wide):
                            for t in range(w, NT):
                                last = nc.tensor.matmul(K.ps[3 + w][:, t * P:(t + 1) * P], qp[hr, t * P:(t + 1) * P], kp[hr, (t - w) * P:(t - w + 1) * P], start=True, stop=True)
                        last.then_inc(N["s_mm"].sem, 1)
                        pe.wait_ge(N["pn"].sem, b["pn"] + 2 * i + hd + 1)
                        for w in range(wide):
                            for t in range(w, NT):
                                last = nc.tensor.transpose(K.ps[5 + w][:, t * P:(t + 1) * P], sm[:, w, t, :], K.ident)
                        last.then_inc(N["pt_mm"].sem, 1)
                        pe.wait_ge(N["pt"].sem, b["pt"] + wide * (2 * i + hd + 1))
                        pe.wait_ge(N["vt"].sem, b["vt"] + i + 1)
                        for t in range(NT):
                            for w in range(min(wide, t + 1)):
                                last = nc.tensor.matmul(K.ps[7][hr, t * P:(t + 1) * P], v_tok[:, t - w, hr], pT[:, w, t, :], start=w == 0, stop=w == min(wide, t + 1) - 1)
                        last.then_inc(N["pv"].sem, 1)

            @block.scalar
            def _(act):
                with act.Fori(0, 2) as i:
                    act.wait_ge(N["vt_mm"].sem, b["vt_mm"] + i + 1)
                    nc.scalar.activation(v_tok[:].rearrange("p t c -> p (t c)"), K.ps[2][:], ACT.Copy).then_inc(N["vt"].sem, 1)
                    for hd in range(2):
                        act.wait_ge(N["arg"].sem, b["arg"] + 2 * i + hd + 1)
                        nc.scalar.activation(sm[:, 0:wide], sm[:, 0:wide], ACT.Exp, scale=float(HD) ** -0.5).then_inc(N["p"].sem, 1)
                        act.wait_ge(N["pt_mm"].sem, b["pt_mm"] + 2 * i + hd + 1)
                        for w in range(wide):
                            nc.scalar.activation(pT[:, w, w:, :].rearrange("p t k -> p (t k)"), K.ps[5 + w][:, w * P:], ACT.Copy).then_inc(N["pt"].sem, 1)

            @block.vector
            def _(dve):
                v = nc.vector
                if g == 0:
                    v.memset(m2[:], 0.0).then_inc(N["o"].sem, 1)
                with dve.Fori(0, 2) as i:
                    for n, dst in ((0, qp), (1, kp)):
                        v.tensor_tensor(t1[:], p1[:, bass.ds(2 + 6 * n + 2 * g + i, 1), :].rearrange("p o s -> p (o s)"), cos[:], ALU.mult).then_inc(N["tq"].sem, 1)
                        dve.wait_ge(N["rot"].sem, b["rot"] + 2 * i + n + 1)
                        v.tensor_tensor(t2[:], K.ps[n][:], sin[:], ALU.mult).then_inc(N["tq"].sem, 1)
                        dve.wait_ge(N["tq"].sem, b["tq"] + 4 * i + 2 * n + 2)
                        v.tensor_tensor(permuted(dst[:]), by_token(t1[:]), by_token(t2[:]), ALU.add).then_inc(N["qk"].sem, 1)
                        dve.wait_ge(N["qk"].sem, b["qk"] + 2 * i + n + 1)
                    for hd in range(2):
                        u = 2 * i + hd
                        mxc, lc = mx[:, g, :, bass.ds(u, 1)], l[:, g, :, bass.ds(u, 1)]
                        dve.wait_ge(N["s_mm"].sem, b["s_mm"] + u + 1)
                        mask = masks[:, P:2 * P] if g == 2 else masks[:, 0:P]
                        v.tensor_tensor(sm[:, 0], K.ps[3][:].rearrange("p (t k) -> p t k", t=NT), mask[:, None, :].to_broadcast([P, NT, P]), ALU.add).then_inc(N["sm"].sem, 1)
                        if wide == 2:
                            v.memset(sm[:, 1, 0, :], NEG).then_inc(N["sm"].sem, 1)
                            v.tensor_tensor(sm[:, 1, 1:, :], K.ps[4][:, P:].rearrange("p (t k) -> p t k", t=NT - 1),
                                            masks[:, None, 2 * P:3 * P].to_broadcast([P, NT - 1, P]), ALU.add).then_inc(N["sm"].sem, 1)
                        per = 3 if wide == 2 else 1
                        dve.wait_ge(N["sm"].sem, b["sm"] + per * (u + 1))
                        v.tensor_reduce(mxc, sm[:, 0], AX_X, ALU.max).then_inc(N["max"].sem, 1)
                        if wide == 2:
                            v.tensor_reduce(m2[:], sm[:, 1], AX_X, ALU.max).then_inc(N["max"].sem, 1)
                            dve.wait_ge(N["max"].sem, b["max"] + 3 * u + 2)
                            v.tensor_tensor(mxc, mxc, m2[:, :, None], ALU.max).then_inc(N["max"].sem, 1)
                        dve.wait_ge(N["max"].sem, b["max"] + per * (u + 1))
                        for w in range(wide):
                            ins = v.tensor_tensor(sm[:, w], sm[:, w], mxc.to_broadcast([P, NT, P]), ALU.subtract)
                        ins.then_inc(N["arg"].sem, 1)
                        dve.wait_ge(N["p"].sem, b["p"] + u + 1)
                        v.tensor_reduce(lc, sm[:, 0], AX_X, ALU.add).then_inc(N["sum"].sem, 1)
                        if wide == 2:
                            v.tensor_reduce(m2[:], sm[:, 1], AX_X, ALU.add).then_inc(N["sum"].sem, 1)
                            dve.wait_ge(N["sum"].sem, b["sum"] + 3 * u + 2)
                            v.tensor_tensor(lc, lc, m2[:, :, None], ALU.add).then_inc(N["sum"].sem, 1)
                        dve.wait_ge(N["sum"].sem, b["sum"] + per * (u + 1))
                        v.tensor_scalar(rl[:, :, None], lc, 1.0, None, ALU.mult).then_inc(N["rl"].sem, 1)
                        dve.wait_ge(N["rl"].sem, b["rl"] + 2 * u + 1)
                        v.reciprocal(rl[:], rl[:]).then_inc(N["rl"].sem, 1)
                        dve.wait_ge(N["rl"].sem, b["rl"] + 2 * u + 2)
                        for w in range(wide):
                            ins = v.tensor_tensor(sm[:, w], sm[:, w], rl[:, :, None].to_broadcast([P, NT, P]), ALU.mult)
                        ins.then_inc(N["pn"].sem, 1)
                    dve.wait_ge(N["pv"].sem, b["pv"] + 2 * i + 2)
                    v.tensor_copy(by_token(o[:, g, bass.ds(i, 1), :].rearrange("p o s -> p (o s)")), permuted(K.ps[7][:])).then_inc(N["o"].sem, 1)
        per = 3 if wide == 2 else 1
        for n, k in (("rot", 4), ("tq", 8), ("qk", 4), ("vp", 2), ("vt_mm", 2), ("vt", 2), ("s_mm", 4), ("sm", 4 * per), ("max", 4 * per), ("arg", 4), ("p", 4),
                     ("sum", 4 * per), ("rl", 8), ("pn", 4), ("pt_mm", 4), ("pt", 4 * wide), ("pv", 4), ("o", 2)):
            N[n].base += k

    order2, ln_done, tr_done, e_done, bc_done, fin, hi_done = (K.count("atw_order"), *(K.sem("atw_" + n) for n in ("ln", "tr", "e", "bc", "fin", "hi")))
    rows_done = K.sem("atw_rows")
    with nc.Block() as block:
        @block.scalar
        def _(act):
            nc.scalar.activation(l[:], l[:], ACT.Ln).then_inc(ln_done, 1)
            act.wait_ge(order2.sem, 7)
            nc.scalar.activation(rows[:], rows[:], ACT.Exp).then_inc(e_done, 1)
            for c in range(2):
                act.wait_ge(fin, c + 1)
                nc.scalar.activation(o_hi[:, c, :], o[:, 0, c, :], ACT.Copy).then_inc(hi_done, 1)

        @block.tensor
        def _(pe):
            pe.wait_ge(order2.sem, 1)
            for g in range(GROUPS):
                for t in range(NT):
                    last = nc.tensor.transpose(K.ps[g][0:4, t * P:(t + 1) * P], lse[:, g, t, :], K.ident)
            last.then_inc(tr_done, 1)
            pe.wait_ge(order2.sem, 11)
            for c in range(2):
                for g in range(GROUPS):
                    nc.tensor.matmul(K.ps[GROUPS * c + g][:], mats[0:4, (1 + c) * P:(2 + c) * P], rows[:, g, :], start=True, stop=True).then_inc(bc_done, 1)

        @block.vector
        def _(dve):
            v = nc.vector
            link = Chain(dve, order2)
            dve.wait_ge(ln_done, 1)
            link(v.scalar_tensor_tensor(lse[:], mx[:], float(HD) ** -0.5, l[:], ALU.mult, ALU.add))
            dve.wait_ge(tr_done, 1)
            for g in range(GROUPS):
                dil = DILATION[g]
                src, dst = K.ps[g][0:4, :], rows[:, g, :]
                if dil > 1:
                    src, dst = src.rearrange("p (r j) -> p j r", r=dil), dst.rearrange("p (j r) -> p j r", r=dil)
                ins = v.tensor_copy(dst, src)
            link(ins)
            link(v.tensor_tensor(wrow[:, 0, :], rows[:, 0, :], rows[:, 1, :], ALU.max))
            link(v.tensor_tensor(wrow[:, 0, :], wrow[:, 0, :], rows[:, 2, :], ALU.max))
            for g in range(GROUPS):
                link(v.tensor_tensor(rows[:, g, :], rows[:, g, :], wrow[:, 0, :], ALU.subtract))
            dve.wait_ge(e_done, 1)
            link(v.tensor_tensor(wrow[:, 0, :], rows[:, 0, :], rows[:, 1, :], ALU.add))
            link(v.tensor_tensor(wrow[:, 0, :], wrow[:, 0, :], rows[:, 2, :], ALU.add))
            link(v.reciprocal(wrow[:, 1, :], wrow[:, 0, :]))
            link(v.tensor_tensor(rows[:], rows[:], wrow[:, 1:2, :].to_broadcast([4, GROUPS, S]), ALU.mult))
            for c in range(2):
                for g in range(GROUPS):
                    dve.wait_ge(bc_done, GROUPS * c + g + 1)
                    link(v.tensor_tensor(o[:, g, c, :], o[:, g, c, :], K.ps[GROUPS * c + g][:], ALU.mult))
                link(v.tensor_tensor(o[:, 0, c, :], o[:, 0, c, :], o[:, 1, c, :], ALU.add))
                v.tensor_tensor(o[:, 0, c, :], o[:, 0, c, :], o[:, 2, c, :], ALU.add).then_inc(fin, 1)
            for c in range(2):
                dve.wait_ge(hi_done, c + 1)
                v.tensor_tensor(o_lo[:, c, :], o[:, 0, c, :], o_hi[:, c, :].bitcast(F32), ALU.subtract)


RWKV_FETCH = 2
RWKV_DECAY = -float(np.exp(-0.5))


def rwkv(K, lora, rkv, base):
    nc, d = K.nc, K.dram
    at = [base]

    def sb(name, shape):
        t = K.at("rw_" + name, shape, F32, at[0])
        at[0] += (int(np.prod(shape[1:])) * 4 + 31) // 32 * 32
        return t
    masks = sb("masks", [P, 10 * P + 2 * LEVELS])
    log_w, a, kkn = (sb(n, [P, S]) for n in ("logw", "a", "kk"))
    raw = K.w_raw_at + RWKV_FETCH * SLOT_BYTES
    names = ("k", "b", "a_dec", "r", "bonus")
    kc, bc, ac, rc, bonus = ([sb(name, [P, S]), K.at(f"rw_{name}1", [P, S], F32, raw + n * S * 4)] for n, name in enumerate(names))
    w_lora, w_gate = sb("w_lora", [P, P]), sb("w_gate", [P, P])
    at_, bt, kt, vt, vs = (sb(n, [P, NT, P]) for n in ("a_tok", "b_tok", "k_tok", "v_tok", "v"))
    spare = [a + SLOT_BYTES + n * S * 4 for a in (K.w_hi_at, K.w_lo_at) for n in range(2)]
    abT = [sb("abT0", [P, NT, P]), K.at("rw_abT1", [P, NT, P], F32, spare[0])]
    T = [sb("T0", [P, NT, P]), K.at("rw_T1", [P, NT, P], F32, spare[1])]
    TT = [sb("TT0", [P, NT, P]), K.at("rw_TT1", [P, NT, P], F32, spare[2])]
    off = [sb("off0", [P, NT, P]), K.at("rw_off1", [P, NT, P], F32, spare[3])]
    W = [sb("W0", [P, NT, P]), sb("W1", [P, NT, P])]
    qs, y = sb("q", [P, S]), sb("y", [P, S])
    G, H = sb("G", [P, NT, HD]), sb("H", [P, NT, HD])
    sh = K.at("rw_sh", [P, P], F32, spare[1] + S * 4)
    s1 = K.at("rw_s1", [P, HD], F32, spare[1] + S * 4 + P * 4)
    mid, ka1 = sb("mid", [P, NT]), sb("ka1", [P, DC])
    pm, pl = ([sb(f"{n}{x}", [P, NT]) for x in range(2)] for n in ("pm", "pl"))
    assert at[0] <= K.nc.sbuf_usable_end, at[0] - K.nc.sbuf_usable_end
    akT, rbT, rkT, cat, xu = abT, T, off, W, TT
    strict, pair_t, pair = masks[:, 0:P], masks[:, P:2 * P], masks[:, 2 * P:3 * P]
    level = [masks[:, (3 + n) * P:(4 + n) * P] for n in range(LEVELS)]
    same = masks[:, 9 * P:10 * P]
    first_half = [masks[:, 10 * P + n:10 * P + n + 1] for n in range(LEVELS)]
    second_half = [masks[:, 10 * P + LEVELS + n:10 * P + LEVELS + n + 1] for n in range(LEVELS)]
    B = [[K.ps[4 * hd + n] for n in range(4)] for hd in range(2)]

    def half(x, lv, second):
        return x.rearrange("p t (n h b) -> p t n h b", h=2, b=2 << lv)[:, :, :, second, :]

    def half_of_chunk(x, lv, second):
        return x.rearrange("p (n h b) -> p n h b", h=2, b=2 << lv)[:, :, second, :]

    PER = {"lora": 2, "sig": 2, "kk": 1, "sq": 1, "ss": 1, "root": 1, "kkn": 4, "k2": 2, "rk": 1, "rk_mm": 1, "bonus": 1, "logw": 1, "cs": 4, "csm": 3,
           "exp": 4, "dec": 5, "vs": 1, "tr": 4, "tok": 4, "score": 10, "mask": 12, "ident": 4, "off": 2 * LEVELS, "w_mm": 2 * LEVELS, "w": 2 * LEVELS,
           "dT": 2 * LEVELS - 2, "dTT": 2 * LEVELS, "T": 2 * LEVELS - 2, "TT": 2 * LEVELS, "akv": 2, "cat": 4, "xu_mm": 2, "xu": 2, "qy": 2, "gh": 4, "qev": 8,
           "s": 10, "y_mm": 3, "s_mm": 2, "yadd": 1, "mean": 1, "yc": 1, "ysq": 1, "var": 1, "r": 2, "yroot": 1, "yn": 3, "g_mm": 1, "out": 1}
    N = {n: K.count("rw_" + n) for n in PER}

    def sig(ins, name):
        ins.then_inc(N[name].sem, 1)

    def after(eng, i, name, n):
        eng.wait_ge(N[name].sem, PER[name] * i + n)

    loaded, lora_act, ka_done = K.sem("rw_loaded"), K.sem("rw_lora_act"), K.sem("rw_ka")
    w_loaded = [K.sem(f"rw_w_loaded{x}") for x in range(2)]
    with nc.Block() as block:
        @block.sync
        def _(sp):
            sp.dma_start(masks[:], d["rwkv_masks"]).then_inc(loaded, 16)
            for n, x in enumerate((w_lora, w_gate)):
                sp.dma_start(x[:], d["w_lora"][0][:, n * P:(n + 1) * P]).then_inc(w_loaded[n], 16)
            sp.wait_ge(loaded, 16)

        @block.scalar
        def _(act):
            nc.scalar.activation(lora[0:HD, 0, :], lora[0:HD, 0, :], ACT.Tanh).then_inc(lora_act, 1)
            nc.scalar.activation(lora[:, 1, :], lora[:, 1, :], ACT.Sigmoid).then_inc(lora_act, 1)

        @block.vector
        def _(dve):
            nc.vector.tensor_scalar(ka1[:], col(K, "k_a", 0, 8), -1.0, 1.0, ALU.mult, ALU.add).then_inc(ka_done, 1)
            for x in (sh, *W, *off):
                nc.vector.memset(x[:], 0.0)

    def t4(x):
        return x.rearrange("p (t k) -> p t k", t=NT)

    def tl(x, t):
        return x[:, t * P:(t + 1) * P]

    halves = [slice(0, HD), slice(HD, P)]
    FREE = [B[0][1], B[1][1]]

    def turns(eng, turn):
        turn(0, 0, False, True)
        with eng.Fori(0, DC // 2 - 1) as i:
            turn(2 * i + 1, 1, True, True)
            turn(2 * i + 2, 0, True, True)
        turn(DC - 1, 1, True, False)

    def flat(x):
        return x.rearrange("p t k -> p (t k)")

    def chunk(n, i):
        return rkv[:, bass.ds(n * DC + i, 1), :].rearrange("p o s -> p (o s)")

    with nc.Block() as block:
        @block.sync
        def _(sp):
            def fetch(n, x, i):
                tile = d["w_lora"][bass.ds(i, 1), :, n * P:(n + 1) * P].rearrange("o p n -> p (o n)")
                sp.dma_start(x[:], tile).then_inc(w_loaded[n], 16)

            after(sp, 0, "lora", 2)
            fetch(0, w_lora, 1)
            with sp.Fori(0, DC - 2) as i:
                after(sp, i + 1, "lora", 2)
                fetch(0, w_lora, i + 2)
                after(sp, i, "g_mm", 1)
                fetch(1, w_gate, i + 1)
            after(sp, DC - 2, "g_mm", 1)
            fetch(1, w_gate, DC - 1)

        @block.gpsimd
        def _(pool):
            def values(i):
                sig(nc.gpsimd.tensor_copy(flat(vs[:]), chunk(2, i)), "vs")

            def turn(i, x, finish, prepare):
                for lv in range(LEVELS):
                    for hd in range(2):
                        if lv == 0:
                            after(pool, i, "mask", 3 * hd + 1)
                        else:
                            after(pool, i, "w_mm", 2 * (lv - 1) + hd + 1)
                        mask = half_of_chunk(level[lv], lv, 1)
                        sig(nc.gpsimd.tensor_tensor(half(off[hd][:], lv, 1), half(abT[hd][:], lv, 1),
                                                    mask[:, None].to_broadcast([P, NT] + list(mask.shape[1:])), ALU.mult), "off")
                if prepare:
                    values(i + 1)
            values(0)
            turns(pool, turn)

        @block.tensor
        def _(pe):
            mm = nc.tensor.matmul

            def lora_w(i, x):
                pe.wait_ge(w_loaded[0], 16 * i + 16)
                sig(mm(FREE[1][:], w_lora[0:HD, :], lora[0:HD, 0, :], start=True, stop=True), "lora")

            def lora_a(i, x):
                sig(mm(FREE[0][:], w_lora[HD:P, :], lora[HD:P, 0, :], start=True, stop=True), "lora")

            def key_norm(i, x):
                after(pe, i, "sq", 1)
                after(pe, i, "sig", 1)
                sig(mm(FREE[1][:], same, ac[x][:], start=True, stop=True), "ss")

            def bonus_sum(i, x):
                after(pe, i, "rk", 1)
                after(pe, i, "root", 1)
                sig(mm(FREE[1][:], same, rc[x][:], start=True, stop=True), "rk_mm")

            def mean(i):
                after(pe, i, "yadd", 1)
                sig(mm(FREE[0][:], same, y[:], start=True, stop=True), "mean")

            def variance(i):
                after(pe, i, "ysq", 1)
                sig(mm(FREE[1][:], same, qs[:], start=True, stop=True), "var")

            def gate(i, x):
                pe.wait_ge(w_loaded[1], 16 * i + 16)
                sig(mm(FREE[0][:], w_gate[:], lora[:, 1, :], start=True, stop=True), "g_mm")

            def turn(i, x, finish, prepare):
                def beside(lv):
                    if lv == 0:
                        after(pe, i, "mask", 6)
                        if finish:
                            mean(i - 1)
                        if prepare:
                            lora_w(i + 1, 1 - x)
                    if lv == 1:
                        if prepare:
                            if finish:
                                after(pe, i - 1, "yc", 1)
                            lora_a(i + 1, 1 - x)
                        if finish:
                            if prepare:
                                after(pe, i + 1, "sig", 1)
                            variance(i - 1)
                    if lv == 2:
                        if finish:
                            if prepare:
                                after(pe, i + 1, "sig", 2)
                            else:
                                after(pe, i - 1, "yc", 1)
                            gate(i - 1, 1 - x)
                        if prepare:
                            if finish:
                                after(pe, i - 1, "r", 1)
                            key_norm(i + 1, 1 - x)
                    if lv == 4 and prepare:
                        bonus_sum(i + 1, 1 - x)

                if finish:
                    after(pe, i - 1, "yadd", 1)
                    after(pe, i - 1, "s", 10)
                for n, (src, name, k) in enumerate(((vs, "vs", 1), (ac[x], "dec", 3), (kc[x], "dec", 4), (bc[x], "dec", 5))):
                    after(pe, i, name, k)
                    for t in range(NT):
                        last = nc.tensor.transpose(tl(K.ps[4 + n], t), src[:, t, :] if src is vs else tl(src, t), K.ident)
                    sig(last, "tr")

                def scores(hd, bank, a_, b_):
                    for t in range(NT):
                        last = mm(tl(B[hd][bank], t), tl(a_, t)[halves[hd]], tl(b_, t)[halves[hd]], start=True, stop=True)
                    sig(last, "score")
                for hd in range(2):
                    if hd == 1:
                        after(pe, i, "tok", 4)
                    scores(hd, 0, bc[x], ac[x])
                    scores(hd, 1, ac[x], bc[x])
                for lv in range(LEVELS):
                    for hd in range(2):
                        after(pe, i, "off", 2 * lv + hd + 1)
                        after(pe, i, "ident", 2 * hd + 2) if lv == 0 else after(pe, i, "T", 2 * (lv - 1) + hd + 1)
                        for t in range(NT):
                            last = mm(tl(B[hd][2], t), off[hd][:, t, :], T[hd][:, t, :], start=True, stop=True)
                        sig(last, "w_mm")
                    for hd in range(2):
                        after(pe, i, "w", 2 * lv + hd + 1)
                        if lv:
                            after(pe, i, "TT", 2 * (lv - 1) + hd + 1)
                        if lv < LEVELS - 1:
                            for t in range(NT):
                                last = mm(tl(B[hd][3], t), TT[hd][:, t, :], W[hd][:, t, :], start=True, stop=True)
                            sig(last, "dT")
                        for t in range(NT):
                            last = mm(tl(B[hd][0], t), W[hd][:, t, :], TT[hd][:, t, :], start=True, stop=True)
                        sig(last, "dTT")
                    beside(lv)
                for hd in range(2):
                    scores(hd, 2, bc[x], rc[x])
                    scores(hd, 3, kc[x], rc[x])
                if finish:
                    after(pe, i - 1, "out", 1)
                if prepare:
                    after(pe, i + 1, "bonus", 1)
                for hd in range(2):
                    scores(hd, 1, kc[x], ac[x])
                for hd, hr in enumerate(halves):
                    after(pe, i, "TT", 2 * (LEVELS - 1) + hd + 1)
                    after(pe, i, "mask", 10 + hd + 1)
                    for t in range(NT):
                        last = mm(B[hd][0][:, t * HD:(t + 1) * HD], akT[hd][:, t, :], vt[:, t, hr], start=True, stop=True)
                    sig(last, "akv")
                for hd in range(2):
                    after(pe, i, "cat", 2 * hd + 2)
                    for t in range(NT):
                        last = mm(tl(B[hd][1], t), TT[hd][:, t, :], cat[hd][:, t, :], start=True, stop=True)
                    sig(last, "xu_mm")
                for hd, hr in enumerate(halves):
                    xr, ur = hr, halves[1 - hd]
                    after(pe, i, "xu", hd + 1)
                    for t in range(NT):
                        mm(tl(B[hd][2], t), xu[hd][:, t, :], rbT[hd][:, t, :], start=True, stop=False, skip_group_check=True)
                        last = mm(tl(B[hd][2], t)[ur], vt[:, t, hr], rkT[hd][:, t, :], start=False, stop=True, skip_group_check=True)
                    sig(last, "qy")
                    for t in range(NT):
                        last = mm(B[hd][3][hr, t * HD:(t + 1) * HD], xu[hd][:, t, xr], bt[:, t, hr], start=True, stop=True)
                    sig(last, "gh")
                    for t in range(NT):
                        mm(B[hd][0][hr, t * HD:(t + 1) * HD], bt[:, t, hr], xu[hd][:, t, ur], start=True, stop=False)
                        last = mm(B[hd][0][hr, t * HD:(t + 1) * HD], kt[:, t, hr], vt[:, t, hr], start=False, stop=True)
                    sig(last, "gh")
                after(pe, i, "qev", 8)
                for t in range(1, NT):
                    after(pe, i, "s", 2 + 4 * (t - 1))
                    sig(mm(tl(K.ps[5], t), sh[:], tl(qs, t), start=True, stop=True), "y_mm")
                    if t < NT - 1:
                        for hr in halves:
                            last = mm(K.ps[6][hr, 0:HD], G[hr, t, :], sh[hr, hr], start=True, stop=True)
                        sig(last, "s_mm")

            lora_w(0, 0)
            lora_a(0, 0)
            key_norm(0, 0)
            bonus_sum(0, 0)
            turns(pe, turn)
            mean(DC - 1)
            variance(DC - 1)
            after(pe, DC - 1, "yc", 1)
            gate(DC - 1, 1)

        @block.scalar
        def _(act):
            A = nc.scalar.activation
            w0, a0 = K.cols_at["w0"][0], K.cols_at["a0"][0]

            def square(i, x):
                after(act, i, "kk", 1)
                sig(A(ac[x][:], kkn[:], ACT.Square), "sq")

            def decay(i, x):
                after(act, i, "lora", 1)
                sig(A(log_w[:], FREE[1][:], ACT.Sigmoid, bias=K.cols[:, bass.ds(w0 + i, 1)]), "sig")

            def rate(i, x):
                after(act, i, "lora", 2)
                sig(A(a[:], FREE[0][:], ACT.Sigmoid, bias=K.cols[:, bass.ds(a0 + i, 1)]), "sig")

            def root(i, x):
                after(act, i, "ss", 1)
                after(act, i, "csm", 3)
                sig(A(log_w[:], FREE[1][:], ACT.Sqrt), "root")

            def decays(i, x):
                after(act, i, "csm", 3)
                after(act, i, "rk_mm", 1)
                sig(A(rc[x][:], bc[x][:], ACT.Exp), "exp")
                sig(A(pm[x][:], mid[:], ACT.Exp), "exp")
                act.wait_ge(N["exp"].sem, PER["exp"] * i + 1)
                sig(A(bc[x][:], bc[x][:], ACT.Exp, scale=-1.0), "exp")
                sig(A(ac[x][:], ac[x][:], ACT.Exp), "exp")

            def y_square(i):
                after(act, i, "yc", 1)
                sig(A(qs[:], y[:], ACT.Square), "ysq")

            def y_root(i):
                after(act, i, "r", 2)
                sig(A(qs[:], qs[:], ACT.Sqrt), "yroot")

            def turn(i, x, finish, prepare):
                for n, dst in ((0, vt), (2, kt)):
                    after(act, i, "tr", n + 1)
                    sig(A(flat(dst[:]), K.ps[4 + n][:], ACT.Copy), "tok")
                for lv in range(LEVELS):
                    for hd in range(2):
                        after(act, i, "w_mm", 2 * lv + hd + 1)
                        if lv:
                            after(act, i, "dTT", 2 * (lv - 1) + hd + 1)
                        sig(A(half(W[hd][:], lv, 0), half(t4(B[hd][2][:]), lv, 0), ACT.Identity, scale=second_half[lv]), "w")
                    if lv == 0 and prepare:
                        square(i + 1, 1 - x)
                    if lv == 1:
                        if prepare:
                            decay(i + 1, 1 - x)
                        if finish:
                            y_square(i - 1)
                    if lv == 2 and prepare:
                        rate(i + 1, 1 - x)
                    if lv == 3:
                        if finish:
                            y_root(i - 1)
                        if prepare:
                            root(i + 1, 1 - x)
                    if lv == 5 and prepare:
                        decays(i + 1, 1 - x)
                for hd, hr in enumerate(halves):
                    after(act, i, "dTT", 2 * (LEVELS - 1) + hd + 1)
                    sig(A(cat[hd][:, :, hr], at_[:, :, hr], ACT.Copy), "cat")
                    after(act, i, "akv", hd + 1)
                    sig(A(cat[hd][:, :, halves[1 - hd]], B[hd][0][:, 0:NT * HD].rearrange("p (t k) -> p t k", t=NT), ACT.Copy), "cat")
                for hd in range(2):
                    after(act, i, "xu_mm", hd + 1)
                    sig(A(flat(xu[hd][:]), B[hd][1][:], ACT.Copy), "xu")

            square(0, 0)
            decay(0, 0)
            rate(0, 0)
            root(0, 0)
            decays(0, 0)
            turns(act, turn)
            y_square(DC - 1)
            y_root(DC - 1)

        @block.vector
        def _(dve):
            v = nc.vector
            c = {n: K.cols_at[n][0] for n in ("k_k", "k_a", "r_k", "gn_w", "gn_b")}

            def colv(n, i):
                return K.cols[:, bass.ds(c[n] + i, 1)]

            def keys(i, x):
                sig(v.tensor_scalar(kkn[:], chunk(1, i), colv("k_k", i), None, ALU.mult), "kk")

            def decay_sum(i, x):
                after(dve, i, "sig", 1)
                sig(v.tensor_scalar(log_w[:], log_w[:], RWKV_DECAY, None, ALU.mult), "logw")
                after(dve, i, "logw", 1)
                for t in range(NT):
                    sig(v.tensor_tensor_scan(tl(bc[x], t), K.ones, tl(log_w, t), 0.0, ALU.mult, ALU.add), "cs")

            def key_rate(i, x):
                after(dve, i, "sig", 2)
                sig(v.tensor_scalar(kc[x][:], a[:], colv("k_a", i), ka1[:, bass.ds(i, 1)], ALU.mult, ALU.add), "k2")
                after(dve, i, "cs", 4)
                sig(v.tensor_copy(mid[:], t4(bc[x][:])[:, :, P // 2 - 1]), "csm")

            def centre(i, x):
                after(dve, i, "csm", 1)
                sig(v.tensor_tensor(t4(bc[x][:]), t4(bc[x][:]), mid[:, :, None].to_broadcast([P, NT, P]), ALU.subtract), "csm")
                after(dve, i, "k2", 1)
                sig(v.tensor_tensor(kc[x][:], kc[x][:], chunk(1, i), ALU.mult), "k2")
                after(dve, i, "csm", 2)
                after(dve, i, "ss", 1)
                sig(v.tensor_tensor(ac[x][:], bc[x][:], log_w[:], ALU.subtract), "csm")
                after(dve, i, "k2", 2)
                sig(v.scalar_tensor_tensor(rc[x][:], chunk(0, i), colv("r_k", i), kc[x][:], ALU.mult, ALU.mult), "rk")

            def unit_keys(i, x):
                rb = log_w[:]
                after(dve, i, "root", 1)
                sig(v.tensor_scalar(rb, rb, 1e-12, None, ALU.max), "kkn")
                after(dve, i, "kkn", 1)
                sig(v.reciprocal(rb, rb), "kkn")
                after(dve, i, "kkn", 2)
                sig(v.tensor_tensor(kkn[:], kkn[:], rb, ALU.mult), "kkn")

            def key_rate_bonus(i, x):
                after(dve, i, "kkn", 3)
                sig(v.tensor_tensor(a[:], a[:], kkn[:], ALU.mult), "kkn")
                after(dve, i, "rk_mm", 1)
                sig(v.tensor_tensor(bonus[x][:], FREE[1][:], chunk(2, i), ALU.mult), "bonus")

            def decayed(i, x):
                after(dve, i, "exp", 4)
                sig(v.tensor_copy(pl[x][:], t4(rc[x][:])[:, :, P - 1]), "dec")
                after(dve, i, "dec", 1)
                sig(v.tensor_tensor(rc[x][:], rc[x][:], chunk(0, i), ALU.mult), "dec")
                sig(v.scalar_tensor_tensor(ac[x][:], kkn[:], -1.0, ac[x][:], ALU.mult, ALU.mult), "dec")
                sig(v.tensor_tensor(kc[x][:], kc[x][:], bc[x][:], ALU.mult), "dec")
                after(dve, i, "dec", 4)
                after(dve, i, "kkn", 4)
                sig(v.tensor_tensor(bc[x][:], bc[x][:], a[:], ALU.mult), "dec")
                after(dve, i, "dec", 5)

            def y_centre(i):
                after(dve, i, "mean", 1)
                sig(v.scalar_tensor_tensor(y[:], FREE[0][:], -1.0 / HD, y[:], ALU.mult, ALU.add), "yc")

            def y_rstd(i):
                after(dve, i, "var", 1)
                sig(v.tensor_scalar(qs[:], FREE[1][:], 1.0 / HD, GN_EPS, ALU.mult, ALU.add), "r")
                after(dve, i, "r", 1)
                sig(v.reciprocal(qs[:], qs[:]), "r")

            def y_norm(i, x):
                after(dve, i, "yroot", 1)
                sig(v.tensor_tensor(y[:], y[:], qs[:], ALU.mult), "yn")
                after(dve, i, "yn", 1)
                sig(v.tensor_scalar(y[:], y[:], colv("gn_w", i), colv("gn_b", i), ALU.mult, ALU.add), "yn")
                after(dve, i, "yn", 2)
                sig(v.tensor_tensor(y[:], y[:], bonus[x][:], ALU.add), "yn")

            def y_gate(i):
                after(dve, i, "yn", 3)
                after(dve, i, "g_mm", 1)
                sig(v.tensor_tensor(chunk(0, i), y[:], FREE[0][:], ALU.mult), "out")

            def turn(i, x, finish, prepare):
                for n, dst in ((1, at_), (3, bt)):
                    after(dve, i, "tr", n + 1)
                    sig(v.tensor_copy(flat(dst[:]), K.ps[4 + n][:]), "tok")

                def masked(score, n, bank, dst, mask):
                    after(dve, i, "score", score)
                    sig(v.tensor_tensor(dst[:], t4(bank[:]), mask[:, None, :].to_broadcast([P, NT, P]), ALU.mult), "mask")
                eye = K.ident[:, None, :].to_broadcast([P, NT, P])
                for hd in range(2):
                    masked(2 * hd + 1, 3 * hd + 1, B[hd][0], abT[hd], strict)
                    masked(2 * hd + 2, 3 * hd + 2, B[hd][1], T[hd], pair_t)
                    after(dve, i, "mask", 3 * hd + 2)
                    sig(v.tensor_tensor(T[hd][:], T[hd][:], eye, ALU.add), "ident")
                    sig(v.tensor_tensor(TT[hd][:], abT[hd][:], pair[:, None, :].to_broadcast([P, NT, P]), ALU.mult), "mask")
                    after(dve, i, "mask", 3 * hd + 3)
                    sig(v.tensor_tensor(TT[hd][:], TT[hd][:], eye, ALU.add), "ident")
                for lv in range(LEVELS):
                    for hd in range(2):
                        if lv < LEVELS - 1:
                            after(dve, i, "dT", 2 * lv + hd + 1)
                            z = half(T[hd][:], lv, 0)
                            sig(v.tensor_tensor(z, z, half(t4(B[hd][3][:]), lv, 0), ALU.add), "T")
                        after(dve, i, "dTT", 2 * lv + hd + 1)
                        z = half(TT[hd][:], lv, 1)
                        sig(v.scalar_tensor_tensor(z, half(t4(B[hd][0][:]), lv, 1), first_half[lv], z, ALU.mult, ALU.add), "TT")
                    if lv == 0:
                        if prepare:
                            keys(i + 1, 1 - x)
                        if finish:
                            y_centre(i - 1)
                    if lv == 1 and prepare:
                        decay_sum(i + 1, 1 - x)
                    if lv == 2:
                        if finish:
                            y_rstd(i - 1)
                        if prepare:
                            key_rate(i + 1, 1 - x)
                    if lv == 3:
                        if prepare:
                            centre(i + 1, 1 - x)
                        if finish:
                            y_norm(i - 1, 1 - x)
                    if lv == 4:
                        if finish:
                            y_gate(i - 1)
                        if prepare:
                            unit_keys(i + 1, 1 - x)
                    if lv == 5 and prepare:
                        key_rate_bonus(i + 1, 1 - x)
                for hd in range(2):
                    masked(4 + 2 * hd + 1, 6 + 2 * hd + 1, B[hd][2], rbT[hd], K.causal)
                    masked(4 + 2 * hd + 2, 6 + 2 * hd + 2, B[hd][3], rkT[hd], K.causal)
                for hd in range(2):
                    masked(8 + hd + 1, 10 + hd + 1, B[hd][1], akT[hd], strict)
                if prepare:
                    decayed(i + 1, 1 - x)
                for hd, hr in enumerate(halves):
                    ur = halves[1 - hd]
                    after(dve, i, "qy", hd + 1)
                    sig(v.tensor_tensor(qs[hr, :], B[hd][2][hr, :], rc[x][hr, :], ALU.add), "qev")
                    sig(v.tensor_copy(y[hr, :], B[hd][2][ur, :]), "qev")
                    after(dve, i, "gh", 2 * hd + 2)
                    sig(v.tensor_copy(G[hr, :, :], B[hd][3][hr, 0:NT * HD].rearrange("p (t k) -> p t k", t=NT)), "qev")
                    sig(v.tensor_tensor(H[hr, :, :], B[hd][0][hr, 0:NT * HD].rearrange("p (t k) -> p t k", t=NT),
                                        pl[x][hr, :, None].to_broadcast([HD, NT, HD]), ALU.mult), "qev")
                after(dve, i, "qev", 8)
                for hr in halves:
                    sig(v.tensor_scalar(sh[hr, hr], H[hr, 0, :], pm[x][hr, 1:2], None, ALU.mult), "s")
                for t in range(1, NT - 1):
                    after(dve, i, "s", 2 + 4 * (t - 1))
                    for hr in halves:
                        ins = v.scalar_tensor_tensor(s1[hr, :], sh[hr, hr], pl[x][hr, t:t + 1], H[hr, t, :], ALU.mult, ALU.add)
                    sig(ins, "s")
                    after(dve, i, "s", 3 + 4 * (t - 1))
                    after(dve, i, "s_mm", t)
                    sig(v.scalar_tensor_tensor(s1[:], K.ps[6][:, 0:HD], pl[x][:, t:t + 1], s1[:], ALU.mult, ALU.add), "s")
                    after(dve, i, "s", 4 + 4 * (t - 1))
                    for hr in halves:
                        sig(v.tensor_scalar(sh[hr, hr], s1[hr, :], pm[x][hr, t + 1:t + 2], None, ALU.mult), "s")
                after(dve, i, "y_mm", NT - 1)
                sig(v.tensor_tensor(y[:, P:], y[:, P:], K.ps[5][:, P:], ALU.add), "yadd")

            keys(0, 0)
            decay_sum(0, 0)
            key_rate(0, 0)
            centre(0, 0)
            unit_keys(0, 0)
            key_rate_bonus(0, 0)
            decayed(0, 0)
            turns(dve, turn)
            after(dve, DC - 1, "yadd", 1)
            y_centre(DC - 1)
            y_rstd(DC - 1)
            y_norm(DC - 1, 1)
            y_gate(DC - 1)


def mod(K, layer, sub, which):
    a = layer * 72 + sub * 24 + which * 8
    return K.mods[:, a:a + 8]


def build(nc, dram, plan=None):
    with ExitStack() as ctx:
        K = setup(nc, ctx, dram)
        K.prod_done = K.count("prod_done")
        K.conv_step = K.count("conv_step")
        d = dram
        heads = {"f00": (d.get("gu00"), DC), "hyb": (d["w_hyb"][0:DC] if "w_hyb" in d else None, DC), "f01": (d.get("gu01"), DC),
                 "f10": (d.get("gu10"), DC), "ml": (d.get("w_xm"), DC), "f11": (d.get("gu11"), DC), "b2": (d.get("w_attn"), DC)}
        plan = plan or ["f00", "hyb", "f01", "f10", "ml", "f11", "final", "b2"]
        with stage(K):
            first_block(K, heads[plan[0]])
        K.stored = K.sem("out_stored")
        for n, step in enumerate(plan):
            nxt = next((heads[k] for k in plan[n + 1:] if k in heads), None)
            if step == "final":
                norm(K, "nf", K.x, col(K, "final_g", 0, 8), squares=Squares(K, "nf", K.h_at + 4 * S * 4))
                continue
            if step == "b2":
                second_block(K)
                continue
            layer, sub = {"f00": (0, 0), "hyb": (0, 1), "f01": (0, 2), "f10": (1, 0), "ml": (1, 1), "f11": (1, 2)}[step]
            head = Modulated(K, col(K, "norm_g", layer * 24 + sub * 8, 8), mod(K, layer, sub, 1), mod(K, layer, sub, 0),
                             mod(K, layer, sub, 2), 0.5 if step[0] == "f" else 1.0)
            if step == "hyb":
                with stage(K):
                    hybrid(K, nxt, head)
            elif step == "ml":
                with stage(K):
                    mlstm(K, nxt, head)
            else:
                s = sub // 2
                turns = 2 * FC // RING + 2 * DC // RING
                ada = {"f00": (len(ADA_UP_FRONT) - 1, 0, turns), "f01": (len(ADA_UP_FRONT) - 1 + turns, 0, turns),
                       "f10": (ADA_FIRST, DC, ADA_GROUPS - 1 - ADA_FIRST)}.get(step)
                swiglu(K, step, d[f"gu{layer}{s}"], d[f"dn{layer}{s}"], nxt, head, ada)


def tiles_of(w, kb):
    k, n = w.shape
    return np.ascontiguousarray(w.reshape(k // P // kb, kb, P, n // P, P).transpose(3, 0, 2, 1, 4)).reshape(-1, P, kb * P)


def chunks(v):
    return np.asarray(v).reshape(-1, P).T


def interleave(a, b):
    return np.stack([a, b], axis=1).reshape((-1,) + a.shape[1:])


def layout(I):
    I = {k: np.asarray(v) for k, v in I.items()}
    out = {}
    mu = I["shift_mu_2"][0]
    inv = (np.float32(THETA) ** (-np.arange(ROPE // 2, dtype=np.float32) * np.float32(2.0) / np.float32(ROPE))).astype(np.float32)
    vec = {"ada_b": np.concatenate([I["ada_b"][0], I["ada_b"][1], I["ada_b_2"][0]]), "norm_g": I["norm_g"], "final_g": I["final_norm_g"],
           "mix_pre": I["norm_mix_pre_2"], "mix_post": I["norm_mix_post_2"], "ffn_pre": I["norm_ffn_pre_2"],
           "ffn_post": I["norm_ffn_post_2"], "c": I["c"], "c2": I["c_2"],
           "hyb_conv_w": np.concatenate([I["lru_conv_w"][0], I["ssd_conv_w"][0]], axis=1),
           "hyb_conv_b": np.concatenate([I["lru_conv_b"][0], I["ssd_conv_b"][0]]),
           "lru_ba": I["lru_ba"], "lru_bx": I["lru_bx"], "lru_lambda": I["lru_lambda"],
           "ssd_d": np.repeat(I["ssd_d"][0], SSD_P), "ssd_norm_g": I["ssd_norm_g"],
           "ssd_dt_bias": np.pad(I["ssd_dt_bias"][0], (0, P - SSD_H)), "ssd_a_log": np.pad(I["ssd_a_log"][0], (0, P - SSD_H)),
           "ml_conv_w": I["mlstm_conv_w"], "ml_conv_b": I["mlstm_conv_b"], "ml_norm_g": I["mlstm_norm_g"], "ml_skip": I["mlstm_skip"],
           "ml_bi": np.pad(I["mlstm_b_gates"][0, :ML_H], (0, P - ML_H)), "ml_bf": np.pad(I["mlstm_b_gates"][0, ML_H:], (0, P - ML_H)),
           "rope_inv": np.tile(np.pad(np.tile(inv, 2), (0, HD - ROPE)), 2),
           "shift_mu": np.concatenate([mu[3 * D:], np.zeros(QKV * P, np.float32), mu[:3 * D]]),
           "w0": I["decay_w0_2"], "a0": I["iclr_a0_2"], "k_k": I["k_k_2"], "k_a": I["k_a_2"], "r_k": I["r_k_2"], "gn_w": I["gn_w_2"], "gn_b": I["gn_b_2"]}
    out["cols"] = np.ascontiguousarray(np.concatenate([chunks(vec[n]) for n, _ in COLUMNS], axis=1))
    row, column = np.arange(P)[:, None], np.arange(P)[None, :]
    masks = {"ident": row == column, "ones": np.ones((P, P)), "causal": row <= column}
    out["consts"] = np.concatenate([masks[n] for n in CONSTANTS], axis=1).astype(np.float32)
    ada = [I["ada_w"][0], I["ada_w"][1], I["ada_w_2"][0]]
    out["ada"] = np.concatenate([w.reshape(ADA_TILES, 2, P, -1, S).transpose(3, 0, 2, 1, 4).reshape(-1, P, 2 * S) for w in ada])
    out["x"] = np.ascontiguousarray(I["x"][0].T.reshape(DC, P, S).transpose(1, 0, 2))
    for l in range(2):
        for s in range(2):
            out[f"gu{l}{s}"] = interleave(tiles_of(I["ffn_w_gate"][l, s], DC), tiles_of(I["ffn_w_up"][l, s], DC))
            out[f"dn{l}{s}"] = tiles_of(I["ffn_w_down"][l, s], KB_MAX)
    w_in = I["hyb_w_in"][0]
    gate, x_lru, z, xbc = w_in[:, :D], w_in[:, D:2 * D], w_in[:, 2 * D:3 * D], w_in[:, 3 * D:3 * D + XBC * P]
    out["w_hyb"] = tiles_of(np.concatenate([x_lru, xbc, gate, z], axis=1), DC)
    out["w_dt"] = np.ascontiguousarray(w_in[:, 3 * D + XBC * P:].reshape(DC, P, SSD_H).transpose(1, 0, 2))
    out["lru_wax"] = np.ascontiguousarray(np.concatenate([I["lru_wa"][0], I["lru_wx"][0]], axis=2))
    out["w_hout"] = tiles_of(I["hyb_w_out"][0], DC)
    up = I["mlstm_w_up"][0]
    out["w_xm"], out["w_z"] = tiles_of(up[:, :2 * D], DC), tiles_of(up[:, 2 * D:], DC)
    out["w_mdown"] = tiles_of(I["mlstm_w_down"][0], DC)
    qkv = np.zeros((MLC, P, 3, P), np.float32)
    for k, n in enumerate(("mlstm_wq", "mlstm_wk", "mlstm_wv")):
        w = I[n][0]
        b = w.shape[1]
        blocks = w.reshape(MLC, P // b, b, b)
        for r in range(P // b):
            qkv[:, r * b:(r + 1) * b, k, r * b:(r + 1) * b] = blocks[:, r]
    out["w_qkv"] = qkv.reshape(MLC, P, 3 * P)
    wg = I["mlstm_w_gates"][0].reshape(3, MLC, P, 2 * ML_H).transpose(1, 2, 0, 3)
    gates = np.zeros((MLC, P, 3, 2 * ML_F), np.float32)
    gates[..., :ML_H], gates[..., ML_F:ML_F + ML_H] = wg[..., :ML_H], wg[..., ML_H:]
    w2 = I["w_in_2"][0]
    n_attn, n_rwkv = QKV * P, 3 * D
    lora, gate2 = w2[:, n_attn + n_rwkv:-2 * D], w2[:, -2 * D:]
    out["w_attn"] = tiles_of(np.concatenate([lora, w2[:, :n_attn]], axis=1), DC)
    out["w_rkv"] = tiles_of(w2[:, n_attn:n_attn + n_rwkv], DC)
    out["w_gate2"] = tiles_of(gate2, DC)
    out["w_lora"] = np.concatenate([np.concatenate([I["decay_w2_2"][0], I["iclr_a2_2"][0]]).reshape(P, DC, P),
                                    I["gate_g2_2"][0].reshape(P, DC, P)], axis=2).transpose(1, 0, 2).copy()
    out["w_branch"] = tiles_of(I["w_branch_2"][0], 2 + DC)
    out["w_out2"] = tiles_of(I["w_out_2"][0], DC)
    ff2 = I["w_ff2_2"][0]
    for h in range(2):
        out[f"w_ff1{h}"] = tiles_of(I["w_ff1_2"][0][:, h * 2 * D:(h + 1) * 2 * D], DC)
        out[f"w_ff2{h}"] = tiles_of(ff2[h * 2 * D:(h + 1) * 2 * D], DC)
    out["positions"] = I["positions_2"].reshape(1, S)
    no = np.float32(NEG)
    own, sub = column <= row, (column <= row) & (column // 32 == row // 32)
    band = column >= row
    out["attn_masks"] = np.concatenate([np.where(m, np.float32(0), no) for m in (own, sub, band)], axis=1).astype(np.float32)
    rot = np.zeros((P, P), np.float32)
    for h in range(0, P, HD):
        for j in range(ROPE // 2):
            rot[h + ROPE // 2 + j, h + j], rot[h + j, h + ROPE // 2 + j] = -1.0, 1.0
    head_of = np.zeros((P, 2 * P), np.float32)
    for c in range(2):
        for h in range(2):
            head_of[2 * c + h, c * P + h * HD:c * P + (h + 1) * HD] = 1.0
    out["attn_mats"] = np.concatenate([rot, head_of], axis=1)
    off = [(row // (2 * b) == column // (2 * b)) & (row % (2 * b) < b) & (column % (2 * b) >= b) for b in (1, 2, 4, 8, 16, 32, 64)]
    same = row // HD == column // HD
    rows = [row % (2 * b) < b for b in (2, 4, 8, 16, 32, 64)]
    out["rwkv_masks"] = np.concatenate([row < column, off[0].T, off[0], *off[1:], same, *rows, *(~r for r in rows)], axis=1).astype(np.float32)
    out["w_gates"] = gates.reshape(MLC, P, 6 * ML_F)
    return out


def kernel(**inputs):
    import numpy as _np
    import concourse.bacc as _bacc
    from concourse import mybir as _mybir
    from concourse.bass_utils import run_bass_kernel_spmd as _run

    nc = _bacc.Bacc("TRN2", target_bir_lowering=False, num_devices=1)
    arrays, dram = {}, {}
    for name, a in layout(inputs).items():
        a = _np.ascontiguousarray(a)
        arrays[f"in_{name}"] = a
        dram[name] = nc.dram_tensor(f"in_{name}", a.shape, _mybir.dt.from_np(a.dtype), kind="ExternalInput").ap()
    dram["out"] = nc.dram_tensor("out", [P, DC, S], F32, kind="ExternalOutput").ap()
    build(nc, dram)
    r = _run(nc, [arrays], core_ids=[0])
    return r.results[0]["out"].transpose(1, 0, 2).reshape(1, D, S).transpose(0, 2, 1)
```

```python
from contextlib import ExitStack, contextmanager

import numpy as np

import concourse.bass as bass
from concourse import mybir

F32 = mybir.dt.float32
F32R = mybir.dt.float32r
I32 = mybir.dt.int32
ALU = mybir.AluOpType
ACT = mybir.ActivationFunctionType
AX_X = mybir.AxisListType.X

P = 128
S = 512
NT = S // P
D = 1024
DC = D // P
FF = 2816
FC = FF // P
RING = 4
SPLIT = 2
KB_MAX = FC // 2
SLOT_BYTES = KB_MAX * P * 4
EPS = 1e-6
ADA_GROUPS = (2 * 9 * D + 6 * D) // S
ADA_FIRST = 2 * 9 * D // S
ADA_TILES = 4
ADA_UP_FRONT = (*range(3 * D // S), ADA_GROUPS - 1)

SSD_H, SSD_P, SSD_G = 16, 64, 2
SSD_PAIRS = SSD_H // SSD_G // 2
XBC = DC + 2 * SSD_G
HYB = DC + XBC + 2 * DC
CONV = 4
ML_H = 4
MLC = 2 * D // P
HC = MLC // ML_H
HEADS, HD = 12, 64
GROUPS = 3
DILATION = (1, 4, 16)
ROPE = HD // 4
THETA = 500000.0
QKV = 3 * HEADS * HD // P
LEVELS = 6
GN_EPS = 64e-5
FF2 = 4 * D // P
ML_F = 32

COLUMNS = [("ada_b", 192), ("norm_g", 48), ("final_g", 8), ("mix_pre", 8), ("mix_post", 8), ("ffn_pre", 8),
           ("ffn_post", 8), ("c", 8), ("c2", 8),
           ("hyb_conv_w", 80), ("hyb_conv_b", 20), ("lru_ba", 8), ("lru_bx", 8), ("lru_lambda", 8),
           ("ssd_d", 8), ("ssd_norm_g", 8), ("ssd_dt_bias", 1), ("ssd_a_log", 1),
           ("ml_conv_w", 64), ("ml_conv_b", 16), ("ml_norm_g", 16), ("ml_skip", 16), ("ml_bi", 1), ("ml_bf", 1),
           ("rope_inv", 1), ("shift_mu", 44), ("w0", 8), ("a0", 8), ("k_k", 8), ("k_a", 8), ("r_k", 8), ("gn_w", 8), ("gn_b", 8)]


def column_map():
    at, out = 0, {}
    for name, n in COLUMNS:
        out[name] = (at, n)
        at += n
    return out, at


class Count:

    def __init__(self, sem):
        self.sem, self.base = sem, 0

    def __call__(self, n):
        return self.base + n


class Chain:

    def __init__(self, eng, count, start=0):
        self.eng, self.count, self.n, self.start = eng, count, 0, start

    def __call__(self, ins):
        self.n += 1
        ins.then_inc(self.count.sem, 1)
        self.eng.wait_ge(self.count.sem, self.count(self.start + self.n))


@contextmanager
def stage(K):
    K.stage_sems = []
    yield
    K.nc.clear_and_free_semaphores(K.stage_sems)
    K.stage_sems = None
    K.nc.all_engine_barrier()


class Core:
    pass


def setup(nc, ctx, dram):
    K = Core()
    K.nc, K.dram, K.ctx = nc, dram, ctx
    K.top = [nc.sbuf_base]

    def at(name, shape, dtype, offset):
        return nc.alloc_sbuf_tensor_at(name, shape, dtype, offset=offset)

    def sb(name, shape, dtype=F32):
        n = int(np.prod(shape[1:])) * 4
        K.top[0] = (K.top[0] + 31) // 32 * 32
        t = at(name, shape, dtype, K.top[0])
        K.top[0] += n
        return t

    K.at, K.sb = at, sb
    K.stage_sems = None

    def sem(name):
        if K.stage_sems is None:
            return ctx.enter_context(nc.semaphore(name))
        K.stage_sems.append(nc.alloc_semaphore(name=name))
        return K.stage_sems[-1]
    K.sem = sem
    K.count = lambda name: Count(K.sem(name))
    K.cols_at, ncols = column_map()
    K.x = sb("residual", [P, DC, S])
    K.h_at = (K.top[0] + 31) // 32 * 32
    K.h_hi = sb("h_hi", [P, DC, S], F32R)
    K.h_lo_at = (K.top[0] + 31) // 32 * 32
    K.h_lo = sb("h_lo", [P, DC, S], F32R)
    K.w_raw_at = (K.top[0] + 31) // 32 * 32
    K.w_raw = sb("w_raw", [P, RING, KB_MAX * P])
    K.w_hi_at = (K.top[0] + 31) // 32 * 32
    K.w_hi = sb("w_hi", [P, SPLIT, KB_MAX * P], F32R)
    K.w_lo_at = (K.top[0] + 31) // 32 * 32
    K.w_lo = sb("w_lo", [P, SPLIT, KB_MAX * P], F32R)
    K.cols = sb("cols", [P, ncols])
    K.consts = sb("consts", [P, NCONST])
    K.mods = sb("mods", [P, 192])
    K.gain = sb("gain", [P, DC])
    K.coef = sb("coef", [P, DC])
    K.c_act = sb("c_act", [P, 16])
    K.arena = (K.top[0] + 31) // 32 * 32
    K.ident = K.consts[:, 0:P]
    K.ones = K.consts[:, P:2 * P]
    K.causal = K.consts[:, 2 * P:3 * P]
    K.ps = [nc.alloc_psum_tensor(f"bank{i}", [P, S], F32) for i in range(8)]

    K.w_loaded = [K.sem(f"w_loaded{i}") for i in range(RING)]
    K.hi_done = K.count("w_hi_done")
    K.lo_done = K.count("w_lo_done")
    K.tile_mm = K.count("tile_mm")
    K.bank_free = K.count("bank_free")
    K.ada_loaded, K.ada_base = [K.sem(f"ada_loaded{i}") for i in range(2)], 0
    K.ada_step, K.ada_mm, K.ada_out = K.count("ada_step"), K.count("ada_mm"), K.count("ada_out")
    K.sq_done, K.sq_added = K.count("sq_done"), K.count("sq_added")
    K.rms_sum, K.rms_step, K.rms_root, K.rms_diag, K.rms_row = (K.count("rms_" + n) for n in ("sum", "step", "root", "diag", "row"))
    K.scaled, K.h_hi_done, K.h_ready, K.x_written = (K.count(n) for n in ("h_scaled", "h_hi_done", "h_ready", "x_written"))
    K.rs, K.pad4 = sb("rms_rs", [P, NT]), sb("rms_pad", [P, NT])
    K.t = at("h_scaled", [P, DC, S], F32, K.h_lo_at)
    K.diag = at("rms_diag", [P, NT, P], F32, K.h_at + 3 * S * 4)
    K.arena = (K.top[0] + 31) // 32 * 32
    K.silu_done, K.gu_hi_done = K.count("silu_done"), K.count("gu_hi_done")
    K.tile0 = 0
    return K


CONSTANTS = ["ident", "ones", "causal"]
NCONST = len(CONSTANTS) * P


def col(K, name, i=0, n=1):
    a, _ = K.cols_at[name]
    return K.cols[:, a + i:a + i + n]


def load_tile(K, sp, w, kb, t, slot, value):
    if value is not None:
        sp.wait_ge(K.lo_done.sem, value)
    sp.dma_start(K.w_raw[:, slot, 0:kb * P], w[bass.ds(t, 1)].rearrange("o p n -> p (o n)")).then_inc(K.w_loaded[slot], 16)


def split_hi(K, act, kb, slot, half, g):
    act.wait_ge(K.w_loaded[slot], 16 * (g // RING + 1) if isinstance(g, int) else (g + (RING - slot)) * (16 // RING))
    act.wait_ge(K.tile_mm.sem, g + PRIMED - 1)
    K.nc.scalar.activation(K.w_hi[:, half, 0:kb * P], K.w_raw[:, slot, 0:kb * P], ACT.Copy).then_inc(K.hi_done.sem, 1)


def split_lo(K, dve, kb, slot, half, g):
    dve.wait_ge(K.hi_done.sem, g + PRIMED + 1)
    K.nc.vector.tensor_tensor(K.w_lo[:, half, 0:kb * P], K.w_raw[:, slot, 0:kb * P],
                              K.w_hi[:, half, 0:kb * P].bitcast(F32), ALU.subtract).then_inc(K.lo_done.sem, 1)


PRIMED = 4


def rolled(eng, n, body):
    if n > 2:
        with eng.Fori(0, n - 1) as i:
            body(i, False)
    elif n == 2:
        body(0, False)
    body(n - 1, True)


def gemm(K, w, kb, n_tiles, nxt, mm, pe_wait, act_evac=None, dve_evac=None, turn=4, post=None, side=None, head=None, squares=None, fetched=RING, fetch=RING):
    nc = K.nc
    g0 = K.tile0
    n = n_tiles // turn
    assert n_tiles % turn == 0 and g0 % RING == 0 and turn % RING == 0
    with nc.Block() as block:
        @block.sync
        def _(sp):
            if side:
                side.first_loads(sp)
            for j in range(fetched, RING):
                load_tile(K, sp, w, kb, j, j, None)

            def body(i, last):
                for j in range(turn):
                    ahead = turn * i + j + RING
                    if not last or j < turn - RING:
                        load_tile(K, sp, w, kb, ahead, j % RING, g0 + ahead + PRIMED - RING + 1)
                    elif nxt is not None and j - turn + RING < fetch:
                        load_tile(K, sp, nxt[0], nxt[1], j - turn + RING, j % RING, g0 + ahead + PRIMED - RING + 1)
                    if side:
                        side.load(sp, i, j, last)
            rolled(sp, n, body)

        @block.scalar
        def _(act):
            if head:
                head.act(act)

            def body(i, last):
                for j in range(turn):
                    t = turn * i + j
                    if not (last and j == turn - 1):
                        split_hi(K, act, kb, (j + 1) % RING, (j + 1) % SPLIT, g0 + t + 1)
                    elif nxt is not None:
                        split_hi(K, act, nxt[1], 0, 0, g0 + t + 1)
                    if act_evac:
                        act_evac(act, i, j, t, g0 + t + PRIMED + 1)
            rolled(act, n, body)

        @block.vector
        def _(dve):
            if head:
                head.dve(dve)

            def body(i, last):
                for j in range(turn):
                    t = turn * i + j
                    if not (last and j == turn - 1):
                        split_lo(K, dve, kb, (j + 1) % RING, (j + 1) % SPLIT, g0 + t + 1)
                    elif nxt is not None:
                        split_lo(K, dve, nxt[1], 0, 0, g0 + t + 1)
                    if dve_evac:
                        dve_evac(dve, i, j, t, g0 + t + PRIMED + 1)
                    if side:
                        side.accumulate(dve, i, j)
            rolled(dve, n, body)

        @block.tensor
        def _(pe):
            if head:
                head.pe(pe)

            def body(i, last):
                for j in range(turn):
                    t = turn * i + j
                    pe.wait_ge(K.lo_done.sem, g0 + t + PRIMED + 1)
                    pe_wait(pe, i, j, t)
                    for k in range(kb):
                        hi, lo, bank, start, stop = mm(k, j)
                        if head:
                            pe.wait_ge(K.h_ready.sem, K.h_ready(k + 1))
                        wh = K.w_hi[:, j % SPLIT, k * P:(k + 1) * P]
                        wl = K.w_lo[:, j % SPLIT, k * P:(k + 1) * P]
                        nc.tensor.matmul(K.ps[bank][:], wh, hi, start=start, stop=False)
                        nc.tensor.matmul(K.ps[bank][:], wh, lo, start=False, stop=False)
                        last_mm = nc.tensor.matmul(K.ps[bank][:], wl, hi, start=False, stop=stop)
                    last_mm.then_inc(K.tile_mm.sem, 1)
                    if side and j == turn - 1:
                        side.reduce(pe, i)
            rolled(pe, n, body)
            if post:
                post(pe)

        if squares:
            @block.gpsimd
            def _(pool):
                squares.clear(pool)

                def body(i, last):
                    for j in range(squares.per):
                        squares.add(pool, squares.per * i + j, j % 2)
                rolled(pool, DC // squares.per, body)
    if side:
        side.advance(n)
    if squares:
        squares.advance()
    if head:
        head.advance()
    K.tile0 += n_tiles
    for c in (K.hi_done, K.lo_done, K.tile_mm):
        c.base = K.tile0 + PRIMED


class Modulation:
    SLOT = (0, 1, 0, 1)
    STEP = ((0, 1), (2,), (3,), ())

    def __init__(self, K, group, c0, base):
        self.K, self.group, self.c0 = K, group, c0
        self.tiles = K.at(f"ada_tiles{group}", [P, 2, 2 * S], F32, base)
        self.acc = K.at(f"ada_acc{group}", [P, S], F32, base + 4 * S * 4)

    def fetch(self, sp, group, tile):
        sp.dma_start(self.tiles[:, self.SLOT[tile], :],
                     self.K.dram["ada"][bass.ds(ADA_TILES * group + tile, 1)].rearrange("o p n -> p (o n)")).then_inc(self.K.ada_loaded[self.SLOT[tile]], 16)

    def first_loads(self, sp):
        for tile in range(2):
            self.fetch(sp, self.group, tile)

    def load(self, sp, i, j, last):
        if last and j >= 2:
            return
        sp.wait_ge(self.K.ada_step.sem, self.K.ada_step(8 * i + 2 * j + 2))
        self.fetch(sp, self.group + i + (j >= 2), (j + 2) % ADA_TILES)

    def accumulate(self, dve, i, j):
        K, v = self.K, self.K.nc.vector
        for tile in self.STEP[j]:
            slot = self.SLOT[tile]
            dve.wait_ge(K.ada_loaded[slot], 32 * i + (K.ada_base + tile // 2 + 1) * 16)
            for k in range(2):
                n = 2 * tile + k
                block = self.tiles[:, slot, k * S:(k + 1) * S]
                c = K.c_act[:, self.c0 + n:self.c0 + n + 1]
                if n == 0:
                    ins = v.tensor_scalar(self.acc[:], block, c, None, ALU.mult)
                else:
                    dve.wait_ge(K.ada_step.sem, K.ada_step(8 * i + n))
                    ins = v.scalar_tensor_tensor(self.acc[:], block, c, self.acc[:], ALU.mult, ALU.add)
                ins.then_inc(K.ada_step.sem, 1)
        if j == 3:
            dve.wait_ge(K.ada_mm.sem, K.ada_mm(i + 1))
            at = 4 * (self.group + i)
            v.tensor_tensor(K.mods[:, bass.ds(at, 4)], K.ps[7][:, 0:4], K.cols[:, bass.ds(K.cols_at["ada_b"][0] + at, 4)],
                            ALU.add).then_inc(K.ada_out.sem, 1)

    def reduce(self, pe, i):
        K = self.K
        pe.wait_ge(K.ada_step.sem, K.ada_step(8 * i + 8))
        pe.wait_ge(K.ada_out.sem, K.ada_out(i))
        for m in range(4):
            last = K.nc.tensor.matmul(K.ps[7][:, m:m + 1], self.acc[:, m * P:(m + 1) * P], K.ones[:, 0:1], start=True, stop=True)
        last.then_inc(K.ada_mm.sem, 1)

    def advance(self, turns):
        K = self.K
        self.group += turns
        K.ada_base += 2 * turns
        for c, per in ((K.ada_step, 8), (K.ada_mm, 1), (K.ada_out, 1)):
            c.base += per * turns


def first_block(K, first):
    nc, dram = K.nc, K.dram
    loaded, x_loaded = K.sem("inputs_loaded"), K.sem("x_loaded")
    silu_done = K.sem("c_silu_done")
    n_up = len(ADA_UP_FRONT)
    ada_loaded = [K.sem(f"ada_up_front{g}") for g in ADA_UP_FRONT]
    step, reduced, out = K.count("ada_up_step"), K.sem("ada_up_reduced"), K.sem("ada_up_out")
    GROUP_BYTES = ADA_TILES * 2 * S * 4
    acc = K.at("ada_up_acc", [P, n_up, S], F32, K.h_at)
    tiny = K.at("prime", [P, 8], F32, K.h_at + n_up * S * 4)
    ada = [K.at(f"ada_up{n}", [P, ADA_TILES, 2 * S], F32, K.arena + n * GROUP_BYTES if n < n_up - 1 else K.h_at + n_up * S * 4 + 32)
           for n in range(n_up)]
    mod_ps = K.ps[0]
    squares = Squares(K, "first", K.arena + (n_up - 1) * GROUP_BYTES + 3 * S * 4)
    K.sq_added.base = PRIMED
    with nc.Block() as block:
        @block.sync
        def _(sp):
            sp.dma_start(K.cols[:], dram["cols"]).then_inc(loaded, 16)
            sp.dma_start(K.consts[:], dram["consts"]).then_inc(loaded, 16)
            for n, g in enumerate(ADA_UP_FRONT):
                sp.dma_start(ada[n][:], dram["ada"][ADA_TILES * g:ADA_TILES * (g + 1)].rearrange("t p n -> p t n")).then_inc(ada_loaded[n], 16)
                if n == 1:
                    sp.dma_start(K.x[:], dram["x"]).then_inc(x_loaded, 16)
            for j in range(RING):
                load_tile(K, sp, first[0], first[1], j, j, None)
            sp.wait_ge(x_loaded, 16)

        @block.scalar
        def _(act):
            act.wait_ge(loaded, 32)
            nc.scalar.activation(K.c_act[:], K.cols[:, K.cols_at["c"][0]:K.cols_at["c"][0] + 16], ACT.Silu).then_inc(silu_done, 1)
            nc.scalar.activation(tiny[:, 4:5], K.consts[:, 0:1], ACT.Copy).then_inc(K.hi_done.sem, PRIMED)
            act.wait_ge(K.tile_mm.sem, PRIMED)
            split_hi(K, act, first[1], 0, 0, 0)
            act.wait_ge(x_loaded, 16)
            for c in range(DC):
                squares.by_act(act, K.x[:, c:c + 1, :], c, c % 2)

        @block.gpsimd
        def _(pool):
            nc.gpsimd.memset(tiny[:, 7:8], 0.0).then_inc(K.sq_added.sem, PRIMED)
            squares.clear(pool)
            for c in range(DC):
                squares.add(pool, c, c % 2)

        @block.vector
        def _(dve):
            v = nc.vector
            v.memset(tiny[:, 0:1], 0.0).then_inc(K.lo_done.sem, PRIMED)
            v.memset(tiny[:, 1:2], 0.0).then_inc(K.tile_mm.sem, PRIMED)
            v.memset(tiny[:, 2:3], 0.0).then_inc(K.bank_free.sem, PRIMED)
            v.memset(tiny[:, 3:4], 0.0).then_inc(K.ada_out.sem, 1)
            for n, c in enumerate((K.prod_done, K.conv_step)):
                v.memset(tiny[:, 5 + n:6 + n], 0.0).then_inc(c.sem, 2 * PRIMED)
            dve.wait_ge(silu_done, 1)
            link = Chain(dve, step)
            for n, g in enumerate(ADA_UP_FRONT):
                dve.wait_ge(ada_loaded[n], 16)
                for k in range(2 * ADA_TILES):
                    block_k = ada[n][:, k // 2, (k % 2) * S:(k % 2 + 1) * S]
                    c0 = (0 if g < ADA_FIRST else DC) + k
                    if k == 0:
                        link(v.tensor_scalar(acc[:, n], block_k, K.c_act[:, c0:c0 + 1], None, ALU.mult))
                    else:
                        link(v.scalar_tensor_tensor(acc[:, n], block_k, K.c_act[:, c0:c0 + 1], acc[:, n], ALU.mult, ALU.add))
            split_lo(K, dve, first[1], 0, 0, 0)
            dve.wait_ge(reduced, n_up)
            for n, g in enumerate(ADA_UP_FRONT):
                a = K.cols_at["ada_b"][0] + 4 * g
                v.tensor_tensor(K.mods[:, 4 * g:4 * g + 4], mod_ps[:, 4 * n:4 * n + 4], K.cols[:, a:a + 4], ALU.add).then_inc(out, 1)
            dve.wait_ge(out, n_up)

        @block.tensor
        def _(pe):
            pe.wait_ge(loaded, 32)
            for n in range(n_up):
                pe.wait_ge(step.sem, 2 * ADA_TILES * (n + 1))
                for m in range(4):
                    last = nc.tensor.matmul(mod_ps[:, 4 * n + m:4 * n + m + 1], acc[:, n, m * P:(m + 1) * P],
                                            K.ones[:, 0:1], start=True, stop=True)
                last.then_inc(reduced, 1)
    for c in (K.hi_done, K.lo_done, K.tile_mm, K.bank_free):
        c.base = PRIMED
    K.ada_out.base = 1
    squares.advance()
    for c in (K.prod_done, K.conv_step):
        c.base = 2 * PRIMED


class Squares:

    def __init__(self, K, name, base, per=2):
        self.K, self.per = K, per
        self.sq = K.at(f"sq_{name}", [P, 2, S], F32, base)
        self.acc = K.at(f"sq_acc_{name}", [P, S], F32, base + 2 * S * 4)

    def clear(self, pool):
        self.K.nc.gpsimd.memset(self.acc[:], 0.0).then_inc(self.K.sq_added.sem, 1)

    def by_act(self, act, src, o, slot):
        act.wait_ge(self.K.sq_added.sem, self.K.sq_added(o))
        self.K.nc.scalar.activation(self.sq[:, slot:slot + 1, :], src, ACT.Square).then_inc(self.K.sq_done.sem, 1)

    def by_dve(self, dve, src, o, slot):
        dve.wait_ge(self.K.sq_added.sem, self.K.sq_added(o))
        self.K.nc.vector.tensor_tensor(self.sq[:, slot:slot + 1, :], src, src, ALU.mult).then_inc(self.K.sq_done.sem, 1)

    def add(self, pool, o, slot):
        K = self.K
        pool.wait_ge(K.sq_done.sem, K.sq_done(o + 1))
        pool.wait_ge(K.sq_added.sem, K.sq_added(o + 1))
        K.nc.gpsimd.tensor_tensor(self.acc[:], self.acc[:], self.sq[:, slot, :], ALU.add).then_inc(K.sq_added.sem, 1)

    def advance(self):
        self.K.sq_done.base += DC
        self.K.sq_added.base += DC + 1
        self.K.sq_acc = self.acc


class Rms:
    SUM, ROW = 4, 5

    def __init__(self, K):
        self.K, self.acc = K, K.sq_acc

    def rms_pe(self, pe):
        K, mm = self.K, self.K.nc.tensor.matmul
        pe.wait_ge(K.sq_added.sem, K.sq_added(0))
        for t in range(NT):
            last = mm(K.ps[self.SUM][:, t:t + 1], self.acc[:, t * P:(t + 1) * P], K.ones[:, 0:1], start=True, stop=True)
        last.then_inc(K.rms_sum.sem, 1)
        pe.wait_ge(K.rms_diag.sem, K.rms_diag(1))
        mm(K.ps[self.ROW][:], K.ones, K.diag[:].rearrange("p t k -> p (t k)"), start=True, stop=True).then_inc(K.rms_row.sem, 1)

    def rms_act(self, act):
        K = self.K
        K.nc.scalar.activation(K.pad4[:], K.consts[:, 0:NT], ACT.Sqrt)
        act.wait_ge(K.rms_step.sem, K.rms_step(1))
        K.nc.scalar.activation(K.rs[:], K.rs[:], ACT.Sqrt).then_inc(K.rms_root.sem, 1)

    def rms_dve(self, dve):
        K, v = self.K, self.K.nc.vector
        dve.wait_ge(K.rms_sum.sem, K.rms_sum(1))
        v.tensor_scalar(K.rs[:], K.ps[self.SUM][:, 0:NT], 1.0 / D, EPS, ALU.mult, ALU.add).then_inc(K.rms_step.sem, 1)
        dve.wait_ge(K.rms_root.sem, K.rms_root(1))
        v.reciprocal(K.rs[:], K.rs[:]).then_inc(K.rms_step.sem, 1)
        dve.wait_ge(K.rms_step.sem, K.rms_step(2))
        v.tensor_tensor(K.diag[:], K.ident[:, None, :].to_broadcast([P, NT, P]), K.rs[:, :, None].to_broadcast([P, NT, P]),
                        ALU.mult).then_inc(K.rms_diag.sem, 1)
        dve.wait_ge(K.rms_row.sem, K.rms_row(1))

    def rms_advance(self):
        K = self.K
        for c, n in ((K.rms_sum, 1), (K.rms_step, 2), (K.rms_root, 1), (K.rms_diag, 1), (K.rms_row, 1)):
            c.base += n


class Modulated(Rms):

    def __init__(self, K, gain, scale, shift, gate, half):
        super().__init__(K)
        self.gain, self.scale, self.shift, self.gate, self.half = gain, scale, shift, gate, half

    def pe(self, pe):
        self.rms_pe(pe)

    def act(self, act):
        K = self.K
        self.rms_act(act)
        for c in range(DC):
            act.wait_ge(K.scaled.sem, K.scaled(c + 1))
            K.nc.scalar.activation(K.h_hi[:, c, :], K.t[:, c, :], ACT.Identity, bias=self.shift[:, c:c + 1]).then_inc(K.h_hi_done.sem, 1)

    def dve(self, dve):
        K, v = self.K, self.K.nc.vector
        v.scalar_tensor_tensor(K.gain[:], self.scale, 1.0, self.gain, ALU.add, ALU.mult).then_inc(K.x_written.sem, 1)
        v.tensor_scalar(K.coef[:], self.gate, 1.0, self.half, ALU.add, ALU.mult).then_inc(K.x_written.sem, 1)
        self.rms_dve(dve)
        dve.wait_ge(K.x_written.sem, K.x_written(2))

        def scale(c):
            v.scalar_tensor_tensor(K.t[:, c, :], K.x[:, c, :], K.gain[:, c:c + 1], K.ps[self.ROW][:], ALU.mult, ALU.mult).then_inc(K.scaled.sem, 1)
        scale(0)
        scale(1)
        for c in range(DC):
            if c + 2 < DC:
                scale(c + 2)
            dve.wait_ge(K.h_hi_done.sem, K.h_hi_done(c + 1))
            v.scalar_tensor_tensor(K.h_lo[:, c, :], K.t[:, c, :], self.shift[:, c:c + 1], K.h_hi[:, c, :].bitcast(F32),
                                   ALU.add, ALU.subtract).then_inc(K.h_ready.sem, 1)

    def advance(self):
        self.rms_advance()
        self.K.x_written.base += 2
        for c in (self.K.scaled, self.K.h_hi_done, self.K.h_ready):
            c.base += DC


def norm(K, name, src, gain, gate=None, squares=None, store=None):
    nc = K.nc
    rms = Rms(K)
    t = K.t
    with nc.Block() as block:
        @block.tensor
        def _(pe):
            rms.rms_pe(pe)

        @block.scalar
        def _(act):
            rms.rms_act(act)
            if squares:
                for c in range(DC):
                    act.wait_ge(K.x_written.sem, K.x_written(c + 2))
                    squares.by_act(act, K.x[:, c:c + 1, :], c, c % 2)

        if squares:
            @block.gpsimd
            def _(pool):
                squares.clear(pool)
                for c in range(DC):
                    squares.add(pool, c, c % 2)

        if store:
            @block.sync
            def _(sp):
                for c in range(DC):
                    sp.wait_ge(K.x_written.sem, K.x_written(c + 2))
                    sp.dma_start(K.dram["out"][:, c, :], K.x[:, c, :]).then_inc(store, 16)
                sp.wait_ge(store, 16 * DC)

        @block.vector
        def _(dve):
            v = nc.vector
            if gate is None:
                v.tensor_copy(K.gain[:], gain).then_inc(K.x_written.sem, 1)
            else:
                v.tensor_tensor(K.gain[:], gain, gate, ALU.mult).then_inc(K.x_written.sem, 1)
            rms.rms_dve(dve)
            dve.wait_ge(K.x_written.sem, K.x_written(1))
            for c in range(DC):
                dst = K.x if gate is None else t
                ins = v.scalar_tensor_tensor(dst[:, c, :], src[:, c, :], K.gain[:, c:c + 1], K.ps[rms.ROW][:], ALU.mult, ALU.mult)
                if gate is None:
                    ins.then_inc(K.x_written.sem, 1)
                    continue
                ins.then_inc(K.scaled.sem, 1)
                dve.wait_ge(K.scaled.sem, K.scaled(c + 1))
                v.tensor_tensor(K.x[:, c, :], K.x[:, c, :], t[:, c, :], ALU.add).then_inc(K.x_written.sem, 1)
    rms.rms_advance()
    K.x_written.base += DC + 1
    if gate is not None:
        K.scaled.base += DC
    if squares:
        squares.advance()


def swiglu(K, name, w_gu, w_down, nxt, head, ada=None):
    nc = K.nc
    sil_done, guhi_done = K.silu_done, K.gu_hi_done
    gu_hi = K.at(f"{name}_gu_hi", [P, FC, S], F32R, K.arena)
    gu_lo = K.at(f"{name}_gu_lo", [P, FC, S], F32R, K.arena + FC * S * 4)
    sil = K.at(f"{name}_sil_t", [P, 2, S], F32, K.arena + 2 * FC * S * 4)
    prod = K.at(f"{name}_prod_t", [P, 2, S], F32, K.arena + 2 * FC * S * 4 + 2 * S * 4)
    side = Modulation(K, ada[0], ada[1], K.arena + 2 * FC * S * 4 + 4 * S * 4) if ada else None
    done = K.prod_done

    def mm(k, j):
        return K.h_hi[:, k, :], K.h_lo[:, k, :], j, k == 0, k == DC - 1

    def pe_wait(pe, i, j, t):
        if j % 2 == 0:
            pe.wait_ge(done.sem, done(2 * i + j // 2 - 1))

    def act_evac(act, i, j, t, mm_done):
        f = 2 * i + j // 2
        if j % 2 == 0:
            act.wait_ge(K.tile_mm.sem, mm_done)
            act.wait_ge(done.sem, done(f - 1))
            nc.scalar.activation(sil[:, j // 2, :], K.ps[j][:], ACT.Silu).then_inc(sil_done.sem, 1)
        else:
            act.wait_ge(done.sem, done(f + 1))
            nc.scalar.activation(gu_hi[:, bass.ds(f, 1), :], prod[:, j // 2:j // 2 + 1, :], ACT.Copy).then_inc(guhi_done.sem, 1)

    def dve_evac(dve, i, j, t, mm_done):
        f = 2 * i + j // 2
        if j % 2 == 1:
            dve.wait_ge(K.tile_mm.sem, mm_done)
            dve.wait_ge(sil_done.sem, sil_done(f + 1))
            nc.vector.tensor_tensor(prod[:, j // 2, :], sil[:, j // 2, :], K.ps[j][:], ALU.mult).then_inc(done.sem, 1)
            dve.wait_ge(guhi_done.sem, guhi_done(f + 1))
            nc.vector.tensor_tensor(gu_lo[:, bass.ds(f, 1), :], prod[:, j // 2:j // 2 + 1, :],
                                    gu_hi[:, bass.ds(f, 1), :].bitcast(F32), ALU.subtract)

    gemm(K, w_gu, DC, 2 * FC, (w_down, KB_MAX), mm, pe_wait, act_evac, dve_evac, side=side, head=head)
    for c in (done, sil_done, guhi_done):
        c.base += FC

    def mm2(k, j):
        kc = (j % 2) * KB_MAX + k
        return gu_hi[:, kc, :], gu_lo[:, kc, :], j // 2, kc == 0, kc == FC - 1

    project(K, w_down, KB_MAX, 2, mm2, nxt, lambda o: (K.coef[:, bass.ds(o, 1)]),
            Squares(K, name, K.h_at), side=side if ada and ada[2] > 2 * FC // RING else None)


def project(K, w, kb, tpo, mm, nxt, coef, squares, turn=4, side=None):
    nc = K.nc
    banks = turn // tpo
    free = K.bank_free

    def pe_wait(pe, i, j, t):
        if j % tpo == 0:
            pe.wait_ge(free.sem, free(banks * i + j // tpo - banks + 1))

    def dve_evac(dve, i, j, t, mm_done):
        if j % tpo == tpo - 1:
            o = banks * i + j // tpo
            dve.wait_ge(K.tile_mm.sem, mm_done)
            nc.vector.scalar_tensor_tensor(K.x[:, bass.ds(o, 1), :], K.ps[j // tpo][:, None, :], coef(o), K.x[:, bass.ds(o, 1), :],
                                           ALU.mult, ALU.add).then_inc(free.sem, 1)

    def act_evac(act, i, j, t, mm_done):
        if j % tpo == tpo - 1:
            o = banks * i + j // tpo
            act.wait_ge(free.sem, free(o + 1))
            squares.by_act(act, K.x[:, bass.ds(o, 1), :], o, j // tpo % 2)

    gemm(K, w, kb, DC * tpo, nxt, mm, pe_wait, act_evac, dve_evac, turn=turn, side=side, squares=squares)
    free.base += DC


def conv_evacs(K, raw, dst, dst0, o0, weights, bias, n_all, ring=True):
    nc, free = K.nc, K.bank_free
    steps = K.conv_step
    wa, ba = K.cols_at[weights][0], K.cols_at[bias][0]

    def act_evac(act, i, j, t, mm_done):
        act.wait_ge(K.tile_mm.sem, mm_done)
        o = j % 2
        if ring:
            act.wait_ge(steps.sem, steps(CONV * (4 * i + j - 1)))
        else:
            o = t
        nc.scalar.activation(raw[:, bass.ds(o, 1), CONV - 1:], K.ps[j][:, None, :], ACT.Copy).then_inc(free.sem, 1)

    def dve_evac(dve, i, j, t, mm_done):
        o = 4 * i + j
        dve.wait_ge(free.sem, free(o + 1))
        y = dst[:, bass.ds(dst0 + o, 1), :]
        for tap in range(CONV):
            src = raw[:, bass.ds(j % 2 if ring else o, 1), tap:tap + S]
            w = K.cols[:, bass.ds(wa + tap * n_all + o0 + o, 1)]
            if tap == 0:
                ins = nc.vector.tensor_scalar(y, src, w, K.cols[:, bass.ds(ba + o0 + o, 1)], ALU.mult, ALU.add)
            else:
                dve.wait_ge(steps.sem, steps(CONV * o + tap))
                ins = nc.vector.scalar_tensor_tensor(y, src, w, y, ALU.mult, ALU.add)
            ins.then_inc(steps.sem, 1)

    return act_evac, dve_evac


def stream_out(K, w, n, nxt, act_evac, dve_evac=None, post=None, head=None, squares=None, fetched=RING, fetch=RING):
    free = K.bank_free

    def mm(k, j):
        return K.h_hi[:, k, :], K.h_lo[:, k, :], j, k == 0, k == DC - 1

    def pe_wait(pe, i, j, t):
        pe.wait_ge(free.sem, free(t - RING + 1))

    gemm(K, w, DC, n, nxt, mm, pe_wait, act_evac, dve_evac, post=post, head=head, squares=squares,
         fetched=fetched, fetch=fetch)
    free.base += n


def act_out(K, dst, dst0, func):
    def act_evac(act, i, j, t, mm_done):
        act.wait_ge(K.tile_mm.sem, mm_done)
        K.nc.scalar.activation(dst[:, bass.ds(dst0 + t, 1), :], K.ps[j][:, None, :], func).then_inc(K.bank_free.sem, 1)
    return act_evac


LOG1P_TERMS = 8
NEG = -1e30


def softplus_steps(nc, link, z, out, e, q, exp_of):
    softplus_abs(nc, link, z, e, q)
    exp_of()
    softplus_log(nc, link, z, out, e, q)


def softplus_abs(nc, link, z, e, q):
    link(nc.vector.tensor_scalar(q, z, -1.0, None, ALU.mult))
    link(nc.vector.tensor_tensor(e, z, q, ALU.max))


def softplus_log(nc, link, z, out, e, q):
    v = nc.vector
    link(v.tensor_scalar(q, e, 2.0, None, ALU.add))
    link(v.reciprocal(q, q))
    link(v.tensor_tensor(e, e, q, ALU.mult))
    link(v.tensor_tensor(q, e, e, ALU.mult))
    link(v.tensor_scalar(out, q, 1.0 / (2 * LOG1P_TERMS - 1), None, ALU.mult))
    for n in range(LOG1P_TERMS - 2, 0, -1):
        link(v.scalar_tensor_tensor(out, out, 1.0 / (2 * n + 1), q, ALU.add, ALU.mult))
    link(v.scalar_tensor_tensor(out, out, 1.0, e, ALU.add, ALU.mult))
    link(v.tensor_scalar(q, z, 0.0, None, ALU.max))
    link(v.scalar_tensor_tensor(out, out, 2.0, q, ALU.mult, ALU.add))


def hybrid(K, nxt, head):
    nc, d = K.nc, K.dram
    A = K.arena
    proj = K.at("proj", [P, HYB, S], F32, A)
    B = A + HYB * S * 4
    raw = K.at("conv_raw", [P, 2, S + CONV - 1], F32, B + 20 * 1024)
    w_dt = K.at("w_dt", [P, DC, SSD_H], F32, B + 26 * 1024)
    w_dt_hi = K.at("w_dt_hi", [P, DC, SSD_H], F32R, B + 26 * 1024 + 512)
    w_dt_lo = K.at("w_dt_lo", [P, DC, SSD_H], F32R, B + 24 * 1024 + 512)
    wax = K.at("lru_wax", [P, 2, 2 * P], F32, B + 27 * 1024)
    dt_raw = K.at("dt_raw", [SSD_H, S], F32, B + 30 * 1024)
    small = K.sem("hyb_small_loaded")
    wax_loaded = [K.sem(f"lru_wax_loaded{i}") for i in range(2)]
    pad_done = K.sem("conv_pad_zeroed")
    dt_mm = K.sem("dt_mm")
    XB, GATE, Z = DC, DC + XBC, DC + XBC + DC

    with nc.Block() as block:
        @block.sync
        def _(sp):
            sp.dma_start(w_dt[:], d["w_dt"]).then_inc(small, 16)
            for j in range(2):
                sp.dma_start(wax[:, j, :], d["lru_wax"][j]).then_inc(wax_loaded[j], 16)
            sp.wait_ge(small, 16)

        @block.scalar
        def _(act):
            act.wait_ge(small, 16)
            nc.scalar.activation(w_dt_hi[:], w_dt[:], ACT.Copy).then_inc(pad_done, 1)

        @block.vector
        def _(dve):
            nc.vector.memset(raw[:, :, 0:CONV - 1], 0.0)
            dve.wait_ge(pad_done, 1)
            nc.vector.tensor_tensor(w_dt_lo[:], w_dt[:], w_dt_hi[:].bitcast(F32), ALU.subtract).then_inc(pad_done, 1)

    def dt_product(pe):
        passes = [(w, h, k) for k in range(DC) for w, h in ((w_dt_hi, K.h_hi), (w_dt_hi, K.h_lo), (w_dt_lo, K.h_hi))]
        for n, (w, h, k) in enumerate(passes):
            last = nc.tensor.matmul(K.ps[7][0:SSD_H, :], w[:, k, :], h[:, k, :], start=n == 0, stop=n == len(passes) - 1)
        last.then_inc(dt_mm, 1)

    ae, de = conv_evacs(K, raw, proj, 0, 0, "hyb_conv_w", "hyb_conv_b", DC + XBC)
    stream_out(K, d["w_hyb"][0:DC], DC, (d["w_hyb"][XB:GATE], DC), ae, de, post=dt_product, head=head)
    K.conv_step.base += CONV * DC
    ae, de = conv_evacs(K, raw, proj, XB, XB, "hyb_conv_w", "hyb_conv_b", DC + XBC)
    stream_out(K, d["w_hyb"][XB:GATE], XBC, (d["w_hyb"][GATE:Z], DC), ae, de)
    K.conv_step.base += CONV * XBC
    stream_out(K, d["w_hyb"][GATE:Z], DC, (d["w_hyb"][Z:HYB], DC), act_out(K, proj, GATE, ACT.Gelu_apprx_tanh))
    stream_out(K, d["w_hyb"][Z:HYB], DC, (d["w_hout"], DC), act_out(K, proj, Z, ACT.Silu))
    dt = lru(K, proj, XB, GATE, wax, wax_loaded, dt_raw, dt_mm)
    ssd(K, proj, XB, Z, B, dt)
    hybrid_out(K, proj, GATE, nxt)


def lru(K, proj, XB, GATE, wax, wax_loaded, dt_raw, dt_mm):
    nc, d = K.nc, K.dram
    B = K.arena + HYB * S * 4
    r_all = K.at("lru_r", [P, DC, S], F32, B)
    ix = K.at("lru_ix", [P, DC, S], F32, K.h_at)
    m2 = K.at("lru_m2", [P, DC, S], F32, K.h_at + DC * S * 4)
    i_t = K.at("lru_i", [P, 2, S], F32, B + DC * S * 4)
    lam = K.at("lru_lam", [P, 4, DC], F32, B + 26 * 1024)
    dt = K.at("ssd_dt", [SSD_H, S], F32, B + DC * S * 4)
    dt_z, dt_e, dt_q = (K.at(f"dt_{n}", [SSD_H, S], F32, B + (DC + 2 + k) * S * 4) for k, n in enumerate("zeq"))
    assert B + (DC + 5) * S * 4 <= B + 26 * 1024
    mm_done, sig_done, ix_done = K.count("lru_mm"), K.count("lru_sig"), K.sem("lru_ix_done")
    lam_order, lam_abs, lam_exp = K.count("lru_lam_order"), K.sem("lru_lam_abs"), K.sem("lru_lam_exp")
    a_done, q_done, root_done, u_done, h_done = (K.sem(f"lru_{n}") for n in ("a", "q", "root", "u", "h"))
    dt_out, dt_order, dt_exp = K.sem("dt_out"), K.count("dt_order"), K.sem("dt_exp")
    dt_bias = K.cols[0:SSD_H, K.cols_at["ssd_dt_bias"][0]:K.cols_at["ssd_dt_bias"][0] + 1]
    la = K.cols_at["lru_lambda"][0]
    ba, bx = K.cols_at["lru_ba"][0], K.cols_at["lru_bx"][0]
    z, e, q, out = (lam[:, k, :] for k in range(4))
    with nc.Block() as block:
        @block.sync
        def _(sp):
            with sp.Fori(0, DC // 2 - 1) as i:
                for j in range(2):
                    sp.wait_ge(mm_done.sem, 2 * i + j + 1)
                    sp.dma_start(wax[:, j:j + 1, :], d["lru_wax"][bass.ds(2 * i + j + 2, 1)].rearrange("o p n -> p o n")).then_inc(wax_loaded[j], 16)

        @block.tensor
        def _(pe):
            def head(i, j, first):
                pe.wait_ge(wax_loaded[j], 16 * i + 16)
                if not first:
                    pe.wait_ge(sig_done.sem, 4 * i + 2 * j - 2)
                c = 2 * i + j
                nc.tensor.matmul(K.ps[2 * j][:], wax[:, j, 0:P], proj[:, bass.ds(c, 1), :], start=True, stop=True)
                nc.tensor.matmul(K.ps[2 * j + 1][:], wax[:, j, P:2 * P], proj[:, bass.ds(c, 1), :], start=True, stop=True).then_inc(mm_done.sem, 1)
            for j in range(2):
                head(0, j, True)
            with pe.Fori(1, DC // 2) as i:
                for j in range(2):
                    head(i, j, False)

        @block.scalar
        def _(act):
            act.wait_ge(dt_mm, 1)
            nc.scalar.activation(dt_raw[:], K.ps[7][0:SSD_H, :], ACT.Copy).then_inc(dt_out, 1)
            act.wait_ge(dt_order.sem, 1 + SOFTPLUS_ABS_STEPS)
            nc.scalar.activation(dt_e[:], dt_e[:], ACT.Exp, scale=-1.0).then_inc(dt_exp, 1)
            act.wait_ge(lam_abs, 1)
            nc.scalar.activation(e, e, ACT.Exp, scale=-1.0).then_inc(lam_exp, 1)

            def head(i, j, first):
                c = 2 * i + j
                act.wait_ge(mm_done.sem, c + 1)
                nc.scalar.activation(r_all[:, bass.ds(c, 1), :], K.ps[2 * j][:, None, :], ACT.Sigmoid, bias=K.cols[:, bass.ds(ba + c, 1)]).then_inc(sig_done.sem, 1)
                if not first:
                    act.wait_ge(ix_done, c - 1)
                nc.scalar.activation(i_t[:, j, :], K.ps[2 * j + 1][:], ACT.Sigmoid, bias=K.cols[:, bass.ds(bx + c, 1)]).then_inc(sig_done.sem, 1)
            for j in range(2):
                head(0, j, True)
            with act.Fori(1, DC // 2) as i:
                for j in range(2):
                    head(i, j, False)
            act.wait_ge(lam_order.sem, LRU_LAM_STEPS)
            act.wait_ge(ix_done, DC)
            with act.Fori(0, DC) as c:
                nc.scalar.activation(m2[:, bass.ds(c, 1), :], r_all[:, bass.ds(c, 1), :], ACT.Tanh, scale=lam[:, 3, bass.ds(c, 1)]).then_inc(a_done, 1)
            with act.Fori(0, DC) as c:
                nc.scalar.activation(proj[:, bass.ds(c, 1), :], r_all[:, bass.ds(c, 1), :], ACT.Exp, scale=lam[:, 3, bass.ds(c, 1)]).then_inc(a_done, 1)
            act.wait_ge(q_done, 2 * DC)
            for c in range(0, DC, DC // 2):
                nc.scalar.activation(m2[:, c:c + DC // 2, :], m2[:, c:c + DC // 2, :], ACT.Sqrt, scale=-1.0).then_inc(root_done, 1)
            nc.scalar.activation(proj[:, XB:XB + XBC, :], proj[:, XB:XB + XBC, :], ACT.Silu)

        @block.vector
        def _(dve):
            link, dt_link = Chain(dve, lam_order), Chain(dve, dt_order)
            dve.wait_ge(dt_out, 1)
            dt_link(nc.vector.tensor_scalar(dt_z[:], dt_raw[:], dt_bias, None, ALU.add))
            softplus_abs(nc, dt_link, dt_z[:], dt_e[:], dt_q[:])

            def exp_of():
                nc.vector.tensor_copy(q, e).then_inc(lam_abs, 1)
                dve.wait_ge(lam_exp, 1)
            link(nc.vector.tensor_scalar(z, K.cols[:, la:la + DC], -1.0, None, ALU.mult))
            softplus_steps(nc, link, z, out, e, q, exp_of)
            link(nc.vector.tensor_scalar(out, out, -8.0, None, ALU.mult))
            assert link.n == LRU_LAM_STEPS, link.n
            with dve.Fori(0, DC // 2) as i:
                for j in range(2):
                    c = 2 * i + j
                    dve.wait_ge(sig_done.sem, 4 * i + 2 * j + 2)
                    nc.vector.tensor_tensor(ix[:, bass.ds(c, 1), :], i_t[:, j:j + 1, :], proj[:, bass.ds(c, 1), :], ALU.mult).then_inc(ix_done, 1)
            dve.wait_ge(dt_exp, 1)
            softplus_log(nc, dt_link, dt_z[:], dt[:], dt_e[:], dt_q[:])
            with dve.Fori(0, DC) as c:
                r_c, a_c, m_c = (t[:, bass.ds(c, 1), :] for t in (r_all, proj, m2))
                dve.wait_ge(a_done, DC + c + 1)
                nc.vector.tensor_tensor(r_c, a_c, a_c, ALU.mult).then_inc(q_done, 1)
                dve.wait_ge(q_done, 2 * c + 1)
                nc.vector.scalar_tensor_tensor(m_c, r_c, 1.0, m_c, ALU.add, ALU.mult).then_inc(q_done, 1)
            for n in range(2):
                half = slice(n * DC // 2, (n + 1) * DC // 2)
                dve.wait_ge(root_done, n + 1)
                nc.vector.tensor_tensor(ix[:, half, :], ix[:, half, :], m2[:, half, :], ALU.mult).then_inc(u_done, 1)
                dve.wait_ge(u_done, n + 1)
                for c in range(half.start, half.stop):
                    nc.vector.tensor_tensor_scan(r_all[:, c, :], proj[:, c, :], ix[:, c, :], 0.0, ALU.mult, ALU.add).then_inc(h_done, 1)
                dve.wait_ge(h_done, half.stop)
                gate = proj[:, GATE + half.start:GATE + half.stop, :]
                nc.vector.tensor_tensor(gate, gate, r_all[:, half, :], ALU.mult)
    return dt


SOFTPLUS_ABS_STEPS = 2
LRU_LAM_STEPS = 10 + LOG1P_TERMS


def ssd(K, proj, XB, Z, B, dt):
    nc = K.nc
    H16 = SSD_H
    off = [B, K.h_at, K.arena]

    def sb(name, shape, where=0):
        t = K.at("ssd_" + name, shape, F32, off[where])
        off[where] += (int(np.prod(shape[1:])) * 4 + 31) // 32 * 32
        return t
    acs, wst = sb("acs", [H16, S]), sb("wst", [H16, S], 1)
    toks = sb("toks", [P, 3, NT, H16])
    edec = sb("edec", [P, NT, H16])
    b_tok, cbm = sb("b_tok", [P, SSD_G, S]), sb("cbm", [P, SSD_G, S])
    xs, xdt, xw = ([sb(f"{n}{g}", shape, 2 * g) for g in range(SSD_G)] for n, shape in (("xs", [P, S]), ("xdt", [P, NT, P]), ("xw", [P, NT, P])))
    rows = [sb(f"rows{g}", [H16, 2, S], 2 * g) for g in range(SSD_G)]
    arg, eb = [sb(f"arg{g}", [P, 2, S], 2 * g) for g in range(SSD_G)], [sb(f"eb{g}", [P, 2, S], 1) for g in range(SSD_G)]
    state = [sb(f"state{g}", [P, NT - 1, P], 1) for g in range(SSD_G)]
    z = sb("z", [H16, S], 1)
    diag = sb("diag", [H16, NT, H16], 1)
    aneg = sb("aneg", [H16, 1], 1)
    assert off[0] <= B + 30 * 1024 and off[1] <= K.h_at + 32 * 1024 and off[2] <= K.arena + DC * S * 4
    CSTEP = S // NT
    order = K.count("ssd_order")
    exp_done, tr_done, cb_done, prep_done, wexp_done, wdone = (
        K.sem(f"ssd_{n}") for n in ("exp", "tr", "cb", "prep", "wexp", "w"))
    alog = K.cols[0:H16, K.cols_at["ssd_a_log"][0]:K.cols_at["ssd_a_log"][0] + 1]

    N = {n: [K.sem(f"ssd_{n}{g}") for g in range(SSD_G)] for n in (
        "rows", "bc", "arg", "eb", "decay", "m", "cd", "xs", "xt", "xdt", "st_mm", "state", "y_mm", "y", "z")}
    def tile(t, c):
        return t[:, c * CSTEP:(c + 1) * CSTEP]

    with nc.Block() as block:
        @block.scalar
        def _(act):
            nc.scalar.activation(aneg[:], alog, ACT.Exp).then_inc(exp_done, 1)
            act.wait_ge(wdone, 1)
            nc.scalar.activation(wst[:], wst[:], ACT.Exp, scale=-1.0).then_inc(wexp_done, 1)
            act.wait_ge(cb_done, 2)
            nc.scalar.activation(edec[:], K.ps[5][:, 0:NT * H16].rearrange("p (c h) -> p c h", c=NT), ACT.Exp).then_inc(prep_done, 1)

        @block.vector
        def _(dve):
            v = nc.vector
            link = Chain(dve, order)
            dve.wait_ge(exp_done, 1)
            link(v.tensor_scalar(aneg[:], aneg[:], -1.0, None, ALU.mult))
            link(v.tensor_scalar(z[:], dt[:], aneg[:, 0:1], None, ALU.mult))
            for c in range(NT):
                ins = v.tensor_tensor_scan(tile(acs, c), K.ones[0:H16, :], tile(z, c), 0.0, ALU.mult, ALU.add)
            link(ins)
            for c in range(NT):
                end = acs[:, (c + 1) * CSTEP - 1:(c + 1) * CSTEP]
                v.tensor_scalar(diag[:, c, :], K.ident[0:H16, 0:H16], end, None, ALU.mult)
                ins = v.tensor_scalar(tile(wst, c), tile(acs, c), end, None, ALU.subtract)
            ins.then_inc(wdone, 1)
            dve.wait_ge(wexp_done, 1)
            v.tensor_tensor(wst[:], wst[:], dt[:], ALU.mult).then_inc(wdone, 1)
            dve.wait_ge(tr_done, 1)
            v.tensor_copy(toks[:], K.ps[0][:, 0:3 * NT * H16].rearrange("p (k c h) -> p k c h", k=3, c=NT))
            dve.wait_ge(cb_done, 1)
            for g in range(SSD_G):
                v.tensor_copy(b_tok[:, g, :], K.ps[1 + g][:])
                v.tensor_tensor(cbm[:, g, :].rearrange("p (c l) -> p c l", c=NT), K.ps[3 + g][:].rearrange("p (c l) -> p c l", c=NT),
                                K.causal[:, None, :].to_broadcast([P, NT, P]), ALU.mult).then_inc(N["y"][g], 1)

        @block.tensor
        def _(pe):
            for g in range(SSD_G):
                bt, ct = proj[:, XB + DC + g, :], proj[:, XB + DC + SSD_G + g, :]
                for c in range(NT):
                    nc.tensor.transpose(K.ps[1 + g][:, c * P:(c + 1) * P], tile(bt, c), K.ident)
                    last = nc.tensor.matmul(K.ps[3 + g][:, c * P:(c + 1) * P], tile(bt, c), tile(ct, c), start=True, stop=True)
            last.then_inc(cb_done, 1)
            pe.wait_ge(wdone, 2)
            for k, t in enumerate((acs, dt, wst)):
                for c in range(NT):
                    last = nc.tensor.transpose(K.ps[0][:, (k * NT + c) * H16:(k * NT + c + 1) * H16], tile(t, c), K.ident[0:H16, 0:H16])
            last.then_inc(tr_done, 1)
            nc.tensor.matmul(K.ps[5][:, 0:NT * H16], K.ones[0:H16, :], diag[:], start=True, stop=True).then_inc(cb_done, 1)

    dcol = K.cols_at["ssd_d"][0]
    toks_v = toks[:]
    CD = [proj[:, XB + DC + SSD_G + g, :] for g in range(SSD_G)]
    BC, XT, ST, Y = (0, 1), 2, 2, 3
    ps = [[K.ps[4 * g + n] for n in range(4)] for g in range(SSD_G)]
    STATES = 1 + 2 * (NT - 2)
    groups = range(SSD_G)
    with nc.Block() as block:
        @block.gpsimd
        def _(pool):
            with pool.Fori(0, SSD_PAIRS) as i:
                for g in groups:
                    pool.wait_ge(N["y"][g], i + 1)
                    nc.gpsimd.tensor_copy(xs[g][:, None, :], proj[:, bass.ds(XB + g * SSD_PAIRS + i, 1), :]).then_inc(N["xs"][g], 1)
                for g in groups:
                    pool.wait_ge(N["eb"][g], 2 * i + 2)
                    nc.gpsimd.tensor_tensor(eb[g][:], eb[g][:], CD[g][:, None, :].to_broadcast([P, 2, S]), ALU.mult).then_inc(N["cd"][g], 1)

        @block.tensor
        def _(pe):
            with pe.Fori(0, SSD_PAIRS) as i:
                for g in groups:
                    pe.wait_ge(N["rows"][g], 2 * i + 2)
                    for hd in range(2):
                        last = nc.tensor.matmul(ps[g][BC[hd]][:], K.ones[0:H16, :], rows[g][:, hd, :], start=True, stop=True)
                    last.then_inc(N["bc"][g], 1)
                for g in groups:
                    pe.wait_ge(N["xs"][g], i + 1)
                    for c in range(NT):
                        last = nc.tensor.transpose(tile(ps[g][XT], c), tile(xs[g], c), K.ident)
                    last.then_inc(N["xt"][g], 1)
                for g in groups:
                    pe.wait_ge(N["xdt"][g], 2 * i + 2)
                    for c in range(NT - 1):
                        last = nc.tensor.matmul(tile(ps[g][ST], c), tile(b_tok[:, g, :], c), xw[g][:, c, :], start=True, stop=True)
                    last.then_inc(N["st_mm"][g], 1)
                for g in groups:
                    pe.wait_ge(N["m"][g], i + 1)
                    pe.wait_ge(N["cd"][g], i + 1)
                    pe.wait_ge(N["state"][g], STATES * i + STATES)
                    for hd in range(2):
                        lo, hi = hd * SSD_P, (hd + 1) * SSD_P
                        for c in range(NT):
                            dst = ps[g][Y][lo:hi, c * P:(c + 1) * P]
                            last = nc.tensor.matmul(dst, xdt[g][:, c, lo:hi], tile(arg[g][:, hd, :], c), start=True, stop=c == 0)
                            if c:
                                last = nc.tensor.matmul(dst, state[g][:, c - 1, lo:hi], tile(eb[g][:, hd, :], c), start=False, stop=True)
                    last.then_inc(N["y_mm"][g], 1)

        @block.scalar
        def _(act):
            with act.Fori(0, SSD_PAIRS) as i:
                for g in groups:
                    act.wait_ge(N["bc"][g], i + 1)
                    act.wait_ge(N["y"][g], i + 1)
                    for hd in range(2):
                        nc.scalar.activation(eb[g][:, hd, :], ps[g][BC[hd]][:], ACT.Exp).then_inc(N["eb"][g], 1)
                for g in groups:
                    act.wait_ge(N["arg"][g], 2 * NT * i + 2 * NT)
                    nc.scalar.activation(arg[g][:], arg[g][:], ACT.Exp).then_inc(N["decay"][g], 1)

        @block.vector
        def _(dve):
            v = nc.vector

            def heads(g, i):
                return 2 * SSD_PAIRS * g + 2 * i

            def one_hot(i):
                for g in groups:
                    for hd in range(2):
                        v.tensor_scalar(rows[g][:, hd, :], acs[:], K.consts[0:H16, bass.ds(heads(g, i) + hd, 1)], None, ALU.mult).then_inc(N["rows"][g], 1)

            def pairs(i, last):
                for g in groups:
                    for hd in range(2):
                        dve.wait_ge(N["eb"][g], 2 * i + hd + 1)
                        for c in range(NT):
                            v.tensor_scalar(tile(arg[g][:, hd, :], c), tile(ps[g][BC[hd]], c), toks[:, 0, c, bass.ds(heads(g, i) + hd, 1)], 0.0,
                                            ALU.subtract, ALU.min).then_inc(N["arg"][g], 1)
                for g in groups:
                    dve.wait_ge(N["xt"][g], i + 1)
                    for k, t in ((1, xdt[g]), (2, xw[g])):
                        v.tensor_tensor(t[:].rearrange("p c (h w) -> p c h w", h=2), ps[g][XT][:].rearrange("p (c h w) -> p c h w", c=NT, h=2),
                                        toks_v[:, k, :, bass.ds(heads(g, i), 2)][:, :, :, None].to_broadcast([P, NT, 2, SSD_P]), ALU.mult).then_inc(N["xdt"][g], 1)
                for g in groups:
                    dve.wait_ge(N["st_mm"][g], i + 1)
                    v.tensor_copy(state[g][:, 0, :], ps[g][ST][:, 0:P]).then_inc(N["state"][g], 1)
                    for c in range(1, NT - 1):
                        dve.wait_ge(N["state"][g], STATES * i + 1 + 2 * (c - 1))
                        for hd in range(2):
                            lo, hi = hd * SSD_P, (hd + 1) * SSD_P
                            v.scalar_tensor_tensor(state[g][:, c, lo:hi], state[g][:, c - 1, lo:hi], edec[:, c, bass.ds(heads(g, i) + hd, 1)],
                                                   ps[g][ST][:, c * P + lo:c * P + hi], ALU.mult, ALU.add).then_inc(N["state"][g], 1)
                    dve.wait_ge(N["decay"][g], i + 1)
                    v.tensor_tensor(arg[g][:], arg[g][:], cbm[:, g:g + 1, :].to_broadcast([P, 2, S]), ALU.mult).then_inc(N["m"][g], 1)
                if not last:
                    one_hot(i + 1)
                for g in groups:
                    dve.wait_ge(N["y_mm"][g], i + 1)
                    y = xdt[g][:].rearrange("p c w -> p (c w)")
                    v.scalar_tensor_tensor(y, xs[g][:], K.cols[:, bass.ds(dcol + g * SSD_PAIRS + i, 1)], ps[g][Y][:], ALU.mult, ALU.add).then_inc(N["z"][g], 1)
                    dve.wait_ge(N["z"][g], i + 1)
                    zc = proj[:, bass.ds(Z + g * SSD_PAIRS + i, 1), :]
                    v.tensor_tensor(zc, zc, y[:, None, :], ALU.mult).then_inc(N["y"][g], 1)
            one_hot(0)
            rolled(dve, SSD_PAIRS, pairs)


def hybrid_out(K, proj, GATE, nxt):
    nc = K.nc
    n = 2 * DC
    hi = K.at("hyb_hi", [P, n, S], F32R, K.h_at)
    lo = K.at("hyb_lo", [P, n, S], F32R, K.arena)
    B = K.arena + HYB * S * 4
    sq = K.at("hyb_sq", [P, DC, S], F32, B)
    rstd = K.at("hyb_rstd", [P, SSD_G, S], F32, B + DC * S * 4)
    sq_done, sum_done, r_done, root_done, v_done, hi_done = (K.sem(f"hyb_{k}") for k in ("sq", "sum", "r", "root", "v", "hi"))
    per = DC // SSD_G
    ng = K.cols_at["ssd_norm_g"][0]
    with nc.Block() as block:
        @block.scalar
        def _(act):
            for g in range(SSD_G):
                nc.scalar.activation(sq[:, per * g:per * (g + 1), :], proj[:, GATE + DC + per * g:GATE + DC + per * (g + 1), :], ACT.Square).then_inc(sq_done, 1)
            with act.Fori(0, DC) as c:
                nc.scalar.activation(hi[:, bass.ds(c, 1), :], proj[:, bass.ds(GATE + c, 1), :], ACT.Copy).then_inc(hi_done, 1)
            for g in range(SSD_G):
                act.wait_ge(r_done, 2 * g + 2)
                nc.scalar.activation(rstd[:, g, :], rstd[:, g, :], ACT.Sqrt).then_inc(root_done, 1)
            with act.Fori(0, DC) as c:
                act.wait_ge(v_done, c + 1)
                nc.scalar.activation(hi[:, bass.ds(DC + c, 1), :], proj[:, bass.ds(GATE + DC + c, 1), :], ACT.Copy).then_inc(hi_done, 1)

        def low(eng, c):
            eng.tensor_tensor(lo[:, bass.ds(c, 1), :], proj[:, bass.ds(GATE + c, 1), :], hi[:, bass.ds(c, 1), :].bitcast(F32), ALU.subtract)

        @block.gpsimd
        def _(pool):
            with pool.Fori(0, DC) as c:
                pool.wait_ge(hi_done, c + 1)
                low(nc.gpsimd, c)

        @block.tensor
        def _(pe):
            for g in range(SSD_G):
                pe.wait_ge(sq_done, g + 1)
                for c in range(per):
                    last = nc.tensor.matmul(K.ps[g][:], K.ones, sq[:, per * g + c, :], start=c == 0, stop=c == per - 1)
                last.then_inc(sum_done, 1)

        @block.vector
        def _(dve):
            v = nc.vector
            for g in range(SSD_G):
                dve.wait_ge(sum_done, g + 1)
                v.tensor_scalar(rstd[:, g, :], K.ps[g][:], 1.0 / (per * P), EPS, ALU.mult, ALU.add).then_inc(r_done, 1)
                dve.wait_ge(r_done, 2 * g + 1)
                v.reciprocal(rstd[:, g, :], rstd[:, g, :]).then_inc(r_done, 1)
            for g in range(SSD_G):
                dve.wait_ge(root_done, g + 1)
                with dve.Fori(per * g, per * (g + 1)) as c:
                    y = proj[:, bass.ds(GATE + DC + c, 1), :]
                    v.scalar_tensor_tensor(y, y, K.cols[:, bass.ds(ng + c, 1)], rstd[:, g:g + 1, :], ALU.mult, ALU.mult).then_inc(v_done, 1)
            with dve.Fori(DC, 2 * DC) as c:
                dve.wait_ge(hi_done, c + 1)
                low(v, c)

    def mm(k, j):
        kc = (j % 2) * DC + k
        return hi[:, kc, :], lo[:, kc, :], j // 2, kc == 0, kc == n - 1

    project(K, K.dram["w_hout"], DC, 2, mm, nxt, lambda o: K.coef[:, bass.ds(o, 1)], Squares(K, "hyb", K.arena + n * S * 4))


def mlstm(K, nxt, head):
    nc, d = K.nc, K.dram
    A = K.arena
    PAD = S + CONV - 1
    xm = K.at("ml_xm", [P, MLC, PAD], F32, A)
    xc = K.at("ml_xc", [P, MLC, S], F32, A + MLC * PAD * 4)
    B = A + MLC * (PAD + S) * 4
    at = [B]

    def sb(name, shape):
        t = K.at("ml_" + name, shape, F32, at[0])
        at[0] += (int(np.prod(shape[1:])) * 4 + 31) // 32 * 32
        return t
    r_row, m_row = sb("r_row", [ML_H, S]), sb("m_row", [ML_H, S])
    ccol = sb("ccol", [P, NT, ML_H])
    sel = sb("sel", [P, S])
    bd = sb("bd", [P, HC, 3 * P])
    mix = at[0]
    q, k, v, e = (sb(n, [P, HC, S]) for n in "qkve")
    pad_done = K.sem("ml_pad_zeroed")

    with nc.Block() as block:
        @block.vector
        def _(dve):
            nc.vector.memset(xm[:, :, 0:CONV - 1], 0.0).then_inc(pad_done, 1)

    ae, de = conv_evacs(K, xm, xc, 0, 0, "ml_conv_w", "ml_conv_b", MLC, ring=False)
    stream_out(K, d["w_xm"], MLC, (d["w_z"], DC), ae, de, head=head, fetch=ML_FETCH)
    K.conv_step.base += CONV * MLC
    ml_gates(K, xm, xc, r_row, m_row, ccol, mix)
    ml_heads(K, xm, xc, r_row, m_row, ccol, sel, bd, q, k, v, e)

    hi = K.at("ml_hi", [P, MLC, S], F32R, A + MLC * PAD * 4)
    lo = K.at("ml_lo", [P, MLC, S], F32R, B)
    sz = K.at("ml_sz", [P, 2, S], F32, B + MLC * S * 4)
    y_done, hi_done = K.count("ml_y"), K.sem("ml_hi_done")
    free = K.bank_free

    def act_evac(act, i, j, t, mm_done):
        act.wait_ge(K.tile_mm.sem, mm_done)
        nc.scalar.activation(sz[:, j % 2, :], K.ps[j][:], ACT.Silu).then_inc(free.sem, 1)
        act.wait_ge(y_done.sem, t + 1)
        nc.scalar.activation(hi[:, bass.ds(t, 1), :], xm[:, bass.ds(t, 1), CONV - 1:], ACT.Copy).then_inc(hi_done, 1)

    def dve_evac(dve, i, j, t, mm_done):
        y = xm[:, bass.ds(t, 1), CONV - 1:]
        dve.wait_ge(free.sem, free(t + 1))
        nc.vector.tensor_tensor(y, y, sz[:, j % 2:j % 2 + 1, :], ALU.mult).then_inc(y_done.sem, 1)
        dve.wait_ge(hi_done, t + 1)
        nc.vector.tensor_tensor(lo[:, bass.ds(t, 1), :], y, hi[:, bass.ds(t, 1), :].bitcast(F32), ALU.subtract)

    stream_out(K, d["w_z"], MLC, (d["w_mdown"], DC), act_evac, dve_evac, fetched=ML_FETCH)

    def mm(kk, j):
        kc = (j % 2) * DC + kk
        return hi[:, kc, :], lo[:, kc, :], j // 2, kc == 0, kc == MLC - 1

    project(K, d["w_mdown"], DC, 2, mm, nxt, lambda o: K.coef[:, bass.ds(o, 1)], Squares(K, "ml", K.h_at))


ML_FETCH = 2


def ml_gates(K, xm, xc, r_row, m_row, ccol, base):
    nc, d = K.nc, K.dram
    at = [base]

    def sb(name, shape):
        t = K.at("mlg_" + name, shape, F32, at[0])
        at[0] += (int(np.prod(shape[1:])) * 4 + 31) // 32 * 32
        return t
    part = HC
    parts = MLC // part
    w = sb("w", [P, 2, part, 3 * P])
    wg = sb("wg", [P, 2, part, 6 * ML_F])
    through = K.at("mlg_through", [P, MLC * 4 * ML_F], F32, K.w_raw_at + ML_FETCH * SLOT_BYTES)
    assert MLC * 4 * ML_F * 4 <= (RING - ML_FETCH) * SLOT_BYTES and part * 4 * ML_F == S
    acc = K.ps[2][0:2 * ML_F, :]
    i_pre, z, lf, e, t2, zero = (sb(n, [ML_H, S]) for n in ("i", "z", "lf", "e", "t2", "zero"))
    silu_done, w_loaded = K.sem("mlg_silu"), [K.sem(f"mlg_w{j}") for j in range(2)]
    through_mm, through_done, gate_mm = (K.sem(f"mlg_{n}") for n in ("through_mm", "through", "gate_mm"))
    order, abs_done, exp_done, m_done, tr_done = K.count("mlg_order"), K.sem("mlg_abs"), K.sem("mlg_exp"), K.sem("mlg_m"), K.sem("mlg_tr")
    bi, bf = (K.cols[0:ML_H, K.cols_at[n][0]:K.cols_at[n][0] + 1] for n in ("ml_bi", "ml_bf"))
    with nc.Block() as block:
        @block.sync
        def _(sp):
            def load(n, j):
                for src, dst in (("w_qkv_t", w), ("w_gates", wg)):
                    sp.dma_start(dst[:, j], d[src][bass.ds(part * n, part)].rearrange("c p n -> p c n")).then_inc(w_loaded[j], 16)
            for j in range(2):
                load(j, j)
            with sp.Fori(0, parts // 2 - 1) as i:
                for j in range(2):
                    sp.wait_ge(through_mm, 2 * i + j + 1)
                    load(2 * i + j + 2, j)

        @block.scalar
        def _(act):
            for c in range(0, MLC, HC):
                nc.scalar.activation(xc[:, c:c + HC, :], xc[:, c:c + HC, :], ACT.Silu).then_inc(silu_done, 1)
            act.wait_ge(abs_done, 1)
            nc.scalar.activation(e[:], e[:], ACT.Exp, scale=-1.0).then_inc(exp_done, 1)
            act.wait_ge(m_done, 1)
            nc.scalar.activation(m_row[:], m_row[:], ACT.Exp, scale=-1.0)

        @block.tensor
        def _(pe):
            def body(i, first):
                for j in range(2):
                    pe.wait_ge(w_loaded[j], 32 * i + 32)
                    if not first:
                        pe.wait_ge(through_done, 2 * i + j - 1)
                    for c in range(part):
                        at = 4 * ML_F * c
                        for n, (to, start) in enumerate(((0, True), (0, False), (2 * ML_F, True))):
                            last = nc.tensor.matmul(K.ps[j][:, at + to:at + to + 2 * ML_F], w[:, j, c, n * P:(n + 1) * P],
                                                    wg[:, j, c, 2 * n * ML_F:2 * (n + 1) * ML_F], start=start, stop=n > 0)
                    last.then_inc(through_mm, 1)
            body(0, True)
            with pe.Fori(1, parts // 2) as i:
                body(i, False)
            pe.wait_ge(silu_done, ML_H)
            pe.wait_ge(through_done, parts)

            for c in range(MLC):
                at = 4 * ML_F * c
                nc.tensor.matmul(acc, through[:, at:at + 2 * ML_F], xc[:, c, :], start=c == 0, stop=False)
                last = nc.tensor.matmul(acc, through[:, at + 2 * ML_F:at + 4 * ML_F], xm[:, c, CONV - 1:], start=False, stop=c == MLC - 1)
            last.then_inc(gate_mm, 1)
            pe.wait_ge(order.sem, ML_GATE_STEPS)
            for c in range(NT):
                last = nc.tensor.transpose(K.ps[0][:, c * ML_H:(c + 1) * ML_H], t2[:, c * P:(c + 1) * P], K.ident[0:ML_H, 0:ML_H])
            last.then_inc(tr_done, 1)

        @block.vector
        def _(dve):
            v = nc.vector
            link = Chain(dve, order)
            with dve.Fori(0, parts // 2) as i:
                for j in range(2):
                    n = 2 * i + j
                    dve.wait_ge(through_mm, n + 1)
                    v.tensor_copy(through[:, bass.ds(S * n, S)], K.ps[j][:]).then_inc(through_done, 1)
            link(v.memset(zero[:], 0.0))
            dve.wait_ge(gate_mm, 1)
            link(v.tensor_scalar(i_pre[:], acc[0:ML_H, :], bi, None, ALU.add))
            link(v.tensor_copy(z[:], acc[ML_F:ML_F + ML_H, :]))
            link(v.tensor_scalar(z[:], z[:], bf, -1.0, ALU.add, ALU.mult))

            def exp_of():
                v.tensor_copy(t2[:], e[:]).then_inc(abs_done, 1)
                dve.wait_ge(exp_done, 1)
            softplus_steps(nc, link, z[:], lf[:], e[:], t2[:], exp_of)
            link(v.tensor_scalar(lf[:], lf[:], -1.0, None, ALU.mult))
            link(v.tensor_tensor_scan(z[:], lf[:], zero[:], 0.0, ALU.add, ALU.add))
            link(v.tensor_tensor_scan(m_row[:], lf[:], i_pre[:], 0.0, ALU.add, ALU.max))
            link(v.tensor_tensor(r_row[:], z[:], m_row[:], ALU.subtract))
            v.tensor_tensor(e[:], z[:], m_row[:], ALU.add).then_inc(m_done, 1)
            link(v.tensor_tensor(t2[:], z[:], i_pre[:], ALU.subtract))
            assert link.n == ML_GATE_STEPS, link.n
            dve.wait_ge(tr_done, 1)
            v.tensor_copy(ccol[:], K.ps[0][:, 0:NT * ML_H].rearrange("p (c h) -> p c h", c=NT))


ML_GATE_STEPS = 17 + LOG1P_TERMS


def ml_heads(K, xm, xc, r_row, m_row, ccol, sel, bd, q, k, v, e):
    nc, d = K.nc, K.dram
    names = ("xs", "q_mm", "k_mm", "q", "k", "v_mm", "v", "sel", "bc", "arg", "e", "s_mm", "s", "den_mm", "rec", "num_mm", "h",
             "mean_mm", "hc", "sq", "var_mm", "r", "root", "mu", "normed")
    N = {n: K.count("mlh_" + n) for n in names}
    bd_loaded = K.sem("mlh_bd_loaded")
    gcol, scol = K.cols_at["ml_norm_g"][0], K.cols_at["ml_skip"][0]
    assert HC * S <= (RING - ML_FETCH) * KB_MAX * P
    h_t = K.at("mlh_out", [P, HC, S], F32, K.w_raw_at + ML_FETCH * SLOT_BYTES)
    sq, xs = k, e
    mu = sel
    rows = slice(0, ML_H)
    with nc.Block() as block:
        @block.sync
        def _(sp):
            def load(h):
                sp.dma_start(bd[:], d["w_qkv"][bass.ds(HC * h, HC)].rearrange("c p n -> p c n")).then_inc(bd_loaded, 16)
            load(0)
            with sp.Fori(0, ML_H - 1) as h:
                sp.wait_ge(N["v_mm"].sem, h + 1)
                load(h + 1)

        @block.gpsimd
        def _(pool):
            with pool.Fori(0, ML_H) as h:
                pool.wait_ge(N["num_mm"].sem, 4 * h)
                nc.gpsimd.tensor_copy(xs[:], xm[:, bass.ds(HC * h, HC), CONV - 1:]).then_inc(N["xs"].sem, 1)

        @block.tensor
        def _(pe):
            mmul = nc.tensor.matmul
            with pe.Fori(0, ML_H) as h:
                pe.wait_ge(bd_loaded, 16 * h + 16)
                pe.wait_ge(N["h"].sem, 4 * h)
                for c in range(HC):
                    last = mmul(K.ps[c][:], bd[:, c, 0:P], xc[:, bass.ds(HC * h + c, 1), :], start=True, stop=True)
                    last.then_inc(N["q_mm"].sem, 1)
                pe.wait_ge(N["r"].sem, 2 * h)
                for c in range(HC):
                    last = mmul(K.ps[4 + c][:], bd[:, c, P:2 * P], xc[:, bass.ds(HC * h + c, 1), :], start=True, stop=True)
                    last.then_inc(N["k_mm"].sem, 1)
                pe.wait_ge(N["xs"].sem, h + 1)
                for t in range(NT):
                    pe.wait_ge(N["q"].sem, 4 * h + t + 1)
                    for c in range(HC):
                        last = mmul(K.ps[t][:, c * P:(c + 1) * P], xs[:, c, t * P:(t + 1) * P], bd[:, c, 2 * P:3 * P], start=True, stop=True)
                last.then_inc(N["v_mm"].sem, 1)
                pe.wait_ge(N["k"].sem, 4 * h + 4)
                pe.wait_ge(N["sel"].sem, 2 * h + 1)
                mmul(K.ps[4][:], K.ones[rows, :], sel[rows, :], start=True, stop=True).then_inc(N["bc"].sem, 1)
                for sb in range(NT):
                    pe.wait_ge(N["v"].sem, 4 * h + sb + 1)
                    for c in range(HC):
                        last = mmul(K.ps[sb][:, sb * P:], k[:, c, sb * P:(sb + 1) * P], q[:, c, sb * P:], start=c == 0, stop=c == HC - 1)
                    last.then_inc(N["s_mm"].sem, 1)
                pe.wait_ge(N["sel"].sem, 2 * h + 2)
                mmul(K.ps[5][:], K.ones[rows, :], sel[rows, :], start=True, stop=True).then_inc(N["bc"].sem, 1)
                for sb in range(NT):
                    pe.wait_ge(N["s"].sem, 4 * h + sb + 1)
                    last = mmul(K.ps[6][:, sb * P:], K.ones, e[:, sb, sb * P:], start=sb == 0, stop=sb == NT - 1, skip_group_check=True)
                last.then_inc(N["den_mm"].sem, 1)
                for c in range(HC):
                    for sb in range(NT):
                        last = mmul(K.ps[c][:, sb * P:], v[:, sb, c * P:(c + 1) * P], e[:, sb, sb * P:], start=sb == 0, stop=sb == NT - 1, skip_group_check=True)
                    last.then_inc(N["num_mm"].sem, 1)
                for c in range(HC):
                    pe.wait_ge(N["h"].sem, 4 * h + c + 1)
                    last = mmul(K.ps[7][:], K.ones, h_t[:, c, :], start=c == 0, stop=c == HC - 1)
                last.then_inc(N["mean_mm"].sem, 1)
                for c in range(HC):
                    pe.wait_ge(N["sq"].sem, 4 * h + c + 1)
                    last = mmul(K.ps[4][:], K.ones, sq[:, c, :], start=c == 0, stop=c == HC - 1)
                last.then_inc(N["var_mm"].sem, 1)

        @block.scalar
        def _(act):
            with act.Fori(0, ML_H) as h:
                for c in range(HC):
                    act.wait_ge(N["q_mm"].sem, 4 * h + c + 1)
                    nc.scalar.activation(q[:, c, :], K.ps[c][:], ACT.Copy).then_inc(N["q"].sem, 1)
                for c in range(HC):
                    act.wait_ge(N["k_mm"].sem, 4 * h + c + 1)
                    nc.scalar.activation(k[:, c, :], K.ps[4 + c][:], ACT.Copy, scale=float(HC * P) ** -0.5).then_inc(N["k"].sem, 1)
                for sb in range(NT):
                    act.wait_ge(N["arg"].sem, 4 * h + sb + 1)
                    nc.scalar.activation(e[:, sb, sb * P:], e[:, sb, sb * P:], ACT.Exp).then_inc(N["e"].sem, 1)
                for c in range(HC):
                    act.wait_ge(N["hc"].sem, 4 * h + c + 1)
                    nc.scalar.activation(sq[:, c, :], h_t[:, c, :], ACT.Square).then_inc(N["sq"].sem, 1)
                act.wait_ge(N["r"].sem, 2 * h + 2)
                nc.scalar.activation(mu[:], mu[:], ACT.Sqrt).then_inc(N["root"].sem, 1)

        @block.vector
        def _(dve):
            vv = nc.vector
            with dve.Fori(0, ML_H) as h:
                one = K.consts[rows, bass.ds(h, 1)]
                vv.tensor_scalar(sel[rows, :], r_row[:], one, None, ALU.mult).then_inc(N["sel"].sem, 1)
                dve.wait_ge(N["v_mm"].sem, h + 1)
                for t in range(NT):
                    vv.tensor_copy(v[:, t, :], K.ps[t][:]).then_inc(N["v"].sem, 1)
                dve.wait_ge(N["bc"].sem, 2 * h + 1)
                vv.tensor_scalar(sel[rows, :], m_row[:], one, None, ALU.mult).then_inc(N["sel"].sem, 1)
                for sb in range(NT):
                    vv.tensor_scalar(e[:, sb, sb * P:], K.ps[4][:, sb * P:], ccol[:, sb, bass.ds(h, 1)], 0.0, ALU.subtract, ALU.min).then_inc(N["arg"].sem, 1)
                for sb in range(NT):
                    dve.wait_ge(N["e"].sem, 4 * h + sb + 1)
                    blk = e[:, sb, sb * P:(sb + 1) * P]
                    vv.tensor_tensor(blk, blk, K.causal, ALU.mult).then_inc(N["mu"].sem, 1)
                    dve.wait_ge(N["s_mm"].sem, 4 * h + sb + 1)
                    dve.wait_ge(N["mu"].sem, 5 * h + sb + 1)
                    vv.tensor_tensor(e[:, sb, sb * P:], e[:, sb, sb * P:], K.ps[sb][:, sb * P:], ALU.mult).then_inc(N["s"].sem, 1)
                rec = sel
                dve.wait_ge(N["den_mm"].sem, h + 1)
                vv.tensor_scalar(rec[:], K.ps[6][:], -1.0, None, ALU.mult).then_inc(N["rec"].sem, 1)
                dve.wait_ge(N["rec"].sem, 4 * h + 1)
                vv.tensor_tensor(rec[:], rec[:], K.ps[6][:], ALU.max).then_inc(N["rec"].sem, 1)
                dve.wait_ge(N["rec"].sem, 4 * h + 2)
                dve.wait_ge(N["bc"].sem, 2 * h + 2)
                vv.tensor_tensor(rec[:], rec[:], K.ps[5][:], ALU.max).then_inc(N["rec"].sem, 1)
                dve.wait_ge(N["rec"].sem, 4 * h + 3)
                vv.reciprocal(rec[:], rec[:]).then_inc(N["rec"].sem, 1)
                dve.wait_ge(N["rec"].sem, 4 * h + 4)
                for c in range(HC):
                    dve.wait_ge(N["num_mm"].sem, 4 * h + c + 1)
                    vv.tensor_tensor(h_t[:, c, :], K.ps[c][:], rec[:], ALU.mult).then_inc(N["h"].sem, 1)
                dve.wait_ge(N["mean_mm"].sem, h + 1)
                dve.wait_ge(N["h"].sem, 4 * h + 4)
                vv.tensor_scalar(mu[:], K.ps[7][:], 1.0 / (HC * P), None, ALU.mult).then_inc(N["mu"].sem, 1)
                dve.wait_ge(N["mu"].sem, 5 * h + 5)
                for c in range(HC):
                    vv.tensor_tensor(h_t[:, c, :], h_t[:, c, :], mu[:], ALU.subtract).then_inc(N["hc"].sem, 1)
                dve.wait_ge(N["var_mm"].sem, h + 1)
                vv.tensor_scalar(mu[:], K.ps[4][:], 1.0 / (HC * P), EPS, ALU.mult, ALU.add).then_inc(N["r"].sem, 1)
                dve.wait_ge(N["r"].sem, 2 * h + 1)
                vv.reciprocal(mu[:], mu[:]).then_inc(N["r"].sem, 1)
                dve.wait_ge(N["root"].sem, h + 1)
                for c in range(HC):
                    vv.scalar_tensor_tensor(h_t[:, c, :], h_t[:, c, :], K.cols[:, bass.ds(gcol + HC * h + c, 1)], mu[:], ALU.mult, ALU.mult).then_inc(N["normed"].sem, 1)
                for c in range(HC):
                    dve.wait_ge(N["normed"].sem, 4 * h + c + 1)
                    vv.scalar_tensor_tensor(xm[:, bass.ds(HC * h + c, 1), CONV - 1:], xc[:, bass.ds(HC * h + c, 1), :],
                                            K.cols[:, bass.ds(scol + HC * h + c, 1)], h_t[:, c:c + 1, :], ALU.mult, ALU.add)


def second_block(K):
    nc, d = K.nc, K.dram
    A = K.arena
    o_hi = K.at("oa_hi", [P, 2, S], F32R, A)
    o_lo = K.at("oa_lo", [P, 2, S], F32R, A + 4096)
    p1 = K.at("attn_proj", [P, 2 + QKV, S], F32, A + 8192)
    raw1 = K.at("shift_raw1", [P, 2, S + 1], F32, A + 8192 + (2 + QKV) * S * 4)
    rkv = K.at("rkv", [P, 3 * DC, S], F32, A + 8192 + 4096)
    raw2 = K.at("shift_raw2", [P, 2, S + 1], F32, A + 8192 + 4096 + 3 * DC * S * 4)
    lora = p1[:, 0:2, :]
    m = [K.mods[:, 144 + 8 * n:152 + 8 * n] for n in range(6)]
    sh1, sc1, gt1, sh2, sc2, gt2 = m
    head = Modulated(K, col(K, "mix_pre", 0, 8), sc1, sh1, gt1, 1.0)
    mu0 = K.cols_at["shift_mu"][0]
    shifted = K.count("shifted")
    for n, (w, n_tiles, raw, dst, o0, nxt) in enumerate((("w_attn", 2 + QKV, raw1, p1, 0, "w_rkv"), ("w_rkv", 3 * DC, raw2, rkv, 2 + QKV, "w_gate2"))):
        pad = K.sem(f"shift_pad{n}")
        with nc.Block() as block:
            @block.vector
            def _(dve):
                nc.vector.memset(raw[:, :, 0:1], 0.0).then_inc(pad, 1)
                if n == 0:
                    nc.vector.memset(K.pad4[:], 0.0).then_inc(shifted.sem, 4)
                    shifted.base = 4
        ae, de = shift_evacs(K, raw, dst, mu0 + o0, shifted)
        stream_out(K, d[w], n_tiles, (d[nxt], DC), ae, de, head=head if n == 0 else None,
                   fetched=RING if n == 0 else RWKV_FETCH, fetch=RWKV_FETCH)
        shifted.base += 2 * n_tiles
        if n == 0:
            with stage(K):
                attention(K, p1, o_hi, o_lo, A + 8192 + (2 + QKV) * S * 4)
    with stage(K):
        rwkv(K, lora, rkv, A + 8192 + 4096 + 3 * DC * S * 4)

    G = A + 8192 + 4096 + 3 * DC * S * 4
    gates = K.at("branch_gates", [P, 2 * DC, S], F32, G)
    r_hi = K.at("or_hi", [P, DC, S], F32R, A + 8192 + 4096 + DC * S * 4)
    r_lo = K.at("or_lo", [P, DC, S], F32R, A + 8192 + 4096 + 2 * DC * S * 4)
    sp_hi = K.sem("or_hi_done")
    with nc.Block() as block:
        @block.scalar
        def _(act):
            for c in range(0, DC, 2):
                nc.scalar.activation(r_hi[:, c:c + 2, :], rkv[:, c:c + 2, :], ACT.Copy).then_inc(sp_hi, 1)

        @block.vector
        def _(dve):
            for c in range(0, DC, 2):
                dve.wait_ge(sp_hi, c // 2 + 1)
                nc.vector.tensor_tensor(r_lo[:, c:c + 2, :], rkv[:, c:c + 2, :], r_hi[:, c:c + 2, :].bitcast(F32), ALU.subtract)
    stream_out(K, d["w_gate2"], 2 * DC, (d["w_branch"], 2 + DC), act_out(K, gates, 0, ACT.Sigmoid), fetched=RWKV_FETCH)

    free, merged, hi_done = K.bank_free, K.count("merged"), K.sem("merged_hi")

    def mm(k, j):
        if k < 2:
            return o_hi[:, k, :], o_lo[:, k, :], 2 * j, k == 0, k == 1
        return r_hi[:, k - 2, :], r_lo[:, k - 2, :], 2 * j + 1, k == 2, k == 1 + DC

    def pe_wait(pe, i, j, t):
        pe.wait_ge(free.sem, free(t - RING + 1))

    def act_evac(act, i, j, t, mm_done):
        act.wait_ge(merged.sem, 2 * t + 2)
        nc.scalar.activation(K.h_hi[:, bass.ds(t, 1), :], gates[:, bass.ds(t, 1), :], ACT.Copy).then_inc(hi_done, 1)

    def dve_evac(dve, i, j, t, mm_done):
        ga, gr = gates[:, bass.ds(t, 1), :], gates[:, bass.ds(DC + t, 1), :]
        dve.wait_ge(K.tile_mm.sem, mm_done)
        nc.vector.tensor_tensor(ga, ga, K.ps[2 * j][:, None, :], ALU.mult).then_inc(merged.sem, 1)
        nc.vector.tensor_tensor(gr, gr, K.ps[2 * j + 1][:, None, :], ALU.mult).then_inc(free.sem, 1)
        dve.wait_ge(merged.sem, 2 * t + 1)
        dve.wait_ge(free.sem, free(t + 1))
        nc.vector.tensor_tensor(ga, ga, gr, ALU.add).then_inc(merged.sem, 1)
        dve.wait_ge(hi_done, t + 1)
        nc.vector.tensor_tensor(K.h_lo[:, bass.ds(t, 1), :], ga, K.h_hi[:, bass.ds(t, 1), :].bitcast(F32), ALU.subtract)

    gemm(K, d["w_branch"], 2 + DC, DC, (d["w_out2"], DC), mm, pe_wait, act_evac, dve_evac)
    free.base += DC
    mix = K.at("mix_out", [P, DC, S], F32, G)
    squares = Squares(K, "mix", A + 8192 + 4096, RING)

    def square_mix(dve, i, j, t, mm_done):
        dve.wait_ge(free.sem, free(t + 1))
        squares.by_dve(dve, mix[:, bass.ds(t, 1), :], t, j % 2)
    stream_out(K, d["w_out2"], DC, (d["w_ff10"], DC), act_out(K, mix, 0, ACT.Copy), square_mix, squares=squares)
    norm(K, "n2p", mix, col(K, "mix_post", 0, 8), gate=gt1, squares=Squares(K, "x2", K.h_at + 4 * S * 4))

    head = Modulated(K, col(K, "ffn_pre", 0, 8), sc2, sh2, gt2, 1.0)
    HF = FF2 // 2
    u_hi = K.at("u_hi", [P, HF, S], F32R, A)
    u_lo = K.at("u_lo", [P, HF, S], F32R, A + HF * S * 4)
    f = K.at("ffn_out", [P, DC, S], F32, A + 2 * HF * S * 4)
    rel = K.at("relu", [P, 2, S], F32, A + (2 * HF + DC) * S * 4)
    squared = K.count("squared")
    uhi = K.count("u_hi_done")
    for half in range(2):
        def act_evac(act, i, j, t, mm_done):
            act.wait_ge(K.tile_mm.sem, mm_done)
            nc.scalar.activation(rel[:, j % 2, :], K.ps[j][:], ACT.Relu).then_inc(free.sem, 1)
            act.wait_ge(squared.sem, squared(t + 1))
            nc.scalar.activation(u_hi[:, bass.ds(t, 1), :], rel[:, j % 2:j % 2 + 1, :], ACT.Copy).then_inc(uhi.sem, 1)

        def dve_evac(dve, i, j, t, mm_done):
            r = rel[:, j % 2:j % 2 + 1, :]
            dve.wait_ge(free.sem, free(t + 1))
            nc.vector.tensor_tensor(r, r, r, ALU.mult).then_inc(squared.sem, 1)
            dve.wait_ge(uhi.sem, uhi(t + 1))
            nc.vector.tensor_tensor(u_lo[:, bass.ds(t, 1), :], r, u_hi[:, bass.ds(t, 1), :].bitcast(F32), ALU.subtract)

        stream_out(K, d[f"w_ff1{half}"], HF, (d[f"w_ff2{half}"], DC), act_evac, dve_evac, head=head if half == 0 else None)
        squared.base += HF
        uhi.base += HF

        def mm(k, j):
            kc = (j % 2) * DC + k
            return u_hi[:, kc, :], u_lo[:, kc, :], j // 2, kc == 0, kc == HF - 1

        def pe_wait(pe, i, j, t):
            if j % 2 == 0:
                pe.wait_ge(free.sem, free(2 * i + j // 2 - 1))

        def dve_evac2(dve, i, j, t, mm_done):
            if j % 2 == 1:
                o = f[:, bass.ds(2 * i + j // 2, 1), :]
                dve.wait_ge(K.tile_mm.sem, mm_done)
                if half == 0:
                    ins = nc.vector.tensor_copy(o, K.ps[j // 2][:, None, :])
                else:
                    ins = nc.vector.tensor_tensor(o, o, K.ps[j // 2][:, None, :], ALU.add)
                ins.then_inc(free.sem, 1)

        squares = Squares(K, "ffn", K.h_at) if half else None

        def square_f(act, i, j, t, mm_done):
            if j % 2 == 1:
                o = 2 * i + j // 2
                act.wait_ge(free.sem, free(o + 1))
                squares.by_act(act, f[:, bass.ds(o, 1), :], o, j // 2)

        gemm(K, d[f"w_ff2{half}"], DC, 2 * DC, (d["w_ff11"], DC) if half == 0 else None, mm, pe_wait, square_f if half else None, dve_evac2,
             squares=squares)
        free.base += DC
    norm(K, "n2f", f, col(K, "ffn_post", 0, 8), gate=gt2, store=K.stored)


def shift_evacs(K, raw, dst, mu0, shifted):
    nc, free = K.nc, K.bank_free

    def act_evac(act, i, j, t, mm_done):
        act.wait_ge(K.tile_mm.sem, mm_done)
        act.wait_ge(shifted.sem, shifted(2 * (t - 1)))
        nc.scalar.activation(raw[:, j % 2, 1:], K.ps[j][:], ACT.Copy).then_inc(free.sem, 1)

    def dve_evac(dve, i, j, t, mm_done):
        u, prev = raw[:, j % 2:j % 2 + 1, 1:], raw[:, j % 2:j % 2 + 1, 0:S]
        o = dst[:, bass.ds(t, 1), :]
        dve.wait_ge(free.sem, free(t + 1))
        nc.vector.tensor_tensor(o, prev, u, ALU.subtract).then_inc(shifted.sem, 1)
        dve.wait_ge(shifted.sem, shifted(2 * t + 1))
        nc.vector.scalar_tensor_tensor(o, o, K.cols[:, bass.ds(mu0 + t, 1)], u, ALU.mult, ALU.add).then_inc(shifted.sem, 1)

    return act_evac, dve_evac


TWO_PI = (6.28125, 1.93500518798828125e-03, 3.0199160983e-07)
ROUND = 12582912.0


def attention(K, p1, o_hi, o_lo, base):
    nc, d = K.nc, K.dram
    at = [base]

    def sb(name, shape, dt=F32):
        t = K.at("at_" + name, shape, dt, at[0])
        at[0] += (int(np.prod(shape[1:])) * 4 + 31) // 32 * 32
        return t
    masks, mats = sb("masks", [P, 3 * P]), sb("mats", [P, 3 * P])
    cos, sin = sb("cos", [P, S]), sb("sin", [P, S])
    qp, kp, vp = sb("qp", [P, S]), sb("kp", [P, S]), sb("vp", [P, S])
    t1, t2 = sb("t1", [P, S]), sb("t2", [P, S])
    v_tok = sb("v_tok", [P, NT, P])
    sm, pT = ([sb(n, [P, 2, NT, P]), K.at(f"at_{n}1", [P, 2, NT, P], F32, K.w_raw_at + RWKV_FETCH * SLOT_BYTES + k * 2 * NT * P * 4)]
              for k, n in enumerate(("sm", "pT")))
    assert 16 * NT * P <= (RING - RWKV_FETCH) * SLOT_BYTES
    S_BANK, T_BANK = (3, 0), (5, 0)
    o = sb("o", [P, GROUPS, 2, S])
    mx, l, lse = sb("mx", [P, GROUPS, NT, 4]), sb("l", [P, GROUPS, NT, 4]), sb("lse", [P, GROUPS, NT, 4])
    m2, rl = sb("m2", [P, 2, NT]), sb("rl", [P, 2, NT])
    rows, wrow = sb("rows", [4, GROUPS, S]), sb("wrow", [4, 2, S])
    pos = K.at("at_pos", [P, S], I32, at[0] - 5 * 2048)
    assert at[0] - base < 58 * 1024, at[0] - base
    rot = mats[:, 0:P]
    loaded, order = K.sem("at_loaded"), K.count("at_order")
    trig_done = K.sem("at_trig")
    inv = K.cols[:, K.cols_at["rope_inv"][0]:K.cols_at["rope_inv"][0] + 1]
    with nc.Block() as block:
        @block.sync
        def _(sp):
            sp.dma_start(masks[:], d["attn_masks"]).then_inc(loaded, 16)
            sp.dma_start(mats[:], d["attn_mats"]).then_inc(loaded, 16)
            sp.dma_start(pos[:], d["positions"].to_broadcast([P, S])).then_inc(loaded, 16)
            sp.wait_ge(loaded, 48)

        @block.vector
        def _(dve):
            v = nc.vector
            link = Chain(dve, order)
            dve.wait_ge(loaded, 48)
            link(v.tensor_copy(t1[:], pos[:]))
            link(v.tensor_scalar(t1[:], t1[:], inv, None, ALU.mult))
            link(v.tensor_scalar(t2[:], t1[:], float(0.5 / np.pi), ROUND, ALU.mult, ALU.add))
            link(v.tensor_scalar(t2[:], t2[:], -ROUND, None, ALU.add))
            for part in TWO_PI:
                link(v.scalar_tensor_tensor(t1[:], t2[:], -part, t1[:], ALU.mult, ALU.add))
            link(v.tensor_scalar(t1[:], t1[:], float(np.float32(3.1415925)), -float(np.float32(3.1415925)), ALU.min, ALU.max))
            dve.wait_ge(trig_done, 2)
            link(v.tensor_tensor(cos[:], cos[:], cos[:], ALU.mult))
            link(v.tensor_scalar(cos[:], cos[:], -2.0, 1.0, ALU.mult, ALU.add))

        @block.scalar
        def _(act):
            act.wait_ge(order.sem, 8)
            nc.scalar.activation(sin[:], t1[:], ACT.Sin).then_inc(trig_done, 1)
            nc.scalar.activation(cos[:], t1[:], ACT.Sin, scale=0.5).then_inc(trig_done, 1)

    names = ("rot", "tq", "qk", "vp", "vt_mm", "vt", "s_mm", "sm", "max", "arg", "p", "sum", "rl", "pn", "pt_mm", "pt", "pv", "o")
    N = {n: K.count("ath_" + n) for n in names}
    for g in range(GROUPS):
        dil = DILATION[g]
        wide = 2 if g == 0 else 1

        def permuted(t):
            return t.rearrange("p (r j) -> p j r", r=dil) if dil > 1 else t

        def by_token(t):
            return t.rearrange("p (j r) -> p j r", r=dil) if dil > 1 else t

        b = {n: c.base for n, c in N.items()}
        with nc.Block() as block:
            @block.gpsimd
            def _(pool):
                with pool.Fori(0, 2) as i:
                    pool.wait_ge(N["o"].sem, b["o"] + i + 1)
                    nc.gpsimd.tensor_copy(permuted(vp[:]), by_token(p1[:, bass.ds(2 + 12 + 2 * g + i, 1), :].rearrange("p o s -> p (o s)"))).then_inc(N["vp"].sem, 1)

            @block.tensor
            def _(pe):
                with pe.Fori(0, 2) as i:
                    pe.wait_ge(N["o"].sem, b["o"] + i + 1)
                    for n in range(2):
                        nc.tensor.matmul(K.ps[n][:], rot, p1[:, bass.ds(2 + 6 * n + 2 * g + i, 1), :], start=True, stop=True).then_inc(N["rot"].sem, 1)
                    pe.wait_ge(N["vp"].sem, b["vp"] + i + 1)
                    for t in range(NT):
                        last = nc.tensor.transpose(K.ps[2][:, t * P:(t + 1) * P], vp[:, t * P:(t + 1) * P], K.ident)
                    last.then_inc(N["vt_mm"].sem, 1)
                    pe.wait_ge(N["qk"].sem, b["qk"] + 2 * i + 2)
                    half = [slice(hd * HD, (hd + 1) * HD) for hd in range(2)]
                    for hd, hr in enumerate(half):
                        for w in range(wide):
                            for t in range(w, NT):
                                last = nc.tensor.matmul(K.ps[S_BANK[hd] + w][:, t * P:(t + 1) * P], qp[hr, t * P:(t + 1) * P], kp[hr, (t - w) * P:(t - w + 1) * P], start=True, stop=True)
                        last.then_inc(N["s_mm"].sem, 1)
                    for hd in range(2):
                        pe.wait_ge(N["pn"].sem, b["pn"] + 2 * i + hd + 1)
                        for w in range(wide):
                            for t in range(w, NT):
                                last = nc.tensor.transpose(K.ps[T_BANK[hd] + w][:, t * P:(t + 1) * P], sm[hd][:, w, t, :], K.ident)
                        last.then_inc(N["pt_mm"].sem, 1)
                    pe.wait_ge(N["vt"].sem, b["vt"] + i + 1)
                    for hd, hr in enumerate(half):
                        pe.wait_ge(N["pt"].sem, b["pt"] + wide * (2 * i + hd + 1))
                        for t in range(NT):
                            for w in range(min(wide, t + 1)):
                                last = nc.tensor.matmul(K.ps[7][hr, t * P:(t + 1) * P], v_tok[:, t - w, hr], pT[hd][:, w, t, :], start=w == 0, stop=w == min(wide, t + 1) - 1)
                        last.then_inc(N["pv"].sem, 1)

            @block.scalar
            def _(act):
                with act.Fori(0, 2) as i:
                    act.wait_ge(N["vt_mm"].sem, b["vt_mm"] + i + 1)
                    nc.scalar.activation(v_tok[:].rearrange("p t c -> p (t c)"), K.ps[2][:], ACT.Copy).then_inc(N["vt"].sem, 1)
                    for hd in range(2):
                        act.wait_ge(N["arg"].sem, b["arg"] + 2 * i + hd + 1)
                        nc.scalar.activation(sm[hd][:, 0:wide], sm[hd][:, 0:wide], ACT.Exp, scale=float(HD) ** -0.5).then_inc(N["p"].sem, 1)
                    for hd in range(2):
                        act.wait_ge(N["pt_mm"].sem, b["pt_mm"] + 2 * i + hd + 1)
                        for w in range(wide):
                            nc.scalar.activation(pT[hd][:, w, w:, :].rearrange("p t k -> p (t k)"), K.ps[T_BANK[hd] + w][:, w * P:], ACT.Copy).then_inc(N["pt"].sem, 1)

            @block.vector
            def _(dve):
                v = nc.vector
                if g == 0:
                    v.memset(m2[:], 0.0).then_inc(N["o"].sem, 1)
                with dve.Fori(0, 2) as i:
                    for n, dst in ((0, qp), (1, kp)):
                        v.tensor_tensor(t1[:], p1[:, bass.ds(2 + 6 * n + 2 * g + i, 1), :].rearrange("p o s -> p (o s)"), cos[:], ALU.mult).then_inc(N["tq"].sem, 1)
                        dve.wait_ge(N["rot"].sem, b["rot"] + 2 * i + n + 1)
                        v.tensor_tensor(t2[:], K.ps[n][:], sin[:], ALU.mult).then_inc(N["tq"].sem, 1)
                        dve.wait_ge(N["tq"].sem, b["tq"] + 4 * i + 2 * n + 2)
                        v.tensor_tensor(permuted(dst[:]), by_token(t1[:]), by_token(t2[:]), ALU.add).then_inc(N["qk"].sem, 1)
                        dve.wait_ge(N["qk"].sem, b["qk"] + 2 * i + n + 1)
                    per = 3 if wide == 2 else 1
                    heads = [(hd, 2 * i + hd, sm[hd], mx[:, g, :, bass.ds(2 * i + hd, 1)], l[:, g, :, bass.ds(2 * i + hd, 1)]) for hd in range(2)]
                    mask = masks[:, P:2 * P] if g == 2 else masks[:, 0:P]
                    for hd, u, s, mxc, lc in heads:
                        dve.wait_ge(N["s_mm"].sem, b["s_mm"] + u + 1)
                        v.tensor_tensor(s[:, 0], K.ps[S_BANK[hd]][:].rearrange("p (t k) -> p t k", t=NT), mask[:, None, :].to_broadcast([P, NT, P]), ALU.add).then_inc(N["sm"].sem, 1)
                        if wide == 2:
                            v.memset(s[:, 1, 0, :], NEG).then_inc(N["sm"].sem, 1)
                            v.tensor_tensor(s[:, 1, 1:, :], K.ps[S_BANK[hd] + 1][:, P:].rearrange("p (t k) -> p t k", t=NT - 1),
                                            masks[:, None, 2 * P:3 * P].to_broadcast([P, NT - 1, P]), ALU.add).then_inc(N["sm"].sem, 1)
                    for hd, u, s, mxc, lc in heads:
                        dve.wait_ge(N["sm"].sem, b["sm"] + per * (u + 1))
                        v.tensor_reduce(mxc, s[:, 0], AX_X, ALU.max).then_inc(N["max"].sem, 1)
                        if wide == 2:
                            v.tensor_reduce(m2[:, hd, :], s[:, 1], AX_X, ALU.max).then_inc(N["max"].sem, 1)
                            dve.wait_ge(N["max"].sem, b["max"] + 3 * u + 2)
                            v.tensor_tensor(mxc, mxc, m2[:, hd, :, None], ALU.max).then_inc(N["max"].sem, 1)
                    for hd, u, s, mxc, lc in heads:
                        dve.wait_ge(N["max"].sem, b["max"] + per * (u + 1))
                        for w in range(wide):
                            ins = v.tensor_tensor(s[:, w], s[:, w], mxc.to_broadcast([P, NT, P]), ALU.subtract)
                        ins.then_inc(N["arg"].sem, 1)
                    for hd, u, s, mxc, lc in heads:
                        dve.wait_ge(N["p"].sem, b["p"] + u + 1)
                        v.tensor_reduce(lc, s[:, 0], AX_X, ALU.add).then_inc(N["sum"].sem, 1)
                        if wide == 2:
                            v.tensor_reduce(m2[:, hd, :], s[:, 1], AX_X, ALU.add).then_inc(N["sum"].sem, 1)
                            dve.wait_ge(N["sum"].sem, b["sum"] + 3 * u + 2)
                            v.tensor_tensor(lc, lc, m2[:, hd, :, None], ALU.add).then_inc(N["sum"].sem, 1)
                        dve.wait_ge(N["sum"].sem, b["sum"] + per * (u + 1))
                        v.tensor_scalar(rl[:, hd, :, None], lc, 1.0, None, ALU.mult).then_inc(N["rl"].sem, 1)
                        dve.wait_ge(N["rl"].sem, b["rl"] + 2 * u + 1)
                        v.reciprocal(rl[:, hd, :], rl[:, hd, :]).then_inc(N["rl"].sem, 1)
                        dve.wait_ge(N["rl"].sem, b["rl"] + 2 * u + 2)
                        for w in range(wide):
                            ins = v.tensor_tensor(s[:, w], s[:, w], rl[:, hd, :, None].to_broadcast([P, NT, P]), ALU.mult)
                        ins.then_inc(N["pn"].sem, 1)
                    dve.wait_ge(N["pv"].sem, b["pv"] + 2 * i + 2)
                    v.tensor_copy(by_token(o[:, g, bass.ds(i, 1), :].rearrange("p o s -> p (o s)")), permuted(K.ps[7][:])).then_inc(N["o"].sem, 1)
        per = 3 if wide == 2 else 1
        for n, k in (("rot", 4), ("tq", 8), ("qk", 4), ("vp", 2), ("vt_mm", 2), ("vt", 2), ("s_mm", 4), ("sm", 4 * per), ("max", 4 * per), ("arg", 4), ("p", 4),
                     ("sum", 4 * per), ("rl", 8), ("pn", 4), ("pt_mm", 4), ("pt", 4 * wide), ("pv", 4), ("o", 2)):
            N[n].base += k

    order2, ln_done, tr_done, e_done, bc_done, fin, hi_done = (K.count("atw_order"), *(K.sem("atw_" + n) for n in ("ln", "tr", "e", "bc", "fin", "hi")))
    with nc.Block() as block:
        @block.scalar
        def _(act):
            nc.scalar.activation(l[:], l[:], ACT.Ln).then_inc(ln_done, 1)
            act.wait_ge(order2.sem, 7)
            nc.scalar.activation(rows[:], rows[:], ACT.Exp).then_inc(e_done, 1)
            for c in range(2):
                act.wait_ge(fin, c + 1)
                nc.scalar.activation(o_hi[:, c, :], o[:, 0, c, :], ACT.Copy).then_inc(hi_done, 1)

        @block.tensor
        def _(pe):
            pe.wait_ge(order2.sem, 1)
            for g in range(GROUPS):
                for t in range(NT):
                    last = nc.tensor.transpose(K.ps[g][0:4, t * P:(t + 1) * P], lse[:, g, t, :], K.ident)
            last.then_inc(tr_done, 1)
            pe.wait_ge(order2.sem, 11)
            for c in range(2):
                for g in range(GROUPS):
                    nc.tensor.matmul(K.ps[GROUPS * c + g][:], mats[0:4, (1 + c) * P:(2 + c) * P], rows[:, g, :], start=True, stop=True).then_inc(bc_done, 1)

        @block.vector
        def _(dve):
            v = nc.vector
            link = Chain(dve, order2)
            dve.wait_ge(ln_done, 1)
            link(v.scalar_tensor_tensor(lse[:], mx[:], float(HD) ** -0.5, l[:], ALU.mult, ALU.add))
            dve.wait_ge(tr_done, 1)
            for g in range(GROUPS):
                dil = DILATION[g]
                src, dst = K.ps[g][0:4, :], rows[:, g, :]
                if dil > 1:
                    src, dst = src.rearrange("p (r j) -> p j r", r=dil), dst.rearrange("p (j r) -> p j r", r=dil)
                ins = v.tensor_copy(dst, src)
            link(ins)
            link(v.tensor_tensor(wrow[:, 0, :], rows[:, 0, :], rows[:, 1, :], ALU.max))
            link(v.tensor_tensor(wrow[:, 0, :], wrow[:, 0, :], rows[:, 2, :], ALU.max))
            for g in range(GROUPS):
                link(v.tensor_tensor(rows[:, g, :], rows[:, g, :], wrow[:, 0, :], ALU.subtract))
            dve.wait_ge(e_done, 1)
            link(v.tensor_tensor(wrow[:, 0, :], rows[:, 0, :], rows[:, 1, :], ALU.add))
            link(v.tensor_tensor(wrow[:, 0, :], wrow[:, 0, :], rows[:, 2, :], ALU.add))
            link(v.reciprocal(wrow[:, 1, :], wrow[:, 0, :]))
            link(v.tensor_tensor(rows[:], rows[:], wrow[:, 1:2, :].to_broadcast([4, GROUPS, S]), ALU.mult))
            for c in range(2):
                for g in range(GROUPS):
                    dve.wait_ge(bc_done, GROUPS * c + g + 1)
                    link(v.tensor_tensor(o[:, g, c, :], o[:, g, c, :], K.ps[GROUPS * c + g][:], ALU.mult))
                link(v.tensor_tensor(o[:, 0, c, :], o[:, 0, c, :], o[:, 1, c, :], ALU.add))
                v.tensor_tensor(o[:, 0, c, :], o[:, 0, c, :], o[:, 2, c, :], ALU.add).then_inc(fin, 1)
            for c in range(2):
                dve.wait_ge(hi_done, c + 1)
                v.tensor_tensor(o_lo[:, c, :], o[:, 0, c, :], o_hi[:, c, :].bitcast(F32), ALU.subtract)


RWKV_FETCH = 2
RWKV_DECAY = -float(np.exp(-0.5))


def rwkv(K, lora, rkv, base):
    nc, d = K.nc, K.dram
    at = [base]

    def sb(name, shape):
        t = K.at("rw_" + name, shape, F32, at[0])
        at[0] += (int(np.prod(shape[1:])) * 4 + 31) // 32 * 32
        return t
    masks = sb("masks", [P, 10 * P + 2 * LEVELS])
    log_w, a, kkn = (sb(n, [P, S]) for n in ("logw", "a", "kk"))
    raw = K.w_raw_at + RWKV_FETCH * SLOT_BYTES
    names = ("k", "b", "a_dec", "r", "bonus")
    kc, bc, ac, rc, bonus = ([sb(name, [P, S]), K.at(f"rw_{name}1", [P, S], F32, raw + n * S * 4)] for n, name in enumerate(names))
    w_lora, w_gate = sb("w_lora", [P, P]), sb("w_gate", [P, P])
    at_, bt, kt, vt, vs = (sb(n, [P, NT, P]) for n in ("a_tok", "b_tok", "k_tok", "v_tok", "v"))
    spare = [a + SLOT_BYTES + n * S * 4 for a in (K.w_hi_at, K.w_lo_at) for n in range(2)]
    abT = [sb("abT0", [P, NT, P]), K.at("rw_abT1", [P, NT, P], F32, spare[0])]
    T = [sb("T0", [P, NT, P]), K.at("rw_T1", [P, NT, P], F32, spare[1])]
    TT = [sb("TT0", [P, NT, P]), K.at("rw_TT1", [P, NT, P], F32, spare[2])]
    off = [sb("off0", [P, NT, P]), K.at("rw_off1", [P, NT, P], F32, spare[3])]
    W = [sb("W0", [P, NT, P]), sb("W1", [P, NT, P])]
    qs, y = sb("q", [P, S]), sb("y", [P, S])
    G, H = sb("G", [P, NT, HD]), sb("H", [P, NT, HD])
    sh = K.at("rw_sh", [P, P], F32, spare[1] + S * 4)
    s1 = K.at("rw_s1", [P, HD], F32, spare[1] + S * 4 + P * 4)
    mid, ka1 = sb("mid", [P, NT]), sb("ka1", [P, DC])
    pm, pl = ([sb(f"{n}{x}", [P, NT]) for x in range(2)] for n in ("pm", "pl"))
    assert at[0] <= K.nc.sbuf_usable_end, at[0] - K.nc.sbuf_usable_end
    akT, rbT, rkT, cat, xu = abT, T, off, W, TT
    strict, pair_t, pair = masks[:, 0:P], masks[:, P:2 * P], masks[:, 2 * P:3 * P]
    level = [masks[:, (3 + n) * P:(4 + n) * P] for n in range(LEVELS)]
    same = masks[:, 9 * P:10 * P]
    first_half = [masks[:, 10 * P + n:10 * P + n + 1] for n in range(LEVELS)]
    second_half = [masks[:, 10 * P + LEVELS + n:10 * P + LEVELS + n + 1] for n in range(LEVELS)]
    B = [[K.ps[4 * hd + n] for n in range(4)] for hd in range(2)]

    def half(x, lv, second):
        return x.rearrange("p t (n h b) -> p t n h b", h=2, b=2 << lv)[:, :, :, second, :]

    def half_of_chunk(x, lv, second):
        return x.rearrange("p (n h b) -> p n h b", h=2, b=2 << lv)[:, :, second, :]

    PER = {"lora": 2, "sig": 2, "kk": 1, "sq": 1, "ss": 1, "root": 1, "kkn": 4, "k2": 2, "rk": 1, "rk_mm": 1, "bonus": 1, "logw": 1, "cs": 4, "csm": 3,
           "exp": 4, "dec": 5, "vs": 1, "tr": 4, "tok": 4, "score": 10, "mask": 12, "ident": 4, "off": 2 * LEVELS, "w_mm": 2 * LEVELS, "w": 2 * LEVELS,
           "dT": 2 * LEVELS - 2, "dTT": 2 * LEVELS, "T": 2 * LEVELS - 2, "TT": 2 * LEVELS, "akv": 2, "cat": 4, "xu_mm": 2, "xu": 2, "qy": 2, "gh": 4, "qev": 8,
           "s": 10, "y_mm": 3, "s_mm": 2, "yadd": 1, "mean": 1, "yc": 1, "ysq": 1, "var": 1, "r": 2, "yroot": 1, "yn": 3, "g_mm": 1, "out": 1}
    N = {n: K.count("rw_" + n) for n in PER}

    def sig(ins, name):
        ins.then_inc(N[name].sem, 1)

    def after(eng, i, name, n):
        eng.wait_ge(N[name].sem, PER[name] * i + n)

    loaded, lora_act, ka_done = K.sem("rw_loaded"), K.sem("rw_lora_act"), K.sem("rw_ka")
    w_loaded = [K.sem(f"rw_w_loaded{x}") for x in range(2)]
    with nc.Block() as block:
        @block.sync
        def _(sp):
            sp.dma_start(masks[:], d["rwkv_masks"]).then_inc(loaded, 16)
            for n, x in enumerate((w_lora, w_gate)):
                sp.dma_start(x[:], d["w_lora"][0][:, n * P:(n + 1) * P]).then_inc(w_loaded[n], 16)
            sp.wait_ge(loaded, 16)

        @block.scalar
        def _(act):
            nc.scalar.activation(lora[0:HD, 0, :], lora[0:HD, 0, :], ACT.Tanh).then_inc(lora_act, 1)
            nc.scalar.activation(lora[:, 1, :], lora[:, 1, :], ACT.Sigmoid).then_inc(lora_act, 1)

        @block.vector
        def _(dve):
            nc.vector.tensor_scalar(ka1[:], col(K, "k_a", 0, 8), -1.0, 1.0, ALU.mult, ALU.add).then_inc(ka_done, 1)
            for x in (sh, *W, *off):
                nc.vector.memset(x[:], 0.0)

    def t4(x):
        return x.rearrange("p (t k) -> p t k", t=NT)

    def tl(x, t):
        return x[:, t * P:(t + 1) * P]

    halves = [slice(0, HD), slice(HD, P)]
    FREE = [B[0][1], B[1][1]]

    def turns(eng, turn):
        turn(0, 0, False, True)
        with eng.Fori(0, DC // 2 - 1) as i:
            turn(2 * i + 1, 1, True, True)
            turn(2 * i + 2, 0, True, True)
        turn(DC - 1, 1, True, False)

    def flat(x):
        return x.rearrange("p t k -> p (t k)")

    def chunk(n, i):
        return rkv[:, bass.ds(n * DC + i, 1), :].rearrange("p o s -> p (o s)")

    with nc.Block() as block:
        @block.sync
        def _(sp):
            def fetch(n, x, i):
                tile = d["w_lora"][bass.ds(i, 1), :, n * P:(n + 1) * P].rearrange("o p n -> p (o n)")
                sp.dma_start(x[:], tile).then_inc(w_loaded[n], 16)

            after(sp, 0, "lora", 2)
            fetch(0, w_lora, 1)
            with sp.Fori(0, DC - 2) as i:
                after(sp, i + 1, "lora", 2)
                fetch(0, w_lora, i + 2)
                after(sp, i, "g_mm", 1)
                fetch(1, w_gate, i + 1)
            after(sp, DC - 2, "g_mm", 1)
            fetch(1, w_gate, DC - 1)

        @block.gpsimd
        def _(pool):
            def values(i):
                sig(nc.gpsimd.tensor_copy(flat(vs[:]), chunk(2, i)), "vs")

            def turn(i, x, finish, prepare):
                for lv in range(LEVELS):
                    for hd in range(2):
                        if lv == 0:
                            after(pool, i, "mask", 3 * hd + 1)
                        else:
                            after(pool, i, "w_mm", 2 * (lv - 1) + hd + 1)
                        mask = half_of_chunk(level[lv], lv, 1)
                        sig(nc.gpsimd.tensor_tensor(half(off[hd][:], lv, 1), half(abT[hd][:], lv, 1),
                                                    mask[:, None].to_broadcast([P, NT] + list(mask.shape[1:])), ALU.mult), "off")
                if prepare:
                    values(i + 1)
            values(0)
            turns(pool, turn)

        @block.tensor
        def _(pe):
            mm = nc.tensor.matmul

            def lora_w(i, x):
                pe.wait_ge(w_loaded[0], 16 * i + 16)
                sig(mm(FREE[1][:], w_lora[0:HD, :], lora[0:HD, 0, :], start=True, stop=True), "lora")

            def lora_a(i, x):
                sig(mm(FREE[0][:], w_lora[HD:P, :], lora[HD:P, 0, :], start=True, stop=True), "lora")

            def key_norm(i, x):
                after(pe, i, "sq", 1)
                after(pe, i, "sig", 1)
                sig(mm(FREE[1][:], same, ac[x][:], start=True, stop=True), "ss")

            def bonus_sum(i, x):
                after(pe, i, "rk", 1)
                after(pe, i, "root", 1)
                sig(mm(FREE[1][:], same, rc[x][:], start=True, stop=True), "rk_mm")

            def state(i, t):
                after(pe, i, "s", 2 + 4 * (t - 1))
                sig(mm(tl(B[0][2], t), sh[:], tl(qs, t), start=True, stop=True), "y_mm")
                if t < NT - 1:
                    for hr in halves:
                        last = mm(B[0][3][hr, 0:HD], G[hr, t, :], sh[hr, hr], start=True, stop=True)
                    sig(last, "s_mm")

            def mean(i):
                after(pe, i, "yadd", 1)
                sig(mm(FREE[0][:], same, y[:], start=True, stop=True), "mean")

            def variance(i):
                after(pe, i, "ysq", 1)
                sig(mm(FREE[1][:], same, qs[:], start=True, stop=True), "var")

            def gate(i, x):
                pe.wait_ge(w_loaded[1], 16 * i + 16)
                sig(mm(FREE[0][:], w_gate[:], lora[:, 1, :], start=True, stop=True), "g_mm")

            def turn(i, x, finish, prepare):
                def beside(lv):
                    if lv == 0:
                        after(pe, i, "mask", 6)
                        if finish:
                            mean(i - 1)
                        if prepare:
                            lora_w(i + 1, 1 - x)
                    if lv == 1:
                        if prepare:
                            if finish:
                                after(pe, i - 1, "yc", 1)
                            lora_a(i + 1, 1 - x)
                        if finish:
                            if prepare:
                                after(pe, i + 1, "sig", 1)
                            variance(i - 1)
                    if lv == 2:
                        if finish:
                            if prepare:
                                after(pe, i + 1, "sig", 2)
                            else:
                                after(pe, i - 1, "yc", 1)
                            gate(i - 1, 1 - x)
                        if prepare:
                            if finish:
                                after(pe, i - 1, "r", 1)
                            key_norm(i + 1, 1 - x)
                    if lv == 4 and prepare:
                        bonus_sum(i + 1, 1 - x)

                if finish:
                    after(pe, i - 1, "qev", 8)
                    state(i - 1, 1)
                for n, (src, name, k) in enumerate(((vs, "vs", 1), (ac[x], "dec", 3), (kc[x], "dec", 4), (bc[x], "dec", 5))):
                    after(pe, i, name, k)
                    for t in range(NT):
                        last = nc.tensor.transpose(tl(K.ps[4 + n], t), src[:, t, :] if src is vs else tl(src, t), K.ident)
                    sig(last, "tr")
                    if finish and n % 2 == 1:
                        state(i - 1, 2 + n // 2)

                def scores(hd, bank, a_, b_):
                    for t in range(NT):
                        last = mm(tl(B[hd][bank], t), tl(a_, t)[halves[hd]], tl(b_, t)[halves[hd]], start=True, stop=True)
                    sig(last, "score")
                for hd in range(2):
                    if hd == 1:
                        after(pe, i, "tok", 4)
                    scores(hd, 0, bc[x], ac[x])
                    scores(hd, 1, ac[x], bc[x])

                def lower(lv, hd):
                    after(pe, i, "off", 2 * lv + hd + 1)
                    after(pe, i, "ident", 2 * hd + 2) if lv == 0 else after(pe, i, "T", 2 * (lv - 1) + hd + 1)
                    for t in range(NT):
                        last = mm(tl(B[hd][2], t), off[hd][:, t, :], T[hd][:, t, :], start=True, stop=True)
                    sig(last, "w_mm")

                def grow(lv, hd):
                    after(pe, i, "w", 2 * lv + hd + 1)
                    if lv:
                        after(pe, i, "TT", 2 * (lv - 1) + hd + 1)
                    if lv < LEVELS - 1:
                        for t in range(NT):
                            last = mm(tl(B[hd][3], t), TT[hd][:, t, :], W[hd][:, t, :], start=True, stop=True)
                        sig(last, "dT")
                    for t in range(NT):
                        last = mm(tl(B[hd][0], t), W[hd][:, t, :], TT[hd][:, t, :], start=True, stop=True)
                    sig(last, "dTT")

                if finish:
                    after(pe, i - 1, "yadd", 1)
                for lv in range(LEVELS):
                    for step, hd in (((lower, 0), (grow, 0), (lower, 1), (grow, 1)) if lv == 0 else
                                     ((lower, 0), (lower, 1), (grow, 0), (grow, 1))):
                        step(lv, hd)
                    beside(lv)
                for hd in range(2):
                    scores(hd, 2, bc[x], rc[x])
                    scores(hd, 3, kc[x], rc[x])
                if finish:
                    after(pe, i - 1, "out", 1)
                if prepare:
                    after(pe, i + 1, "bonus", 1)
                for hd in range(2):
                    scores(hd, 1, kc[x], ac[x])
                for hd, hr in enumerate(halves):
                    after(pe, i, "TT", 2 * (LEVELS - 1) + hd + 1)
                    after(pe, i, "mask", 10 + hd + 1)
                    for t in range(NT):
                        last = mm(B[hd][0][:, t * HD:(t + 1) * HD], akT[hd][:, t, :], vt[:, t, hr], start=True, stop=True)
                    sig(last, "akv")
                for hd in range(2):
                    after(pe, i, "cat", 2 * hd + 2)
                    for t in range(NT):
                        last = mm(tl(B[hd][1], t), TT[hd][:, t, :], cat[hd][:, t, :], start=True, stop=True)
                    sig(last, "xu_mm")
                for hd, hr in enumerate(halves):
                    xr, ur = hr, halves[1 - hd]
                    after(pe, i, "xu", hd + 1)
                    for t in range(NT):
                        mm(tl(B[hd][2], t), xu[hd][:, t, :], rbT[hd][:, t, :], start=True, stop=False, skip_group_check=True)
                        last = mm(tl(B[hd][2], t)[ur], vt[:, t, hr], rkT[hd][:, t, :], start=False, stop=True, skip_group_check=True)
                    sig(last, "qy")
                    for t in range(NT):
                        last = mm(B[hd][3][hr, t * HD:(t + 1) * HD], xu[hd][:, t, xr], bt[:, t, hr], start=True, stop=True)
                    sig(last, "gh")
                    for t in range(NT):
                        mm(B[hd][0][hr, t * HD:(t + 1) * HD], bt[:, t, hr], xu[hd][:, t, ur], start=True, stop=False)
                        last = mm(B[hd][0][hr, t * HD:(t + 1) * HD], kt[:, t, hr], vt[:, t, hr], start=False, stop=True)
                    sig(last, "gh")

            lora_w(0, 0)
            lora_a(0, 0)
            key_norm(0, 0)
            bonus_sum(0, 0)
            turns(pe, turn)
            after(pe, DC - 1, "qev", 8)
            for t in range(1, NT):
                state(DC - 1, t)
            mean(DC - 1)
            variance(DC - 1)
            after(pe, DC - 1, "yc", 1)
            gate(DC - 1, 1)

        @block.scalar
        def _(act):
            A = nc.scalar.activation
            w0, a0 = K.cols_at["w0"][0], K.cols_at["a0"][0]

            def square(i, x):
                after(act, i, "kk", 1)
                sig(A(ac[x][:], kkn[:], ACT.Square), "sq")

            def decay(i, x):
                after(act, i, "lora", 1)
                sig(A(log_w[:], FREE[1][:], ACT.Sigmoid, bias=K.cols[:, bass.ds(w0 + i, 1)]), "sig")

            def rate(i, x):
                after(act, i, "lora", 2)
                sig(A(a[:], FREE[0][:], ACT.Sigmoid, bias=K.cols[:, bass.ds(a0 + i, 1)]), "sig")

            def root(i, x):
                after(act, i, "ss", 1)
                after(act, i, "csm", 3)
                sig(A(log_w[:], FREE[1][:], ACT.Sqrt), "root")

            def decays(i, x):
                after(act, i, "csm", 3)
                after(act, i, "rk_mm", 1)
                sig(A(rc[x][:], bc[x][:], ACT.Exp), "exp")
                sig(A(pm[x][:], mid[:], ACT.Exp), "exp")
                act.wait_ge(N["exp"].sem, PER["exp"] * i + 1)
                sig(A(bc[x][:], bc[x][:], ACT.Exp, scale=-1.0), "exp")
                sig(A(ac[x][:], ac[x][:], ACT.Exp), "exp")

            def y_square(i):
                after(act, i, "yc", 1)
                sig(A(qs[:], y[:], ACT.Square), "ysq")

            def y_root(i):
                after(act, i, "r", 2)
                sig(A(qs[:], qs[:], ACT.Sqrt), "yroot")

            def turn(i, x, finish, prepare):
                for n, dst in ((0, vt), (2, kt)):
                    after(act, i, "tr", n + 1)
                    sig(A(flat(dst[:]), K.ps[4 + n][:], ACT.Copy), "tok")
                for lv in range(LEVELS):
                    for hd in range(2):
                        after(act, i, "w_mm", 2 * lv + hd + 1)
                        if lv:
                            after(act, i, "dTT", 2 * (lv - 1) + hd + 1)
                        sig(A(half(W[hd][:], lv, 0), half(t4(B[hd][2][:]), lv, 0), ACT.Identity, scale=second_half[lv]), "w")
                    if lv == 0 and prepare:
                        square(i + 1, 1 - x)
                    if lv == 1:
                        if prepare:
                            decay(i + 1, 1 - x)
                        if finish:
                            y_square(i - 1)
                    if lv == 2 and prepare:
                        rate(i + 1, 1 - x)
                    if lv == 3:
                        if finish:
                            y_root(i - 1)
                        if prepare:
                            root(i + 1, 1 - x)
                    if lv == 5 and prepare:
                        decays(i + 1, 1 - x)
                for hd, hr in enumerate(halves):
                    after(act, i, "dTT", 2 * (LEVELS - 1) + hd + 1)
                    sig(A(cat[hd][:, :, hr], at_[:, :, hr], ACT.Copy), "cat")
                    after(act, i, "akv", hd + 1)
                    sig(A(cat[hd][:, :, halves[1 - hd]], B[hd][0][:, 0:NT * HD].rearrange("p (t k) -> p t k", t=NT), ACT.Copy), "cat")
                for hd in range(2):
                    after(act, i, "xu_mm", hd + 1)
                    sig(A(flat(xu[hd][:]), B[hd][1][:], ACT.Copy), "xu")

            square(0, 0)
            decay(0, 0)
            rate(0, 0)
            root(0, 0)
            decays(0, 0)
            turns(act, turn)
            y_square(DC - 1)
            y_root(DC - 1)

        @block.vector
        def _(dve):
            v = nc.vector
            c = {n: K.cols_at[n][0] for n in ("k_k", "k_a", "r_k", "gn_w", "gn_b")}

            def colv(n, i):
                return K.cols[:, bass.ds(c[n] + i, 1)]

            def keys(i, x):
                sig(v.tensor_scalar(kkn[:], chunk(1, i), colv("k_k", i), None, ALU.mult), "kk")

            def decay_sum(i, x):
                after(dve, i, "sig", 1)
                sig(v.tensor_scalar(log_w[:], log_w[:], RWKV_DECAY, None, ALU.mult), "logw")
                after(dve, i, "logw", 1)
                for t in range(NT):
                    sig(v.tensor_tensor_scan(tl(bc[x], t), K.ones, tl(log_w, t), 0.0, ALU.mult, ALU.add), "cs")

            def key_rate(i, x):
                after(dve, i, "sig", 2)
                sig(v.tensor_scalar(kc[x][:], a[:], colv("k_a", i), ka1[:, bass.ds(i, 1)], ALU.mult, ALU.add), "k2")
                after(dve, i, "cs", 4)
                sig(v.tensor_copy(mid[:], t4(bc[x][:])[:, :, P // 2 - 1]), "csm")

            def centre(i, x):
                after(dve, i, "csm", 1)
                sig(v.tensor_tensor(t4(bc[x][:]), t4(bc[x][:]), mid[:, :, None].to_broadcast([P, NT, P]), ALU.subtract), "csm")
                after(dve, i, "k2", 1)
                sig(v.tensor_tensor(kc[x][:], kc[x][:], chunk(1, i), ALU.mult), "k2")
                after(dve, i, "csm", 2)
                after(dve, i, "ss", 1)
                sig(v.tensor_tensor(ac[x][:], bc[x][:], log_w[:], ALU.subtract), "csm")
                after(dve, i, "k2", 2)
                sig(v.scalar_tensor_tensor(rc[x][:], chunk(0, i), colv("r_k", i), kc[x][:], ALU.mult, ALU.mult), "rk")

            def unit_keys(i, x):
                rb = log_w[:]
                after(dve, i, "root", 1)
                sig(v.tensor_scalar(rb, rb, 1e-12, None, ALU.max), "kkn")
                after(dve, i, "kkn", 1)
                sig(v.reciprocal(rb, rb), "kkn")
                after(dve, i, "kkn", 2)
                sig(v.tensor_tensor(kkn[:], kkn[:], rb, ALU.mult), "kkn")

            def key_rate_bonus(i, x):
                after(dve, i, "kkn", 3)
                sig(v.tensor_tensor(a[:], a[:], kkn[:], ALU.mult), "kkn")
                after(dve, i, "rk_mm", 1)
                sig(v.tensor_tensor(bonus[x][:], FREE[1][:], chunk(2, i), ALU.mult), "bonus")

            def decayed(i, x):
                after(dve, i, "exp", 4)
                sig(v.tensor_copy(pl[x][:], t4(rc[x][:])[:, :, P - 1]), "dec")
                after(dve, i, "dec", 1)
                sig(v.tensor_tensor(rc[x][:], rc[x][:], chunk(0, i), ALU.mult), "dec")
                sig(v.scalar_tensor_tensor(ac[x][:], kkn[:], -1.0, ac[x][:], ALU.mult, ALU.mult), "dec")
                sig(v.tensor_tensor(kc[x][:], kc[x][:], bc[x][:], ALU.mult), "dec")
                after(dve, i, "dec", 4)
                after(dve, i, "kkn", 4)
                sig(v.tensor_tensor(bc[x][:], bc[x][:], a[:], ALU.mult), "dec")
                after(dve, i, "dec", 5)

            def state_first(i, x):
                for hr in halves:
                    sig(v.tensor_scalar(sh[hr, hr], H[hr, 0, :], pm[x][hr, 1:2], None, ALU.mult), "s")
                after(dve, i, "s", 2)

            def state_next(i, x, t):
                for hr in halves:
                    ins = v.scalar_tensor_tensor(s1[hr, :], sh[hr, hr], pl[x][hr, t:t + 1], H[hr, t, :], ALU.mult, ALU.add)
                sig(ins, "s")
                after(dve, i, "s", 3 + 4 * (t - 1))
                after(dve, i, "s_mm", t)
                sig(v.scalar_tensor_tensor(s1[:], B[0][3][:, 0:HD], pl[x][:, t:t + 1], s1[:], ALU.mult, ALU.add), "s")
                after(dve, i, "s", 4 + 4 * (t - 1))
                for hr in halves:
                    sig(v.tensor_scalar(sh[hr, hr], s1[hr, :], pm[x][hr, t + 1:t + 2], None, ALU.mult), "s")
                after(dve, i, "s", 6 + 4 * (t - 1))

            def state_out(i):
                after(dve, i, "y_mm", NT - 1)
                sig(v.tensor_tensor(y[:, P:], y[:, P:], B[0][2][:, P:], ALU.add), "yadd")

            def y_centre(i):
                after(dve, i, "mean", 1)
                sig(v.scalar_tensor_tensor(y[:], FREE[0][:], -1.0 / HD, y[:], ALU.mult, ALU.add), "yc")

            def y_rstd(i):
                after(dve, i, "var", 1)
                sig(v.tensor_scalar(qs[:], FREE[1][:], 1.0 / HD, GN_EPS, ALU.mult, ALU.add), "r")
                after(dve, i, "r", 1)
                sig(v.reciprocal(qs[:], qs[:]), "r")

            def y_norm(i, x):
                after(dve, i, "yroot", 1)
                sig(v.tensor_tensor(y[:], y[:], qs[:], ALU.mult), "yn")
                after(dve, i, "yn", 1)
                sig(v.tensor_scalar(y[:], y[:], colv("gn_w", i), colv("gn_b", i), ALU.mult, ALU.add), "yn")
                after(dve, i, "yn", 2)
                sig(v.tensor_tensor(y[:], y[:], bonus[x][:], ALU.add), "yn")

            def y_gate(i):
                after(dve, i, "yn", 3)
                after(dve, i, "g_mm", 1)
                sig(v.tensor_tensor(chunk(0, i), y[:], FREE[0][:], ALU.mult), "out")

            def turn(i, x, finish, prepare):
                if finish:
                    state_first(i - 1, 1 - x)
                    state_next(i - 1, 1 - x, 1)
                for n, dst in ((1, at_), (3, bt)):
                    after(dve, i, "tr", n + 1)
                    sig(v.tensor_copy(flat(dst[:]), K.ps[4 + n][:]), "tok")
                    if finish:
                        state_next(i - 1, 1 - x, 2) if n == 1 else state_out(i - 1)

                def masked(score, n, bank, dst, mask):
                    after(dve, i, "score", score)
                    sig(v.tensor_tensor(dst[:], t4(bank[:]), mask[:, None, :].to_broadcast([P, NT, P]), ALU.mult), "mask")
                eye = K.ident[:, None, :].to_broadcast([P, NT, P])
                for hd in range(2):
                    masked(2 * hd + 1, 3 * hd + 1, B[hd][0], abT[hd], strict)
                    masked(2 * hd + 2, 3 * hd + 2, B[hd][1], T[hd], pair_t)
                    after(dve, i, "mask", 3 * hd + 2)
                    sig(v.tensor_tensor(T[hd][:], T[hd][:], eye, ALU.add), "ident")
                    sig(v.tensor_tensor(TT[hd][:], abT[hd][:], pair[:, None, :].to_broadcast([P, NT, P]), ALU.mult), "mask")
                    after(dve, i, "mask", 3 * hd + 3)
                    sig(v.tensor_tensor(TT[hd][:], TT[hd][:], eye, ALU.add), "ident")
                for lv in range(LEVELS):
                    for hd in range(2):
                        if lv < LEVELS - 1:
                            after(dve, i, "dT", 2 * lv + hd + 1)
                            z = half(T[hd][:], lv, 0)
                            sig(v.tensor_tensor(z, z, half(t4(B[hd][3][:]), lv, 0), ALU.add), "T")
                        after(dve, i, "dTT", 2 * lv + hd + 1)
                        z = half(TT[hd][:], lv, 1)
                        sig(v.scalar_tensor_tensor(z, half(t4(B[hd][0][:]), lv, 1), first_half[lv], z, ALU.mult, ALU.add), "TT")
                    if lv == 0:
                        if prepare:
                            keys(i + 1, 1 - x)
                        if finish:
                            y_centre(i - 1)
                    if lv == 1 and prepare:
                        decay_sum(i + 1, 1 - x)
                    if lv == 2:
                        if finish:
                            y_rstd(i - 1)
                        if prepare:
                            key_rate(i + 1, 1 - x)
                    if lv == 3:
                        if prepare:
                            centre(i + 1, 1 - x)
                        if finish:
                            y_norm(i - 1, 1 - x)
                    if lv == 4:
                        if finish:
                            y_gate(i - 1)
                        if prepare:
                            unit_keys(i + 1, 1 - x)
                    if lv == 5 and prepare:
                        key_rate_bonus(i + 1, 1 - x)
                for hd in range(2):
                    masked(4 + 2 * hd + 1, 6 + 2 * hd + 1, B[hd][2], rbT[hd], K.causal)
                    masked(4 + 2 * hd + 2, 6 + 2 * hd + 2, B[hd][3], rkT[hd], K.causal)
                for hd in range(2):
                    masked(8 + hd + 1, 10 + hd + 1, B[hd][1], akT[hd], strict)
                if prepare:
                    decayed(i + 1, 1 - x)
                for hd, hr in enumerate(halves):
                    ur = halves[1 - hd]
                    after(dve, i, "qy", hd + 1)
                    sig(v.tensor_tensor(qs[hr, :], B[hd][2][hr, :], rc[x][hr, :], ALU.add), "qev")
                    sig(v.tensor_copy(y[hr, :], B[hd][2][ur, :]), "qev")
                    after(dve, i, "gh", 2 * hd + 2)
                    sig(v.tensor_copy(G[hr, :, :], B[hd][3][hr, 0:NT * HD].rearrange("p (t k) -> p t k", t=NT)), "qev")
                    sig(v.tensor_tensor(H[hr, :, :], B[hd][0][hr, 0:NT * HD].rearrange("p (t k) -> p t k", t=NT),
                                        pl[x][hr, :, None].to_broadcast([HD, NT, HD]), ALU.mult), "qev")
                after(dve, i, "qev", 8)

            keys(0, 0)
            decay_sum(0, 0)
            key_rate(0, 0)
            centre(0, 0)
            unit_keys(0, 0)
            key_rate_bonus(0, 0)
            decayed(0, 0)
            turns(dve, turn)
            state_first(DC - 1, 1)
            for t in range(1, NT - 1):
                state_next(DC - 1, 1, t)
            state_out(DC - 1)
            after(dve, DC - 1, "yadd", 1)
            y_centre(DC - 1)
            y_rstd(DC - 1)
            y_norm(DC - 1, 1)
            y_gate(DC - 1)


def mod(K, layer, sub, which):
    a = layer * 72 + sub * 24 + which * 8
    return K.mods[:, a:a + 8]


def build(nc, dram, plan=None):
    with ExitStack() as ctx:
        K = setup(nc, ctx, dram)
        K.prod_done = K.count("prod_done")
        K.conv_step = K.count("conv_step")
        d = dram
        heads = {"f00": (d.get("gu00"), DC), "hyb": (d["w_hyb"][0:DC] if "w_hyb" in d else None, DC), "f01": (d.get("gu01"), DC),
                 "f10": (d.get("gu10"), DC), "ml": (d.get("w_xm"), DC), "f11": (d.get("gu11"), DC), "b2": (d.get("w_attn"), DC)}
        plan = plan or ["f00", "hyb", "f01", "f10", "ml", "f11", "final", "b2"]
        with stage(K):
            first_block(K, heads[plan[0]])
        K.stored = K.sem("out_stored")
        for n, step in enumerate(plan):
            nxt = next((heads[k] for k in plan[n + 1:] if k in heads), None)
            if step == "final":
                norm(K, "nf", K.x, col(K, "final_g", 0, 8), squares=Squares(K, "nf", K.h_at + 4 * S * 4))
                continue
            if step == "b2":
                second_block(K)
                continue
            layer, sub = {"f00": (0, 0), "hyb": (0, 1), "f01": (0, 2), "f10": (1, 0), "ml": (1, 1), "f11": (1, 2)}[step]
            head = Modulated(K, col(K, "norm_g", layer * 24 + sub * 8, 8), mod(K, layer, sub, 1), mod(K, layer, sub, 0),
                             mod(K, layer, sub, 2), 0.5 if step[0] == "f" else 1.0)
            if step == "hyb":
                with stage(K):
                    hybrid(K, nxt, head)
            elif step == "ml":
                with stage(K):
                    mlstm(K, nxt, head)
            else:
                s = sub // 2
                turns = 2 * FC // RING + 2 * DC // RING
                ada = {"f00": (len(ADA_UP_FRONT) - 1, 0, turns), "f01": (len(ADA_UP_FRONT) - 1 + turns, 0, turns),
                       "f10": (ADA_FIRST, DC, ADA_GROUPS - 1 - ADA_FIRST)}.get(step)
                swiglu(K, step, d[f"gu{layer}{s}"], d[f"dn{layer}{s}"], nxt, head, ada)


def tiles_of(w, kb):
    k, n = w.shape
    return np.ascontiguousarray(w.reshape(k // P // kb, kb, P, n // P, P).transpose(3, 0, 2, 1, 4)).reshape(-1, P, kb * P)


def chunks(v):
    return np.asarray(v).reshape(-1, P).T


def interleave(a, b):
    return np.stack([a, b], axis=1).reshape((-1,) + a.shape[1:])


def layout(I):
    I = {k: np.asarray(v) for k, v in I.items()}
    out = {}
    mu = I["shift_mu_2"][0]
    inv = (np.float32(THETA) ** (-np.arange(ROPE // 2, dtype=np.float32) * np.float32(2.0) / np.float32(ROPE))).astype(np.float32)
    vec = {"ada_b": np.concatenate([I["ada_b"][0], I["ada_b"][1], I["ada_b_2"][0]]), "norm_g": I["norm_g"], "final_g": I["final_norm_g"],
           "mix_pre": I["norm_mix_pre_2"], "mix_post": I["norm_mix_post_2"], "ffn_pre": I["norm_ffn_pre_2"],
           "ffn_post": I["norm_ffn_post_2"], "c": I["c"], "c2": I["c_2"],
           "hyb_conv_w": np.concatenate([I["lru_conv_w"][0], I["ssd_conv_w"][0]], axis=1),
           "hyb_conv_b": np.concatenate([I["lru_conv_b"][0], I["ssd_conv_b"][0]]),
           "lru_ba": I["lru_ba"], "lru_bx": I["lru_bx"], "lru_lambda": I["lru_lambda"],
           "ssd_d": np.repeat(I["ssd_d"][0], SSD_P), "ssd_norm_g": I["ssd_norm_g"],
           "ssd_dt_bias": np.pad(I["ssd_dt_bias"][0], (0, P - SSD_H)), "ssd_a_log": np.pad(I["ssd_a_log"][0], (0, P - SSD_H)),
           "ml_conv_w": I["mlstm_conv_w"], "ml_conv_b": I["mlstm_conv_b"], "ml_norm_g": I["mlstm_norm_g"], "ml_skip": I["mlstm_skip"],
           "ml_bi": np.pad(I["mlstm_b_gates"][0, :ML_H], (0, P - ML_H)), "ml_bf": np.pad(I["mlstm_b_gates"][0, ML_H:], (0, P - ML_H)),
           "rope_inv": np.tile(np.pad(np.tile(inv, 2), (0, HD - ROPE)), 2),
           "shift_mu": np.concatenate([mu[3 * D:], np.zeros(QKV * P, np.float32), mu[:3 * D]]),
           "w0": I["decay_w0_2"], "a0": I["iclr_a0_2"], "k_k": I["k_k_2"], "k_a": I["k_a_2"], "r_k": I["r_k_2"], "gn_w": I["gn_w_2"], "gn_b": I["gn_b_2"]}
    out["cols"] = np.ascontiguousarray(np.concatenate([chunks(vec[n]) for n, _ in COLUMNS], axis=1))
    row, column = np.arange(P)[:, None], np.arange(P)[None, :]
    masks = {"ident": row == column, "ones": np.ones((P, P)), "causal": row <= column}
    out["consts"] = np.concatenate([masks[n] for n in CONSTANTS], axis=1).astype(np.float32)
    ada = [I["ada_w"][0], I["ada_w"][1], I["ada_w_2"][0]]
    out["ada"] = np.concatenate([w.reshape(ADA_TILES, 2, P, -1, S).transpose(3, 0, 2, 1, 4).reshape(-1, P, 2 * S) for w in ada])
    out["x"] = np.ascontiguousarray(I["x"][0].T.reshape(DC, P, S).transpose(1, 0, 2))
    for l in range(2):
        for s in range(2):
            out[f"gu{l}{s}"] = interleave(tiles_of(I["ffn_w_gate"][l, s], DC), tiles_of(I["ffn_w_up"][l, s], DC))
            out[f"dn{l}{s}"] = tiles_of(I["ffn_w_down"][l, s], KB_MAX)
    w_in = I["hyb_w_in"][0]
    gate, x_lru, z, xbc = w_in[:, :D], w_in[:, D:2 * D], w_in[:, 2 * D:3 * D], w_in[:, 3 * D:3 * D + XBC * P]
    out["w_hyb"] = tiles_of(np.concatenate([x_lru, xbc, gate, z], axis=1), DC)
    out["w_dt"] = np.ascontiguousarray(w_in[:, 3 * D + XBC * P:].reshape(DC, P, SSD_H).transpose(1, 0, 2))
    out["lru_wax"] = np.ascontiguousarray(np.concatenate([I["lru_wa"][0], I["lru_wx"][0]], axis=2))
    out["w_hout"] = tiles_of(I["hyb_w_out"][0], DC)
    up = I["mlstm_w_up"][0]
    out["w_xm"], out["w_z"] = tiles_of(up[:, :2 * D], DC), tiles_of(up[:, 2 * D:], DC)
    out["w_mdown"] = tiles_of(I["mlstm_w_down"][0], DC)
    qkv = np.zeros((MLC, P, 3, P), np.float32)
    for k, n in enumerate(("mlstm_wq", "mlstm_wk", "mlstm_wv")):
        w = I[n][0]
        b = w.shape[1]
        blocks = w.reshape(MLC, P // b, b, b)
        for r in range(P // b):
            qkv[:, r * b:(r + 1) * b, k, r * b:(r + 1) * b] = blocks[:, r]
    out["w_qkv"] = qkv.reshape(MLC, P, 3 * P)
    out["w_qkv_t"] = qkv.reshape(MLC, P, 3, P).transpose(0, 3, 2, 1).reshape(MLC, P, 3 * P)
    wg = I["mlstm_w_gates"][0].reshape(3, MLC, P, 2 * ML_H).transpose(1, 2, 0, 3)
    gates = np.zeros((MLC, P, 3, 2 * ML_F), np.float32)
    gates[..., :ML_H], gates[..., ML_F:ML_F + ML_H] = wg[..., :ML_H], wg[..., ML_H:]
    w2 = I["w_in_2"][0]
    n_attn, n_rwkv = QKV * P, 3 * D
    lora, gate2 = w2[:, n_attn + n_rwkv:-2 * D], w2[:, -2 * D:]
    out["w_attn"] = tiles_of(np.concatenate([lora, w2[:, :n_attn]], axis=1), DC)
    out["w_rkv"] = tiles_of(w2[:, n_attn:n_attn + n_rwkv], DC)
    out["w_gate2"] = tiles_of(gate2, DC)
    out["w_lora"] = np.concatenate([np.concatenate([I["decay_w2_2"][0], I["iclr_a2_2"][0]]).reshape(P, DC, P),
                                    I["gate_g2_2"][0].reshape(P, DC, P)], axis=2).transpose(1, 0, 2).copy()
    out["w_branch"] = tiles_of(I["w_branch_2"][0], 2 + DC)
    out["w_out2"] = tiles_of(I["w_out_2"][0], DC)
    ff2 = I["w_ff2_2"][0]
    for h in range(2):
        out[f"w_ff1{h}"] = tiles_of(I["w_ff1_2"][0][:, h * 2 * D:(h + 1) * 2 * D], DC)
        out[f"w_ff2{h}"] = tiles_of(ff2[h * 2 * D:(h + 1) * 2 * D], DC)
    out["positions"] = I["positions_2"].reshape(1, S)
    no = np.float32(NEG)
    own, sub = column <= row, (column <= row) & (column // 32 == row // 32)
    band = column >= row
    out["attn_masks"] = np.concatenate([np.where(m, np.float32(0), no) for m in (own, sub, band)], axis=1).astype(np.float32)
    rot = np.zeros((P, P), np.float32)
    for h in range(0, P, HD):
        for j in range(ROPE // 2):
            rot[h + ROPE // 2 + j, h + j], rot[h + j, h + ROPE // 2 + j] = -1.0, 1.0
    head_of = np.zeros((P, 2 * P), np.float32)
    for c in range(2):
        for h in range(2):
            head_of[2 * c + h, c * P + h * HD:c * P + (h + 1) * HD] = 1.0
    out["attn_mats"] = np.concatenate([rot, head_of], axis=1)
    off = [(row // (2 * b) == column // (2 * b)) & (row % (2 * b) < b) & (column % (2 * b) >= b) for b in (1, 2, 4, 8, 16, 32, 64)]
    same = row // HD == column // HD
    rows = [row % (2 * b) < b for b in (2, 4, 8, 16, 32, 64)]
    out["rwkv_masks"] = np.concatenate([row < column, off[0].T, off[0], *off[1:], same, *rows, *(~r for r in rows)], axis=1).astype(np.float32)
    out["w_gates"] = gates.reshape(MLC, P, 6 * ML_F)
    return out


def kernel(**inputs):
    import numpy as _np
    import concourse.bacc as _bacc
    from concourse import mybir as _mybir
    from concourse.bass_utils import run_bass_kernel_spmd as _run

    nc = _bacc.Bacc("TRN2", target_bir_lowering=False, num_devices=1)
    arrays, dram = {}, {}
    for name, a in layout(inputs).items():
        a = _np.ascontiguousarray(a)
        arrays[f"in_{name}"] = a
        dram[name] = nc.dram_tensor(f"in_{name}", a.shape, _mybir.dt.from_np(a.dtype), kind="ExternalInput").ap()
    dram["out"] = nc.dram_tensor("out", [P, DC, S], F32, kind="ExternalOutput").ap()
    build(nc, dram)
    r = _run(nc, [arrays], core_ids=[0])
    return r.results[0]["out"].transpose(1, 0, 2).reshape(1, D, S).transpose(0, 2, 1)
```
